# Optimizing a Trainium2 kernel written in Bass

```python
import jax, jax.numpy as jnp
from jax import lax
import numpy as np
import math

D_MODEL = 1024
BATCH = 1
SEQ = 1024
DEPTH = 2

HEAD_DIM = 64
ATTN_HEADS = 8
ATTN_KV_HEADS = 2
ATTN_GROUP = ATTN_HEADS // ATTN_KV_HEADS
WINDOW = 128
ATTN_BLOCK = 128
ROPE_THETA = 10000.0

RET_HEADS = 4
RET_DK = 64
RET_DV = 64
RET_CHUNK = 128

GLA_HEADS = 4
GLA_DK = 32
GLA_DV = 64
GLA_CHUNK = 64
GLA_GATE_RANK = 16
GLA_GATE_NORMALIZER = 16.0

EPS = 1e-6

ATTN_W = ATTN_HEADS * HEAD_DIM
RET_W = RET_HEADS * RET_DV
GLA_W = GLA_HEADS * GLA_DV
D_MIX = ATTN_W + RET_W + GLA_W

IN_SIZES = (
    ATTN_HEADS * HEAD_DIM, ATTN_KV_HEADS * HEAD_DIM, ATTN_KV_HEADS * HEAD_DIM, ATTN_W,
    RET_HEADS * RET_DK, RET_HEADS * RET_DK, RET_HEADS * RET_DV, RET_W,
    GLA_HEADS * GLA_DK, GLA_HEADS * GLA_DK, GLA_HEADS * GLA_DV, GLA_W,
    GLA_GATE_RANK,
)
D_IN = sum(IN_SIZES)
IN_SPLITS = [int(s) for s in np.cumsum(IN_SIZES)[:-1]]


def rms_norm(x, gain=None):
    xf = x.astype(jnp.float32)
    y = xf * lax.rsqrt(jnp.mean(xf * xf, axis=-1, keepdims=True) + EPS)
    if gain is not None:
        y = y * gain.astype(jnp.float32)
    return y.astype(x.dtype)

def apply_rotary(x, positions, inv_freq):
    ang = positions.astype(jnp.float32)[..., None] * inv_freq
    cos = jnp.cos(ang)[:, :, None, :]
    sin = jnp.sin(ang)[:, :, None, :]
    x1, x2 = jnp.split(x.astype(jnp.float32), 2, axis=-1)
    out = jnp.concatenate([x1 * cos - x2 * sin, x2 * cos + x1 * sin], axis=-1)
    return out.astype(x.dtype)

def sliding_window_attention(q, k, v, sinks):
    B, S, H, D = q.shape
    nb = S // ATTN_BLOCK
    qb = q.reshape(B, nb, ATTN_BLOCK, ATTN_KV_HEADS, ATTN_GROUP, D)
    kb = k.reshape(B, nb, ATTN_BLOCK, ATTN_KV_HEADS, D)
    vb = v.reshape(B, nb, ATTN_BLOCK, ATTN_KV_HEADS, D)

    def with_prev(t):
        prev = jnp.pad(t, ((0, 0), (1, 0), (0, 0), (0, 0), (0, 0)))[:, :-1]
        return jnp.concatenate([prev, t], axis=2)

    kk, vv = with_prev(kb), with_prev(vb)
    s = jnp.einsum('bnqhgd,bnkhd->bnhgqk', qb, kk).astype(jnp.float32) * (D ** -0.5)
    i = jnp.arange(ATTN_BLOCK)[:, None]
    j = jnp.arange(2 * ATTN_BLOCK)[None, :]
    rel = i + ATTN_BLOCK - j
    kpos = (jnp.arange(nb)[:, None] - 1) * ATTN_BLOCK + jnp.arange(2 * ATTN_BLOCK)[None, :]
    valid = ((rel >= 0) & (rel < WINDOW))[None] & (kpos >= 0)[:, None, :]
    s = jnp.where(valid[None, :, None, None], s, -1e30)
    sink = sinks.astype(jnp.float32).reshape(ATTN_KV_HEADS, ATTN_GROUP)[None, None, :, :, None, None]
    sink = jnp.broadcast_to(sink, s.shape[:-1] + (1,))
    p = jax.nn.softmax(jnp.concatenate([s, sink], axis=-1), axis=-1)[..., :-1]
    o = jnp.einsum('bnhgqk,bnkhd->bnqhgd', p.astype(v.dtype), vv)
    return o.reshape(B, S, H * D)

def retention(q, k, v):
    B, S, H, Dk = q.shape
    Dv = v.shape[-1]
    C = RET_CHUNK
    nc = S // C
    f32 = jnp.float32
    log_g = jnp.log(1.0 - 2.0 ** (-5.0 - jnp.arange(H, dtype=f32)))
    idx = jnp.arange(C, dtype=f32)
    diff = idx[:, None] - idx[None, :]
    dmask = jnp.where(diff >= 0, jnp.exp(log_g[:, None, None] * jnp.maximum(diff, 0.0)), 0.0)
    q_decay = jnp.exp(log_g[:, None] * (idx + 1.0))[..., None]
    k_decay = jnp.exp(log_g[:, None] * (C - 1.0 - idx))[..., None]
    chunk_decay = jnp.exp(log_g * C)[:, None, None]

    def to_chunks(t):
        return t.astype(f32).reshape(B, nc, C, H, t.shape[-1]).transpose(1, 0, 3, 2, 4)

    qc, kc, vc = to_chunks(q), to_chunks(k * (Dk ** -0.5)), to_chunks(v)

    def step(state, inp):
        qi, ki, vi = inp
        sc = jnp.einsum('bhid,bhjd->bhij', qi, ki) * dmask
        intra = jnp.einsum('bhij,bhjv->bhiv', sc, vi)
        inter = jnp.einsum('bhid,bhdv->bhiv', qi * q_decay, state)
        new_state = chunk_decay * state + jnp.einsum('bhjd,bhjv->bhdv', ki * k_decay, vi)
        return new_state, intra + inter

    state0 = jnp.zeros((B, H, Dk, Dv), f32)
    _, out = lax.scan(step, state0, (qc, kc, vc))
    return out.transpose(1, 0, 3, 2, 4).reshape(B, S, H, Dv).astype(v.dtype)

def gated_linear_attention(q, k, v, log_a):
    B, S, H, Dk = q.shape
    Dv = v.shape[-1]
    C = GLA_CHUNK
    nc = S // C
    f32 = jnp.float32

    def to_chunks(t):
        return t.astype(f32).reshape(B, nc, C, H, t.shape[-1]).transpose(1, 0, 3, 2, 4)

    qc, kc, vc, gc = to_chunks(q * (Dk ** -0.5)), to_chunks(k), to_chunks(v), to_chunks(log_a)
    causal = jnp.tril(jnp.ones((C, C), dtype=bool))[..., None]

    def step(state, inp):
        qi, ki, vi, gi = inp
        b = jnp.cumsum(gi, axis=2)
        rel = b[:, :, :, None, :] - b[:, :, None, :, :]
        decay = jnp.where(causal, jnp.exp(jnp.minimum(rel, 0.0)), 0.0)
        sc = jnp.einsum('bhid,bhijd,bhjd->bhij', qi, decay, ki)
        intra = jnp.einsum('bhij,bhjv->bhiv', sc, vi)
        inter = jnp.einsum('bhid,bhdv->bhiv', qi * jnp.exp(b), state)
        b_last = b[:, :, -1:, :]
        new_state = (jnp.exp(b_last)[:, :, 0, :, None] * state
                     + jnp.einsum('bhjd,bhjv->bhdv', ki * jnp.exp(b_last - b), vi))
        return new_state, intra + inter

    state0 = jnp.zeros((B, H, Dk, Dv), f32)
    _, out = lax.scan(step, state0, (qc, kc, vc, gc))
    return out.transpose(1, 0, 3, 2, 4).reshape(B, S, H, Dv).astype(v.dtype)

def hybrid_layer(x, c_act, positions, w_mod, b_mod, pre_gain, post_gain, w_in, sinks,
                 gla_gate_w, gla_gate_b, gla_norm_gain, w_out):
    B, S, _ = x.shape
    mod = c_act @ w_mod + b_mod
    shift, scale, gate = jnp.split(mod[:, None, :], 3, axis=-1)
    h = rms_norm(x, pre_gain) * (1.0 + scale) + shift
    proj = h @ w_in
    (aq, ak, av, ag, rq, rk, rv, rg, gq, gk, gv, gg, ga) = jnp.split(proj, IN_SPLITS, axis=-1)

    rope_freq = ROPE_THETA ** (-jnp.arange(0, HEAD_DIM, 2, dtype=jnp.float32) / HEAD_DIM)
    aq = apply_rotary(aq.reshape(B, S, ATTN_HEADS, HEAD_DIM), positions, rope_freq)
    ak = apply_rotary(ak.reshape(B, S, ATTN_KV_HEADS, HEAD_DIM), positions, rope_freq)
    av = av.reshape(B, S, ATTN_KV_HEADS, HEAD_DIM)
    a_out = sliding_window_attention(aq, ak, av, sinks) * jax.nn.silu(ag)

    ret_freq = 1.0 / (10000.0 ** jnp.linspace(0.0, 1.0, RET_DK // 2, dtype=jnp.float32))
    rq = apply_rotary(rq.reshape(B, S, RET_HEADS, RET_DK), positions, ret_freq)
    rk = apply_rotary(rk.reshape(B, S, RET_HEADS, RET_DK), positions, ret_freq)
    r = retention(rq, rk, rv.reshape(B, S, RET_HEADS, RET_DV))
    r_out = rms_norm(r).reshape(B, S, RET_W) * jax.nn.silu(rg)

    gate_logits = (ga @ gla_gate_w + gla_gate_b).astype(jnp.float32)
    log_a = (jax.nn.log_sigmoid(gate_logits) / GLA_GATE_NORMALIZER).reshape(B, S, GLA_HEADS, GLA_DK)
    g = gated_linear_attention(gq.reshape(B, S, GLA_HEADS, GLA_DK), gk.reshape(B, S, GLA_HEADS, GLA_DK),
                               gv.reshape(B, S, GLA_HEADS, GLA_DV), log_a)
    g_out = rms_norm(g, gla_norm_gain).reshape(B, S, GLA_W) * jax.nn.silu(gg)

    y = jnp.concatenate([a_out, r_out, g_out], axis=-1) @ w_out
    return x + gate * rms_norm(y, post_gain)

def first_inputs(seed: int = 0) -> dict:
    key = jax.random.key(seed)
    ks = jax.random.split(key, 16)
    f32 = jnp.float32
    x = jax.random.normal(ks[0], (BATCH, SEQ, D_MODEL), f32)
    c = jax.random.normal(ks[1], (BATCH, D_MODEL), f32)
    positions = jnp.broadcast_to(jnp.arange(SEQ, dtype=jnp.int32)[None, :], (BATCH, SEQ))
    w_mod = jax.random.normal(ks[2], (DEPTH, D_MODEL, 3 * D_MODEL), f32) * (0.5 * D_MODEL ** -0.5)
    b_mod = jax.random.normal(ks[3], (DEPTH, 3 * D_MODEL), f32) * 0.01
    pre_norm_gain = 1.0 + 0.02 * jax.random.normal(ks[4], (DEPTH, D_MODEL), f32)
    post_norm_gain = 1.0 + 0.02 * jax.random.normal(ks[5], (DEPTH, D_MODEL), f32)
    w_in = jax.random.normal(ks[6], (DEPTH, D_MODEL, D_IN), f32) * (D_MODEL ** -0.5)
    attn_sinks = 0.5 * jax.random.normal(ks[7], (DEPTH, ATTN_HEADS), f32)
    gla_gate_w = jax.random.normal(ks[8], (DEPTH, GLA_GATE_RANK, GLA_HEADS * GLA_DK), f32) * (GLA_GATE_RANK ** -0.5)
    gla_gate_b = 0.01 * jax.random.normal(ks[9], (DEPTH, GLA_HEADS * GLA_DK), f32)
    gla_norm_gain = 1.0 + 0.02 * jax.random.normal(ks[10], (DEPTH, GLA_DV), f32)
    w_out = jax.random.normal(ks[11], (DEPTH, D_MIX, D_MODEL), f32) * (D_MIX ** -0.5)
    return {"x": x, "c": c, "positions": positions, "w_mod": w_mod, "b_mod": b_mod,
            "pre_norm_gain": pre_norm_gain, "post_norm_gain": post_norm_gain, "w_in": w_in,
            "attn_sinks": attn_sinks, "gla_gate_w": gla_gate_w, "gla_gate_b": gla_gate_b,
            "gla_norm_gain": gla_norm_gain, "w_out": w_out}

def first_block(x, c, positions, w_mod, b_mod, pre_norm_gain, post_norm_gain, w_in,
              attn_sinks, gla_gate_w, gla_gate_b, gla_norm_gain, w_out):
    c_act = jax.nn.silu(c)
    for l in range(DEPTH):
        x = hybrid_layer(x, c_act, positions, w_mod[l], b_mod[l], pre_norm_gain[l], post_norm_gain[l],
                         w_in[l], attn_sinks[l], gla_gate_w[l], gla_gate_b[l], gla_norm_gain[l], w_out[l])
    return x


CTX_LEN = 256
GRID_W = 64
ATTN_WIDTH = D_MODEL // 2
SGU_WIDTH = D_MODEL // 4
FOURIER_WIDTH = D_MODEL // 4
MIX_WIDTH = ATTN_WIDTH + SGU_WIDTH + FOURIER_WIDTH
N_Q_HEADS = ATTN_WIDTH // HEAD_DIM
N_KV_HEADS = N_Q_HEADS // 4
KV_WIDTH = N_KV_HEADS * HEAD_DIM
SGU_HEAD_DIM = 64
N_SGU_HEADS = SGU_WIDTH // SGU_HEAD_DIM
FOURIER_GROUP_DIM = 64
N_FOURIER_GROUPS = FOURIER_WIDTH // FOURIER_GROUP_DIM
IN_WIDTH = ATTN_WIDTH + 2 * KV_WIDTH + 2 * SGU_WIDTH + FOURIER_WIDTH
Q_END = ATTN_WIDTH
K_END = Q_END + KV_WIDTH
V_END = K_END + KV_WIDTH
U_END = V_END + SGU_WIDTH
G_END = U_END + SGU_WIDTH
BLOCK = 128
CHUNK = 128
D_FF = 4 * D_MODEL
NEG_INF = -1e30


def rmsnorm(x, g):
    xf = x.astype(jnp.float32)
    y = xf * lax.rsqrt(jnp.mean(xf * xf, axis=-1, keepdims=True) + EPS)
    return (y * g.astype(jnp.float32)).astype(x.dtype)

def axial_rope_tables(rows):
    row = jnp.repeat(jnp.arange(rows), GRID_W).astype(jnp.float32)
    col = jnp.tile(jnp.arange(GRID_W), rows).astype(jnp.float32)
    n_freq = HEAD_DIM // 4
    inv_freq = ROPE_THETA ** (-jnp.arange(n_freq, dtype=jnp.float32) / n_freq)
    ang_r = row[:, None] * inv_freq[None, :]
    ang_c = col[:, None] * inv_freq[None, :]
    ang = jnp.concatenate([ang_r, ang_r, ang_c, ang_c], axis=-1)
    return jnp.cos(ang), jnp.sin(ang)

def apply_rope(x, cos, sin):
    x1, x2, x3, x4 = jnp.split(x, 4, axis=-1)
    rot = jnp.concatenate([-x2, x1, -x4, x3], axis=-1)
    out = x * cos[None, :, None, :] + rot * sin[None, :, None, :]
    return out.astype(x.dtype)

def neighbour_blocks(t):
    z = jnp.zeros_like(t[:, :1])
    prev = jnp.concatenate([z, t[:, :-1]], axis=1)
    nxt = jnp.concatenate([t[:, 1:], z], axis=1)
    return jnp.concatenate([prev, t, nxt], axis=2)

def latent_window_attention(q, k, v, ck, cv, sink):
    B, S, H, hd = q.shape
    G = H // N_KV_HEADS
    nb = S // BLOCK
    scale = hd ** -0.5
    qb = q.reshape(B, nb, BLOCK, N_KV_HEADS, G, hd)
    kw = neighbour_blocks(k.reshape(B, nb, BLOCK, N_KV_HEADS, hd))
    vw = neighbour_blocks(v.reshape(B, nb, BLOCK, N_KV_HEADS, hd))
    s_loc = jnp.einsum('bnqhgd,bnkhd->bnhgqk', qb, kw, preferred_element_type=jnp.float32) * scale
    qpos = jnp.arange(BLOCK)[:, None]
    kpos = jnp.arange(3 * BLOCK)[None, :] - BLOCK
    band = jnp.abs(kpos - qpos) <= WINDOW
    kabs = jnp.arange(nb)[:, None, None] * BLOCK + kpos[None]
    valid = band[None] & (kabs >= 0) & (kabs < S)
    s_loc = jnp.where(valid[None, :, None, None], s_loc, NEG_INF)
    s_ctx = jnp.einsum('bnqhgd,bchd->bnhgqc', qb, ck, preferred_element_type=jnp.float32) * scale
    s_sink = jnp.broadcast_to(sink.astype(jnp.float32).reshape(1, 1, N_KV_HEADS, G, 1, 1),
                              s_loc.shape[:-1] + (1,))
    p = jax.nn.softmax(jnp.concatenate([s_loc, s_ctx, s_sink], axis=-1), axis=-1)
    n_loc = 3 * BLOCK
    n_ctx = ck.shape[1]
    p_loc = p[..., :n_loc].astype(v.dtype)
    p_ctx = p[..., n_loc:n_loc + n_ctx].astype(v.dtype)
    out = (jnp.einsum('bnhgqk,bnkhd->bnqhgd', p_loc, vw)
           + jnp.einsum('bnhgqc,bchd->bnqhgd', p_ctx, cv))
    return out.reshape(B, S, H * hd)

def context_attention(cq, ck, cv, sink):
    B, L, H, hd = cq.shape
    G = H // N_KV_HEADS
    qg = cq.reshape(B, L, N_KV_HEADS, G, hd)
    s = jnp.einsum('bqhgd,bkhd->bhgqk', qg, ck, preferred_element_type=jnp.float32) * (hd ** -0.5)
    s_sink = jnp.broadcast_to(sink.astype(jnp.float32).reshape(1, N_KV_HEADS, G, 1, 1),
                              s.shape[:-1] + (1,))
    p = jax.nn.softmax(jnp.concatenate([s, s_sink], axis=-1), axis=-1)[..., :L]
    out = jnp.einsum('bhgqk,bkhd->bqhgd', p.astype(cv.dtype), cv)
    return out.reshape(B, L, H * hd)

def spatial_gating(u, v, w_s, b_s, g_s):
    B, S, _ = u.shape
    vh = rmsnorm(v.reshape(B, S, N_SGU_HEADS, SGU_HEAD_DIM), g_s)
    vc = vh.reshape(B, S // CHUNK, CHUNK, N_SGU_HEADS, SGU_HEAD_DIM)
    mixed = jnp.einsum('hpq,bnqhd->bnphd', w_s, vc) + b_s.T[None, None, :, :, None]
    return u * mixed.reshape(B, S, SGU_WIDTH)

def fourier_mix(f):
    B, S, _ = f.shape
    fg = f.reshape(B, S, N_FOURIER_GROUPS, FOURIER_GROUP_DIM).astype(jnp.float32)
    y = jnp.real(jnp.fft.fft2(fg, axes=(1, 3), norm='ortho'))
    return y.reshape(B, S, FOURIER_WIDTH).astype(f.dtype)

def merge_heads(attn, sgu, four, g_mix, w_out):
    a = rmsnorm(attn, g_mix[:ATTN_WIDTH])
    s = rmsnorm(sgu, g_mix[ATTN_WIDTH:ATTN_WIDTH + SGU_WIDTH])
    f = rmsnorm(four, g_mix[ATTN_WIDTH + SGU_WIDTH:])
    return jnp.concatenate([a, s, f], axis=-1) @ w_out

def squared_relu_mlp(h, w1, w2):
    return jnp.square(jax.nn.relu(h @ w1)) @ w2

def second_inputs(seed: int = 0) -> dict:
    key = jax.random.key(seed)
    ks = jax.random.split(key, 24)
    f32 = jnp.float32
    nrm = lambda k, shape, s: jax.random.normal(k, shape, f32) * s
    gain = lambda k, shape: 1.0 + 0.05 * jax.random.normal(k, shape, f32)
    return {
        "x": nrm(ks[0], (BATCH, SEQ, D_MODEL), 1.0),
        "c": nrm(ks[1], (BATCH, D_MODEL), 1.0),
        "ctx": nrm(ks[2], (BATCH, CTX_LEN, D_MODEL), 1.0),
        "c_ctx": nrm(ks[3], (D_MODEL,), 1.0),
        "w_ada": nrm(ks[4], (DEPTH, D_MODEL, 6 * D_MODEL), 0.5 * D_MODEL ** -0.5),
        "b_ada": nrm(ks[5], (DEPTH, 6 * D_MODEL), 0.02),
        "g_pre_mix": gain(ks[6], (DEPTH, D_MODEL)),
        "w_in": nrm(ks[7], (DEPTH, D_MODEL, IN_WIDTH), D_MODEL ** -0.5),
        "sink": nrm(ks[8], (DEPTH, N_Q_HEADS), 0.5),
        "w_sgu": nrm(ks[9], (DEPTH, N_SGU_HEADS, CHUNK, CHUNK), 0.5 * CHUNK ** -0.5),
        "b_sgu": gain(ks[10], (DEPTH, N_SGU_HEADS, CHUNK)),
        "g_sgu": gain(ks[11], (DEPTH, N_SGU_HEADS, SGU_HEAD_DIM)),
        "g_mix": gain(ks[12], (DEPTH, MIX_WIDTH)),
        "w_out": nrm(ks[13], (DEPTH, MIX_WIDTH, D_MODEL), MIX_WIDTH ** -0.5),
        "g_post_mix": gain(ks[14], (DEPTH, D_MODEL)),
        "g_pre_ff": gain(ks[15], (DEPTH, D_MODEL)),
        "w_ff1": nrm(ks[16], (DEPTH, D_MODEL, D_FF), D_MODEL ** -0.5),
        "w_ff2": nrm(ks[17], (DEPTH, D_FF, D_MODEL), D_FF ** -0.5),
        "g_post_ff": gain(ks[18], (DEPTH, D_MODEL)),
    }

def second_block(x, c, ctx, c_ctx, w_ada, b_ada, g_pre_mix, w_in, sink, w_sgu, b_sgu, g_sgu,
              g_mix, w_out, g_post_mix, g_pre_ff, w_ff1, w_ff2, g_post_ff):
    B, S, _ = x.shape
    ROWS = S // GRID_W
    cos, sin = axial_rope_tables(ROWS)
    h_ctx = ctx
    for l in range(DEPTH):
        last = l == DEPTH - 1
        mod_x = (jax.nn.silu(c) @ w_ada[l] + b_ada[l])[:, None, :]
        sh1, sc1, g1, sh2, sc2, g2 = jnp.split(mod_x, 6, axis=-1)
        mod_c = jax.nn.silu(c_ctx) @ w_ada[l] + b_ada[l]
        csh1, csc1, cg1, csh2, csc2, cg2 = jnp.split(mod_c, 6, axis=-1)

        hc = rmsnorm(h_ctx, g_pre_mix[l]) * (1.0 + csc1) + csh1
        if last:
            ckv = hc @ w_in[l][:, Q_END:V_END]
            ck, cv = jnp.split(ckv, 2, axis=-1)
        else:
            pc = hc @ w_in[l]
            cq, ck, cv, cu, cg, cf = jnp.split(pc, [Q_END, K_END, V_END, U_END, G_END], axis=-1)
        ck = ck.reshape(B, CTX_LEN, N_KV_HEADS, HEAD_DIM)
        cv = cv.reshape(B, CTX_LEN, N_KV_HEADS, HEAD_DIM)
        if not last:
            c_attn = context_attention(cq.reshape(B, CTX_LEN, N_Q_HEADS, HEAD_DIM), ck, cv, sink[l])
            c_sgu = spatial_gating(jax.nn.gelu(cu), jax.nn.gelu(cg), w_sgu[l], b_sgu[l], g_sgu[l])
            c_four = fourier_mix(cf)
            yc = merge_heads(c_attn, c_sgu, c_four, g_mix[l], w_out[l])
            h_ctx = h_ctx + cg1 * rmsnorm(yc, g_post_mix[l])
            hc2 = rmsnorm(h_ctx, g_pre_ff[l]) * (1.0 + csc2) + csh2
            h_ctx = h_ctx + cg2 * rmsnorm(squared_relu_mlp(hc2, w_ff1[l], w_ff2[l]), g_post_ff[l])

        hx = rmsnorm(x, g_pre_mix[l]) * (1.0 + sc1) + sh1
        px = hx @ w_in[l]
        q, k, v, u, gv, f = jnp.split(px, [Q_END, K_END, V_END, U_END, G_END], axis=-1)
        q = apply_rope(q.reshape(B, S, N_Q_HEADS, HEAD_DIM), cos, sin)
        k = apply_rope(k.reshape(B, S, N_KV_HEADS, HEAD_DIM), cos, sin)
        v = v.reshape(B, S, N_KV_HEADS, HEAD_DIM)
        attn = latent_window_attention(q, k, v, ck, cv, sink[l])
        sgu = spatial_gating(jax.nn.gelu(u), jax.nn.gelu(gv), w_sgu[l], b_sgu[l], g_sgu[l])
        four = fourier_mix(f)
        y = merge_heads(attn, sgu, four, g_mix[l], w_out[l])
        x = x + g1 * rmsnorm(y, g_post_mix[l])
        hx2 = rmsnorm(x, g_pre_ff[l]) * (1.0 + sc2) + sh2
        x = x + g2 * rmsnorm(squared_relu_mlp(hx2, w_ff1[l], w_ff2[l]), g_post_ff[l])
    return x


def setup_inputs(seed=0):
    out = dict(first_inputs(seed))
    for name, value in second_inputs(seed + 1).items():
        if name != "x":
            out[name + "_2"] = value
    return out


def reference(
    x, c, positions, w_mod, b_mod, pre_norm_gain, post_norm_gain, w_in, attn_sinks, gla_gate_w,
    gla_gate_b, gla_norm_gain, w_out, c_2, ctx_2, c_ctx_2, w_ada_2, b_ada_2, g_pre_mix_2,
    w_in_2, sink_2, w_sgu_2, b_sgu_2, g_sgu_2, g_mix_2, w_out_2, g_post_mix_2, g_pre_ff_2,
    w_ff1_2, w_ff2_2, g_post_ff_2,
):
    x = first_block(
        x, c, positions, w_mod, b_mod, pre_norm_gain, post_norm_gain, w_in, attn_sinks,
        gla_gate_w, gla_gate_b, gla_norm_gain, w_out,
    )
    return second_block(
        x, c_2, ctx_2, c_ctx_2, w_ada_2, b_ada_2, g_pre_mix_2, w_in_2, sink_2, w_sgu_2, b_sgu_2,
        g_sgu_2, g_mix_2, w_out_2, g_post_mix_2, g_pre_ff_2, w_ff1_2, w_ff2_2, g_post_ff_2,
    )


_drawn_inputs = setup_inputs


def setup_inputs(seed=0):
    import zlib

    import numpy as np

    out = dict(_drawn_inputs(seed))
    spreads = {}
    factors = {'b_mod': 2.882,
     'pre_norm_gain': 3.61,
     'post_norm_gain': 6.476,
     'attn_sinks': 8.0,
     'gla_gate_b': 8.0,
     'gla_norm_gain': 8.0,
     'g_pre_mix_2': 3.226,
     'sink_2': 64.0,
     'b_sgu_2': 39.45,
     'g_sgu_2': 63.909,
     'g_mix_2': 2.868,
     'g_post_mix_2': 2.831,
     'g_pre_ff_2': 2.906,
     'g_post_ff_2': 2.858}
    for name, (base, spread) in spreads.items():
        noise = np.random.default_rng([zlib.crc32(name.encode()), seed]).standard_normal(out[name].shape)
        drawn = base * np.exp(spread * noise) if base else spread * noise
        out[name] = __import__('jax').numpy.asarray(drawn.astype(out[name].dtype))
    for name, factor in factors.items():
        out[name] = (out[name] * factor).astype(out[name].dtype)
    return out
```

```python
from contextlib import ExitStack

import numpy as np

import concourse.bass as bass
from concourse import mybir

F32 = mybir.dt.float32
F32R = mybir.dt.float32r
BF16 = mybir.dt.bfloat16
I32 = mybir.dt.int32
U8 = mybir.dt.uint8
ALU = mybir.AluOpType
ACT = mybir.ActivationFunctionType
AX_X = mybir.AxisListType.X

P = 128
D = 1024
KB = D // P
SEQ = 1024
W = 512
NB = SEQ // W
NT = W // P
DEPTH = 2
EPS = 1e-6

ROPE1 = 9
GQ, GK, AV, RV, GV = 9, 10, 11, 12, 14
GATE1 = 16
OUT1 = 24
CH1 = 32
GATE_RANK = 16
LEVELS = 7
ATT_SCALE = 64 ** -0.5
HEAD_PAIRS = [0, 4, 1, 5, 2, 6, 3, 7]

CTX = 256
GRID_W = 64
TOKENS = SEQ + CTX
VEC = 3
MOD1, MOD2 = 3 * KB, 6 * KB
GV2, U2, Q2, K2, F2, V2 = 0, 2, 4, 8, 9, 11
IN2 = 12
FF_GROUPS = 4
FF_CH = 8
FF2 = FF_GROUPS * 2 * FF_CH
CH2 = IN2 + KB + FF2
DFT = 16
A1, B1, G1, A2, B2, G2 = range(0, 48, 8)

C_A, C_B, C_G, C_GB, C_GN, C_ONE, C_SINK = 0, 8, 16, 24, 25, 26, 32
NCOL1 = 40


class Sig:

    def __init__(self, sem, per=0, start=0):
        self.sem, self.per, self.start = sem, per, start

    def after(self, it, n):
        if isinstance(it, int):
            return self.sem, self.start + it * self.per + n
        return self.sem, it * self.per + (self.start + n)

    @property
    def one(self):
        return self.sem, 1


class Order:

    def __init__(self, eng, sig):
        self.eng, self.sig, self.n, self.it = eng, sig, 0, 0

    def begin(self, it):
        self.it, self.n = it, 0

    def link(self, ins):
        self.n += 1
        ins.then_inc(self.sig.sem, 1)
        self.eng.wait_ge(*self.sig.after(self.it, self.n))

    def end(self):
        assert self.n == self.sig.per, (self.n, self.sig.per)


def constants():
    f = np.float32
    c = {}
    c["ident"] = np.eye(P, dtype=f)
    c["ones"] = np.ones((P, P), f)
    half = np.arange(P) // 64
    c["ones64"] = (half[:, None] == half[None, :]).astype(f)
    rot = np.zeros((P, P), f)
    for m in range(P):
        d = m % 64
        if d < 32:
            rot[m + 32, m] = -1
        else:
            rot[m - 32, m] = 1
    c["rot1"] = rot
    inv_a = (10000.0 ** (-np.arange(0, 64, 2, dtype=np.float64) / 64)).astype(f)
    steps = np.arange(32, dtype=f) * f(1 / 31)
    steps[-1] = 1
    inv_r = f(1) / np.power(10000.0, steps.astype(np.float64)).astype(f)
    c["inv_freq"] = np.stack([np.tile(inv_a, 4), np.tile(inv_r, 4)], 1)
    i, j = np.arange(P)[:, None], np.arange(2 * P)[None, :]
    rel = i + P - j
    ok = (rel >= 0) & (rel < P)
    c["mask1"] = np.stack([np.where(ok & (j >= P), 0, -1e30), np.where(ok, 0, -1e30)], 1).astype(f)
    log_g = np.log(1.0 - 2.0 ** (-5.0 - np.arange(4)))
    idx = np.arange(P, dtype=np.float64)
    diff = idx[None, :] - idx[:, None]
    dm = np.where(diff >= 0, np.exp(log_g[:, None, None] * np.maximum(diff, 0)), 0) * 64 ** -0.5
    c["ret_mask"] = dm.transpose(1, 0, 2).astype(f)
    qd = np.exp(log_g[:, None] * (idx + 1))
    c["ret_qdecay"] = np.stack([qd[2 * n + half] for n in range(2)], 1).astype(f)
    kd = np.exp(log_g[:, None] * (P - 1 - idx)) * 64 ** -0.5
    c["ret_kdecay"] = np.repeat(kd.T, 64, axis=1).astype(f)
    c["ret_cdecay"] = np.stack([np.exp(log_g * P)[2 * n + half] for n in range(2)], 1).astype(f)
    c["gla_heads"] = (np.arange(P)[:, None] // 32 == np.arange(256)[None, :] // 64).astype(f)
    m = np.zeros((P, LEVELS + 1, P), f)
    a = np.arange(P)
    for lv in range(LEVELS):
        s = 64 >> lv
        m[:, lv] = (a[:, None] // s % 2 == 0) & (a[None, :] // s == a[:, None] // s + 1)
    m[:, LEVELS] = np.eye(P)
    c["gla_mask"] = m
    rot = np.zeros((P, P), f)
    for m in range(P):
        d = m % 32
        if d < 16:
            rot[m + 16, m] = -1
        else:
            rot[m - 16, m] = 1
    c["rot2"] = rot
    inv = (10000.0 ** (-np.arange(16, dtype=np.float64) / 16)).astype(f)
    tok = np.arange(SEQ)
    row, column = (tok // GRID_W).astype(f), (tok % GRID_W).astype(f)
    ang = np.concatenate([np.tile(inv[:, None] * row[None], (2, 1)), np.tile(inv[:, None] * column[None], (2, 1))])
    ang = np.tile(ang, (2, 1)).astype(np.float64)
    c["rope2"] = np.stack([np.cos(ang), np.sin(ang)], 1).astype(f)
    i, j = np.arange(P)[:, None], np.arange(3 * P)[None, :] - P
    band = np.abs(j - i) <= P
    c["mask2"] = np.stack([np.where(ok, 0, -1e30) for ok in (band & (j >= 0), band, band & (j < P))], 1).astype(f)
    w = 2 * np.pi * np.outer(np.arange(64), np.arange(64)) / 64
    two = np.kron(np.eye(2), np.ones((64, 64)))
    c["dft_dims"] = (np.concatenate([np.tile(np.cos(w), (2, 2)) * two, np.tile(np.sin(w), (2, 2)) * two], 1) / 256).astype(f)
    w = 2 * np.pi * (np.outer(np.arange(SEQ), np.arange(SEQ)) % SEQ) / SEQ
    c["dft_tokens"] = np.stack([chunked(np.cos(w).astype(f)), chunked(-np.sin(w).astype(f))], 1).reshape(-1, P, SEQ)
    w = 2 * np.pi * (np.outer(np.arange(CTX), np.arange(CTX)) % CTX) / CTX
    both = np.stack([2 * np.cos(w), -2 * np.sin(w)])
    c["dft_ctx"] = both.reshape(2, 2, P, CTX).transpose(2, 0, 1, 3).astype(f)
    return c


TWO_PI = 2 * np.pi
C1 = 6.28125
C2 = 0.0019350051879882812
C3 = TWO_PI - C1 - C2
MAGIC = 12582912.0
PI_IN = 3.1415925


def load_and_modulate(nc, t, a, sems):
    sem = sems
    NRING = 6
    n1, n2 = DEPTH * MOD1, DEPTH * MOD2
    chunks = n1 + n2
    with ExitStack() as ctx:
        ring = ctx.enter_context(nc.sbuf_tensor("mod_ring", [P, NRING, D], F32))
        pos_i = ctx.enter_context(nc.sbuf_tensor("pos_i", [P, SEQ], I32))
        pos_f = ctx.enter_context(nc.sbuf_tensor("pos_f", [P, SEQ], F32))
        ang = ctx.enter_context(nc.sbuf_tensor("ang", [P, SEQ], F32))
        turns = ctx.enter_context(nc.sbuf_tensor("turns", [P, SEQ], F32))
        arg = ctx.enter_context(nc.sbuf_tensor("arg", [P, 4, SEQ], F32))
        cvec = ctx.enter_context(nc.sbuf_tensor("cvec", [P, KB, VEC], F32))
        cact = ctx.enter_context(nc.sbuf_tensor("cact", [P, KB, VEC], F32))
        bias = ctx.enter_context(nc.sbuf_tensor("mod_bias", [P, chunks], F32))
        mod = ctx.enter_context(nc.sbuf_tensor("mod", [P, DEPTH, MOD1], F32))
        mod2 = ctx.enter_context(nc.sbuf_tensor("mod2", [P, DEPTH, 2, MOD2], F32))
        gains2 = ctx.enter_context(nc.sbuf_tensor("gains2", [P, DEPTH, 4, KB], F32))
        gains = ctx.enter_context(nc.sbuf_tensor("gains", [P, DEPTH, 18], F32))
        sinks = ctx.enter_context(nc.sbuf_tensor("sinks", [P, DEPTH, 8], F32))
        mask_f = ctx.enter_context(nc.sbuf_tensor("mask_f", [P, 2, 2 * P], F32))
        levels_f = ctx.enter_context(nc.sbuf_tensor("levels_f", [P, LEVELS + 1, P], F32))
        inv = ctx.enter_context(nc.sbuf_tensor("inv", [P, 2], F32))
        psM = ctx.enter_context(nc.psum_tensor("psM", [P, 512], F32))

        chunk_in = [sem(f"mod_chunk_in{s}") for s in range(NRING)]
        chunk_used = sem("mod_chunk_used")
        vec_in, pos_in, small_in = sem("vec_in"), sem("pos_in"), sem("small_in")
        cact_ready, mod_done, args_ready = sem("cact_ready"), sem("mod_done"), sem("args_ready")
        tables_ready = sem("tables_ready")
        order = Order(nc.vector, Sig(sem("prep_order")))
        block = ctx.enter_context(nc.Block())

        @block.sync
        def _(sp):
            sp.dma_start(cvec[:], a["c"]).then_inc(vec_in, 16)
            sp.dma_start(pos_i[:], a["positions"]).then_inc(pos_in, 16)
            sp.dma_start(inv[:], a["inv_freq"]).then_inc(pos_in, 16)
            for s in range(NRING):
                sp.dma_start(ring[:, s, :], a["w_mod"][s]).then_inc(chunk_in[s], 16)
            loads = [(bias, "b_mod"), (gains, "gains1"), (sinks, "sinks1"), (mask_f, "mask1"), (gains2, "gains2"),
                     (levels_f, "gla_mask")]
            for dst, name in loads:
                sp.dma_start(dst[:], a[name]).then_inc(small_in, 16)
            with sp.Fori(0, n1 // NRING - 1) as i:
                for s in range(NRING):
                    sp.wait_ge(chunk_used, i * NRING + (s + 1))
                    sp.dma_start(ring[:, s, :], a["w_mod"][bass.ds(i * NRING + (NRING + s), 1)]
                                 .rearrange("o p n -> p (o n)")).then_inc(chunk_in[s], 16)
            with sp.Fori(n1 // NRING - 1, chunks // NRING - 1) as i:
                for s in range(NRING):
                    sp.wait_ge(chunk_used, i * NRING + (s + 1))
                    sp.dma_start(ring[:, s, :], a["w_ada"][bass.ds(i * NRING + (NRING - n1 + s), 1)]
                                 .rearrange("o p n -> p (o n)")).then_inc(chunk_in[s], 16)

        @block.gpsimd
        def _(pool):
            pool.dma_start(t["x"][:], a["x"]).then_inc(t["x_in"], 16)
            for name in ("ident", "ones", "ones64", "rot1", "ret_mask", "ret_qdecay", "ret_kdecay", "ret_cdecay",
                         "gla_heads", "gate_w"):
                pool.dma_start(t[name][:], a[name]).then_inc(t["const_in"], 16)
            pool.wait_ge(t["x_in"], 16)
            pool.wait_ge(t["const_in"], 16 * 10)

        @block.scalar
        def _(act):
            act.wait_ge(vec_in, 16)
            nc.scalar.activation(cact[:], cvec[:], ACT.Silu).then_inc(cact_ready, 1)
            for n in range(4):
                act.wait_ge(args_ready, n + 1)
                nc.scalar.activation(t["rope1"][:, n, :], arg[:, n, :], ACT.Sin).then_inc(tables_ready, 1)
            act.wait_ge(tables_ready, 4)

        @block.tensor
        def _(pe):
            pe.wait_ge(cact_ready, 1)
            with pe.Fori(0, chunks // NRING) as i:
                for s in range(NRING):
                    pe.wait_ge(chunk_in[s], i * 16 + 16)
                    for k in range(KB):
                        last = nc.tensor.matmul(psM[:, bass.ds((i * NRING + s) * VEC, VEC)], ring[:, s, k * P:(k + 1) * P],
                                                cact[:, k, :], start=(k == 0), stop=(k == KB - 1))
                    last.then_inc(chunk_used, 1)

        @block.vector
        def _(dve):
            link = order.link
            dve.wait_ge(pos_in, 32)
            link(nc.vector.tensor_copy(pos_f[:], pos_i[:]))
            for j in range(2):
                link(nc.vector.tensor_scalar(ang[:], pos_f[:], inv[:, j:j + 1], None, ALU.mult))
                for cosine in (1, 0):
                    out = arg[:, 2 * j + 1 - cosine, :]
                    link(nc.vector.tensor_scalar(turns[:], ang[:], 1 / TWO_PI, 0.25 * cosine, ALU.mult, ALU.add))
                    link(nc.vector.tensor_scalar(turns[:], turns[:], MAGIC, None, ALU.add))
                    link(nc.vector.tensor_scalar(turns[:], turns[:], MAGIC, None, ALU.subtract))
                    link(nc.vector.scalar_tensor_tensor(out, turns[:], -C1, ang[:], ALU.mult, ALU.add))
                    link(nc.vector.scalar_tensor_tensor(out, turns[:], -C2, out, ALU.mult, ALU.add))
                    link(nc.vector.scalar_tensor_tensor(out, turns[:], -C3, out, ALU.mult, ALU.add))
                    link(nc.vector.tensor_scalar(out, out, np.pi / 2 * cosine, PI_IN, ALU.add, ALU.min))
                    nc.vector.tensor_scalar(out, out, -PI_IN, None, ALU.max).then_inc(args_ready, 1)
            dve.wait_ge(small_in, 16 * 6)
            link(nc.vector.tensor_copy(t["mask1"][:], mask_f[:]))
            link(nc.vector.tensor_copy(t["gla_mask"][:], levels_f[:]))
            dve.wait_ge(t["const_in"], 16 * 10)
            link(nc.vector.tensor_copy(t["identb"][:], t["ident"][:]))
            cols = t["cols1"]
            dve.wait_ge(chunk_used, chunks)
            products = psM[:, 0:chunks * VEC].rearrange("p (n v) -> p n v", v=VEC)
            link(nc.vector.tensor_tensor(mod[:].rearrange("p l n -> p (l n)"), products[:, 0:n1, 0], bias[:, 0:n1],
                                         ALU.add))
            for v in range(2):
                for l in range(DEPTH):
                    part = slice(n1 + l * MOD2, n1 + (l + 1) * MOD2)
                    link(nc.vector.tensor_tensor(mod2[:, l, v, :], products[:, part, 1 + v], bias[:, part], ALU.add))
                    for half in range(2):
                        m, out = mod2[:, l, v, 24 * half:], t["cols2"][:, l, v, 24 * half:]
                        nc.vector.scalar_tensor_tensor(out[:, A1:A1 + 8], m[:, 8:16], 1.0, gains2[:, l, 2 * half, :],
                                                       ALU.add, ALU.mult)
                        nc.vector.tensor_copy(out[:, B1:B1 + 8], m[:, 0:8])
                        link(nc.vector.tensor_tensor(out[:, G1:G1 + 8], m[:, 16:24], gains2[:, l, 2 * half + 1, :],
                                                     ALU.mult))
            link(nc.vector.scalar_tensor_tensor(cols[:, :, C_A:C_A + 8], mod[:, :, 8:16], 1.0, gains[:, :, 0:8],
                                                ALU.add, ALU.mult))
            link(nc.vector.tensor_copy(cols[:, :, C_B:C_B + 8], mod[:, :, 0:8]))
            link(nc.vector.tensor_tensor(cols[:, :, C_G:C_G + 8], mod[:, :, 16:24], gains[:, :, 8:16], ALU.mult))
            link(nc.vector.tensor_copy(cols[:, :, C_GB:C_GB + 2], gains[:, :, 16:18]))
            link(nc.vector.memset(cols[:, :, C_ONE:C_ONE + 6], 1.0))
            link(nc.vector.tensor_scalar(cols[:, :, C_SINK:C_SINK + 8], sinks[:], -1.0, None, ALU.mult))


def first_block(nc, t, a, sems, debug=None):
    sem = sems
    with ExitStack() as ctx:
        def sb(name, shape, dt=F32):
            return ctx.enter_context(nc.sbuf_tensor(name, shape, dt))

        x, wraw, whi, wlo = t["x"], t["wraw"], t["whi"], t["wlo"]
        cols1, rope1, mask1 = t["cols1"], t["rope1"], t["mask1"]
        h_hi, h_lo = sb("h_hi", [P, KB, W], F32R), sb("h_lo", [P, KB, W], F32R)
        aq = sb("aq", [P, 4, W])
        ak = sb("ak", [P, P + W])
        av = sb("av", [P, 1 + NT, P])
        rq, rk = sb("rq", [P, 2, W]), sb("rk", [P, 2, W])
        rv, gv = sb("rv", [P, NT, 256]), sb("gv", [P, NT, 256])
        gq, gk = sb("gq", [P, W]), sb("gk", [P, W])
        gate_y = sb("gate_y", [P, KB, W])
        ga = sb("ga", [GATE_RANK, W])
        gw = sb("gw", [GATE_RANK, P])
        col = sb("col", [P, NCOL1])
        tmp = sb("tmp", [P, 8, W])
        rstd = sb("rstd", [P, W])
        probs = [tmp[:, 2 * n:2 * n + 2, :].rearrange("p a b -> p (a b)").rearrange("p (g k) -> p g k", g=4)
                 for n in range(2)]
        probsT = [tmp[:, 4 + 2 * n:6 + 2 * n, :] for n in range(2)]
        mx = sb("mx", [P, 2, 4])
        nmax, sink_arg, esum, esink, rden = (sb(n, [P, 2, 4]) for n in ("nmax", "sink_arg", "esum", "esink", "rden"))
        scm = sb("scm", [P, 2, 4, P])
        kd = sb("kd", [P, 2, 256])
        qd = sb("qd", [P, 2, 2, P])
        rstate, rnew = sb("rstate", [P, 2, P]), sb("rnew", [P, 2, P])
        gstate, gnew = sb("gstate", [P, 256]), rnew[:].rearrange("p c v -> p (c v)")
        bsum = sb("bsum", [P, W])
        zed = sb("zed", [P, 2, W])
        lq, lk = tmp[:, 4:6, :], tmp[:, 6:8, :]
        gsc = aq[:].rearrange("p t (h i) -> p t h i", h=4)
        khT = sb("khT", [P, 2, P])
        elast = sb("elast", [P, NT])
        lin0, lin1 = (ctx.enter_context(nc.psum_tensor(f"lin{n}", [P, 512], F32)) for n in range(2))
        scores = [ctx.enter_context(nc.psum_tensor(f"scores{n}", [P, 1024], F32)) for n in range(2)]
        bank = [lin0[:], lin1[:]] + [s[:, 512 * n:512 * n + 512] for s in scores for n in range(2)]
        bankT = ctx.enter_context(nc.psum_tensor("bankT", [P, 2, 512], F32))
        bankS = bank[2:]
        eb, qe, khat, logs = tmp[:, 0, :], tmp[:, 1, :], tmp[:, 2, :], tmp[:, 7, :]

        def score(j):
            return scores[j % 2][:].rearrange("p (g k) -> p g k", g=4)

        def mixed(j):
            return rq[:, j, :] if j < 2 else gv[:, :, (j - 2) * P:(j - 1) * P]

        def sig(name, per, start=0):
            return Sig(sem(name), per, start)

        layer_ready = sig("layer_ready", 1)
        carried = sig("carried", 1)
        sq_ready, sq_used = sig("sq_ready", 20), sig("sq_used", 20)
        rstd_ready = sig("rstd_ready", 6)
        scaled, shifted = sig("scaled", 8), sig("shifted", 8)
        h_ready = sig("h_ready", 8)
        rope_raw, rope_mm, rope_done = sig("rope_raw", 9), sig("rope_mm", 9), sig("rope_done", 9)
        raw_in, w_hi, w_split = t["raw_in"], t["w_hi"], t["w_split"]
        lin_done, lin_free = t["lin_done"], t["lin_free"]
        ga_in = sig("ga_in", 16)
        ga_ready = sig("ga_ready", 1)
        logit_done, sig_ready = sig("logit_done", 1), sig("sig_ready", 1)
        bsum_ready = sig("bsum_ready", 1)
        s_ready, nm_ready, exp_done = sig("s_ready", 8), sig("nm_ready", 8), sig("exp_done", 8)
        rden_ready, pn_ready = sig("rden_ready", 8), sig("pn_ready", 8)
        pt_done, pt_evac_a, pt_evac_d = sig("pt_done", 8), sig("pt_evac_a", 8), sig("pt_evac_d", 8)
        pv_done, ao_done = sig("pv_done", 8), sig("ao_done", 4)
        r_scores, r_kd, r_qd = (sig(n, 4) for n in ("r_scores", "r_kd", "r_qd"))
        r_out, r_evac, r_state = (sig(n, 4) for n in ("r_out", "r_evac", "r_state"))
        z_ready, e_ready = sig("z_ready", LEVELS + 1), sig("e_ready", LEVELS + 1)
        eb_ready = sig("eb_ready", 2)
        lev_ready = sig("lev_ready", LEVELS)
        g_scores, g_picked = sig("g_scores", 4 * (LEVELS + 1)), sig("g_picked", 4 * (LEVELS + 1))
        qe_ready, kh_ready = sig("qe_ready", 1), sig("kh_ready", 1)
        kh_done, kh_evac = sig("kh_done", 4), sig("kh_evac", 4)
        g_out, g_evac, g_state = (sig(n, 4) for n in ("g_out", "g_evac", "g_state"))
        mix_hi, mix_ready = sig("mix_hi", 4), sig("mix_ready", 8)
        x_done = sig("x_done", 8, 1)
        dve_order = Order(nc.vector, sig("dve_order", 72))
        act_order = Order(nc.scalar, sig("act_order", 17))

        wait_seat = sem("wait_seat")
        block = ctx.enter_context(nc.Block())

        def layers_and_blocks(eng, layer_start=None):
            with eng.Fori(0, DEPTH) as l:
                if layer_start:
                    layer_start(l)
                with eng.Fori(0, NB) as b:
                    yield l, b, l * NB + b

        def rows(b):
            return bass.ds(b * W, W)

        def lin_product(pe, out, slot, first_wait=None):
            for k in range(KB):
                kw = slice(k * P, (k + 1) * P)
                for n, (w, h) in enumerate(((whi, h_hi), (whi, h_lo), (wlo, h_hi))):
                    last = nc.tensor.matmul(out, w[:, slot, kw], h[:, k, :], start=(k == 0 and n == 0),
                                            stop=(k == KB - 1 and n == 2))
            return last

        def token_product(slot, n_bank):
            for tile in range(NT):
                for k in range(KB):
                    for n, (h, w) in enumerate(((h_hi, whi), (h_lo, whi), (h_hi, wlo))):
                        last = nc.tensor.matmul(bank[n_bank][:, tile * P:(tile + 1) * P],
                                                h[:, k, tile * P:(tile + 1) * P], w[:, slot, k * P:(k + 1) * P],
                                                start=(k == 0 and n == 0), stop=(k == KB - 1 and n == 2))
            return last

        @block.sync
        def _(sp):
            def load(dst, src, s):
                sp.dma_start(dst, src).then_inc(raw_in[s].sem, 16)

            for s in range(2):
                load(wraw[:, s, 0:D], a["w1"][0, s], s)
            for l, b, it in layers_and_blocks(sp):
                sp.dma_start(wraw[:, 1, D:], a["w1_gate"][bass.ds(l, 1)].rearrange("o p n -> p (o n)"))\
                  .then_inc(ga_in.sem, 16)
                with sp.Fori(0, CH1 // 2 - 1) as i:
                    for s in range(2):
                        sp.wait_ge(*w_split.after(it, 2 * i + (s + 1)))
                        load(wraw[:, s, 0:D], a["w1"][bass.ds(l, 1), bass.ds(2 * i + (s + 2), 1)]
                             .rearrange("l c p n -> p (l c n)"), s)
                for s in range(2):
                    sp.wait_ge(*w_split.after(it, CH1 - 1 + s))
                    load(wraw[:, s, 0:D], a["w1_next"][bass.ds(it, 1), s].rearrange("o p n -> p (o n)"), s)

        @block.gpsimd
        def _(pool):
            def split_low(it, c, s, n=D):
                pool.wait_ge(*w_hi.after(it, c + 1))
                nc.gpsimd.tensor_tensor(wlo[:, s, 0:n], wraw[:, s, 0:n], whi[:, s, 0:n].bitcast(F32), ALU.subtract)\
                  .then_inc(*w_split.one)

            for s in range(2):
                split_low(0, s, s)
            for l, b, it in layers_and_blocks(pool):
                with pool.Fori(1, AV // 2) as i:
                    for s in range(2):
                        split_low(it, 2 * i + s, s)
                split_low(it, AV - 1, 0)
                split_low(it, AV, 1, D + KB * GATE_RANK)
                with pool.Fori(AV // 2 + 1, OUT1 // 2 + 1) as i:
                    for s in range(2):
                        split_low(it, 2 * i + s, s)
                for s in range(8):
                    pool.wait_ge(*rden_ready.after(it, s + 1))
                    nc.gpsimd.tensor_tensor(probs[s % 2], probs[s % 2],
                                            rden[:, s % 2, :].rearrange("p (g o) -> p g o", o=1)
                                            .to_broadcast([P, 4, 2 * P]), ALU.mult).then_inc(*pn_ready.one)
                for n in range(NT):
                    pool.wait_ge(*rope_done.after(it, ROPE1))
                    if n >= 2:
                        pool.wait_ge(*r_out.after(it, n - 1))
                    nc.gpsimd.tensor_tensor(qd[:, n % 2], rq[:, :, n * P:(n + 1) * P], t["ret_qdecay"][:], ALU.mult)\
                      .then_inc(*r_qd.one)
                for lv in range(LEVELS):
                    pool.wait_ge(*e_ready.after(it, lv + 1))
                    if lv == 0:
                        pool.wait_ge(*pv_done.after(it, 8))
                    if lv >= 2:
                        pool.wait_ge(*g_scores.after(it, 4 * (lv - 1)))
                    nc.gpsimd.tensor_tensor(lq[:, lv % 2], gq[:], zed[:, lv % 2], ALU.mult)
                    nc.gpsimd.tensor_tensor(lk[:, lv % 2], gk[:], zed[:, lv % 2], ALU.mult).then_inc(*lev_ready.one)
                pool.wait_ge(*eb_ready.after(it, 2))
                nc.gpsimd.tensor_tensor(qe, gq[:], eb, ALU.mult).then_inc(*qe_ready.one)
                pool.wait_ge(*e_ready.after(it, LEVELS + 1))
                nc.gpsimd.tensor_tensor(khat, gk[:], zed[:, LEVELS % 2], ALU.mult).then_inc(*kh_ready.one)
                with pool.Fori(OUT1 // 2 + 1, CH1 // 2 + 1) as i:
                    for s in range(2):
                        split_low(it, 2 * i + s, s)

        @block.scalar
        def _(act):
            link = act_order.link

            def split_high(it, c, s, n=D):
                act.wait_ge(raw_in[s].sem, raw_in[s].after(it, 16 * (c // 2 + 1))[1] if isinstance(c, int)
                            else raw_in[s].after(it, c * 8 + (16 - 8 * s))[1])
                nc.scalar.activation(whi[:, s, 0:n], wraw[:, s, 0:n], ACT.Copy).then_inc(*w_hi.one)

            def product(it, c):
                act.wait_ge(*lin_done.after(it, c + 1))

            def square(it, u, src):
                if u not in (0, 1):
                    act.wait_ge(*sq_used.after(it, u - 1))
                nc.scalar.activation(tmp[:, u % 2, :] if len(src.shape) == 2 else
                                     tmp[:, u % 2, :].rearrange("p (a b) -> p a b", b=P), src, ACT.Square)\
                  .then_inc(*sq_ready.one)

            def root(it, n, ps, width):
                if 2 <= n < 5:
                    act.wait_ge(*rstd_ready.after(it, n))
                link(nc.scalar.activation(logs, ps[:], ACT.Ln, scale=1.0 / width, bias=EPS))
                if 2 <= n < 5:
                    act.wait_ge(*mix_ready.after(it, 3 + n))
                nc.scalar.activation(rstd[:], logs, ACT.Exp, scale=-0.5).then_inc(*rstd_ready.one)

            act.sem_inc(lin_free.sem, 2)
            for s in range(2):
                split_high(0, s, s)
            for l, b, it in layers_and_blocks(act, lambda l: act.wait_ge(*layer_ready.after(l, 1))):
                act_order.begin(it)
                act.wait_ge(*x_done.after(it, 0))
                for k in range(KB):
                    square(it, k, x[:, k, rows(b)])
                act.wait_ge(*sq_used.after(it, KB))
                root(it, 0, bank[2], D)
                for k in range(KB):
                    act.wait_ge(*scaled.after(it, k + 1))
                    if k >= 2:
                        act.wait_ge(*h_ready.after(it, k - 1))
                    nc.scalar.activation(tmp[:, 4 + k % 2, :], tmp[:, 2 + k % 2, :], ACT.Identity,
                                         scale=col[:, C_A + k:C_A + k + 1], bias=col[:, C_B + k:C_B + k + 1])\
                      .then_inc(*shifted.one)
                for r in range(ROPE1):
                    product(it, r)
                    if r >= 2:
                        act.wait_ge(*rope_done.after(it, r - 1))
                    nc.scalar.activation(tmp[:, 6 + r % 2, :], bank[r % 2][:], ACT.Copy).then_inc(*rope_raw.one)
                    act.wait_ge(*rope_raw.after(it, r + 1))
                    act.sem_inc(lin_free.sem, 1)
                    split_high(it, r + 2, r % 2)
                product(it, GQ)
                nc.scalar.activation(gq[:], bank[1][:], ACT.Copy, scale=32 ** -0.5).then_inc(*lin_free.one)
                act.wait_ge(*ga_in.after(it, 16))
                split_high(it, AV, 1, D + KB * GATE_RANK)
                product(it, GK)
                nc.scalar.activation(gk[:], bank[0][:], ACT.Copy).then_inc(*lin_free.one)
                split_high(it, GK + 2, 0)
                product(it, AV)
                act.wait_ge(*carried.after(it, 1))
                nc.scalar.activation(ga[:], bank[4][0:GATE_RANK, :], ACT.Copy).then_inc(*ga_ready.one)
                nc.scalar.activation(av[:, 1:, :].rearrange("p t n -> p (t n)"), bank[1][:], ACT.Copy)\
                  .then_inc(*lin_free.one)
                split_high(it, AV + 2, 1)
                for c in range(RV, GATE1):
                    product(it, c)
                    dst = (rv if c < GV else gv)[:, :, (c % 2) * P:(c % 2 + 1) * P]
                    nc.scalar.activation(dst, bank[c % 2][:].rearrange("p (t n) -> p t n", n=P), ACT.Copy)\
                      .then_inc(*lin_free.one)
                    split_high(it, c + 2, c % 2)
                act.wait_ge(*logit_done.after(it, 1))
                link(nc.scalar.activation(zed[:, 0, :], bank[5][:], ACT.Identity, bias=col[:, C_GB:C_GB + 1]))
                link(nc.scalar.activation(zed[:, 1, :], zed[:, 0, :], ACT.Abs))
                link(nc.scalar.activation(zed[:, 1, :], zed[:, 1, :], ACT.Exp, scale=-1.0))
                nc.scalar.activation(zed[:, 1, :], zed[:, 1, :], ACT.Ln, bias=1.0).then_inc(*sig_ready.one)
                with act.Fori(0, (OUT1 - GATE1) // 2) as i:
                    for s in range(2):
                        product(it, 2 * i + (GATE1 + s))
                        nc.scalar.activation(gate_y[:, bass.ds(2 * i + s, 1), :].rearrange("p o n -> p (o n)"),
                                             bank[s][:], ACT.Silu).then_inc(*lin_free.one)
                        split_high(it, 2 * i + (GATE1 + s + 2), s)
                for j in range(10):
                    if j < 8:
                        act.wait_ge(*nm_ready.after(it, j + 1))
                        if j >= 2:
                            act.wait_ge(*pt_done.after(it, j - 1))
                        for g in range(4):
                            nc.scalar.activation(probs[j % 2][:, g, :], score(j)[:, g, :], ACT.Exp, scale=ATT_SCALE,
                                                 bias=nmax[:, j % 2, g:g + 1], accum_out=esum[:, j % 2, g:g + 1])
                        nc.scalar.activation(esink[:, j % 2, :], sink_arg[:, j % 2, :], ACT.Exp).then_inc(*exp_done.one)
                    if j >= 2:
                        s = j - 2
                        act.wait_ge(*pt_done.after(it, s + 1))
                        if s >= 2:
                            act.wait_ge(*pv_done.after(it, s - 1))
                        nc.scalar.activation(probsT[s % 2][:, 0, :], bankT[:, 0, :], ACT.Copy).then_inc(*pt_evac_a.one)
                act.wait_ge(*ao_done.after(it, NT))
                for j in range(4):
                    nc.scalar.activation(h_hi[:, j, :], aq[:, j, :], ACT.Copy).then_inc(*mix_hi.one)
                for n in range(NT):
                    act.wait_ge(*r_out.after(it, n + 1))
                    nc.scalar.activation(rq[:, :, n * P:(n + 1) * P],
                                         bank[n % 2][:, 0:256].rearrange("p (c n) -> p c n", n=P), ACT.Copy)\
                      .then_inc(*r_evac.one)
                act.wait_ge(*bsum_ready.after(it, 1))
                act.wait_ge(*pt_done.after(it, 8))
                nc.scalar.activation(eb, bsum[:], ACT.Exp).then_inc(*eb_ready.one)
                nc.scalar.activation(elast[:], bsum[:, P - 1::P], ACT.Exp).then_inc(*eb_ready.one)
                for lv in range(LEVELS + 1):
                    act.wait_ge(*z_ready.after(it, lv + 1))
                    link(nc.scalar.activation(zed[:, lv % 2], zed[:, lv % 2], ACT.Abs))
                    nc.scalar.activation(zed[:, lv % 2], zed[:, lv % 2], ACT.Exp, scale=-1.0).then_inc(*e_ready.one)
                for n in range(NT + 1):
                    if n < NT:
                        act.wait_ge(*kh_done.after(it, n + 1))
                        if n >= 2:
                            act.wait_ge(*g_out.after(it, n - 1))
                        nc.scalar.activation(khT[:, n % 2, :], bankT[:, n % 2, 0:P], ACT.Copy).then_inc(*kh_evac.one)
                    if n:
                        act.wait_ge(*g_out.after(it, n))
                        nc.scalar.activation(gv[:, n - 1, :], bank[(n - 1) % 2][:, 0:256], ACT.Copy)\
                          .then_inc(*g_evac.one)
                act.wait_ge(*r_evac.after(it, NT))
                act.wait_ge(*g_evac.after(it, NT))
                for j in range(4):
                    square(it, KB + j, mixed(j))
                for j in range(4):
                    act.wait_ge(*sq_used.after(it, KB + j + 1))
                    root(it, 1 + j, bankS[j], 64)
                with act.Fori(0, KB // 2) as i:
                    for s in range(2):
                        product(it, 2 * i + (OUT1 + s))
                        act.wait_ge(*sq_used.after(it, 2 * i + (KB + 4 + s - 1)))
                        nc.scalar.activation(tmp[:, s, :], bank[s][:], ACT.Square).then_inc(*sq_ready.one)
                        nc.scalar.activation(gate_y[:, bass.ds(2 * i + s, 1), :].rearrange("p o n -> p (o n)"),
                                             bank[s][:], ACT.Copy).then_inc(*lin_free.one)
                        split_high(it, 2 * i + (OUT1 + s + 2), s)
                act.wait_ge(*sq_used.after(it, 2 * KB + 4))
                root(it, 5, bank[2], D)
                act_order.end()

        @block.vector
        def _(dve):
            link = dve_order.link

            def layer_start(l):
                nc.vector.tensor_copy(col[:], cols1[:, bass.ds(l, 1), :].rearrange("p o n -> p (o n)"))
                nc.vector.tensor_copy(gw[:], t["gate_w"][:, bass.ds(l, 1), :].rearrange("p o n -> p (o n)"))
                for state in (ak[:], av[:], rstate[:], gstate[:]):
                    last = nc.vector.memset(state, 0.0)
                last.then_inc(*layer_ready.one)
                dve.wait_ge(*layer_ready.after(l, 1))
                dve.sem_inc(wait_seat, 1)

            def inverse_root(it, n):
                dve.wait_ge(*rstd_ready.after(it, n + 1))

            dve.sem_inc(x_done.sem, 1)
            for l, b, it in layers_and_blocks(dve, layer_start):
                dve_order.begin(it)
                link(nc.vector.tensor_copy(ak[:, 0:P], ak[:, W:W + P]))
                nc.vector.tensor_copy(av[:, 0, :], av[:, NT, :]).then_inc(*carried.one)
                inverse_root(it, 0)
                for k in range(KB + 1):
                    if k < KB:
                        if k >= 2:
                            dve.wait_ge(*shifted.after(it, k - 1))
                        nc.vector.tensor_tensor(tmp[:, 2 + k % 2, :], x[:, k, rows(b)], rstd[:], ALU.mult)\
                          .then_inc(*scaled.one)
                    if k:
                        n = k - 1
                        dve.wait_ge(*shifted.after(it, k))
                        link(nc.vector.tensor_copy(h_hi[:, n, :], tmp[:, 4 + n % 2, :]))
                        nc.vector.tensor_tensor(h_lo[:, n, :], tmp[:, 4 + n % 2, :], h_hi[:, n, :].bitcast(F32),
                                                ALU.subtract).then_inc(*h_ready.one)
                for r in range(ROPE1):
                    table = 0 if r < 5 else 2
                    out = aq[:, r, :] if r < 4 else ak[:, P:] if r == 4 else rq[:, r - 5, :] if r < 7 else rk[:, r - 7, :]
                    dve.wait_ge(*rope_raw.after(it, r + 1))
                    if r == 0:
                        dve.wait_ge(*h_ready.after(it, KB))
                    nc.vector.tensor_tensor(tmp[:, 2 + r % 2, :], tmp[:, 6 + r % 2, :], rope1[:, table, rows(b)],
                                            ALU.mult)
                    dve.wait_ge(*rope_mm.after(it, r + 1))
                    link(nc.vector.tensor_tensor(tmp[:, 4 + r % 2, :], bankS[r % 2][:], rope1[:, table + 1, rows(b)],
                                                 ALU.mult))
                    nc.vector.tensor_tensor(out, tmp[:, 2 + r % 2, :], tmp[:, 4 + r % 2, :], ALU.add)\
                      .then_inc(*rope_done.one)
                dve.wait_ge(*sig_ready.after(it, 1))
                link(nc.vector.tensor_scalar(zed[:, 0, :], zed[:, 0, :], 0.0, 1 / 16, ALU.min, ALU.mult))
                link(nc.vector.scalar_tensor_tensor(zed[:, 0, :], zed[:, 1, :], -1 / 16, zed[:, 0, :], ALU.mult, ALU.add))
                for n in range(NT):
                    part = slice(n * P, (n + 1) * P)
                    last = nc.vector.tensor_tensor_scan(bsum[:, part], t["ones"][:], zed[:, 0, part], 0.0,
                                                        ALU.mult, ALU.add)
                last.then_inc(*bsum_ready.one)
                dve.wait_ge(*bsum_ready.after(it, 1))
                for j in range(13):
                    if j < 8:
                        neg_sink = col[:, C_SINK + 4 * (j % 2):C_SINK + 4 * (j % 2) + 4]
                        dve.wait_ge(*s_ready.after(it, j + 1))
                        link(nc.vector.reduce_max(mx[:, j % 2, :], score(j), AX_X))
                        if j >= 2:
                            dve.wait_ge(*exp_done.after(it, j - 1))
                        link(nc.vector.scalar_tensor_tensor(nmax[:, j % 2, :], mx[:, j % 2, :], -ATT_SCALE, neg_sink,
                                                            ALU.mult, ALU.min))
                        nc.vector.tensor_tensor(sink_arg[:, j % 2, :], nmax[:, j % 2, :], neg_sink, ALU.subtract)\
                          .then_inc(*nm_ready.one)
                    if 1 <= j < 9:
                        s = j - 1
                        dve.wait_ge(*exp_done.after(it, s + 1))
                        link(nc.vector.tensor_tensor(esum[:, s % 2, :], esum[:, s % 2, :], esink[:, s % 2, :], ALU.add))
                        if s >= 2:
                            dve.wait_ge(*pn_ready.after(it, s - 1))
                        nc.vector.reciprocal(rden[:, s % 2, :], esum[:, s % 2, :]).then_inc(*rden_ready.one)
                    if 2 <= j < 10:
                        s = j - 2
                        dve.wait_ge(*pt_done.after(it, s + 1))
                        if s >= 2:
                            dve.wait_ge(*pv_done.after(it, s - 1))
                        nc.vector.tensor_copy(probsT[s % 2][:, 1, :], bankT[:, 1, :]).then_inc(*pt_evac_d.one)
                    if j >= 5 and j % 2:
                        n = (j - 5) // 2
                        part = slice(n * P, (n + 1) * P)
                        dve.wait_ge(*pv_done.after(it, 2 * n + 2))
                        nc.vector.tensor_tensor(aq[:, :, part], bank[n % 2][:].rearrange("p (g n) -> p g n", n=P),
                                                gate_y[:, 0:4, part], ALU.mult).then_inc(*ao_done.one)
                for j in range(4):
                    dve.wait_ge(*mix_hi.after(it, j + 1))
                    nc.vector.tensor_tensor(h_lo[:, j, :], aq[:, j, :], h_hi[:, j, :].bitcast(F32), ALU.subtract)\
                      .then_inc(*mix_ready.one)
                for n in range(NT + 1):
                    if n < NT:
                        dve.wait_ge(*r_scores.after(it, n + 1))
                        if n >= 2:
                            dve.wait_ge(*r_out.after(it, n - 1))
                        def by_parity(v):
                            return v.rearrange("p (c a) i -> p a c i", a=2)
                        nc.vector.tensor_tensor(by_parity(scm[:, n % 2]),
                                                scores[0][:].rearrange("p (a c i) -> p a c i", a=2, i=P)[:, :, 0:2, :],
                                                by_parity(t["ret_mask"][:]), ALU.mult)
                        nc.vector.tensor_tensor(kd[:, n % 2], bankS[2 + n % 2][:, 0:256], t["ret_kdecay"][:], ALU.mult)\
                          .then_inc(*r_kd.one)
                    if n:
                        dve.wait_ge(*r_out.after(it, n))
                        link(nc.vector.tensor_tensor(rnew[:], bankT[:, (n - 1) % 2, 0:256].rearrange("p (c v) -> p c v", c=2),
                                                     t["ones64"][:].rearrange("p (o v) -> p o v", o=1)
                                                     .to_broadcast([P, 2, P]), ALU.mult))
                        for c in range(2):
                            last = nc.vector.scalar_tensor_tensor(rstate[:, c, :], rstate[:, c, :],
                                                                  t["ret_cdecay"][:, c:c + 1], rnew[:, c, :],
                                                                  ALU.mult, ALU.add)
                        last.then_inc(*r_state.one)
                        dve.wait_ge(*r_state.after(it, n))
                def z_of(lv):
                    if lv >= 2:
                        dve.wait_ge(*lev_ready.after(it, lv - 1))
                    s = P >> (lv + 1)
                    if lv < LEVELS:
                        pairs = bsum[:].rearrange("p (n s) -> p n s", s=2 * s)
                        ref, n_ref, width = pairs[:, :, s - 1:s], W // (2 * s), 2 * s
                    else:
                        pairs = bsum[:].rearrange("p (n s) -> p n s", s=P)
                        ref, n_ref, width = pairs[:, :, P - 1:P], NT, P
                    nc.vector.tensor_tensor(zed[:, lv % 2].rearrange("p (n s) -> p n s", s=width), pairs,
                                            ref.to_broadcast([P, n_ref, width]), ALU.subtract).then_inc(*z_ready.one)

                z_of(0)
                z_of(1)
                for lv in range(LEVELS + 1):
                    if lv + 2 <= LEVELS:
                        z_of(lv + 2)
                    for h in range(4):
                        dve.wait_ge(*g_scores.after(it, 4 * lv + h + 1))
                        mask = t["gla_mask"][:, lv:lv + 1, :].to_broadcast([P, NT, P])
                        level = bankS[h][:].rearrange("p (n i) -> p n i", i=P)
                        dve.sem_inc(wait_seat, 1)
                        if lv == 0:
                            pick = nc.vector.tensor_tensor(gsc[:, :, h, :], level, mask, ALU.mult)
                        else:
                            pick = nc.vector.copy_predicated(gsc[:, :, h, :], mask, level)
                        pick.then_inc(*g_picked.one)
                for n in range(NT):
                    dve.wait_ge(*g_out.after(it, n + 1))
                    if n == 0:
                        dve.wait_ge(*eb_ready.after(it, 2))
                    link(nc.vector.tensor_tensor(gnew, bankS[n % 2][:, 0:256], t["gla_heads"][:], ALU.mult))
                    nc.vector.scalar_tensor_tensor(gstate[:], gstate[:], elast[:, n:n + 1], gnew, ALU.mult, ALU.add)\
                      .then_inc(*g_state.one)
                    dve.wait_ge(*g_state.after(it, n + 1))
                for j in range(4):
                    src = mixed(j)
                    view = (lambda v: v) if j < 2 else (lambda v: v.rearrange("p (t k) -> p t k", k=P))
                    gain = C_ONE if j < 2 else C_GN
                    inverse_root(it, 1 + j)
                    link(nc.vector.tensor_tensor(view(tmp[:, 2 + j % 2, :]), src, view(rstd[:]), ALU.mult))
                    link(nc.vector.scalar_tensor_tensor(tmp[:, 4 + j % 2, :], tmp[:, 2 + j % 2, :],
                                                        col[:, gain:gain + 1], gate_y[:, 4 + j, :], ALU.mult, ALU.mult))
                    link(nc.vector.tensor_copy(h_hi[:, 4 + j, :], tmp[:, 4 + j % 2, :]))
                    nc.vector.tensor_tensor(h_lo[:, 4 + j, :], tmp[:, 4 + j % 2, :], h_hi[:, 4 + j, :].bitcast(F32),
                                            ALU.subtract).then_inc(*mix_ready.one)
                inverse_root(it, 5)
                dve.wait_ge(*lin_free.after(it, CH1 + 2))
                for k in range(KB):
                    link(nc.vector.tensor_tensor(tmp[:, 2 + k % 2, :], gate_y[:, k, :], rstd[:], ALU.mult))
                    nc.vector.scalar_tensor_tensor(x[:, k, rows(b)], tmp[:, 2 + k % 2, :], col[:, C_G + k:C_G + k + 1],
                                                   x[:, k, rows(b)], ALU.mult, ALU.add).then_inc(*x_done.one)
                dve.wait_ge(*x_done.after(it, KB))
                dve_order.end()

        @block.tensor
        def _(pe):
            def ready(it, c):
                pe.wait_ge(*w_split.after(it, c + 1))
                pe.wait_ge(*lin_free.after(it, c + 1))

            def sum_squares(it, u, ps, start, stop, weights=t["ones"]):
                pe.wait_ge(*sq_ready.after(it, u + 1))
                return nc.tensor.matmul(ps[:], weights[:], tmp[:, (u if isinstance(u, int) else u[1]) % 2, :],
                                        start=start, stop=stop)

            def chunk(it, c, s):
                ready(it, c)
                lin_product(pe, bank[s][:], s).then_inc(*lin_done.one)

            def rotate(it, r, s):
                pe.wait_ge(*rope_raw.after(it, r + 1))
                if not isinstance(r, int) or r >= 2:
                    pe.wait_ge(*rope_done.after(it, r - 1))
                nc.tensor.matmul(bankS[s][:], t["rot1"][:], tmp[:, 6 + s, :], start=True, stop=True)\
                  .then_inc(*rope_mm.one)

            def layer_start(l):
                pe.wait_ge(*layer_ready.after(l, 1))
                pe.sem_inc(wait_seat, 1)

            for l, b, it in layers_and_blocks(pe, layer_start):
                for k in range(KB):
                    sum_squares(it, k, bank[2], k == 0, k == KB - 1).then_inc(*sq_used.one)
                pe.wait_ge(*h_ready.after(it, KB))
                chunk(it, 0, 0)
                chunk(it, 1, 1)
                rotate(it, 0, 0)
                with pe.Fori(1, 5) as i:
                    chunk(it, 2 * i, 0)
                    rotate(it, 2 * i - 1, 1)
                    chunk(it, 2 * i + 1, 1)
                    rotate(it, 2 * i, 0)
                chunk(it, GK, 0)
                ready(it, AV)
                for k in range(KB):
                    gate_cols = slice(D + k * GATE_RANK, D + (k + 1) * GATE_RANK)
                    for n, (w, h) in enumerate(((whi, h_hi), (whi, h_lo), (wlo, h_hi))):
                        nc.tensor.matmul(bank[4][0:GATE_RANK, :], w[:, 1, gate_cols], h[:, k, :],
                                         start=(k == 0 and n == 0), stop=(k == KB - 1 and n == 2))
                token_product(1, 1).then_inc(*lin_done.one)
                for c in range(RV, GATE1):
                    ready(it, c)
                    token_product(c % 2, c % 2).then_inc(*lin_done.one)
                    if c == RV:
                        pe.wait_ge(*ga_ready.after(it, 1))
                        nc.tensor.matmul(bank[5][:], gw[:], ga[:], start=True, stop=True).then_inc(*logit_done.one)
                with pe.Fori(GATE1 // 2, OUT1 // 2) as i:
                    for s in range(2):
                        chunk(it, 2 * i + s, s)
                pe.wait_ge(*rope_done.after(it, ROPE1))
                pe.wait_ge(*lin_free.after(it, OUT1 + 2))
                pe.wait_ge(*sig_ready.after(it, 1))
                for j in range(11):
                    if j < 8:
                        n, kv = j // 2, j % 2
                        half = slice(64 * kv, 64 * kv + 64)
                        if j >= 2:
                            pe.wait_ge(*exp_done.after(it, j - 1))
                        mask = mask1[:, bass.ds(b, 1), :].rearrange("p o n -> p (o n)") if n == 0 else mask1[:, 1, :]
                        for g in range(4):
                            nc.tensor.matmul(score(j)[:, g, :], aq[half, g, n * P:(n + 1) * P],
                                             ak[half, n * P:n * P + 2 * P], start=True, stop=False)
                            last = nc.tensor.matmul(score(j)[:, g, :], t["identb"][:], mask, start=False, stop=True)
                        last.then_inc(*s_ready.one)
                    if 2 <= j < 10:
                        s = j - 2
                        pe.wait_ge(*pn_ready.after(it, s + 1))
                        if s:
                            pe.wait_ge(*pt_evac_a.after(it, s))
                            pe.wait_ge(*pt_evac_d.after(it, s))
                        for kb in range(2):
                            for g in range(4):
                                last = nc.tensor.transpose(bankT[:, kb, g * P:(g + 1) * P],
                                                           probs[s % 2][:, g, kb * P:(kb + 1) * P], t["ident"][:])
                        last.then_inc(*pt_done.one)
                    if j >= 3:
                        s = j - 3
                        n, kv = s // 2, s % 2
                        half = slice(64 * kv, 64 * kv + 64)
                        pe.wait_ge(*pt_evac_a.after(it, s + 1))
                        pe.wait_ge(*pt_evac_d.after(it, s + 1))
                        if n >= 2:
                            pe.wait_ge(*ao_done.after(it, n - 1))
                        for kb in range(2):
                            last = nc.tensor.matmul(bank[n % 2][half, :], av[:, n + kb, half], probsT[s % 2][:, kb, :],
                                                    start=(kb == 0), stop=(kb == 1))
                        last.then_inc(*pv_done.one)
                pe.wait_ge(*ao_done.after(it, NT))
                for n in range(NT + 1):
                    if n < NT:
                        part = slice(n * P, (n + 1) * P)
                        if n:
                            pe.wait_ge(*r_kd.after(it, n))
                        for h in range(4):
                            half = slice(64 * (h % 2), 64 * (h % 2) + 64)
                            nc.tensor.matmul(bankS[h % 2][:, h // 2 * P:(h // 2 + 1) * P], rk[half, h // 2, part],
                                             rq[half, h // 2, part], start=True, stop=True)
                        for c in range(2):
                            last = nc.tensor.transpose(bankS[2 + n % 2][:, c * P:(c + 1) * P], rk[:, c, part], t["ident"][:])
                        last.then_inc(*r_scores.one)
                    if n:
                        m = n - 1
                        pe.wait_ge(*r_kd.after(it, m + 1))
                        pe.wait_ge(*r_qd.after(it, m + 1))
                        if m:
                            pe.wait_ge(*r_state.after(it, m))
                        if m >= 2:
                            pe.wait_ge(*r_evac.after(it, m - 1))
                        for c in range(2):
                            both = slice(c * P, (c + 1) * P)
                            nc.tensor.matmul(bankT[:, m % 2, both], kd[:, m % 2, both], rv[:, m, both],
                                             start=True, stop=True)
                        for c in range(2):
                            both = slice(c * P, (c + 1) * P)
                            nc.tensor.matmul(bank[m % 2][:, both], rstate[:, c, :], qd[:, m % 2, c, :],
                                             start=True, stop=False, skip_group_check=True)
                            for h in (2 * c, 2 * c + 1):
                                half = slice(64 * (h % 2), 64 * (h % 2) + 64)
                                last = nc.tensor.matmul(bank[m % 2][half, both], rv[:, m, 64 * h:64 * h + 64],
                                                        scm[:, m % 2, h, :], start=False, stop=(h % 2 == 1),
                                                        skip_group_check=True)
                        last.then_inc(*r_out.one)
                for lv in range(LEVELS + 1):
                    if lv < LEVELS:
                        pe.wait_ge(*lev_ready.after(it, lv + 1))
                    for h in range(4):
                        u = 4 * lv + h
                        dims = slice(32 * h, 32 * h + 32)
                        if lv:
                            pe.wait_ge(*g_picked.after(it, u - 3))
                        for n in range(NT):
                            part = slice(n * P, (n + 1) * P)
                            q = lq[dims, lv % 2, part] if lv < LEVELS else gq[dims, part]
                            k = lk[dims, lv % 2, part] if lv < LEVELS else gk[dims, part]
                            last = nc.tensor.matmul(bankS[h][:, part], k, q, start=True, stop=True)
                        last.then_inc(*g_scores.one)
                pe.wait_ge(*kh_ready.after(it, 1))
                pe.wait_ge(*qe_ready.after(it, 1))
                pe.wait_ge(*r_evac.after(it, NT))
                pe.wait_ge(*r_state.after(it, NT))
                pe.wait_ge(*g_picked.after(it, 4 * (LEVELS + 1)))
                for n in range(NT + 1):
                    if n < NT:
                        if n >= 2:
                            pe.wait_ge(*kh_evac.after(it, n - 1))
                        nc.tensor.transpose(bankT[:, n % 2, 0:P], khat[:, n * P:(n + 1) * P], t["ident"][:])\
                          .then_inc(*kh_done.one)
                    if n:
                        m = n - 1
                        pe.wait_ge(*kh_evac.after(it, m + 1))
                        if m:
                            pe.wait_ge(*g_state.after(it, m))
                        if m >= 2:
                            pe.wait_ge(*g_evac.after(it, m - 1))
                        nc.tensor.matmul(bankS[m % 2][:, 0:256], khT[:, m % 2, :], gv[:, m, :], start=True, stop=True)
                        for c in range(2):
                            both = slice(c * P, (c + 1) * P)
                            nc.tensor.matmul(bank[m % 2][:, both], gstate[:, both], qe[:, m * P:(m + 1) * P],
                                             start=True, stop=False, skip_group_check=True)
                            for h in (2 * c, 2 * c + 1):
                                half = slice(64 * (h % 2), 64 * (h % 2) + 64)
                                last = nc.tensor.matmul(bank[m % 2][half, both], gv[:, m, 64 * h:64 * h + 64],
                                                        gsc[:, m, h, :], start=False, stop=(h % 2 == 1),
                                                        skip_group_check=True)
                        last.then_inc(*g_out.one)
                pe.wait_ge(*g_state.after(it, NT))
                pe.wait_ge(*g_evac.after(it, NT))
                for j in range(4):
                    sum_squares(it, KB + j, bankS[j], True, True, t["ones64"]).then_inc(*sq_used.one)
                pe.wait_ge(*rstd_ready.after(it, 5))
                pe.wait_ge(*mix_ready.after(it, KB))
                base = KB + 4
                chunk(it, OUT1, 0)
                chunk(it, OUT1 + 1, 1)
                sum_squares(it, base, bank[2], True, False).then_inc(*sq_used.one)
                with pe.Fori(1, KB // 2) as i:
                    chunk(it, 2 * i + OUT1, 0)
                    pe.wait_ge(*sq_ready.after(it, 2 * i + base))
                    nc.tensor.matmul(bank[2][:], t["ones"][:], tmp[:, 1, :], start=False, stop=False).then_inc(*sq_used.one)
                    chunk(it, 2 * i + (OUT1 + 1), 1)
                    pe.wait_ge(*sq_ready.after(it, 2 * i + (base + 1)))
                    nc.tensor.matmul(bank[2][:], t["ones"][:], tmp[:, 0, :], start=False, stop=False).then_inc(*sq_used.one)
                sum_squares(it, base + KB - 1, bank[2], False, True).then_inc(*sq_used.one)


class Chain:

    def __init__(self, eng, sem):
        self.eng, self.sem, self.base, self.n = eng, sem, 0, 0
        self.reg, self.per, self.trips = 0, 0, 1

    def enter(self, reg, trips, per):
        self.base, self.n = self.base + self.n, 0
        self.reg, self.per, self.trips = reg, per, trips

    def leave(self):
        assert self.n == self.per, (self.n, self.per)
        self.base, self.n = self.base + self.per * self.trips, 0
        self.reg, self.per, self.trips = 0, 0, 1

    def link(self, ins):
        self.n += 1
        ins.then_inc(self.sem, 1)
        value = self.base + self.n
        self.eng.wait_ge(self.sem, value if isinstance(self.reg, int) else self.reg * self.per + value)


class Rows:

    def __init__(self, l, b, context=False):
        self.l, self.b, self.context = l, b, context
        self.w = CTX if context else W
        self.tiles = self.w // P
        self.it = 3 * l + 2 if context else b + 3 * l
        self.latent_it = b + NB * l
        self.v = 1 if context else 0
        self.cols = slice(SEQ, TOKENS) if context else bass.ds(b * W, W)

    def chunk(self, base, per):
        return base + NB * per if self.context else self.b * per + base


S1_AT, DFT_AT, WO_AT, FF_AT = [], [], [], []
_at = 0
for _l in range(DEPTH):
    _n = NB + 1 if _l == 0 else NB
    S1_AT.append(_at)
    _at += NB * IN2 + (IN2 if _l == 0 else 2)
    DFT_AT.append(_at)
    _at += DFT
    WO_AT.append(_at)
    _at += _n * KB
    FF_AT.append(_at)
    _at += _n * FF2
CHUNKS2 = _at


def second_block(nc, t, a, sems, out):
    sem = sems
    with ExitStack() as ctx:
        def sb(name, shape, dt=F32):
            return ctx.enter_context(nc.sbuf_tensor(name, shape, dt))

        x, wraw, whi, wlo, cols2 = t["x"], t["wraw"], t["whi"], t["wlo"], t["cols2"]
        xc = sb("xc", [P, KB, CTX])
        h_hi, h_lo = sb("h2_hi", [P, KB, W], F32R), sb("h2_lo", [P, KB, W], F32R)
        y, tmp, rstd = sb("y", [P, KB, W]), sb("tmp2", [P, 8, W]), sb("rstd2", [P, W])
        kz, kcz = sb("kz", [P, 2, SEQ + 2 * P]), sb("kcz", [P, 2, CTX])
        vx, vc = sb("vx", [P, SEQ // P + 2, P]), sb("vc", [P, CTX // P, P])
        qt = sb("qt", [P, 4, P])
        stats = [sb(n, [P, TOKENS // P, 8]) for n in ("nmax2", "esum2", "sink_arg2", "esink2", "rden2")]
        nmax, esum, sink_arg, esink, rden = stats
        mx = sb("mx2", [P, 2])
        ms = sb("ms", [P, 16])
        rot, mask, dims = sb("rot", [P, P]), sb("mask_band", [P, 3, 3 * P], BF16), sb("dims", [P, 256])
        w_s, b_s = sb("w_s", [P, DEPTH, 4, P]), sb("b_s", [P, DEPTH, 2, P])
        g_s, g_m, neg_sink = sb("g_s", [P, DEPTH, 2]), sb("g_m", [P, DEPTH, KB]), sb("neg_sink", [P, DEPTH, 8])
        with ExitStack() as mixers:
            q, u, f = (mixers.enter_context(nc.sbuf_tensor(n, [P, c, TOKENS], F32))
                       for n, c in (("q", 4), ("u", 2), ("f", 2)))
        a_hi, a_lo = sb("a_hi", [P, FF_CH, W], F32R), sb("a_lo", [P, FF_CH, W], F32R)
        table, gvn = y[:, 0:2, :], y[:, 2:4, :].rearrange("p a (n c) -> p (a n) c", c=256)
        dft_ctx = y[:, 4:6, :].rearrange("p a (k n) -> p a k n", k=2)
        y_flat = y[:].rearrange("p a n -> p (a n)")
        KEYS = 3 * P + CTX
        probs = [y_flat[:, KEYS * n:KEYS * (n + 1)] for n in range(2)]
        probsT = [y_flat[:, KEYS * (2 + n):KEYS * (3 + n)] for n in range(2)]
        o_tile = y_flat[:, 4 * KEYS:4 * KEYS + 512]
        mix_rstd = [y[:, 5 + n, :] for n in range(3)]
        mask_f = tmp[:, 0:3, 0:3 * P]

        lin0, lin1 = (ctx.enter_context(nc.psum_tensor(f"lin2_{n}", [P, 512], F32)) for n in range(2))
        scores = [ctx.enter_context(nc.psum_tensor(f"scores2_{n}", [P, 1024], F32)) for n in range(2)]
        bank = [lin0[:], lin1[:]] + [s[:, 512 * n:512 * n + 512] for s in scores for n in range(2)]
        bankT = ctx.enter_context(nc.psum_tensor("bankT2", [P, 1024], F32))

        def residual(p, k):
            return xc[:, k, :] if p.context else x[:, k, p.cols]

        def mixed(p, j):
            return (q[:, j, p.cols] if j < 4 else u[:, j - 4, p.cols] if j < 6 else f[:, j - 6, p.cols])

        def column(p, at):
            return cols2[:, p.l, p.v, at:at + 1]

        before = DEPTH * NB * CH1
        chunk_in = [Sig(t["raw_in"][s].sem, 8, before // 2 * 16 + 16 - 8 * s) for s in range(2)]
        w_hi, w_split = (Sig(t[n].sem, 1, before) for n in ("w_hi", "w_split"))
        lin_done, lin_free = (Sig(t[n].sem, 1, before) for n in ("lin_done", "lin_free"))
        EVACUATED = 3

        def sig(name, per, start=0):
            return Sig(sem("c_" + name), per, start)

        consts_in, consts_ready, table_in = sig("consts_in", 0), sig("consts_ready", 0), sig("table_in", 16)
        norms = {n: {s: sig(f"{n}_{s}", per) for s, per in
                     (("sq", 8 + m), ("sq_used", 8 + m), ("rstd", r), ("scaled", 8), ("hi", 8), ("ready", 8))}
                 for n, m, r in (("s1", 0, 1), ("wo", 8, 4), ("ff", 8, 2))}
        rope_mm, rope_done = sig("rope_mm", 5), sig("rope_done", 5, 1)
        gv_ms, gv_rs, gv_ready = sig("gv_ms", 1), sig("gv_rs", 1), sig("gv_ready", 1)
        sgu_mm, sgu_done = sig("sgu_mm", 1), sig("sgu_done", 1, 1)
        NDIM = [TOKENS // P, SEQ // P]
        dim_mm, dim_hi, dim_ready = sig("dim_mm", TOKENS // P), sig("dim_hi", TOKENS // P), sig("dim_ready", SEQ // P)
        ctx_dft, ctx_dft_done = sig("ctx_dft", 0), sig("ctx_dft_done", 0)
        s_ready, nm_ready, exp_done = sig("s_ready", 8), sig("nm_ready", 8), sig("exp_done", 8)
        pt_done, pt_evac_a, pt_evac_d, pv_done = (sig(n, 8) for n in ("pt_done", "pt_evac_a", "pt_evac_d", "pv_done"))
        qt_ready = sig("qt_ready", 4)
        sink_ready, esink_ready = sig("sink_ready", 1), sig("esink_ready", 1)
        o_done, ot_done, attn_done = sig("o_done", 1), sig("ot_done", 1), sig("attn_done", 1)
        wo_done, ff_done = sig("wo_done", 8, 1), sig("ff_done", 8, 1)
        a_sq = sig("a_sq", FF_CH)
        a_hi_ready, a_ready = sig("a_hi_ready", FF_CH), sig("a_ready", FF_CH, 2)
        saved = sig("saved", 0)
        wait_seat = sem("c_wait_seat")
        dve_chain, act_chain = Chain(nc.vector, sem("c_dve_chain")), Chain(nc.scalar, sem("c_act_chain"))
        block = ctx.enter_context(nc.Block())

        def passes(eng, l, kv_pass=False, chain=None, per=0):
            with eng.Fori(0, NB) as b:
                if chain:
                    chain.enter(b, NB, per)
                yield Rows(l, b)
            if chain:
                chain.leave()
            if l == 0 or kv_pass:
                yield Rows(l, 0, context=True)

        def attention_tiles(eng, l, body, chain=None, per=0):
            n = SEQ // P
            base = l * (TOKENS // P)
            body(0, base, 0, True, False)
            with eng.Fori(1, n - 1) as i:
                if chain:
                    chain.enter(i - 1, n - 2, per)
                body(i, i + base, 1, False, False)
            if chain:
                chain.leave()
            body(n - 1, base + n - 1, 2, False, True)
            if l == 0:
                body(n, base + n, None, True, False)
                body(n + 1, base + n + 1, None, False, True)

        def keys_of(mask_no):
            return (slice(P, 4 * P + CTX), 5) if mask_no is not None else (slice(4 * P, 4 * P + CTX), 2)

        def starts(no):
            return isinstance(no, int) and no == 0

        def lagging(tile, no, j, lag, first):
            if j >= lag:
                return tile, no, j - lag
            return None if first else (tile - 1, no - 1, j - lag + 8)

        def of_tile(v, tile):
            return v[:, tile, :] if isinstance(tile, int) else v[:, bass.ds(tile, 1), :].rearrange("p o h -> p (o h)")

        def of_head(v, tile, j):
            return v[:, tile, j:j + 1] if isinstance(tile, int) else v[:, bass.ds(tile, 1), j:j + 1].rearrange("p o h -> p (o h)")

        def token_cols(tile):
            return slice(tile * P, (tile + 1) * P) if isinstance(tile, int) else bass.ds(tile * P, P)

        @block.sync
        def _(sp):
            def load(g, s, src):
                sp.wait_ge(*w_split.after(g, -1))
                sp.dma_start(wraw[:, s, 0:D], src).then_inc(chunk_in[s].sem, 16)

            def run(g, l, at, n, skip=0):
                with sp.Fori(skip // 2, n // 2) as i:
                    for s in range(2):
                        load(2 * i + (g + s), s, a["w2"][l, bass.ds(2 * i + (at + s), 1)].rearrange("o p n -> p (o n)"))

            for l in range(DEPTH):
                blocks = NB + 1 if l == 0 else NB
                for b in range(blocks):
                    run(S1_AT[l] + b * IN2, l, 0, IN2, 2 if l == b == 0 else 0)
                if l:
                    for s, c in enumerate((K2, V2)):
                        load(S1_AT[l] + NB * IN2 + s, s, a["w2"][l, c])
                with sp.Fori(0, DFT // 2) as i:
                    for s in range(2):
                        load(2 * i + (DFT_AT[l] + s), s, a["dft_tokens"][bass.ds(2 * i + s, 1)].rearrange("o p n -> p (o n)"))
                for b in range(blocks):
                    run(WO_AT[l] + b * KB, l, IN2, KB)
                for b in range(blocks):
                    run(FF_AT[l] + b * FF2, l, IN2 + KB, FF2)
            for s in range(2):
                load(CHUNKS2 + s, s, a["w2"][0, s])
            sp.wait_ge(*ff_done.after(3 * DEPTH - 1, 0))
            sp.dma_start(out, x[:]).then_inc(saved.sem, 16)
            sp.wait_ge(saved.sem, 16)

        @block.gpsimd
        def _(pool):
            def split_low(g, s):
                pool.wait_ge(*w_hi.after(g, 1))
                nc.gpsimd.tensor_tensor(wlo[:, s, 0:D], wraw[:, s, 0:D], whi[:, s, 0:D].bitcast(F32), ALU.subtract)\
                  .then_inc(*w_split.one)

            def run(g, n):
                with pool.Fori(0, n // 2) as i:
                    for s in range(2):
                        split_low(2 * i + (g + 2 + s), s)

            def query_tile(tile, r):
                cols = slice(tile * P, (tile + 1) * P) if isinstance(tile, int) else bass.ds(tile * P, P)
                nc.gpsimd.tensor_copy(qt[:, r, :], q[:, r, cols]).then_inc(*qt_ready.one)

            for name, dst in (("ctx", xc[:]), ("rot2", rot[:]), ("mask2", mask_f), ("dft_dims", dims[:]),
                              ("dft_ctx", dft_ctx), ("w_sgu", w_s[:]), ("b_sgu", b_s[:]), ("g_sgu", g_s[:]),
                              ("g_mix", g_m[:]), ("sinks2", neg_sink[:])):
                pool.dma_start(dst, a[name]).then_inc(consts_in.sem, 16)
            for l in range(DEPTH):
                run(S1_AT[l], DFT_AT[l] - S1_AT[l])
                run(DFT_AT[l], DFT)

                def tile_queries(tile, no, mask_no, first, last):
                    for r in range(4):
                        if not starts(no):
                            pool.wait_ge(*s_ready.after(no - 1, 2 * r + 2))
                        query_tile(tile, r)

                pool.wait_ge(*lin_free.after(DFT_AT[l], 2))
                pool.wait_ge(*sgu_done.after(3 * l + (3 if l == 0 else 2), 0))
                attention_tiles(pool, l, tile_queries)
                run(WO_AT[l], FF_AT[l] - WO_AT[l])
                run(FF_AT[l], (NB + 1 if l == 0 else NB) * FF2)

        @block.scalar
        def _(act):
            link = act_chain.link

            def split_high(g, s):
                act.wait_ge(*chunk_in[s].after(g, 0))
                nc.scalar.activation(whi[:, s, 0:D], wraw[:, s, 0:D], ACT.Copy).then_inc(*w_hi.one)

            def square(n, p, k, src):
                if k >= 2:
                    act.wait_ge(*n["sq_used"].after(p.it, k - 1))
                nc.scalar.activation(tmp[:, k % 2, 0:p.w], src, ACT.Square).then_inc(*n["sq"].one)

            def root(n, ps, dst, width):
                link(nc.scalar.activation(dst, ps, ACT.Ln, scale=1.0 / width, bias=EPS))
                nc.scalar.activation(dst, dst, ACT.Exp, scale=-0.5).then_inc(*n["rstd"].one)

            def high(n, p, shift=None):
                for k in range(KB):
                    act.wait_ge(*n["scaled"].after(p.it, k + 1))
                    if shift is None:
                        ins = nc.scalar.activation(h_hi[:, k, 0:p.w], tmp[:, 2 + k % 2, 0:p.w], ACT.Copy)
                    else:
                        ins = nc.scalar.activation(h_hi[:, k, 0:p.w], tmp[:, 2 + k % 2, 0:p.w], ACT.Identity,
                                                   bias=column(p, shift + k))
                    ins.then_inc(*n["hi"].one)

            def norm(n, p, shift):
                for k in range(KB):
                    square(n, p, k, residual(p, k))
                act.wait_ge(*n["sq_used"].after(p.it, KB))
                root(n, bank[2][:, 0:p.w], rstd[:, 0:p.w], D)
                high(n, p, shift)

            def evacuate(g, s, dst, src, func=ACT.Copy):
                act.wait_ge(*lin_done.after(g, 1))
                nc.scalar.activation(dst, src, func).then_inc(*lin_free.one)
                split_high(g + 2, s)

            def project(p):
                n = norms["s1"]
                g = p.chunk(S1_AT[p.l], IN2)
                full = not (p.context and p.l)
                act.wait_ge(*ff_done.after(3 * p.l, 0))
                if not p.context:
                    act.wait_ge(*rope_done.after(p.latent_it, 0))
                    act.dma_start(table, a["rope2"][:, :, p.cols]).then_inc(table_in.sem, 16)
                norm(n, p, B1)

                def tokens(s):
                    return bank[s][:, 0:p.w].rearrange("p (t n) -> p t n", n=P)

                if not full:
                    for s, c in enumerate((K2, V2)):
                        context_kv(g + s, s, c)
                    return
                act.wait_ge(*sgu_done.after(p.it, 0))
                for c in range(GV2, GV2 + 2):
                    evacuate(g + c, c % 2, gvn[:, 0:p.tiles, (c - GV2) * P:(c - GV2 + 1) * P], tokens(c % 2),
                             ACT.Gelu_apprx_tanh)
                for c in range(U2, U2 + 2):
                    evacuate(g + c, c % 2, u[:, c - U2, p.cols], bank[c % 2][:, 0:p.w], ACT.Gelu_apprx_tanh)
                for r in range(5):
                    c = Q2 + r
                    if p.context:
                        if r < 4:
                            evacuate(g + c, c % 2, q[:, r, p.cols], bank[c % 2][:, 0:p.w])
                        else:
                            context_kv(g + c, c % 2, K2)
                    else:
                        if r >= 2:
                            act.wait_ge(*rope_done.after(p.latent_it, r - 1))
                        evacuate(g + c, c % 2, tmp[:, 6 + r % 2, :], bank[c % 2][:])
                    if r == 1:
                        act.wait_ge(*gv_ms.after(p.it, 1))
                        part = ms[:, 0:4 * p.tiles]
                        link(nc.scalar.activation(part, part, ACT.Ln, scale=1.0 / 64, bias=EPS))
                        nc.scalar.activation(part, part, ACT.Exp, scale=-0.5).then_inc(*gv_rs.one)
                for c in range(F2, F2 + 2):
                    evacuate(g + c, c % 2, f[:, c - F2, p.cols], bank[c % 2][:, 0:p.w])
                if p.context:
                    context_kv(g + V2, V2 % 2, V2)
                else:
                    evacuate(g + V2, V2 % 2, vx[:, bass.ds(p.b * NT + 1, NT), :], tokens(V2 % 2))

            def context_kv(g, s, c):
                if c == V2:
                    evacuate(g, s, vc[:], bank[s][:, 0:CTX].rearrange("p (t n) -> p t n", n=P))
                    return
                act.wait_ge(*lin_done.after(g, 1))
                link(nc.scalar.activation(kcz[0:64, 0, :], bank[s][0:64, 0:CTX], ACT.Copy))
                evacuate(g, s, kcz[64:P, 1, :], bank[s][64:P, 0:CTX])

            def fourier(l):
                for n in range(NDIM[l]):
                    act.wait_ge(*dim_mm.after(l, n + 1))
                    if n < SEQ // P:
                        nc.scalar.activation(h_hi[:, n, :], bank[2 + n % 4], ACT.Copy).then_inc(*dim_hi.one)
                    else:
                        nc.scalar.activation(tmp[:, n - SEQ // P, :], bank[2 + n % 4], ACT.Copy).then_inc(*dim_hi.one)
                with act.Fori(0, DFT // 2) as i:
                    for s in range(2):
                        g = 2 * i + (DFT_AT[l] + s)
                        act.wait_ge(*lin_done.after(g, 1))
                        split_high(g + 2, s)

            def attend(l):
                def sinks(tile, no):
                    act.wait_ge(*sink_ready.after(no, 1))
                    nc.scalar.activation(of_tile(esink, tile), of_tile(sink_arg, tile), ACT.Exp).then_inc(*esink_ready.one)

                def transposed(tile, no, j, n):
                    act.wait_ge(*pt_done.after(no, j + 1))
                    if j >= 2 or not starts(no):
                        act.wait_ge(*pv_done.after(no, j - 1))
                    rest = n // 2 * P
                    nc.scalar.activation(probsT[j % 2][:, n * P - rest:n * P], bankT[:, 512:512 + rest], ACT.Copy)\
                      .then_inc(*pt_evac_a.one)

                def outputs(tile, no):
                    act.wait_ge(*ot_done.after(no, 1))
                    nc.scalar.activation(q[:, :, token_cols(tile)], lin1[:].rearrange("p (c n) -> p c n", n=P), ACT.Copy)\
                      .then_inc(*attn_done.one)

                def body(tile, no, mask_no, first, last):
                    keys, n = keys_of(mask_no)
                    for j in range(8):
                        if j == 0 and not first:
                            sinks(tile - 1, no - 1)
                        act.wait_ge(*nm_ready.after(no, j + 1))
                        if j >= 2 or not starts(no):
                            act.wait_ge(*pt_done.after(no, j - 1))
                        nc.scalar.activation(probs[j % 2][:, 0:n * P], scores[j % 2][:, keys], ACT.Exp, scale=ATT_SCALE,
                                             bias=of_head(nmax, tile, j), accum_out=of_head(esum, tile, j))\
                          .then_inc(*exp_done.one)
                        step = lagging(tile, no, j, 2, first)
                        if step:
                            transposed(*step, n)
                        if j == 5 and not first:
                            outputs(tile - 1, no - 1)
                    if last:
                        sinks(tile, no)
                        for j in range(6, 8):
                            transposed(tile, no, j, n)
                        outputs(tile, no)

                attention_tiles(act, l, body)

            def merge(p):
                n = norms["wo"]
                act.wait_ge(*attn_done.after((p.l + 1) * (TOKENS // P) - (2 if p.l else 0), 0))
                act.wait_ge(*wo_done.after(p.it, 0))
                for j in range(KB):
                    square(n, p, j, mixed(p, j))
                act.wait_ge(*n["sq_used"].after(p.it, KB))
                for i, width in enumerate((512, 256, 256)):
                    root(n, bank[2 + i][:, 0:p.w], mix_rstd[i][:, 0:p.w], width)
                high(n, p)
                g = p.chunk(WO_AT[p.l], KB)
                act.sem_inc(wait_seat, 1)
                with act.Fori(0, KB // 2) as i:
                    for s in range(2):
                        gi = g + (2 * i + s)
                        act.wait_ge(*lin_done.after(gi, 1))
                        act.wait_ge(*n["sq_used"].after(p.it, 2 * i + (KB + s - 1)))
                        nc.scalar.activation(tmp[:, s, 0:p.w], bank[s][:, 0:p.w], ACT.Square).then_inc(*n["sq"].one)
                        nc.scalar.activation(y[:, bass.ds(2 * i + s, 1), 0:p.w].rearrange("p o n -> p (o n)"),
                                             bank[s][:, 0:p.w], ACT.Copy).then_inc(*lin_free.one)
                        split_high(gi + 2, s)
                act.wait_ge(*n["sq_used"].after(p.it, 2 * KB))
                root(n, bank[2][:, 0:p.w], rstd[:, 0:p.w], D)

            def feed_forward(p):
                n = norms["ff"]
                act.wait_ge(*wo_done.after(3 * (p.l + 1) - (1 if p.l else 0), 0))
                act.wait_ge(*ff_done.after(p.it, 0))
                norm(n, p, B2)

                def group(q_no, last):
                    g = p.chunk(FF_AT[p.l], FF2) + q_no * (2 * FF_CH)
                    grp = p.it * FF_GROUPS + q_no
                    act.wait_ge(*lin_free.after(g, 2))
                    act.sem_inc(wait_seat, 1)
                    with act.Fori(0, FF_CH // 2) as i:
                        for s in range(2):
                            gi = g + (2 * i + s)
                            act.wait_ge(*lin_done.after(gi, 1))
                            act.wait_ge(*a_ready.after(grp, 2 * i + (s - 1)))
                            nc.scalar.activation(tmp[:, 4 + s, 0:p.w], bank[s][:, 0:p.w], ACT.Relu).then_inc(*lin_free.one)
                            split_high(gi + 2, s)
                            act.wait_ge(*lin_free.after(gi, EVACUATED))
                            nc.scalar.activation(a_hi[:, bass.ds(2 * i + s, 1), 0:p.w].rearrange("p o n -> p (o n)"),
                                                 tmp[:, 4 + s, 0:p.w], ACT.Square).then_inc(*a_hi_ready.one)
                    with act.Fori(0, FF_CH // 2) as i:
                        for s in range(2):
                            gi = g + (2 * i + (FF_CH + s))
                            act.wait_ge(*lin_done.after(gi, 1))
                            split_high(gi + 2, s)
                            if last:
                                act.wait_ge(*n["sq_used"].after(p.it, 2 * i + (KB + s - 1)))
                                act.wait_ge(*lin_free.after(gi, EVACUATED))
                                nc.scalar.activation(tmp[:, s, 0:p.w],
                                                     y[:, bass.ds(2 * i + s, 1), 0:p.w].rearrange("p o n -> p (o n)"),
                                                     ACT.Square).then_inc(*n["sq"].one)

                with act.Fori(0, FF_GROUPS - 1) as q_no:
                    group(q_no, False)
                group(FF_GROUPS - 1, True)
                act.wait_ge(*n["sq_used"].after(p.it, 2 * KB))
                root(n, bank[2][:, 0:p.w], rstd[:, 0:p.w], D)

            act.wait_ge(consts_ready.sem, 1)
            for l in range(DEPTH):
                for p in passes(act, l, True, act_chain, 2):
                    project(p)
                fourier(l)
                attend(l)
                for p in passes(act, l, False, act_chain, 4):
                    merge(p)
                for p in passes(act, l, False, act_chain, 2):
                    feed_forward(p)

        @block.vector
        def _(dve):
            link = dve_chain.link

            def split(n, p, src, gain, rs, shift=None):
                for k in range(KB + 1):
                    if k < KB:
                        nc.vector.scalar_tensor_tensor(tmp[:, 2 + k % 2, 0:p.w], src(k), gain(k), rs(k), ALU.mult, ALU.mult)\
                          .then_inc(*n["scaled"].one)
                    if k:
                        j = k - 1
                        dve.wait_ge(*n["hi"].after(p.it, j + 1))
                        if shift:
                            ins = nc.vector.scalar_tensor_tensor(h_lo[:, j, 0:p.w], tmp[:, 2 + j % 2, 0:p.w], shift(j),
                                                                 h_hi[:, j, 0:p.w].bitcast(F32), ALU.add, ALU.subtract)
                        else:
                            ins = nc.vector.tensor_tensor(h_lo[:, j, 0:p.w], tmp[:, 2 + j % 2, 0:p.w],
                                                          h_hi[:, j, 0:p.w].bitcast(F32), ALU.subtract)
                        ins.then_inc(*n["ready"].one)
                        dve.wait_ge(*n["ready"].after(p.it, j + 1))

            def norm(n, p, gain, shift):
                dve.wait_ge(*n["rstd"].after(p.it, 1))
                split(n, p, lambda k: residual(p, k), lambda k: column(p, gain + k), lambda k: rstd[:, 0:p.w],
                      lambda k: column(p, shift + k))

            def add_to_residual(n, p, at, gate, done):
                dve.wait_ge(*n["rstd"].after(p.it, at))
                for k in range(KB):
                    link(nc.vector.tensor_tensor(tmp[:, 2 + k % 2, 0:p.w], y[:, k, 0:p.w], rstd[:, 0:p.w], ALU.mult))
                    nc.vector.scalar_tensor_tensor(residual(p, k), tmp[:, 2 + k % 2, 0:p.w], column(p, gate + k),
                                                   residual(p, k), ALU.mult, ALU.add).then_inc(*done.one)
                dve.wait_ge(*done.after(p.it, KB))

            def project(p):
                norm(norms["s1"], p, A1, B1)
                if p.context and p.l:
                    return
                g = p.chunk(S1_AT[p.l], IN2)
                values = gvn[:, 0:p.tiles, :]
                n_heads = 4 * p.tiles
                by_head = values.rearrange("p t (h d) -> p (t h) d", d=64)
                squares = tmp[:, 0:2, :].rearrange("p a n -> p (a n)")[:, 0:n_heads * 64].rearrange("p (h d) -> p h d", d=64)
                dve.wait_ge(*lin_free.after(g + (GV2 + 1), EVACUATED))
                link(nc.vector.tensor_tensor(squares, by_head, by_head, ALU.mult))
                nc.vector.reduce_sum(ms[:, 0:n_heads], squares, AX_X).then_inc(*gv_ms.one)
                for r in range(5):
                    if r == (0 if p.context else 2):
                        dve.wait_ge(*gv_rs.after(p.it, 1))
                        nc.vector.tensor_tensor(by_head, by_head,
                                                ms[:, 0:n_heads].rearrange("p (h o) -> p h o", o=1).to_broadcast([P, n_heads, 64]),
                                                ALU.mult).then_inc(*gv_ready.one)
                    if p.context:
                        continue
                    if r == 0:
                        dve.wait_ge(*table_in.after(p.latent_it, 16))
                    dve.wait_ge(*lin_free.after(g + (Q2 + r), EVACUATED))
                    nc.vector.tensor_tensor(tmp[:, 2 + r % 2, :], tmp[:, 6 + r % 2, :], table[:, 0, :], ALU.mult)
                    dve.wait_ge(*rope_mm.after(p.latent_it, r + 1))
                    link(nc.vector.tensor_tensor(tmp[:, 4 + r % 2, :], bank[4 + r % 2], table[:, 1, :], ALU.mult))
                    if r < 4:
                        nc.vector.tensor_tensor(q[:, r, p.cols], tmp[:, 2 + r % 2, :], tmp[:, 4 + r % 2, :], ALU.add)\
                          .then_inc(*rope_done.one)
                    else:
                        keys = bass.ds(p.b * W + P, W)
                        link(nc.vector.tensor_tensor(kz[0:64, 0, keys], tmp[0:64, 2, :], tmp[0:64, 4, :], ALU.add))
                        nc.vector.tensor_tensor(kz[64:P, 1, keys], tmp[64:P, 2, :], tmp[64:P, 4, :], ALU.add)\
                          .then_inc(*rope_done.one)
                        dve.wait_ge(*rope_done.after(p.latent_it, 5))
                dve.wait_ge(*sgu_mm.after(p.it, 1))
                sums = scores[0][:].rearrange("p (t c n) -> p c t n", c=2, n=P)
                dve.wait_ge(*lin_free.after(g + (U2 + 1), EVACUATED))
                for c in range(2):
                    gated = tmp[:, 4 + c, 0:p.w].rearrange("p (t n) -> p t n", n=P)
                    link(nc.vector.scalar_tensor_tensor(gated, sums[:, c, 0:p.tiles, :], g_s[:, p.l, c:c + 1],
                                                        b_s[:, p.l, c:c + 1, :].to_broadcast([P, p.tiles, P]),
                                                        ALU.mult, ALU.add))
                    ins = nc.vector.tensor_tensor(u[:, c, p.cols], u[:, c, p.cols], tmp[:, 4 + c, 0:p.w], ALU.mult)
                    if c == 0:
                        link(ins)
                ins.then_inc(*sgu_done.one)
                dve.wait_ge(*sgu_done.after(p.it, 1))

            def fourier(l):
                for n in range(SEQ // P):
                    dve.wait_ge(*dim_hi.after(l, n + 1))
                    nc.vector.tensor_tensor(h_lo[:, n, :], bank[2 + n % 4], h_hi[:, n, :].bitcast(F32), ALU.subtract)\
                      .then_inc(*dim_ready.one)
                with dve.Fori(0, DFT // 4) as i:
                    for s in range(2):
                        g = 4 * i + (DFT_AT[l] + 2 * s)
                        dve.wait_ge(*lin_done.after(g, 2))
                        nc.vector.tensor_copy(f[:, :, bass.ds(i * (2 * P) + s * P, P)],
                                              scores[s][:].rearrange("p (c n) -> p c n", c=2)[:, :, 0:P])\
                          .then_inc(lin_free.sem, 2)
                if l == 0:
                    dve.wait_ge(ctx_dft.sem, 1)
                    nc.vector.tensor_copy(f[:, :, SEQ:], bankT[:].rearrange("p (c n) -> p c n", c=2)[:, :, 0:CTX])\
                      .then_inc(*ctx_dft_done.one)

            def attend(l):
                def maximum(tile, no, j, keys):
                    dve.wait_ge(*s_ready.after(no, j + 1))
                    link(nc.vector.reduce_max(mx[:, j % 2:j % 2 + 1], scores[j % 2][:, keys], AX_X))
                    nc.vector.scalar_tensor_tensor(of_head(nmax, tile, j), mx[:, j % 2:j % 2 + 1], -ATT_SCALE,
                                                   neg_sink[:, l, j:j + 1], ALU.mult, ALU.min).then_inc(*nm_ready.one)
                    if j == 7:
                        dve.wait_ge(*nm_ready.after(no, 8))
                        nc.vector.tensor_tensor(of_tile(sink_arg, tile), of_tile(nmax, tile), neg_sink[:, l, :],
                                                ALU.subtract).then_inc(*sink_ready.one)

                def transposed(tile, no, j, n):
                    dve.wait_ge(*pt_done.after(no, j + 1))
                    if j >= 2 or not starts(no):
                        dve.wait_ge(*pv_done.after(no, j - 1))
                    half = (n + 1) // 2 * P
                    nc.vector.tensor_copy(probsT[j % 2][:, 0:half], bankT[:, 0:half]).then_inc(*pt_evac_d.one)

                def denominators(tile, no):
                    dve.wait_ge(*esink_ready.after(no, 1))
                    link(nc.vector.tensor_tensor(of_tile(esum, tile), of_tile(esum, tile), of_tile(esink, tile), ALU.add))
                    link(nc.vector.reciprocal(of_tile(rden, tile), of_tile(esum, tile)))

                def outputs(tile, no):
                    dve.wait_ge(*pv_done.after(no, 8))
                    if not starts(no):
                        dve.wait_ge(*ot_done.after(no, 0))
                    share = of_tile(rden, tile).rearrange("p (r k) -> p k r", k=2)
                    for kv in range(2):
                        half = slice(256 * kv, 256 * kv + 256)
                        ins = nc.vector.tensor_tensor(o_tile[:, half].rearrange("p (h d) -> p h d", d=64),
                                                      lin0[:, half].rearrange("p (h d) -> p h d", d=64),
                                                      share[:, kv, :].rearrange("p (h o) -> p h o", o=1)
                                                      .to_broadcast([P, 4, 64]), ALU.mult)
                        if kv == 0:
                            link(ins)
                    ins.then_inc(*o_done.one)

                def body(tile, no, mask_no, first, last):
                    keys, n = keys_of(mask_no)
                    for j in range(8):
                        maximum(tile, no, j, keys)
                        step = lagging(tile, no, j, 2, first)
                        if step:
                            transposed(*step, n)
                        if j == 1 and not first:
                            denominators(tile - 1, no - 1)
                        if j == 3 and not first:
                            outputs(tile - 1, no - 1)
                    if last:
                        for j in range(6, 8):
                            transposed(tile, no, j, n)
                        denominators(tile, no)
                        outputs(tile, no)

                attention_tiles(dve, l, body, dve_chain, 8 + 3)

            def merge(p):
                n = norms["wo"]
                dve.wait_ge(*n["rstd"].after(p.it, 3))
                split(n, p, lambda j: mixed(p, j), lambda j: g_m[:, p.l, j:j + 1],
                      lambda j: mix_rstd[0 if j < 4 else 1 if j < 6 else 2][:, 0:p.w])
                dve.wait_ge(*lin_free.after(p.chunk(WO_AT[p.l], KB) + (KB - 1), EVACUATED))
                add_to_residual(n, p, 4, G1, wo_done)

            def feed_forward(p):
                n = norms["ff"]
                norm(n, p, A2, B2)
                link(nc.vector.memset(y[:, :, 0:p.w], 0.0))

                def group(q_no):
                    g = p.chunk(FF_AT[p.l], FF2) + q_no * (2 * FF_CH)
                    grp = p.it * FF_GROUPS + q_no
                    with dve.Fori(0, FF_CH // 2) as i:
                        for s in range(2):
                            dve.wait_ge(*lin_free.after(g + (2 * i + s), EVACUATED))
                            nc.vector.tensor_tensor(tmp[:, 2 + s, 0:p.w], tmp[:, 4 + s, 0:p.w], tmp[:, 4 + s, 0:p.w],
                                                    ALU.mult).then_inc(*a_sq.one)
                            dve.wait_ge(*a_sq.after(grp, 2 * i + (s + 1)))
                            unit = bass.ds(2 * i + s, 1)
                            dve.wait_ge(*a_hi_ready.after(grp, 2 * i + (s + 1)))
                            nc.vector.tensor_tensor(a_lo[:, unit, 0:p.w].rearrange("p o n -> p (o n)"), tmp[:, 2 + s, 0:p.w],
                                                    a_hi[:, unit, 0:p.w].rearrange("p o n -> p (o n)").bitcast(F32),
                                                    ALU.subtract).then_inc(*a_ready.one)
                            dve.wait_ge(*a_ready.after(grp, 2 * i + (s + 1)))
                            dve.sem_inc(wait_seat, 1)
                    with dve.Fori(0, FF_CH // 2) as i:
                        for s in range(2):
                            dve.wait_ge(*lin_done.after(g + (2 * i + (FF_CH + s)), 1))
                            part = y[:, bass.ds(2 * i + s, 1), 0:p.w].rearrange("p o n -> p (o n)")
                            nc.vector.tensor_tensor(part, bank[s][:, 0:p.w], part, ALU.add).then_inc(*lin_free.one)

                dve.sem_inc(wait_seat, 1)
                with dve.Fori(0, FF_GROUPS - 1) as q_no:
                    group(q_no)
                group(FF_GROUPS - 1)
                add_to_residual(n, p, 2, G2, ff_done)

            dve.wait_ge(consts_in.sem, 16 * 10)
            link(nc.vector.tensor_copy(mask[:], mask_f))
            link(nc.vector.tensor_scalar(neg_sink[:], neg_sink[:], -1.0, None, ALU.mult))
            for pad in (kz[:], kcz[:], vx[:]):
                link(nc.vector.memset(pad, 0.0))
            dve.sem_inc(consts_ready.sem, 1)
            for s in (rope_done, sgu_done, wo_done, ff_done):
                dve.sem_inc(s.sem, 1)
            dve.sem_inc(a_ready.sem, 2)
            for l in range(DEPTH):
                for p in passes(dve, l, True, dve_chain, 10):
                    project(p)
                fourier(l)
                attend(l)
                for p in passes(dve, l, False, dve_chain, 8):
                    merge(p)
                for p in passes(dve, l, False, dve_chain, 9):
                    feed_forward(p)

        @block.tensor
        def _(pe):
            def ready(g):
                pe.wait_ge(*w_split.after(g, 1))
                pe.wait_ge(*lin_free.after(g, 1))

            def sum_squares(n, p, u, ps, start, stop):
                pe.wait_ge(*n["sq"].after(p.it, u + 1))
                nc.tensor.matmul(ps[:, 0:p.w], t["ones"][:], tmp[:, (u if isinstance(u, int) else u[1]) % 2, 0:p.w],
                                 start=start, stop=stop).then_inc(*n["sq_used"].one)

            def product(g, s, p, parts, when=None):
                ready(g)
                hi, lo = parts
                for k in range(KB):
                    if when:
                        pe.wait_ge(*when(k))
                    for n, (w, h) in enumerate(((whi, hi), (whi, lo), (wlo, hi))):
                        last = nc.tensor.matmul(bank[s][:, 0:p.w], w[:, s, k * P:(k + 1) * P], h[:, k, 0:p.w],
                                                start=(k == 0 and n == 0), stop=(k == KB - 1 and n == 2))
                last.then_inc(*lin_done.one)

            def token_product(g, s, p, when=None):
                ready(g)
                for tile in range(p.tiles):
                    for k in range(KB):
                        if when and tile == 0:
                            pe.wait_ge(*when(k))
                        for n, (h, w) in enumerate(((h_hi, whi), (h_lo, whi), (h_hi, wlo))):
                            last = nc.tensor.matmul(bank[s][:, tile * P:(tile + 1) * P],
                                                    h[:, k, tile * P:(tile + 1) * P], w[:, s, k * P:(k + 1) * P],
                                                    start=(k == 0 and n == 0), stop=(k == KB - 1 and n == 2))
                last.then_inc(*lin_done.one)

            h_parts, a_parts = (h_hi, h_lo), (a_hi, a_lo)

            def project(p):
                n = norms["s1"]
                pe.wait_ge(*sgu_done.after(p.it, 0))
                for k in range(KB):
                    sum_squares(n, p, k, bank[2], k == 0, k == KB - 1)
                g = p.chunk(S1_AT[p.l], IN2)

                def part_ready(k):
                    return n["ready"].after(p.it, k + 1)

                if p.context and p.l:
                    product(g, 0, p, h_parts, part_ready)
                    token_product(g + 1, 1, p)
                    return
                token_product(g + GV2, GV2 % 2, p, part_ready)
                token_product(g + (GV2 + 1), (GV2 + 1) % 2, p)
                for c in range(U2, U2 + 2):
                    product(g + c, c % 2, p, h_parts)

                def rotate(r):
                    pe.wait_ge(*lin_free.after(g + (Q2 + r), EVACUATED))
                    if r >= 2:
                        pe.wait_ge(*rope_done.after(p.latent_it, r - 1))
                    nc.tensor.matmul(bank[4 + r % 2], rot[:], tmp[:, 6 + r % 2, :], start=True, stop=True)\
                      .then_inc(*rope_mm.one)

                for r in range(5):
                    product(g + (Q2 + r), (Q2 + r) % 2, p, h_parts)
                    if r and not p.context:
                        rotate(r - 1)
                product(g + F2, F2 % 2, p, h_parts)
                if not p.context:
                    rotate(4)
                pe.wait_ge(*gv_ready.after(p.it, 1))
                for tile in range(p.tiles):
                    for h in range(4):
                        at = (2 * tile + h // 2) * P
                        last = nc.tensor.matmul(scores[0][64 * (h % 2):64 * (h % 2) + 64, at:at + P],
                                                gvn[:, tile, 64 * h:64 * h + 64], w_s[:, p.l, h, :], start=True, stop=True)
                last.then_inc(*sgu_mm.one)
                product(g + (F2 + 1), (F2 + 1) % 2, p, h_parts)
                token_product(g + V2, V2 % 2, p)

            def fourier(l):
                pe.wait_ge(*lin_free.after(DFT_AT[l], 2))
                pe.wait_ge(*sgu_done.after(3 * l + (3 if l == 0 else 2), 0))
                for n in range(NDIM[l]):
                    if n >= 4:
                        pe.wait_ge(*dim_ready.after(l, n - 3))
                    for c in range(2):
                        last = nc.tensor.matmul(bank[2 + n % 4][:, 256 * c:256 * c + 256], f[:, c, n * P:(n + 1) * P],
                                                dims[:], start=True, stop=True)
                    last.then_inc(*dim_mm.one)
                pe.wait_ge(*dim_ready.after(l, SEQ // P))
                pe.wait_ge(*dim_hi.after(l, NDIM[l]))
                if l == 0:
                    for c in range(2):
                        for part in range(2):
                            for k in range(CTX // P):
                                at = 256 * c + P * part
                                last = nc.tensor.matmul(bankT[:, 512 * c:512 * c + CTX], tmp[:, k, at:at + P],
                                                        dft_ctx[:, part, k, :], start=(part == k == 0),
                                                        stop=(part == k == 1))
                    last.then_inc(*ctx_dft.one)
                pe.sem_inc(wait_seat, 1)
                with pe.Fori(0, DFT // 4) as i:
                    for s in range(2):
                        g = 4 * i + (DFT_AT[l] + 2 * s)
                        pe.wait_ge(*lin_free.after(g, 0))
                        for part in range(2):
                            pe.wait_ge(*w_split.after(g + part, 1))
                            for c in range(2):
                                cols = slice(256 * c + P * part, 256 * c + P * part + P)
                                for k in range(KB):
                                    for n, (h, w) in enumerate(((h_hi, whi), (h_lo, whi), (h_hi, wlo))):
                                        last = nc.tensor.matmul(scores[s][:, 512 * c:512 * c + P], h[:, k, cols],
                                                                w[:, part, k * P:(k + 1) * P],
                                                                start=(part == k == n == 0),
                                                                stop=(part == 1 and k == KB - 1 and n == 2))
                            last.then_inc(*lin_done.one)

            def attend(l):
                pe.wait_ge(*lin_free.after(WO_AT[l], 2))
                if l == 0:
                    pe.wait_ge(ctx_dft_done.sem, 1)

                def score(tile, no, j, mask_no):
                    r, kv = j // 2, j % 2
                    if j % 2 == 0:
                        pe.wait_ge(*qt_ready.after(no, r + 1))
                    if j >= 2 or not starts(no):
                        pe.wait_ge(*exp_done.after(no, j - 1))
                    if mask_no is not None:
                        local = scores[kv][:, P:4 * P]
                        keys = slice(tile * P, tile * P + 3 * P) if isinstance(tile, int) else bass.ds(tile * P, 3 * P)
                        nc.tensor.matmul(local, qt[:, r, :], kz[:, kv, keys], start=True, stop=False)
                        nc.tensor.matmul(local, t["identb"][:], mask[:, mask_no, :], start=False, stop=True)
                    nc.tensor.matmul(scores[kv][:, 4 * P:4 * P + CTX], qt[:, r, :], kcz[:, kv, :], start=True, stop=True)\
                      .then_inc(*s_ready.one)

                def transpose(tile, no, j, n):
                    pe.wait_ge(*exp_done.after(no, j + 1))
                    if j or not starts(no):
                        pe.wait_ge(*pt_evac_a.after(no, j))
                        pe.wait_ge(*pt_evac_d.after(no, j))
                    for k in range(n):
                        at = k * P if k < (n + 1) // 2 else 512 + (k - (n + 1) // 2) * P
                        last = nc.tensor.transpose(bankT[:, at:at + P], probs[j % 2][:, k * P:(k + 1) * P],
                                                   t["ident"][:])
                    last.then_inc(*pt_done.one)

                def values(tile, no, j, n):
                    r, kv = j // 2, j % 2
                    pe.wait_ge(*pt_evac_a.after(no, j + 1))
                    pe.wait_ge(*pt_evac_d.after(no, j + 1))
                    if j == 0 and not starts(no):
                        pe.wait_ge(*o_done.after(no, 0))
                    head = (r + 4 * kv) * 64
                    half = slice(64 * kv, 64 * kv + 64)
                    for k in range(n):
                        c = k - (n - CTX // P)
                        if c >= 0:
                            v = vc[:, c, half]
                        elif isinstance(tile, int):
                            v = vx[:, tile + k, half]
                        else:
                            v = vx[:, bass.ds(tile + k, 1), half].rearrange("p o n -> p (o n)")
                        last = nc.tensor.matmul(lin0[:, head:head + 64], probsT[j % 2][:, k * P:(k + 1) * P], v,
                                                start=(k == 0), stop=(k == n - 1))
                    last.then_inc(*pv_done.one)

                def outputs(tile, no):
                    pe.wait_ge(*o_done.after(no, 1))
                    if not starts(no):
                        pe.wait_ge(*attn_done.after(no, 0))
                    for c in range(4):
                        last = nc.tensor.transpose(lin1[:, c * P:(c + 1) * P], o_tile[:, c * P:(c + 1) * P], t["ident"][:])
                    last.then_inc(*ot_done.one)

                def body(tile, no, mask_no, first, last):
                    n = keys_of(mask_no)[1]
                    for j in range(8):
                        score(tile, no, j, mask_no)
                        for lag, work in ((2, transpose), (3, values)):
                            step = lagging(tile, no, j, lag, first)
                            if step:
                                work(*step, n)
                        if j == 4 and not first:
                            outputs(tile - 1, no - 1)
                    if last:
                        for j in range(5, 8):
                            if j > 5:
                                transpose(tile, no, j, n)
                            values(tile, no, j, n)
                        outputs(tile, no)

                attention_tiles(pe, l, body)

            def merge(p):
                n = norms["wo"]
                for j in range(KB):
                    ps, start, stop = (bank[2], j == 0, j == 3) if j < 4 else (bank[3 + (j - 4) // 2], j % 2 == 0, j % 2 == 1)
                    sum_squares(n, p, j, ps, start, stop)
                g = p.chunk(WO_AT[p.l], KB)
                product(g, 0, p, h_parts, lambda k: n["ready"].after(p.it, k + 1))
                norm_of_products(n, p, g, h_parts)

            def norm_of_products(n, p, g, parts):
                product(g + 1, 1, p, parts)
                sum_squares(n, p, KB, bank[2], True, False)
                with pe.Fori(1, KB // 2) as i:
                    for s in range(2):
                        product(g + (2 * i + s), s, p, parts)
                        pe.wait_ge(*n["sq"].after(p.it, 2 * i + (KB + s)))
                        nc.tensor.matmul(bank[2][:, 0:p.w], t["ones"][:], tmp[:, 1 - s, 0:p.w], start=False, stop=False)\
                          .then_inc(*n["sq_used"].one)
                sum_squares(n, p, 2 * KB - 1, bank[2], False, True)

            def feed_forward(p):
                n = norms["ff"]
                for k in range(KB):
                    sum_squares(n, p, k, bank[2], k == 0, k == KB - 1)

                def group(q_no, last):
                    g = p.chunk(FF_AT[p.l], FF2) + q_no * (2 * FF_CH)
                    grp = p.it * FF_GROUPS + q_no
                    pe.sem_inc(wait_seat, 1)
                    with pe.Fori(0, FF_CH // 2) as i:
                        for s in range(2):
                            product(g + (2 * i + s), s, p, h_parts)
                    product(g + FF_CH, 0, p, a_parts, lambda k: a_ready.after(grp, k + 1))
                    if last:
                        norm_of_products(n, p, g + FF_CH, a_parts)
                        return
                    product(g + (FF_CH + 1), 1, p, a_parts)
                    with pe.Fori(1, FF_CH // 2) as i:
                        for s in range(2):
                            product(g + (2 * i + (FF_CH + s)), s, p, a_parts)

                pe.wait_ge(*n["ready"].after(p.it, KB))
                pe.sem_inc(wait_seat, 1)
                with pe.Fori(0, FF_GROUPS - 1) as q_no:
                    group(q_no, False)
                group(FF_GROUPS - 1, True)

            pe.wait_ge(consts_ready.sem, 1)
            for l in range(DEPTH):
                for p in passes(pe, l, True):
                    project(p)
                fourier(l)
                attend(l)
                for p in passes(pe, l):
                    merge(p)
                for p in passes(pe, l):
                    feed_forward(p)


CONSTS1 = ["ones64", "rot1", "ret_mask", "ret_qdecay", "ret_kdecay", "ret_cdecay", "gla_heads", "gla_mask"]


def program(nc, a, out):
    with ExitStack() as ctx:
        def sem(name):
            return ctx.enter_context(nc.semaphore(name))

        def sb(name, shape, dt=F32):
            return ctx.enter_context(nc.sbuf_tensor(name, shape, dt))

        wide = D + KB * GATE_RANK
        t = {"x": sb("x", [P, KB, SEQ]), "wraw": sb("wraw", [P, 2, wide]), "whi": sb("whi", [P, 2, wide], F32R),
             "wlo": sb("wlo", [P, 2, wide], F32R), "ident": sb("ident", [P, P]), "ones": sb("ones", [P, P]),
             "identb": sb("identb", [P, P], BF16), "cols2": sb("cols2", [P, DEPTH, 2, 2 * 24])}
        t["x_in"], t["const_in"] = sem("x_in"), sem("const_in")
        t["raw_in"] = [Sig(sem(f"raw_in{s}"), 8 * CH1) for s in range(2)]
        t["w_hi"], t["w_split"] = Sig(sem("w_hi"), CH1), Sig(sem("w_split"), CH1)
        t["lin_done"], t["lin_free"] = Sig(sem("lin_done"), CH1), Sig(sem("lin_free"), CH1)
        with ExitStack() as first:
            def sb1(name, shape, dt=F32):
                return first.enter_context(nc.sbuf_tensor(name, shape, dt))

            t["cols1"], t["rope1"] = sb1("cols1", [P, DEPTH, NCOL1]), sb1("rope1", [P, 4, SEQ])
            t["mask1"] = sb1("mask1", [P, 2, 2 * P], BF16)
            t["gate_w"] = sb1("gate_w", [GATE_RANK, DEPTH, P])
            for name in CONSTS1:
                t[name] = sb1(name, list(a[name].shape), U8 if name == "gla_mask" else F32)
            load_and_modulate(nc, t, a, sem)
            first_block(nc, t, a, sem)
        second_block(nc, t, a, sem, out)


def chunked(w):
    k, n = w.shape
    return w.reshape(k // P, P, n // P, P).transpose(2, 1, 0, 3).reshape(n // P, P, k)


def columns(v):
    return np.moveaxis(v.reshape(*v.shape[:-1], -1, P), -1, 0)


def kernel(**inp):
    import concourse.bacc as bacc
    from concourse.bass_utils import run_bass_kernel_spmd as run

    inp = {k: np.asarray(v) for k, v in inp.items()}
    heads = np.concatenate([np.arange(64 * h, 64 * h + 64) for h in HEAD_PAIRS])
    order1 = np.concatenate([heads, np.arange(512, 640), np.arange(1280, 1792), np.arange(2304, 2560),
                             np.arange(640, 768), np.arange(1792, 2048), np.arange(2560, 2816),
                             768 + heads, np.arange(2048, 2304), np.arange(2816, 3072)])
    out_rows = np.concatenate([heads, np.arange(512, 1024)])
    a = {}
    a["x"] = inp["x"][0].T.reshape(KB, P, SEQ).transpose(1, 0, 2)
    a["c"] = np.stack([inp[n].reshape(KB, P).T for n in ("c", "c_2", "c_ctx_2")], 2)
    a["positions"] = np.broadcast_to(inp["positions"][0], (P, SEQ))
    a["w_mod"] = np.concatenate([chunked(w) for w in inp["w_mod"]])
    a["w_ada"] = np.concatenate([chunked(w) for w in inp["w_ada_2"]])
    a["b_mod"] = np.concatenate([columns(inp[n]).reshape(P, -1) for n in ("b_mod", "b_ada_2")], 1)
    a["gains2"] = np.stack([columns(inp[f"g_{n}_2"]) for n in ("pre_mix", "post_mix", "pre_ff", "post_ff")], 2)
    gn = np.tile(inp["gla_norm_gain"], (1, 2))
    a["gains1"] = np.concatenate([columns(inp["pre_norm_gain"]), columns(inp["post_norm_gain"]),
                                  inp["gla_gate_b"].T[:, :, None], gn.T[:, :, None]], 2)
    a["sinks1"] = np.broadcast_to(inp["attn_sinks"], (P, DEPTH, 8))
    a["gate_w"] = inp["gla_gate_w"].transpose(1, 0, 2)
    a["w1"] = np.stack([np.concatenate([chunked(inp["w_in"][l][:, order1]), chunked(inp["w_out"][l][out_rows])])
                        for l in range(DEPTH)])
    a["w1_gate"] = np.stack([inp["w_in"][l][:, 3072:].reshape(KB, P, GATE_RANK).transpose(1, 0, 2).reshape(P, -1)
                             for l in range(DEPTH)])
    order2 = np.concatenate([np.arange(1024, 1280), np.arange(768, 1024), heads, np.arange(512, 640),
                             np.arange(1280, 1536), np.arange(640, 768)])
    hidden = KB * P
    a["w2"] = np.stack([np.concatenate(
        [chunked(inp["w_in_2"][l][:, order2]), chunked(inp["w_out_2"][l])]
        + [chunked(w) for g in range(FF_GROUPS) for w in (inp["w_ff1_2"][l][:, g * hidden:(g + 1) * hidden],
                                                          inp["w_ff2_2"][l][g * hidden:(g + 1) * hidden])])
        for l in range(DEPTH)])
    a["w1_next"] = np.stack([a["w1"][0, :2], a["w1"][1, :2], a["w1"][1, :2], a["w2"][0, :2]])
    a["ctx"] = inp["ctx_2"][0].T.reshape(KB, P, CTX).transpose(1, 0, 2)
    a["sinks2"] = np.broadcast_to(inp["sink_2"][:, HEAD_PAIRS], (P, DEPTH, 8))
    a["w_sgu"] = inp["w_sgu_2"].transpose(3, 0, 1, 2)
    a["b_sgu"] = np.repeat(inp["b_sgu_2"].reshape(DEPTH, 2, 2, P).transpose(2, 0, 1, 3), 64, axis=0)
    a["g_sgu"] = columns(inp["g_sgu_2"].reshape(DEPTH, 256))
    a["g_mix"] = columns(inp["g_mix_2"])
    a.update(constants())

    nc = bacc.Bacc("TRN2", target_bir_lowering=False, num_devices=1)
    a = {k: np.ascontiguousarray(v) for k, v in a.items()}
    aps = {k: nc.dram_tensor(f"in_{k}", v.shape, mybir.dt.from_np(v.dtype), kind="ExternalInput").ap() for k, v in a.items()}
    out = nc.dram_tensor("out", (P, KB, SEQ), F32, kind="ExternalOutput").ap()
    program(nc, aps, out)
    r = run(nc, [{f"in_{k}": v for k, v in a.items()}], core_ids=[0])
    got = r.results[0]["out"]
    return got.transpose(2, 1, 0).reshape(1, SEQ, D)
```

```python
from contextlib import ExitStack

import numpy as np

import concourse.bass as bass
from concourse import mybir

F32 = mybir.dt.float32
F32R = mybir.dt.float32r
BF16 = mybir.dt.bfloat16
I32 = mybir.dt.int32
U8 = mybir.dt.uint8
ALU = mybir.AluOpType
ACT = mybir.ActivationFunctionType
AX_X = mybir.AxisListType.X

P = 128
D = 1024
KB = D // P
SEQ = 1024
W = 512
NB = SEQ // W
NT = W // P
DEPTH = 2
EPS = 1e-6

ROPE1 = 9
GQ, GK, AV, RV, GV = 9, 10, 11, 12, 14
GATE1 = 16
OUT1 = 24
CH1 = 32
GATE_RANK = 16
LEVELS = 7
ATT_SCALE = 64 ** -0.5
HEAD_PAIRS = [0, 4, 1, 5, 2, 6, 3, 7]

CTX = 256
GRID_W = 64
TOKENS = SEQ + CTX
VEC = 3
MOD1, MOD2 = 3 * KB, 6 * KB
GV2, U2, Q2, K2, F2, V2 = 0, 2, 4, 8, 9, 11
IN2 = 12
FF_GROUPS = 4
FF_CH = 8
FF2 = FF_GROUPS * 2 * FF_CH
CH2 = IN2 + KB + FF2
DFT = 16
A1, B1, G1, A2, B2, G2 = range(0, 48, 8)

C_A, C_B, C_G, C_GB, C_GN, C_ONE, C_SINK = 0, 8, 16, 24, 25, 26, 32
NCOL1 = 40


class Sig:

    def __init__(self, sem, per=0, start=0):
        self.sem, self.per, self.start = sem, per, start

    def after(self, it, n):
        if isinstance(it, int):
            return self.sem, self.start + it * self.per + n
        return self.sem, it * self.per + (self.start + n)

    @property
    def one(self):
        return self.sem, 1


class Order:

    def __init__(self, eng, sig):
        self.eng, self.sig, self.n, self.it = eng, sig, 0, 0

    def begin(self, it):
        self.it, self.n = it, 0

    def link(self, ins):
        self.n += 1
        ins.then_inc(self.sig.sem, 1)
        self.eng.wait_ge(*self.sig.after(self.it, self.n))

    def end(self):
        assert self.n == self.sig.per, (self.n, self.sig.per)


def constants():
    f = np.float32
    c = {}
    c["ident"] = np.eye(P, dtype=f)
    c["ones"] = np.ones((P, P), f)
    half = np.arange(P) // 64
    c["ones64"] = (half[:, None] == half[None, :]).astype(f)
    rot = np.zeros((P, P), f)
    for m in range(P):
        d = m % 64
        if d < 32:
            rot[m + 32, m] = -1
        else:
            rot[m - 32, m] = 1
    c["rot1"] = rot
    inv_a = (10000.0 ** (-np.arange(0, 64, 2, dtype=np.float64) / 64)).astype(f)
    steps = np.arange(32, dtype=f) * f(1 / 31)
    steps[-1] = 1
    inv_r = f(1) / np.power(10000.0, steps.astype(np.float64)).astype(f)
    c["inv_freq"] = np.stack([np.tile(inv_a, 4), np.tile(inv_r, 4)], 1)
    i, j = np.arange(P)[:, None], np.arange(2 * P)[None, :]
    rel = i + P - j
    ok = (rel >= 0) & (rel < P)
    c["mask1"] = np.stack([np.where(ok & (j >= P), 0, -1e30), np.where(ok, 0, -1e30)], 1).astype(f)
    log_g = np.log(1.0 - 2.0 ** (-5.0 - np.arange(4)))
    idx = np.arange(P, dtype=np.float64)
    diff = idx[None, :] - idx[:, None]
    dm = np.where(diff >= 0, np.exp(log_g[:, None, None] * np.maximum(diff, 0)), 0) * 64 ** -0.5
    c["ret_mask"] = dm.transpose(1, 0, 2).astype(f)
    qd = np.exp(log_g[:, None] * (idx + 1))
    c["ret_qdecay"] = np.stack([qd[2 * n + half] for n in range(2)], 1).astype(f)
    kd = np.exp(log_g[:, None] * (P - 1 - idx)) * 64 ** -0.5
    c["ret_kdecay"] = np.repeat(kd.T, 64, axis=1).astype(f)
    c["ret_cdecay"] = np.stack([np.exp(log_g * P)[2 * n + half] for n in range(2)], 1).astype(f)
    c["gla_heads"] = (np.arange(P)[:, None] // 32 == np.arange(256)[None, :] // 64).astype(f)
    m = np.zeros((P, LEVELS + 1, P), f)
    a = np.arange(P)
    for lv in range(LEVELS):
        s = 64 >> lv
        m[:, lv] = (a[:, None] // s % 2 == 0) & (a[None, :] // s == a[:, None] // s + 1)
    m[:, LEVELS] = np.eye(P)
    c["gla_mask"] = m
    rot = np.zeros((P, P), f)
    for m in range(P):
        d = m % 32
        if d < 16:
            rot[m + 16, m] = -1
        else:
            rot[m - 16, m] = 1
    c["rot2"] = rot
    inv = (10000.0 ** (-np.arange(16, dtype=np.float64) / 16)).astype(f)
    tok = np.arange(SEQ)
    row, column = (tok // GRID_W).astype(f), (tok % GRID_W).astype(f)
    ang = np.concatenate([np.tile(inv[:, None] * row[None], (2, 1)), np.tile(inv[:, None] * column[None], (2, 1))])
    ang = np.tile(ang, (2, 1)).astype(np.float64)
    c["rope2"] = np.stack([np.cos(ang), np.sin(ang)], 1).astype(f)
    i, j = np.arange(P)[:, None], np.arange(3 * P)[None, :] - P
    band = np.abs(j - i) <= P
    c["mask2"] = np.stack([np.where(ok, 0, -1e30) for ok in (band & (j >= 0), band, band & (j < P))], 1).astype(f)
    w = 2 * np.pi * np.outer(np.arange(64), np.arange(64)) / 64
    two = np.kron(np.eye(2), np.ones((64, 64)))
    c["dft_dims"] = (np.concatenate([np.tile(np.cos(w), (2, 2)) * two, np.tile(np.sin(w), (2, 2)) * two], 1) / 256).astype(f)
    w = 2 * np.pi * (np.outer(np.arange(SEQ), np.arange(SEQ)) % SEQ) / SEQ
    c["dft_tokens"] = np.stack([chunked(v.astype(f)).reshape(-1, 2, P, SEQ) for v in (np.cos(w), -np.sin(w))], 1)\
        .reshape(-1, P, SEQ)
    w = 2 * np.pi * (np.outer(np.arange(CTX), np.arange(CTX)) % CTX) / CTX
    both = np.stack([2 * np.cos(w), -2 * np.sin(w)])
    c["dft_ctx"] = both.reshape(2, 2, P, CTX).transpose(2, 0, 1, 3).astype(f)
    return c


TWO_PI = 2 * np.pi
C1 = 6.28125
C2 = 0.0019350051879882812
C3 = TWO_PI - C1 - C2
MAGIC = 12582912.0
PI_IN = 3.1415925


def load_and_modulate(nc, t, a, sems):
    sem = sems
    GROUP = 4
    NRING = 2 * GROUP
    n1, n2 = DEPTH * MOD1, DEPTH * MOD2
    chunks = n1 + n2
    with ExitStack() as ctx:
        ring = ctx.enter_context(nc.sbuf_tensor("mod_ring", [P, NRING, D], F32))
        pos_i = ctx.enter_context(nc.sbuf_tensor("pos_i", [P, SEQ], I32))
        pos_f = ctx.enter_context(nc.sbuf_tensor("pos_f", [P, SEQ], F32))
        ang = ctx.enter_context(nc.sbuf_tensor("ang", [P, SEQ], F32))
        turns = ctx.enter_context(nc.sbuf_tensor("turns", [P, SEQ], F32))
        arg = ctx.enter_context(nc.sbuf_tensor("arg", [P, 4, SEQ], F32))
        cvec = ctx.enter_context(nc.sbuf_tensor("cvec", [P, KB, VEC], F32))
        cact = ctx.enter_context(nc.sbuf_tensor("cact", [P, KB, VEC], F32))
        bias = ctx.enter_context(nc.sbuf_tensor("mod_bias", [P, chunks], F32))
        mod = ctx.enter_context(nc.sbuf_tensor("mod", [P, DEPTH, MOD1], F32))
        mod2 = ctx.enter_context(nc.sbuf_tensor("mod2", [P, DEPTH, 2, MOD2], F32))
        gains2 = ctx.enter_context(nc.sbuf_tensor("gains2", [P, DEPTH, 4, KB], F32))
        gains = ctx.enter_context(nc.sbuf_tensor("gains", [P, DEPTH, 18], F32))
        sinks = ctx.enter_context(nc.sbuf_tensor("sinks", [P, DEPTH, 8], F32))
        mask_f = ctx.enter_context(nc.sbuf_tensor("mask_f", [P, 2, 2 * P], F32))
        levels_f = ctx.enter_context(nc.sbuf_tensor("levels_f", [P, LEVELS + 1, P], F32))
        inv = ctx.enter_context(nc.sbuf_tensor("inv", [P, 2], F32))
        psM = ctx.enter_context(nc.psum_tensor("psM", [P, 512], F32))
        psR = [ctx.enter_context(nc.psum_tensor(f"psR{n}", [P, 512], F32)) for n in range(2)]
        row = ctx.enter_context(nc.sbuf_tensor("mod_row", [VEC, 2, GROUP * P], F32))

        chunk_in = [sem(f"mod_chunk_in{s}") for s in range(NRING)]
        chunk_used = sem("mod_chunk_used")
        vec_in, pos_in, small_in = sem("vec_in"), sem("pos_in"), sem("small_in")
        cact_ready, mod_done, args_ready = sem("cact_ready"), sem("mod_done"), sem("args_ready")
        tables_ready = sem("tables_ready")
        row_ready, row_used = sem("row_ready"), sem("row_used")
        order = Order(nc.vector, Sig(sem("prep_order")))
        block = ctx.enter_context(nc.Block())

        @block.sync
        def _(sp):
            sp.dma_start(cvec[:], a["c"]).then_inc(vec_in, 16)
            sp.dma_start(pos_i[:], a["positions"]).then_inc(pos_in, 16)
            sp.dma_start(inv[:], a["inv_freq"]).then_inc(pos_in, 16)
            for s in range(NRING):
                sp.dma_start(ring[:, s, :], a["w_mod"][s]).then_inc(chunk_in[s], 16)
            loads = [(bias, "b_mod"), (gains, "gains1"), (sinks, "sinks1"), (mask_f, "mask1"), (gains2, "gains2"),
                     (levels_f, "gla_mask")]
            for dst, name in loads:
                sp.dma_start(dst[:], a[name]).then_inc(small_in, 16)
            with sp.Fori(0, n1 // NRING - 1) as i:
                for s in range(NRING):
                    sp.wait_ge(chunk_used, i * NRING + (s + 1))
                    sp.dma_start(ring[:, s, :], a["w_mod"][bass.ds(i * NRING + (NRING + s), 1)]
                                 .rearrange("o p n -> p (o n)")).then_inc(chunk_in[s], 16)
            with sp.Fori(n1 // NRING - 1, chunks // NRING - 1) as i:
                for s in range(NRING):
                    sp.wait_ge(chunk_used, i * NRING + (s + 1))
                    sp.dma_start(ring[:, s, :], a["w_ada"][bass.ds(i * NRING + (NRING - n1 + s), 1)]
                                 .rearrange("o p n -> p (o n)")).then_inc(chunk_in[s], 16)

        @block.gpsimd
        def _(pool):
            for name in ("ident", "ones", "ones64", "rot1", "ret_mask", "ret_qdecay", "ret_kdecay", "ret_cdecay",
                         "gla_heads", "gate_w"):
                pool.dma_start(t[name][:], a[name]).then_inc(t["const_in"], 16)
            pool.dma_start(t["x"][:], a["x"]).then_inc(t["x_in"], 16)
            pool.wait_ge(t["x_in"], 16)
            pool.wait_ge(t["const_in"], 16 * 10)

        @block.scalar
        def _(act):
            act.wait_ge(vec_in, 16)
            nc.scalar.activation(cact[:], cvec[:], ACT.Silu).then_inc(cact_ready, 1)
            for n in range(4):
                act.wait_ge(args_ready, n + 1)
                nc.scalar.activation(t["rope1"][:, n, :], arg[:, n, :], ACT.Sin).then_inc(tables_ready, 1)
            act.wait_ge(tables_ready, 4)
            with act.Fori(0, chunks // NRING) as i:
                for s in range(2):
                    act.wait_ge(chunk_used, i * NRING + GROUP * (s + 1))
                    act.wait_ge(row_used, i * 2 + (s + 1))
                    nc.scalar.activation(row[:, s, :], psR[s][0:VEC, :], ACT.Copy).then_inc(row_ready, 1)

        @block.tensor
        def _(pe):
            pe.wait_ge(cact_ready, 1)
            pe.sem_inc(row_used, 2)

            def products(i, s):
                for c in range(GROUP):
                    slot = s * GROUP + c
                    pe.wait_ge(chunk_in[slot], i * 16 + 16)
                    for k in range(KB):
                        last = nc.tensor.matmul(psR[s][0:VEC, c * P:(c + 1) * P], cact[:, k, :],
                                                ring[:, slot, k * P:(k + 1) * P], start=(k == 0), stop=(k == KB - 1))
                    last.then_inc(chunk_used, 1)

            def to_columns(i, s):
                pe.wait_ge(row_ready, i * 2 + (s + 1))
                for c in range(GROUP):
                    at = (s * GROUP + c) * VEC
                    col = bass.ds(i * (NRING * VEC) + at, VEC)
                    last = nc.tensor.matmul(psM[:, col], row[:, s, c * P:(c + 1) * P], t["ident"][0:VEC, 0:VEC],
                                            start=True, stop=True)
                last.then_inc(row_used, 1)

            products(0, 0)
            products(0, 1)
            pe.wait_ge(t["const_in"], 16 * 10)
            to_columns(0, 0)
            with pe.Fori(1, chunks // NRING) as i:
                products(i, 0)
                to_columns(i - 1, 1)
                products(i, 1)
                to_columns(i, 0)
            to_columns(chunks // NRING - 1, 1)

        @block.vector
        def _(dve):
            link = order.link
            dve.wait_ge(pos_in, 32)
            link(nc.vector.tensor_copy(pos_f[:], pos_i[:]))
            for j in range(2):
                link(nc.vector.tensor_scalar(ang[:], pos_f[:], inv[:, j:j + 1], None, ALU.mult))
                for cosine in (1, 0):
                    out = arg[:, 2 * j + 1 - cosine, :]
                    link(nc.vector.tensor_scalar(turns[:], ang[:], 1 / TWO_PI, 0.25 * cosine, ALU.mult, ALU.add))
                    link(nc.vector.tensor_scalar(turns[:], turns[:], MAGIC, None, ALU.add))
                    link(nc.vector.tensor_scalar(turns[:], turns[:], MAGIC, None, ALU.subtract))
                    link(nc.vector.scalar_tensor_tensor(out, turns[:], -C1, ang[:], ALU.mult, ALU.add))
                    link(nc.vector.scalar_tensor_tensor(out, turns[:], -C2, out, ALU.mult, ALU.add))
                    link(nc.vector.scalar_tensor_tensor(out, turns[:], -C3, out, ALU.mult, ALU.add))
                    link(nc.vector.tensor_scalar(out, out, np.pi / 2 * cosine, PI_IN, ALU.add, ALU.min))
                    nc.vector.tensor_scalar(out, out, -PI_IN, None, ALU.max).then_inc(args_ready, 1)
            dve.wait_ge(small_in, 16 * 6)
            link(nc.vector.tensor_copy(t["mask1"][:], mask_f[:]))
            link(nc.vector.tensor_copy(t["gla_mask"][:], levels_f[:]))
            dve.wait_ge(t["const_in"], 16 * 10)
            link(nc.vector.tensor_copy(t["identb"][:], t["ident"][:]))
            cols = t["cols1"]
            dve.wait_ge(row_used, 2 + chunks // GROUP)
            products = psM[:, 0:chunks * VEC].rearrange("p (n v) -> p n v", v=VEC)
            link(nc.vector.tensor_tensor(mod[:].rearrange("p l n -> p (l n)"), products[:, 0:n1, 0], bias[:, 0:n1],
                                         ALU.add))
            for v in range(2):
                for l in range(DEPTH):
                    part = slice(n1 + l * MOD2, n1 + (l + 1) * MOD2)
                    link(nc.vector.tensor_tensor(mod2[:, l, v, :], products[:, part, 1 + v], bias[:, part], ALU.add))
                    for half in range(2):
                        m, out = mod2[:, l, v, 24 * half:], t["cols2"][:, l, v, 24 * half:]
                        nc.vector.scalar_tensor_tensor(out[:, A1:A1 + 8], m[:, 8:16], 1.0, gains2[:, l, 2 * half, :],
                                                       ALU.add, ALU.mult)
                        nc.vector.tensor_copy(out[:, B1:B1 + 8], m[:, 0:8])
                        link(nc.vector.tensor_tensor(out[:, G1:G1 + 8], m[:, 16:24], gains2[:, l, 2 * half + 1, :],
                                                     ALU.mult))
            link(nc.vector.scalar_tensor_tensor(cols[:, :, C_A:C_A + 8], mod[:, :, 8:16], 1.0, gains[:, :, 0:8],
                                                ALU.add, ALU.mult))
            link(nc.vector.tensor_copy(cols[:, :, C_B:C_B + 8], mod[:, :, 0:8]))
            link(nc.vector.tensor_tensor(cols[:, :, C_G:C_G + 8], mod[:, :, 16:24], gains[:, :, 8:16], ALU.mult))
            link(nc.vector.tensor_copy(cols[:, :, C_GB:C_GB + 2], gains[:, :, 16:18]))
            link(nc.vector.memset(cols[:, :, C_ONE:C_ONE + 6], 1.0))
            link(nc.vector.tensor_scalar(cols[:, :, C_SINK:C_SINK + 8], sinks[:], -1.0, None, ALU.mult))


def first_block(nc, t, a, sems, debug=None):
    sem = sems
    with ExitStack() as ctx:
        def sb(name, shape, dt=F32):
            return ctx.enter_context(nc.sbuf_tensor(name, shape, dt))

        x, wraw, whi, wlo = t["x"], t["wraw"], t["whi"], t["wlo"]
        cols1, rope1, mask1 = t["cols1"], t["rope1"], t["mask1"]
        h_hi, h_lo = sb("h_hi", [P, KB, W], F32R), sb("h_lo", [P, KB, W], F32R)
        aq = sb("aq", [P, 4, W])
        ak = sb("ak", [P, P + W])
        av = sb("av", [P, 1 + NT, P])
        rq, rk = sb("rq", [P, 2, W]), sb("rk", [P, 2, W])
        rv, gv = sb("rv", [P, NT, 256]), sb("gv", [P, NT, 256])
        gq, gk = sb("gq", [P, W]), sb("gk", [P, W])
        gate_y = sb("gate_y", [P, KB, W])
        ga = sb("ga", [GATE_RANK, W])
        gw = sb("gw", [GATE_RANK, P])
        col = sb("col", [P, NCOL1])
        tmp = sb("tmp", [P, 8, W])
        rstd = sb("rstd", [P, W])
        probs = [tmp[:, 2 * n:2 * n + 2, :].rearrange("p a b -> p (a b)").rearrange("p (g k) -> p g k", g=4)
                 for n in range(2)]
        probsT = [tmp[:, 4 + 2 * n:6 + 2 * n, :] for n in range(2)]
        mx = sb("mx", [P, 2, 4])
        nmax, sink_arg, esum, esink, rden = (sb(n, [P, 2, 4]) for n in ("nmax", "sink_arg", "esum", "esink", "rden"))
        scm = sb("scm", [P, 2, 4, P])
        kd = sb("kd", [P, 2, 256])
        qd = sb("qd", [P, 2, 2, P])
        rstate, rnew = sb("rstate", [P, 2, P]), sb("rnew", [P, 2, P])
        gstate, gnew = sb("gstate", [P, 256]), rnew[:].rearrange("p c v -> p (c v)")
        bsum = sb("bsum", [P, W])
        zed = sb("zed", [P, 2, W])
        lq, lk = tmp[:, 4:6, :], tmp[:, 6:8, :]
        gsc = aq[:].rearrange("p t (h i) -> p t h i", h=4)
        khT = sb("khT", [P, 2, P])
        elast = sb("elast", [P, NT])
        lin0, lin1 = (ctx.enter_context(nc.psum_tensor(f"lin{n}", [P, 512], F32)) for n in range(2))
        scores = [ctx.enter_context(nc.psum_tensor(f"scores{n}", [P, 1024], F32)) for n in range(2)]
        bank = [lin0[:], lin1[:]] + [s[:, 512 * n:512 * n + 512] for s in scores for n in range(2)]
        bankT = ctx.enter_context(nc.psum_tensor("bankT", [P, 2, 512], F32))
        bankS = bank[2:]
        eb, qe, khat, logs = tmp[:, 0, :], tmp[:, 1, :], tmp[:, 2, :], tmp[:, 7, :]

        def score(j):
            return scores[j % 2][:].rearrange("p (g k) -> p g k", g=4)

        def mixed(j):
            return rq[:, j, :] if j < 2 else gv[:, :, (j - 2) * P:(j - 1) * P]

        def sig(name, per, start=0):
            return Sig(sem(name), per, start)

        layer_ready = sig("layer_ready", 1)
        carried = sig("carried", 1)
        sq_ready, sq_used = sig("sq_ready", 20), sig("sq_used", 20)
        rstd_ready = sig("rstd_ready", 6)
        scaled, shifted = sig("scaled", 8), sig("shifted", 8)
        h_ready = sig("h_ready", 8)
        rope_raw, rope_mm, rope_done = sig("rope_raw", 9), sig("rope_mm", 9), sig("rope_done", 9)
        raw_in, w_hi, w_split = t["raw_in"], t["w_hi"], t["w_split"]
        lin_done, lin_free = t["lin_done"], t["lin_free"]
        ga_in = sig("ga_in", 16)
        ga_ready = sig("ga_ready", 1)
        logit_done, sig_ready = sig("logit_done", 1), sig("sig_ready", 1)
        bsum_ready = sig("bsum_ready", 1)
        s_ready, nm_ready, exp_done = sig("s_ready", 8), sig("nm_ready", 8), sig("exp_done", 8)
        rden_ready, pn_ready = sig("rden_ready", 8), sig("pn_ready", 8)
        pt_done, pt_evac_a, pt_evac_d = sig("pt_done", 8), sig("pt_evac_a", 8), sig("pt_evac_d", 8)
        pv_done, ao_done = sig("pv_done", 8), sig("ao_done", 4)
        r_scores, r_kd, r_qd = (sig(n, 4) for n in ("r_scores", "r_kd", "r_qd"))
        r_out, r_evac, r_state = (sig(n, 4) for n in ("r_out", "r_evac", "r_state"))
        z_ready, e_ready = sig("z_ready", LEVELS + 1), sig("e_ready", LEVELS + 1)
        eb_ready = sig("eb_ready", 2)
        lev_ready = sig("lev_ready", LEVELS)
        g_scores, g_picked = sig("g_scores", 4 * (LEVELS + 1)), sig("g_picked", 4 * (LEVELS + 1))
        qe_ready, kh_ready = sig("qe_ready", 1), sig("kh_ready", 1)
        kh_done, kh_evac = sig("kh_done", 4), sig("kh_evac", 4)
        g_out, g_evac, g_state = (sig(n, 4) for n in ("g_out", "g_evac", "g_state"))
        mix_hi, mix_ready = sig("mix_hi", 4), sig("mix_ready", 8)
        x_done = sig("x_done", 8, 1)
        dve_order = Order(nc.vector, sig("dve_order", 72))
        act_order = Order(nc.scalar, sig("act_order", 17))

        wait_seat = sem("wait_seat")
        block = ctx.enter_context(nc.Block())

        def layers_and_blocks(eng, layer_start=None):
            with eng.Fori(0, DEPTH) as l:
                if layer_start:
                    layer_start(l)
                with eng.Fori(0, NB) as b:
                    yield l, b, l * NB + b

        def rows(b):
            return bass.ds(b * W, W)

        def lin_product(pe, out, slot, first_wait=None):
            for k in range(KB):
                kw = slice(k * P, (k + 1) * P)
                for n, (w, h) in enumerate(((whi, h_hi), (whi, h_lo), (wlo, h_hi))):
                    last = nc.tensor.matmul(out, w[:, slot, kw], h[:, k, :], start=(k == 0 and n == 0),
                                            stop=(k == KB - 1 and n == 2))
            return last

        def token_product(slot, n_bank):
            for tile in range(NT):
                for k in range(KB):
                    for n, (h, w) in enumerate(((h_hi, whi), (h_lo, whi), (h_hi, wlo))):
                        last = nc.tensor.matmul(bank[n_bank][:, tile * P:(tile + 1) * P],
                                                h[:, k, tile * P:(tile + 1) * P], w[:, slot, k * P:(k + 1) * P],
                                                start=(k == 0 and n == 0), stop=(k == KB - 1 and n == 2))
            return last

        @block.sync
        def _(sp):
            def load(dst, src, s):
                sp.dma_start(dst, src).then_inc(raw_in[s].sem, 16)

            for s in range(2):
                load(wraw[:, s, 0:D], a["w1"][0, s], s)
            for l, b, it in layers_and_blocks(sp):
                sp.dma_start(wraw[:, 1, D:], a["w1_gate"][bass.ds(l, 1)].rearrange("o p n -> p (o n)"))\
                  .then_inc(ga_in.sem, 16)
                with sp.Fori(0, CH1 // 2 - 1) as i:
                    for s in range(2):
                        sp.wait_ge(*w_split.after(it, 2 * i + (s + 1)))
                        load(wraw[:, s, 0:D], a["w1"][bass.ds(l, 1), bass.ds(2 * i + (s + 2), 1)]
                             .rearrange("l c p n -> p (l c n)"), s)
                for s in range(2):
                    sp.wait_ge(*w_split.after(it, CH1 - 1 + s))
                    load(wraw[:, s, 0:D], a["w1_next"][bass.ds(it, 1), s].rearrange("o p n -> p (o n)"), s)

        @block.gpsimd
        def _(pool):
            def split_low(it, c, s, n=D):
                pool.wait_ge(*w_hi.after(it, c + 1))
                nc.gpsimd.tensor_tensor(wlo[:, s, 0:n], wraw[:, s, 0:n], whi[:, s, 0:n].bitcast(F32), ALU.subtract)\
                  .then_inc(*w_split.one)

            for s in range(2):
                split_low(0, s, s)
            for l, b, it in layers_and_blocks(pool):
                with pool.Fori(1, AV // 2) as i:
                    for s in range(2):
                        split_low(it, 2 * i + s, s)
                split_low(it, AV - 1, 0)
                split_low(it, AV, 1, D + KB * GATE_RANK)
                with pool.Fori(AV // 2 + 1, OUT1 // 2 + 1) as i:
                    for s in range(2):
                        split_low(it, 2 * i + s, s)
                for s in range(8):
                    pool.wait_ge(*rden_ready.after(it, s + 1))
                    nc.gpsimd.tensor_tensor(probs[s % 2], probs[s % 2],
                                            rden[:, s % 2, :].rearrange("p (g o) -> p g o", o=1)
                                            .to_broadcast([P, 4, 2 * P]), ALU.mult).then_inc(*pn_ready.one)
                for n in range(NT):
                    pool.wait_ge(*rope_done.after(it, ROPE1))
                    if n >= 2:
                        pool.wait_ge(*r_out.after(it, n - 1))
                    nc.gpsimd.tensor_tensor(qd[:, n % 2], rq[:, :, n * P:(n + 1) * P], t["ret_qdecay"][:], ALU.mult)\
                      .then_inc(*r_qd.one)
                for lv in range(LEVELS):
                    pool.wait_ge(*e_ready.after(it, lv + 1))
                    if lv == 0:
                        pool.wait_ge(*pv_done.after(it, 8))
                    if lv >= 2:
                        pool.wait_ge(*g_scores.after(it, 4 * (lv - 1)))
                    nc.gpsimd.tensor_tensor(lq[:, lv % 2], gq[:], zed[:, lv % 2], ALU.mult)
                    nc.gpsimd.tensor_tensor(lk[:, lv % 2], gk[:], zed[:, lv % 2], ALU.mult).then_inc(*lev_ready.one)
                pool.wait_ge(*eb_ready.after(it, 2))
                nc.gpsimd.tensor_tensor(qe, gq[:], eb, ALU.mult).then_inc(*qe_ready.one)
                pool.wait_ge(*e_ready.after(it, LEVELS + 1))
                nc.gpsimd.tensor_tensor(khat, gk[:], zed[:, LEVELS % 2], ALU.mult).then_inc(*kh_ready.one)
                with pool.Fori(OUT1 // 2 + 1, CH1 // 2 + 1) as i:
                    for s in range(2):
                        split_low(it, 2 * i + s, s)

        @block.scalar
        def _(act):
            link = act_order.link

            def split_high(it, c, s, n=D):
                act.wait_ge(raw_in[s].sem, raw_in[s].after(it, 16 * (c // 2 + 1))[1] if isinstance(c, int)
                            else raw_in[s].after(it, c * 8 + (16 - 8 * s))[1])
                nc.scalar.activation(whi[:, s, 0:n], wraw[:, s, 0:n], ACT.Copy).then_inc(*w_hi.one)

            def product(it, c):
                act.wait_ge(*lin_done.after(it, c + 1))

            def square(it, u, src):
                if u not in (0, 1):
                    act.wait_ge(*sq_used.after(it, u - 1))
                nc.scalar.activation(tmp[:, u % 2, :] if len(src.shape) == 2 else
                                     tmp[:, u % 2, :].rearrange("p (a b) -> p a b", b=P), src, ACT.Square)\
                  .then_inc(*sq_ready.one)

            def root(it, n, ps, width):
                if 2 <= n < 5:
                    act.wait_ge(*rstd_ready.after(it, n))
                link(nc.scalar.activation(logs, ps[:], ACT.Ln, scale=1.0 / width, bias=EPS))
                if 2 <= n < 5:
                    act.wait_ge(*mix_ready.after(it, 3 + n))
                nc.scalar.activation(rstd[:], logs, ACT.Exp, scale=-0.5).then_inc(*rstd_ready.one)

            act.sem_inc(lin_free.sem, 2)
            for s in range(2):
                split_high(0, s, s)
            for l, b, it in layers_and_blocks(act, lambda l: act.wait_ge(*layer_ready.after(l, 1))):
                act_order.begin(it)
                act.wait_ge(*x_done.after(it, 0))
                for k in range(KB):
                    square(it, k, x[:, k, rows(b)])
                act.wait_ge(*sq_used.after(it, KB))
                root(it, 0, bank[2], D)
                for k in range(KB):
                    act.wait_ge(*scaled.after(it, k + 1))
                    if k >= 2:
                        act.wait_ge(*h_ready.after(it, k - 1))
                    nc.scalar.activation(tmp[:, 4 + k % 2, :], tmp[:, 2 + k % 2, :], ACT.Identity,
                                         scale=col[:, C_A + k:C_A + k + 1], bias=col[:, C_B + k:C_B + k + 1])\
                      .then_inc(*shifted.one)
                for r in range(ROPE1):
                    product(it, r)
                    if r >= 2:
                        act.wait_ge(*rope_done.after(it, r - 1))
                    nc.scalar.activation(tmp[:, 6 + r % 2, :], bank[r % 2][:], ACT.Copy).then_inc(*rope_raw.one)
                    act.wait_ge(*rope_raw.after(it, r + 1))
                    act.sem_inc(lin_free.sem, 1)
                    split_high(it, r + 2, r % 2)
                product(it, GQ)
                nc.scalar.activation(gq[:], bank[1][:], ACT.Copy, scale=32 ** -0.5).then_inc(*lin_free.one)
                act.wait_ge(*ga_in.after(it, 16))
                split_high(it, AV, 1, D + KB * GATE_RANK)
                product(it, GK)
                nc.scalar.activation(gk[:], bank[0][:], ACT.Copy).then_inc(*lin_free.one)
                split_high(it, GK + 2, 0)
                product(it, AV)
                act.wait_ge(*carried.after(it, 1))
                nc.scalar.activation(ga[:], bank[4][0:GATE_RANK, :], ACT.Copy).then_inc(*ga_ready.one)
                nc.scalar.activation(av[:, 1:, :].rearrange("p t n -> p (t n)"), bank[1][:], ACT.Copy)\
                  .then_inc(*lin_free.one)
                split_high(it, AV + 2, 1)
                for c in range(RV, GATE1):
                    product(it, c)
                    dst = (rv if c < GV else gv)[:, :, (c % 2) * P:(c % 2 + 1) * P]
                    nc.scalar.activation(dst, bank[c % 2][:].rearrange("p (t n) -> p t n", n=P), ACT.Copy)\
                      .then_inc(*lin_free.one)
                    split_high(it, c + 2, c % 2)
                act.wait_ge(*logit_done.after(it, 1))
                link(nc.scalar.activation(zed[:, 0, :], bank[5][:], ACT.Identity, bias=col[:, C_GB:C_GB + 1]))
                link(nc.scalar.activation(zed[:, 1, :], zed[:, 0, :], ACT.Abs))
                link(nc.scalar.activation(zed[:, 1, :], zed[:, 1, :], ACT.Exp, scale=-1.0))
                nc.scalar.activation(zed[:, 1, :], zed[:, 1, :], ACT.Ln, bias=1.0).then_inc(*sig_ready.one)
                with act.Fori(0, (OUT1 - GATE1) // 2) as i:
                    for s in range(2):
                        product(it, 2 * i + (GATE1 + s))
                        nc.scalar.activation(gate_y[:, bass.ds(2 * i + s, 1), :].rearrange("p o n -> p (o n)"),
                                             bank[s][:], ACT.Silu).then_inc(*lin_free.one)
                        split_high(it, 2 * i + (GATE1 + s + 2), s)
                for j in range(10):
                    if j < 8:
                        act.wait_ge(*nm_ready.after(it, j + 1))
                        if j >= 2:
                            act.wait_ge(*pt_done.after(it, j - 1))
                        for g in range(4):
                            nc.scalar.activation(probs[j % 2][:, g, :], score(j)[:, g, :], ACT.Exp, scale=ATT_SCALE,
                                                 bias=nmax[:, j % 2, g:g + 1], accum_out=esum[:, j % 2, g:g + 1])
                        nc.scalar.activation(esink[:, j % 2, :], sink_arg[:, j % 2, :], ACT.Exp).then_inc(*exp_done.one)
                    if j >= 2:
                        s = j - 2
                        act.wait_ge(*pt_done.after(it, s + 1))
                        if s >= 2:
                            act.wait_ge(*pv_done.after(it, s - 1))
                        nc.scalar.activation(probsT[s % 2][:, 0, :], bankT[:, 0, :], ACT.Copy).then_inc(*pt_evac_a.one)
                act.wait_ge(*ao_done.after(it, NT))
                for j in range(4):
                    nc.scalar.activation(h_hi[:, j, :], aq[:, j, :], ACT.Copy).then_inc(*mix_hi.one)
                for n in range(NT):
                    act.wait_ge(*r_out.after(it, n + 1))
                    nc.scalar.activation(rq[:, :, n * P:(n + 1) * P],
                                         bank[n % 2][:, 0:256].rearrange("p (c n) -> p c n", n=P), ACT.Copy)\
                      .then_inc(*r_evac.one)
                act.wait_ge(*bsum_ready.after(it, 1))
                act.wait_ge(*pt_done.after(it, 8))
                nc.scalar.activation(eb, bsum[:], ACT.Exp).then_inc(*eb_ready.one)
                nc.scalar.activation(elast[:], bsum[:, P - 1::P], ACT.Exp).then_inc(*eb_ready.one)
                for lv in range(LEVELS + 1):
                    act.wait_ge(*z_ready.after(it, lv + 1))
                    link(nc.scalar.activation(zed[:, lv % 2], zed[:, lv % 2], ACT.Abs))
                    nc.scalar.activation(zed[:, lv % 2], zed[:, lv % 2], ACT.Exp, scale=-1.0).then_inc(*e_ready.one)
                for n in range(NT + 1):
                    if n < NT:
                        act.wait_ge(*kh_done.after(it, n + 1))
                        if n >= 2:
                            act.wait_ge(*g_out.after(it, n - 1))
                        nc.scalar.activation(khT[:, n % 2, :], bankT[:, n % 2, 0:P], ACT.Copy).then_inc(*kh_evac.one)
                    if n:
                        act.wait_ge(*g_out.after(it, n))
                        nc.scalar.activation(gv[:, n - 1, :], bank[(n - 1) % 2][:, 0:256], ACT.Copy)\
                          .then_inc(*g_evac.one)
                act.wait_ge(*r_evac.after(it, NT))
                act.wait_ge(*g_evac.after(it, NT))
                for j in range(4):
                    square(it, KB + j, mixed(j))
                for j in range(4):
                    act.wait_ge(*sq_used.after(it, KB + j + 1))
                    root(it, 1 + j, bankS[j], 64)
                with act.Fori(0, KB // 2) as i:
                    for s in range(2):
                        product(it, 2 * i + (OUT1 + s))
                        act.wait_ge(*sq_used.after(it, 2 * i + (KB + 4 + s - 1)))
                        nc.scalar.activation(tmp[:, s, :], bank[s][:], ACT.Square).then_inc(*sq_ready.one)
                        nc.scalar.activation(gate_y[:, bass.ds(2 * i + s, 1), :].rearrange("p o n -> p (o n)"),
                                             bank[s][:], ACT.Copy).then_inc(*lin_free.one)
                        split_high(it, 2 * i + (OUT1 + s + 2), s)
                act.wait_ge(*sq_used.after(it, 2 * KB + 4))
                root(it, 5, bank[2], D)
                act_order.end()

        @block.vector
        def _(dve):
            link = dve_order.link

            def layer_start(l):
                nc.vector.tensor_copy(col[:], cols1[:, bass.ds(l, 1), :].rearrange("p o n -> p (o n)"))
                nc.vector.tensor_copy(gw[:], t["gate_w"][:, bass.ds(l, 1), :].rearrange("p o n -> p (o n)"))
                for state in (ak[:], av[:], rstate[:], gstate[:]):
                    last = nc.vector.memset(state, 0.0)
                last.then_inc(*layer_ready.one)
                dve.wait_ge(*layer_ready.after(l, 1))
                dve.sem_inc(wait_seat, 1)

            def inverse_root(it, n):
                dve.wait_ge(*rstd_ready.after(it, n + 1))

            dve.sem_inc(x_done.sem, 1)
            for l, b, it in layers_and_blocks(dve, layer_start):
                dve_order.begin(it)
                link(nc.vector.tensor_copy(ak[:, 0:P], ak[:, W:W + P]))
                nc.vector.tensor_copy(av[:, 0, :], av[:, NT, :]).then_inc(*carried.one)
                inverse_root(it, 0)
                for k in range(KB + 1):
                    if k < KB:
                        if k >= 2:
                            dve.wait_ge(*shifted.after(it, k - 1))
                        nc.vector.tensor_tensor(tmp[:, 2 + k % 2, :], x[:, k, rows(b)], rstd[:], ALU.mult)\
                          .then_inc(*scaled.one)
                    if k:
                        n = k - 1
                        dve.wait_ge(*shifted.after(it, k))
                        link(nc.vector.tensor_copy(h_hi[:, n, :], tmp[:, 4 + n % 2, :]))
                        nc.vector.tensor_tensor(h_lo[:, n, :], tmp[:, 4 + n % 2, :], h_hi[:, n, :].bitcast(F32),
                                                ALU.subtract).then_inc(*h_ready.one)
                for r in range(ROPE1):
                    table = 0 if r < 5 else 2
                    out = aq[:, r, :] if r < 4 else ak[:, P:] if r == 4 else rq[:, r - 5, :] if r < 7 else rk[:, r - 7, :]
                    dve.wait_ge(*rope_raw.after(it, r + 1))
                    if r == 0:
                        dve.wait_ge(*h_ready.after(it, KB))
                    nc.vector.tensor_tensor(tmp[:, 2 + r % 2, :], tmp[:, 6 + r % 2, :], rope1[:, table, rows(b)],
                                            ALU.mult)
                    dve.wait_ge(*rope_mm.after(it, r + 1))
                    link(nc.vector.tensor_tensor(tmp[:, 4 + r % 2, :], bankS[r % 2][:], rope1[:, table + 1, rows(b)],
                                                 ALU.mult))
                    nc.vector.tensor_tensor(out, tmp[:, 2 + r % 2, :], tmp[:, 4 + r % 2, :], ALU.add)\
                      .then_inc(*rope_done.one)
                dve.wait_ge(*sig_ready.after(it, 1))
                link(nc.vector.tensor_scalar(zed[:, 0, :], zed[:, 0, :], 0.0, 1 / 16, ALU.min, ALU.mult))
                link(nc.vector.scalar_tensor_tensor(zed[:, 0, :], zed[:, 1, :], -1 / 16, zed[:, 0, :], ALU.mult, ALU.add))
                for n in range(NT):
                    part = slice(n * P, (n + 1) * P)
                    last = nc.vector.tensor_tensor_scan(bsum[:, part], t["ones"][:], zed[:, 0, part], 0.0,
                                                        ALU.mult, ALU.add)
                last.then_inc(*bsum_ready.one)
                dve.wait_ge(*bsum_ready.after(it, 1))
                for j in range(13):
                    if j < 8:
                        neg_sink = col[:, C_SINK + 4 * (j % 2):C_SINK + 4 * (j % 2) + 4]
                        dve.wait_ge(*s_ready.after(it, j + 1))
                        link(nc.vector.reduce_max(mx[:, j % 2, :], score(j), AX_X))
                        if j >= 2:
                            dve.wait_ge(*exp_done.after(it, j - 1))
                        link(nc.vector.scalar_tensor_tensor(nmax[:, j % 2, :], mx[:, j % 2, :], -ATT_SCALE, neg_sink,
                                                            ALU.mult, ALU.min))
                        nc.vector.tensor_tensor(sink_arg[:, j % 2, :], nmax[:, j % 2, :], neg_sink, ALU.subtract)\
                          .then_inc(*nm_ready.one)
                    if 1 <= j < 9:
                        s = j - 1
                        dve.wait_ge(*exp_done.after(it, s + 1))
                        link(nc.vector.tensor_tensor(esum[:, s % 2, :], esum[:, s % 2, :], esink[:, s % 2, :], ALU.add))
                        if s >= 2:
                            dve.wait_ge(*pn_ready.after(it, s - 1))
                        nc.vector.reciprocal(rden[:, s % 2, :], esum[:, s % 2, :]).then_inc(*rden_ready.one)
                    if 2 <= j < 10:
                        s = j - 2
                        dve.wait_ge(*pt_done.after(it, s + 1))
                        if s >= 2:
                            dve.wait_ge(*pv_done.after(it, s - 1))
                        nc.vector.tensor_copy(probsT[s % 2][:, 1, :], bankT[:, 1, :]).then_inc(*pt_evac_d.one)
                    if j >= 5 and j % 2:
                        n = (j - 5) // 2
                        part = slice(n * P, (n + 1) * P)
                        dve.wait_ge(*pv_done.after(it, 2 * n + 2))
                        nc.vector.tensor_tensor(aq[:, :, part], bank[n % 2][:].rearrange("p (g n) -> p g n", n=P),
                                                gate_y[:, 0:4, part], ALU.mult).then_inc(*ao_done.one)
                for j in range(4):
                    dve.wait_ge(*mix_hi.after(it, j + 1))
                    nc.vector.tensor_tensor(h_lo[:, j, :], aq[:, j, :], h_hi[:, j, :].bitcast(F32), ALU.subtract)\
                      .then_inc(*mix_ready.one)
                for n in range(NT + 1):
                    if n < NT:
                        dve.wait_ge(*r_scores.after(it, n + 1))
                        if n >= 2:
                            dve.wait_ge(*r_out.after(it, n - 1))
                        def by_parity(v):
                            return v.rearrange("p (c a) i -> p a c i", a=2)
                        nc.vector.tensor_tensor(by_parity(scm[:, n % 2]),
                                                scores[0][:].rearrange("p (a c i) -> p a c i", a=2, i=P)[:, :, 0:2, :],
                                                by_parity(t["ret_mask"][:]), ALU.mult)
                        nc.vector.tensor_tensor(kd[:, n % 2], bankS[2 + n % 2][:, 0:256], t["ret_kdecay"][:], ALU.mult)\
                          .then_inc(*r_kd.one)
                    if n:
                        dve.wait_ge(*r_out.after(it, n))
                        link(nc.vector.tensor_tensor(rnew[:], bankT[:, (n - 1) % 2, 0:256].rearrange("p (c v) -> p c v", c=2),
                                                     t["ones64"][:].rearrange("p (o v) -> p o v", o=1)
                                                     .to_broadcast([P, 2, P]), ALU.mult))
                        for c in range(2):
                            last = nc.vector.scalar_tensor_tensor(rstate[:, c, :], rstate[:, c, :],
                                                                  t["ret_cdecay"][:, c:c + 1], rnew[:, c, :],
                                                                  ALU.mult, ALU.add)
                        last.then_inc(*r_state.one)
                        dve.wait_ge(*r_state.after(it, n))
                def z_of(lv):
                    if lv >= 2:
                        dve.wait_ge(*lev_ready.after(it, lv - 1))
                    s = P >> (lv + 1)
                    if lv < LEVELS:
                        pairs = bsum[:].rearrange("p (n s) -> p n s", s=2 * s)
                        ref, n_ref, width = pairs[:, :, s - 1:s], W // (2 * s), 2 * s
                    else:
                        pairs = bsum[:].rearrange("p (n s) -> p n s", s=P)
                        ref, n_ref, width = pairs[:, :, P - 1:P], NT, P
                    nc.vector.tensor_tensor(zed[:, lv % 2].rearrange("p (n s) -> p n s", s=width), pairs,
                                            ref.to_broadcast([P, n_ref, width]), ALU.subtract).then_inc(*z_ready.one)

                z_of(0)
                z_of(1)
                for lv in range(LEVELS + 1):
                    if lv + 2 <= LEVELS:
                        z_of(lv + 2)
                    for h in range(4):
                        dve.wait_ge(*g_scores.after(it, 4 * lv + h + 1))
                        mask = t["gla_mask"][:, lv:lv + 1, :].to_broadcast([P, NT, P])
                        level = bankS[h][:].rearrange("p (n i) -> p n i", i=P)
                        dve.sem_inc(wait_seat, 1)
                        if lv == 0:
                            pick = nc.vector.tensor_tensor(gsc[:, :, h, :], level, mask, ALU.mult)
                        else:
                            pick = nc.vector.copy_predicated(gsc[:, :, h, :], mask, level)
                        pick.then_inc(*g_picked.one)
                for n in range(NT):
                    dve.wait_ge(*g_out.after(it, n + 1))
                    if n == 0:
                        dve.wait_ge(*eb_ready.after(it, 2))
                    link(nc.vector.tensor_tensor(gnew, bankS[n % 2][:, 0:256], t["gla_heads"][:], ALU.mult))
                    nc.vector.scalar_tensor_tensor(gstate[:], gstate[:], elast[:, n:n + 1], gnew, ALU.mult, ALU.add)\
                      .then_inc(*g_state.one)
                    dve.wait_ge(*g_state.after(it, n + 1))
                for j in range(4):
                    src = mixed(j)
                    view = (lambda v: v) if j < 2 else (lambda v: v.rearrange("p (t k) -> p t k", k=P))
                    gain = C_ONE if j < 2 else C_GN
                    inverse_root(it, 1 + j)
                    link(nc.vector.tensor_tensor(view(tmp[:, 2 + j % 2, :]), src, view(rstd[:]), ALU.mult))
                    link(nc.vector.scalar_tensor_tensor(tmp[:, 4 + j % 2, :], tmp[:, 2 + j % 2, :],
                                                        col[:, gain:gain + 1], gate_y[:, 4 + j, :], ALU.mult, ALU.mult))
                    link(nc.vector.tensor_copy(h_hi[:, 4 + j, :], tmp[:, 4 + j % 2, :]))
                    nc.vector.tensor_tensor(h_lo[:, 4 + j, :], tmp[:, 4 + j % 2, :], h_hi[:, 4 + j, :].bitcast(F32),
                                            ALU.subtract).then_inc(*mix_ready.one)
                inverse_root(it, 5)
                dve.wait_ge(*lin_free.after(it, CH1 + 2))
                for k in range(KB):
                    link(nc.vector.tensor_tensor(tmp[:, 2 + k % 2, :], gate_y[:, k, :], rstd[:], ALU.mult))
                    nc.vector.scalar_tensor_tensor(x[:, k, rows(b)], tmp[:, 2 + k % 2, :], col[:, C_G + k:C_G + k + 1],
                                                   x[:, k, rows(b)], ALU.mult, ALU.add).then_inc(*x_done.one)
                dve.wait_ge(*x_done.after(it, KB))
                dve_order.end()

        @block.tensor
        def _(pe):
            def ready(it, c):
                pe.wait_ge(*w_split.after(it, c + 1))
                pe.wait_ge(*lin_free.after(it, c + 1))

            def sum_squares(it, u, ps, start, stop, weights=t["ones"]):
                pe.wait_ge(*sq_ready.after(it, u + 1))
                return nc.tensor.matmul(ps[:], weights[:], tmp[:, (u if isinstance(u, int) else u[1]) % 2, :],
                                        start=start, stop=stop)

            def chunk(it, c, s):
                ready(it, c)
                lin_product(pe, bank[s][:], s).then_inc(*lin_done.one)

            def rotate(it, r, s):
                pe.wait_ge(*rope_raw.after(it, r + 1))
                if not isinstance(r, int) or r >= 2:
                    pe.wait_ge(*rope_done.after(it, r - 1))
                nc.tensor.matmul(bankS[s][:], t["rot1"][:], tmp[:, 6 + s, :], start=True, stop=True)\
                  .then_inc(*rope_mm.one)

            def layer_start(l):
                pe.wait_ge(*layer_ready.after(l, 1))
                pe.sem_inc(wait_seat, 1)

            for l, b, it in layers_and_blocks(pe, layer_start):
                for k in range(KB):
                    sum_squares(it, k, bank[2], k == 0, k == KB - 1).then_inc(*sq_used.one)
                pe.wait_ge(*h_ready.after(it, KB))
                chunk(it, 0, 0)
                chunk(it, 1, 1)
                rotate(it, 0, 0)
                with pe.Fori(1, 5) as i:
                    chunk(it, 2 * i, 0)
                    rotate(it, 2 * i - 1, 1)
                    chunk(it, 2 * i + 1, 1)
                    rotate(it, 2 * i, 0)
                chunk(it, GK, 0)
                ready(it, AV)
                for k in range(KB):
                    gate_cols = slice(D + k * GATE_RANK, D + (k + 1) * GATE_RANK)
                    for n, (w, h) in enumerate(((whi, h_hi), (whi, h_lo), (wlo, h_hi))):
                        nc.tensor.matmul(bank[4][0:GATE_RANK, :], w[:, 1, gate_cols], h[:, k, :],
                                         start=(k == 0 and n == 0), stop=(k == KB - 1 and n == 2))
                token_product(1, 1).then_inc(*lin_done.one)
                for c in range(RV, GATE1):
                    ready(it, c)
                    token_product(c % 2, c % 2).then_inc(*lin_done.one)
                    if c == RV:
                        pe.wait_ge(*ga_ready.after(it, 1))
                        nc.tensor.matmul(bank[5][:], gw[:], ga[:], start=True, stop=True).then_inc(*logit_done.one)
                with pe.Fori(GATE1 // 2, OUT1 // 2) as i:
                    for s in range(2):
                        chunk(it, 2 * i + s, s)
                pe.wait_ge(*rope_done.after(it, ROPE1))
                pe.wait_ge(*lin_free.after(it, OUT1 + 2))
                pe.wait_ge(*sig_ready.after(it, 1))
                for j in range(11):
                    if j < 8:
                        n, kv = j // 2, j % 2
                        half = slice(64 * kv, 64 * kv + 64)
                        if j >= 2:
                            pe.wait_ge(*exp_done.after(it, j - 1))
                        mask = mask1[:, bass.ds(b, 1), :].rearrange("p o n -> p (o n)") if n == 0 else mask1[:, 1, :]
                        for g in range(4):
                            nc.tensor.matmul(score(j)[:, g, :], aq[half, g, n * P:(n + 1) * P],
                                             ak[half, n * P:n * P + 2 * P], start=True, stop=False)
                            last = nc.tensor.matmul(score(j)[:, g, :], t["identb"][:], mask, start=False, stop=True)
                        last.then_inc(*s_ready.one)
                    if 2 <= j < 10:
                        s = j - 2
                        pe.wait_ge(*pn_ready.after(it, s + 1))
                        if s:
                            pe.wait_ge(*pt_evac_a.after(it, s))
                            pe.wait_ge(*pt_evac_d.after(it, s))
                        for kb in range(2):
                            for g in range(4):
                                last = nc.tensor.transpose(bankT[:, kb, g * P:(g + 1) * P],
                                                           probs[s % 2][:, g, kb * P:(kb + 1) * P], t["ident"][:])
                        last.then_inc(*pt_done.one)
                    if j >= 3:
                        s = j - 3
                        n, kv = s // 2, s % 2
                        half = slice(64 * kv, 64 * kv + 64)
                        pe.wait_ge(*pt_evac_a.after(it, s + 1))
                        pe.wait_ge(*pt_evac_d.after(it, s + 1))
                        if n >= 2:
                            pe.wait_ge(*ao_done.after(it, n - 1))
                        for kb in range(2):
                            last = nc.tensor.matmul(bank[n % 2][half, :], av[:, n + kb, half], probsT[s % 2][:, kb, :],
                                                    start=(kb == 0), stop=(kb == 1))
                        last.then_inc(*pv_done.one)
                pe.wait_ge(*ao_done.after(it, NT))
                for n in range(NT + 1):
                    if n < NT:
                        part = slice(n * P, (n + 1) * P)
                        if n:
                            pe.wait_ge(*r_kd.after(it, n))
                        for h in range(4):
                            half = slice(64 * (h % 2), 64 * (h % 2) + 64)
                            nc.tensor.matmul(bankS[h % 2][:, h // 2 * P:(h // 2 + 1) * P], rk[half, h // 2, part],
                                             rq[half, h // 2, part], start=True, stop=True)
                        for c in range(2):
                            last = nc.tensor.transpose(bankS[2 + n % 2][:, c * P:(c + 1) * P], rk[:, c, part], t["ident"][:])
                        last.then_inc(*r_scores.one)
                    if n:
                        m = n - 1
                        pe.wait_ge(*r_kd.after(it, m + 1))
                        pe.wait_ge(*r_qd.after(it, m + 1))
                        if m:
                            pe.wait_ge(*r_state.after(it, m))
                        if m >= 2:
                            pe.wait_ge(*r_evac.after(it, m - 1))
                        for c in range(2):
                            both = slice(c * P, (c + 1) * P)
                            nc.tensor.matmul(bankT[:, m % 2, both], kd[:, m % 2, both], rv[:, m, both],
                                             start=True, stop=True)
                        for c in range(2):
                            both = slice(c * P, (c + 1) * P)
                            nc.tensor.matmul(bank[m % 2][:, both], rstate[:, c, :], qd[:, m % 2, c, :],
                                             start=True, stop=False, skip_group_check=True)
                            for h in (2 * c, 2 * c + 1):
                                half = slice(64 * (h % 2), 64 * (h % 2) + 64)
                                last = nc.tensor.matmul(bank[m % 2][half, both], rv[:, m, 64 * h:64 * h + 64],
                                                        scm[:, m % 2, h, :], start=False, stop=(h % 2 == 1),
                                                        skip_group_check=True)
                        last.then_inc(*r_out.one)
                for lv in range(LEVELS + 1):
                    if lv < LEVELS:
                        pe.wait_ge(*lev_ready.after(it, lv + 1))
                    for h in range(4):
                        u = 4 * lv + h
                        dims = slice(32 * h, 32 * h + 32)
                        if lv:
                            pe.wait_ge(*g_picked.after(it, u - 3))
                        for n in range(NT):
                            part = slice(n * P, (n + 1) * P)
                            q = lq[dims, lv % 2, part] if lv < LEVELS else gq[dims, part]
                            k = lk[dims, lv % 2, part] if lv < LEVELS else gk[dims, part]
                            last = nc.tensor.matmul(bankS[h][:, part], k, q, start=True, stop=True)
                        last.then_inc(*g_scores.one)
                pe.wait_ge(*kh_ready.after(it, 1))
                pe.wait_ge(*qe_ready.after(it, 1))
                pe.wait_ge(*r_evac.after(it, NT))
                pe.wait_ge(*r_state.after(it, NT))
                pe.wait_ge(*g_picked.after(it, 4 * (LEVELS + 1)))
                for n in range(NT + 1):
                    if n < NT:
                        if n >= 2:
                            pe.wait_ge(*kh_evac.after(it, n - 1))
                        nc.tensor.transpose(bankT[:, n % 2, 0:P], khat[:, n * P:(n + 1) * P], t["ident"][:])\
                          .then_inc(*kh_done.one)
                    if n:
                        m = n - 1
                        pe.wait_ge(*kh_evac.after(it, m + 1))
                        if m:
                            pe.wait_ge(*g_state.after(it, m))
                        if m >= 2:
                            pe.wait_ge(*g_evac.after(it, m - 1))
                        nc.tensor.matmul(bankS[m % 2][:, 0:256], khT[:, m % 2, :], gv[:, m, :], start=True, stop=True)
                        for c in range(2):
                            both = slice(c * P, (c + 1) * P)
                            nc.tensor.matmul(bank[m % 2][:, both], gstate[:, both], qe[:, m * P:(m + 1) * P],
                                             start=True, stop=False, skip_group_check=True)
                            for h in (2 * c, 2 * c + 1):
                                half = slice(64 * (h % 2), 64 * (h % 2) + 64)
                                last = nc.tensor.matmul(bank[m % 2][half, both], gv[:, m, 64 * h:64 * h + 64],
                                                        gsc[:, m, h, :], start=False, stop=(h % 2 == 1),
                                                        skip_group_check=True)
                        last.then_inc(*g_out.one)
                pe.wait_ge(*g_state.after(it, NT))
                pe.wait_ge(*g_evac.after(it, NT))
                for j in range(4):
                    sum_squares(it, KB + j, bankS[j], True, True, t["ones64"]).then_inc(*sq_used.one)
                pe.wait_ge(*rstd_ready.after(it, 5))
                pe.wait_ge(*mix_ready.after(it, KB))
                base = KB + 4
                chunk(it, OUT1, 0)
                chunk(it, OUT1 + 1, 1)
                sum_squares(it, base, bank[2], True, False).then_inc(*sq_used.one)
                with pe.Fori(1, KB // 2) as i:
                    chunk(it, 2 * i + OUT1, 0)
                    pe.wait_ge(*sq_ready.after(it, 2 * i + base))
                    nc.tensor.matmul(bank[2][:], t["ones"][:], tmp[:, 1, :], start=False, stop=False).then_inc(*sq_used.one)
                    chunk(it, 2 * i + (OUT1 + 1), 1)
                    pe.wait_ge(*sq_ready.after(it, 2 * i + (base + 1)))
                    nc.tensor.matmul(bank[2][:], t["ones"][:], tmp[:, 0, :], start=False, stop=False).then_inc(*sq_used.one)
                sum_squares(it, base + KB - 1, bank[2], False, True).then_inc(*sq_used.one)


class Chain:

    def __init__(self, eng, sem):
        self.eng, self.sem, self.base, self.n = eng, sem, 0, 0
        self.reg, self.per, self.trips = 0, 0, 1

    def enter(self, reg, trips, per):
        self.base, self.n = self.base + self.n, 0
        self.reg, self.per, self.trips = reg, per, trips

    def leave(self):
        assert self.n == self.per, (self.n, self.per)
        self.base, self.n = self.base + self.per * self.trips, 0
        self.reg, self.per, self.trips = 0, 0, 1

    def link(self, ins):
        self.n += 1
        ins.then_inc(self.sem, 1)
        value = self.base + self.n
        self.eng.wait_ge(self.sem, value if isinstance(self.reg, int) else self.reg * self.per + value)


class Rows:

    def __init__(self, l, b):
        self.l, self.b, self.context = l, b, b == NB
        self.w = CTX if self.context else W
        self.tiles = self.w // P
        self.it = 3 * l + b
        self.latent_it = NB * l + b
        self.v = 1 if self.context else 0
        self.cols = slice(SEQ, TOKENS) if self.context else slice(b * W, b * W + W)


class Norm:

    def __init__(self, rows, no, gain=None, shift=None, after=None):
        self.rows, self.no, self.gain, self.shift = rows, no, gain, shift
        self.after = after


S1_AT, DFT_AT, WO_AT, FF_AT = [], [], [], []
_at = 0
for _l in range(DEPTH):
    _n = NB + 1 if _l == 0 else NB
    S1_AT.append(_at)
    _at += NB * IN2 + (IN2 if _l == 0 else 2)
    DFT_AT.append(_at)
    _at += DFT
    WO_AT.append(_at)
    _at += _n * KB
    FF_AT.append(_at)
    _at += _n * FF2
CHUNKS2 = _at
S1_STATS = [(), (0,), (1, 2), (3, 4), (5, 6), (7,)]


def second_block(nc, t, a, sems, out):
    sem = sems
    with ExitStack() as ctx:
        def sb(name, shape, dt=F32):
            return ctx.enter_context(nc.sbuf_tensor(name, shape, dt))

        x, wraw, whi, wlo, cols2 = t["x"], t["wraw"], t["whi"], t["wlo"], t["cols2"]
        xc = sb("xc", [P, KB, CTX])
        h_hi, h_lo = sb("h2_hi", [P, KB, W], F32R), sb("h2_lo", [P, KB, W], F32R)
        y, tmp, rstd = sb("y", [P, KB, W]), sb("tmp2", [P, 8, W]), sb("rstd2", [P, W])
        kz, kcz = sb("kz", [P, 2, SEQ + 2 * P]), sb("kcz", [P, 2, CTX])
        vx, vc = sb("vx", [P, SEQ // P + 2, P]), sb("vc", [P, CTX // P, P])
        qt = sb("qt", [P, 4, P])
        stats = [sb(n, [P, TOKENS // P, 8]) for n in ("nmax2", "esum2", "sink_arg2", "esink2", "rden2")]
        nmax, esum, sink_arg, esink, rden = stats
        mx = sb("mx2", [P, 2])
        ms = sb("ms", [P, 16])
        rot, mask, dims = sb("rot", [P, P]), sb("mask_band", [P, 3, 3 * P], BF16), sb("dims", [P, 256])
        w_s, b_s = sb("w_s", [P, DEPTH, 4, P]), sb("b_s", [P, DEPTH, 2, P])
        g_s, g_m, neg_sink = sb("g_s", [P, DEPTH, 2]), sb("g_m", [P, DEPTH, KB]), sb("neg_sink", [P, DEPTH, 8])
        with ExitStack() as mixers:
            q, u, f = (mixers.enter_context(nc.sbuf_tensor(n, [P, c, TOKENS], F32))
                       for n, c in (("q", 4), ("u", 2), ("f", 2)))
        a_hi, a_lo = sb("a_hi", [P, FF_CH, W], F32R), sb("a_lo", [P, FF_CH, W], F32R)
        table, gvn = y[:, 0:2, :], y[:, 2:4, :].rearrange("p a (n c) -> p (a n) c", c=256)
        dft_ctx = y[:, 4:6, :].rearrange("p a (k n) -> p a k n", k=2)
        y_flat = y[:].rearrange("p a n -> p (a n)")
        KEYS = 3 * P + CTX
        probs = [y_flat[:, KEYS * n:KEYS * (n + 1)] for n in range(2)]
        probsT = [y_flat[:, KEYS * (2 + n):KEYS * (3 + n)] for n in range(2)]
        o_tile = y_flat[:, 4 * KEYS:4 * KEYS + 512]
        mix_rstd = [y[:, 5 + n, :] for n in range(3)]
        mask_f = tmp[:, 0:3, 0:3 * P]

        lin0, lin1 = (ctx.enter_context(nc.psum_tensor(f"lin2_{n}", [P, 512], F32)) for n in range(2))
        scores = [ctx.enter_context(nc.psum_tensor(f"scores2_{n}", [P, 1024], F32)) for n in range(2)]
        bank = [lin0[:], lin1[:]] + [s[:, 512 * n:512 * n + 512] for s in scores for n in range(2)]
        bankT = ctx.enter_context(nc.psum_tensor("bankT2", [P, 1024], F32))

        def residual(p, k):
            return xc[:, k, :] if p.context else x[:, k, p.cols]

        def mixed(p, j):
            return (q[:, j, p.cols] if j < 4 else u[:, j - 4, p.cols] if j < 6 else f[:, j - 6, p.cols])

        def column(p, at):
            return cols2[:, p.l, p.v, at:at + 1]

        before = DEPTH * NB * CH1
        chunk_in = [Sig(t["raw_in"][s].sem, 8, before // 2 * 16 + 16 - 8 * s) for s in range(2)]
        w_hi, w_split = (Sig(t[n].sem, 1, before) for n in ("w_hi", "w_split"))
        lin_done, lin_free = (Sig(t[n].sem, 1, before) for n in ("lin_done", "lin_free"))
        EVACUATED = 3

        def sig(name, per, start=0):
            return Sig(sem("c_" + name), per, start)

        consts_in, consts_ready, table_in = sig("consts_in", 0), sig("consts_ready", 0), sig("table_in", 16)
        norms = {n: {s: sig(f"{n}_{s}", per) for s, per in
                     (("sq", KB), ("add", KB - sums), ("sum", sums), ("rstd", sums), ("scaled", KB), ("hi", KB), ("ready", KB))}
                 for n, sums in (("pre", 1), ("mix", 3), ("post", 1))}
        updated = sig("updated", KB)
        rope_mm, rope_done = sig("rope_mm", 5), sig("rope_done", 5)
        gv_ms, gv_rs, gv_ready = sig("gv_ms", 1), sig("gv_rs", 1), sig("gv_ready", 1)
        sgu_mm, sgu_done = sig("sgu_mm", 1), sig("sgu_done", 1)
        NDIM = [TOKENS // P, SEQ // P]
        dim_mm, dim_hi, dim_ready = sig("dim_mm", TOKENS // P), sig("dim_hi", TOKENS // P), sig("dim_ready", SEQ // P)
        ctx_dft, ctx_dft_done = sig("ctx_dft", 0), sig("ctx_dft_done", 0)
        s_ready, nm_ready, exp_done = sig("s_ready", 8), sig("nm_ready", 8), sig("exp_done", 8)
        pt_done, pt_evac_a, pt_evac_d, pv_done = (sig(n, 8) for n in ("pt_done", "pt_evac_a", "pt_evac_d", "pv_done"))
        qt_ready = sig("qt_ready", 4)
        sink_ready, esink_ready = sig("sink_ready", 1), sig("esink_ready", 1)
        o_done, ot_done, attn_done = sig("o_done", 1), sig("ot_done", 1), sig("attn_done", 1)
        a_sq = sig("a_sq", FF_CH)
        a_hi_ready, a_ready = sig("a_hi_ready", FF_CH), sig("a_ready", FF_CH, 2)
        saved = sig("saved", 0)
        wait_seat = sem("c_wait_seat")
        dve_chain, act_chain = Chain(nc.vector, sem("c_dve_chain")), Chain(nc.scalar, sem("c_act_chain"))
        block = ctx.enter_context(nc.Block())

        def rows_of(l):
            return [Rows(l, b) for b in range(NB + 1 if l == 0 else NB)]

        n_rows = [len(rows_of(l)) for l in range(DEPTH)]

        def pre_mix(l, b):
            return Norm(Rows(l, b), 2 * 3 * l + b, A1, B1, post_ff(l - 1, b) if l else None)

        def pre_ff(l, b):
            return Norm(Rows(l, b), 2 * 3 * l + 3 + b, A2, B2, post_mix(l, b))

        def mix(l, b):
            return Norm(Rows(l, b), 3 * l + b)

        def post_mix(l, b):
            return Norm(Rows(l, b), 2 * 3 * l + b, G1)

        def post_ff(l, b):
            return Norm(Rows(l, b), 2 * 3 * l + n_rows[l] + b, G2)

        def sources(n, kind, k):
            p = n.rows
            return mixed(p, k) if kind == "mix" else residual(p, k)

        S1_SUMS, FF_SUMS, MIX_SUMS, POST_SUMS = ([0], [1]), ([6], [7]), ([4, 5, 6], [7]), ([0], [1])
        MIX_OF = [0, 0, 0, 0, 1, 1, 2, 2]

        def part_of(kind, k):
            return (MIX_OF[k], k in (0, 4, 6)) if kind == "mix" else (0, k == 0)

        def adds_before(kind, k):
            return sum(not part_of(kind, j)[1] for j in range(k))

        def slot_of(kind, slots, k):
            return slots[adds_before(kind, k) % len(slots)]

        def attention_tiles(eng, l, body, chain=None, per=0):
            n = SEQ // P
            base = l * (TOKENS // P)
            body(0, base, 0, True, False)
            with eng.Fori(1, n - 1) as i:
                if chain:
                    chain.enter(i - 1, n - 2, per)
                body(i, i + base, 1, False, False)
            if chain:
                chain.leave()
            body(n - 1, base + n - 1, 2, False, True)
            if l == 0:
                body(n, base + n, None, True, False)
                body(n + 1, base + n + 1, None, False, True)

        def keys_of(mask_no):
            return (slice(P, 4 * P + CTX), 5) if mask_no is not None else (slice(4 * P, 4 * P + CTX), 2)

        def starts(no):
            return isinstance(no, int) and no == 0

        def lagging(tile, no, j, lag, first):
            if j >= lag:
                return tile, no, j - lag
            return None if first else (tile - 1, no - 1, j - lag + 8)

        def of_tile(v, tile):
            return v[:, tile, :] if isinstance(tile, int) else v[:, bass.ds(tile, 1), :].rearrange("p o h -> p (o h)")

        def of_head(v, tile, j):
            return v[:, tile, j:j + 1] if isinstance(tile, int) else v[:, bass.ds(tile, 1), j:j + 1].rearrange("p o h -> p (o h)")

        def token_cols(tile):
            return slice(tile * P, (tile + 1) * P) if isinstance(tile, int) else bass.ds(tile * P, P)

        @block.sync
        def _(sp):
            def load(g, s, src):
                sp.wait_ge(*w_split.after(g, -1))
                sp.dma_start(wraw[:, s, 0:D], src).then_inc(chunk_in[s].sem, 16)

            def run(g, l, at, n, skip=0):
                with sp.Fori(skip // 2, n // 2) as i:
                    for s in range(2):
                        load(2 * i + (g + s), s, a["w2"][l, bass.ds(2 * i + (at + s), 1)].rearrange("o p n -> p (o n)"))

            for l in range(DEPTH):
                blocks = NB + 1 if l == 0 else NB
                for b in range(blocks):
                    run(S1_AT[l] + b * IN2, l, 0, IN2, 2 if l == b == 0 else 0)
                if l:
                    for s, c in enumerate((K2, V2)):
                        load(S1_AT[l] + NB * IN2 + s, s, a["w2"][l, c])
                with sp.Fori(0, DFT // 2) as i:
                    for s in range(2):
                        load(2 * i + (DFT_AT[l] + s), s, a["dft_tokens"][bass.ds(2 * i + s, 1)].rearrange("o p n -> p (o n)"))
                for b in range(blocks):
                    run(WO_AT[l] + b * KB, l, IN2, KB)
                for b in range(blocks):
                    run(FF_AT[l] + b * FF2, l, IN2 + KB, FF2)
            for s in range(2):
                load(CHUNKS2 + s, s, a["w2"][0, s])
            sp.wait_ge(*updated.after(post_ff(DEPTH - 1, NB - 1).no, KB))
            sp.dma_start(out, x[:]).then_inc(saved.sem, 16)
            sp.wait_ge(saved.sem, 16)

        @block.gpsimd
        def _(pool):
            def split_low(g, s):
                pool.wait_ge(*w_hi.after(g, 1))
                nc.gpsimd.tensor_tensor(wlo[:, s, 0:D], wraw[:, s, 0:D], whi[:, s, 0:D].bitcast(F32), ALU.subtract)\
                  .then_inc(*w_split.one)

            def run(g, n):
                with pool.Fori(0, n // 2) as i:
                    for s in range(2):
                        split_low(2 * i + (g + 2 + s), s)

            def query_tile(tile, r):
                cols = slice(tile * P, (tile + 1) * P) if isinstance(tile, int) else bass.ds(tile * P, P)
                nc.gpsimd.tensor_copy(qt[:, r, :], q[:, r, cols]).then_inc(*qt_ready.one)

            for name, dst in (("ctx", xc[:]), ("rot2", rot[:]), ("mask2", mask_f), ("dft_dims", dims[:]),
                              ("dft_ctx", dft_ctx), ("w_sgu", w_s[:]), ("b_sgu", b_s[:]), ("g_sgu", g_s[:]),
                              ("g_mix", g_m[:]), ("sinks2", neg_sink[:])):
                pool.dma_start(dst, a[name]).then_inc(consts_in.sem, 16)
            for l in range(DEPTH):
                run(S1_AT[l], DFT_AT[l] - S1_AT[l])
                run(DFT_AT[l], DFT)

                def tile_queries(tile, no, mask_no, first, last):
                    for r in range(4):
                        if not starts(no):
                            pool.wait_ge(*s_ready.after(no - 1, 2 * r + 2))
                        query_tile(tile, r)

                pool.wait_ge(*lin_free.after(DFT_AT[l], 2))
                pool.wait_ge(*sgu_done.after(3 * l + n_rows[l], 0))
                attention_tiles(pool, l, tile_queries)
                run(WO_AT[l], FF_AT[l] - WO_AT[l])
                run(FF_AT[l], (NB + 1 if l == 0 else NB) * FF2)

        @block.scalar
        def _(act):
            link = act_chain.link

            def split_high(g, s):
                act.wait_ge(*chunk_in[s].after(g, 0))
                nc.scalar.activation(whi[:, s, 0:D], wraw[:, s, 0:D], ACT.Copy).then_inc(*w_hi.one)

            def square(kind, n, k, buffers, src):
                sig, w = norms[kind], n.rows.w
                sums, slots = buffers
                part, first = part_of(kind, k)
                done = adds_before(kind, k)
                if first:
                    dst = tmp[:, sums[part], 0:w]
                else:
                    dst = tmp[:, slot_of(kind, slots, k), 0:w]
                    if done >= len(slots):
                        act.wait_ge(*sig["add"].after(n.no, done - len(slots) + 1))
                nc.scalar.activation(dst, src, ACT.Square).then_inc(*sig["sq"].one)

            def residual_square(n, k, buffers):
                if n.after:
                    act.wait_ge(*updated.after(n.after.no, k + 1))
                square("pre", n, k, buffers, residual(n.rows, k))

            def roots(kind, n, dsts, banks, widths):
                w = n.rows.w
                for i, (dst, ps, width) in enumerate(zip(dsts, banks, widths)):
                    act.wait_ge(*norms[kind]["sum"].after(n.no, i + 1))
                    link(nc.scalar.activation(dst[:, 0:w], ps[:, 0:w], ACT.Ln, scale=1.0 / width, bias=EPS))
                for dst in dsts:
                    nc.scalar.activation(dst[:, 0:w], dst[:, 0:w], ACT.Exp, scale=-0.5).then_inc(*norms[kind]["rstd"].one)

            def root_pre(n, buffers):
                roots("pre", n, [tmp[:, buffers[0][0], :]], [bankT[:, 0:512]], [D])

            def root_post(n):
                if n.no:
                    act.wait_ge(*updated.after(n.no - 1, KB))
                roots("post", n, [rstd[:]], [bankT[:, 512:1024]], [D])

            def high(kind, n, k):
                sig, w = norms[kind], n.rows.w
                act.wait_ge(*sig["scaled"].after(n.no, k + 1))
                if kind == "mix":
                    ins = nc.scalar.activation(h_hi[:, k, 0:w], tmp[:, 2 + k % 2, 0:w], ACT.Copy)
                else:
                    ins = nc.scalar.activation(h_hi[:, k, 0:w], tmp[:, 2 + k % 2, 0:w], ACT.Identity,
                                               bias=column(n.rows, n.shift + k))
                ins.then_inc(*sig["hi"].one)

            def evacuate(g, s, dst, src, func=ACT.Copy):
                act.wait_ge(*lin_done.after(g, 1))
                nc.scalar.activation(dst, src, func).then_inc(*lin_free.one)
                split_high(g + 2, s)

            def project(l, b, last):
                n, p, g = pre_mix(l, b), Rows(l, b), S1_AT[l] + b * IN2
                nxt = None if last else pre_mix(l, b + 1)
                if b or l == 0:
                    for k in range(KB):
                        high("pre", n, k)
                if p.context and l:
                    for s, c in enumerate((K2, V2)):
                        context_kv(g + s, s, c)
                    return
                if not p.context:
                    if b:
                        act.wait_ge(*rope_done.after(p.latent_it, 0))
                    elif l:
                        act.wait_ge(*updated.after(post_ff(l - 1, NB).no, KB))
                    act.dma_start(table, a["rope2"][:, :, p.cols]).then_inc(table_in.sem, 16)
                if p.it:
                    act.wait_ge(*sgu_done.after(p.it, 0))
                act.wait_ge(*lin_done.after(g, 2))
                pairs = p.tiles // 2
                for s in range(pairs):
                    nc.scalar.activation(gvn[:, 2 * s:2 * s + 2, :].rearrange("p t n -> p (t n)"), bank[s], ACT.Gelu_apprx_tanh)\
                      .then_inc(lin_free.sem, 2 // pairs)
                for s in range(2):
                    split_high(g + 2 + s, s)
                for c in range(U2, U2 + 2):
                    evacuate(g + c, c % 2, u[:, c - U2, p.cols], bank[c % 2][:, 0:p.w], ACT.Gelu_apprx_tanh)
                for c in range(Q2, F2 + 2):
                    r = c - Q2
                    if r >= 5:
                        evacuate(g + c, c % 2, f[:, c - F2, p.cols], bank[c % 2][:, 0:p.w])
                    elif p.context:
                        if r < 4:
                            evacuate(g + c, c % 2, q[:, r, p.cols], bank[c % 2][:, 0:p.w])
                        else:
                            context_kv(g + c, c % 2, K2)
                    else:
                        if r >= 2:
                            act.wait_ge(*rope_done.after(p.latent_it, r - 1))
                        elif p.latent_it:
                            act.wait_ge(*rope_done.after(p.latent_it, 0))
                        evacuate(g + c, c % 2, tmp[:, 6 + r % 2, :], bank[c % 2][:])
                    if r == 1:
                        act.wait_ge(*gv_ms.after(p.it, 1))
                        part = ms[:, 0:4 * p.tiles]
                        link(nc.scalar.activation(part, part, ACT.Ln, scale=1.0 / 64, bias=EPS))
                        nc.scalar.activation(part, part, ACT.Exp, scale=-0.5).then_inc(*gv_rs.one)
                    if nxt and r < 6:
                        for k in S1_STATS[r]:
                            residual_square(nxt, k, S1_SUMS)
                if nxt:
                    root_pre(nxt, S1_SUMS)
                if p.context:
                    context_kv(g + V2, V2 % 2, V2)
                else:
                    evacuate(g + V2, V2 % 2, vx[:, b * NT + 1:b * NT + 1 + NT, :],
                             bank[V2 % 2][:].rearrange("p (t n) -> p t n", n=P))

            def context_kv(g, s, c):
                if c == V2:
                    evacuate(g, s, vc[:], bank[s][:, 0:CTX].rearrange("p (t n) -> p t n", n=P))
                    return
                act.wait_ge(*lin_done.after(g, 1))
                link(nc.scalar.activation(kcz[0:64, 0, :], bank[s][0:64, 0:CTX], ACT.Copy))
                evacuate(g, s, kcz[64:P, 1, :], bank[s][64:P, 0:CTX])

            def fourier(l):
                for n in range(NDIM[l]):
                    act.wait_ge(*dim_mm.after(l, n + 1))
                    if n < SEQ // P:
                        nc.scalar.activation(h_hi[:, n, :], bank[2 + n % 4], ACT.Copy).then_inc(*dim_hi.one)
                    else:
                        nc.scalar.activation(tmp[:, n - SEQ // P, :], bank[2 + n % 4], ACT.Copy).then_inc(*dim_hi.one)
                with act.Fori(0, DFT // 2) as i:
                    act.wait_ge(*lin_done.after(2 * i + DFT_AT[l], 2))
                    for s in range(2):
                        split_high(2 * i + (DFT_AT[l] + 2 + s), s)

            def attend(l):
                def sinks(tile, no):
                    act.wait_ge(*sink_ready.after(no, 1))
                    nc.scalar.activation(of_tile(esink, tile), of_tile(sink_arg, tile), ACT.Exp).then_inc(*esink_ready.one)

                def transposed(tile, no, j, n):
                    act.wait_ge(*pt_done.after(no, j + 1))
                    if j >= 2 or not starts(no):
                        act.wait_ge(*pv_done.after(no, j - 1))
                    rest = n // 2 * P
                    nc.scalar.activation(probsT[j % 2][:, n * P - rest:n * P], bankT[:, 512:512 + rest], ACT.Copy)\
                      .then_inc(*pt_evac_a.one)

                def outputs(tile, no):
                    act.wait_ge(*ot_done.after(no, 1))
                    nc.scalar.activation(q[:, :, token_cols(tile)], lin1[:].rearrange("p (c n) -> p c n", n=P), ACT.Copy)\
                      .then_inc(*attn_done.one)

                def body(tile, no, mask_no, first, last):
                    keys, n = keys_of(mask_no)
                    for j in range(8):
                        if j == 0 and not first:
                            sinks(tile - 1, no - 1)
                        act.wait_ge(*nm_ready.after(no, j + 1))
                        if j >= 2 or not starts(no):
                            act.wait_ge(*pt_done.after(no, j - 1))
                        nc.scalar.activation(probs[j % 2][:, 0:n * P], scores[j % 2][:, keys], ACT.Exp, scale=ATT_SCALE,
                                             bias=of_head(nmax, tile, j), accum_out=of_head(esum, tile, j))\
                          .then_inc(*exp_done.one)
                        step = lagging(tile, no, j, 2, first)
                        if step:
                            transposed(*step, n)
                        if j == 5 and not first:
                            outputs(tile - 1, no - 1)
                    if last:
                        sinks(tile, no)
                        for j in range(6, 8):
                            transposed(tile, no, j, n)
                        outputs(tile, no)

                attention_tiles(act, l, body)

            def mix_roots(n):
                roots("mix", n, [tmp[:, 4 + i, :] for i in range(3)], bank[2:5], (512, 256, 256))

            def merge(l, b, last):
                n, p, post, g = mix(l, b), Rows(l, b), post_mix(l, b), WO_AT[l] + b * KB
                prev = post_mix(l, b - 1) if b else None
                nxt = None if last else mix(l, b + 1)
                ff = pre_ff(l, 0) if last else None
                if b == 0:
                    act.wait_ge(*attn_done.after(l * (TOKENS // P), TOKENS // P if l == 0 else SEQ // P))
                    for k in range(KB):
                        square("mix", n, k, MIX_SUMS, mixed(p, k))
                    mix_roots(n)
                for k in range(KB):
                    high("mix", n, k)
                if prev:
                    root_post(prev)
                for k in range(KB):
                    s = k % 2
                    act.wait_ge(*lin_done.after(g + k, 1))
                    square("post", post, k, POST_SUMS, bank[s][:, 0:p.w])
                    if prev:
                        act.wait_ge(*updated.after(prev.no, k + 1))
                    nc.scalar.activation(y[:, k, 0:p.w], bank[s][:, 0:p.w], ACT.Copy).then_inc(*lin_free.one)
                    split_high(g + k + 2, s)
                    if nxt and k < 4:
                        for j in (2 * k, 2 * k + 1):
                            square("mix", nxt, j, MIX_SUMS, mixed(nxt.rows, j))
                    if nxt and k == 6:
                        mix_roots(nxt)
                    if ff and k:
                        residual_square(ff, k - 1, FF_SUMS)
                if ff:
                    residual_square(ff, KB - 1, FF_SUMS)
                    root_pre(ff, FF_SUMS)

            def hidden(gi, grp, j, s, w):
                act.wait_ge(*lin_done.after(gi, 1))
                act.wait_ge(*a_ready.after(grp, j - 1))
                nc.scalar.activation(tmp[:, 4 + s, 0:w], bank[s][:, 0:w], ACT.Relu).then_inc(*lin_free.one)
                split_high(gi + 2, s)
                act.wait_ge(*lin_free.after(gi, EVACUATED))
                unit = a_hi[:, j, 0:w] if isinstance(j, int) else a_hi[:, bass.ds(j, 1), 0:w].rearrange("p o n -> p (o n)")
                nc.scalar.activation(unit, tmp[:, 4 + s, 0:w], ACT.Square).then_inc(*a_hi_ready.one)

            def feed_forward(l, b, last):
                p, post, g0 = Rows(l, b), post_ff(l, b), FF_AT[l] + b * FF2
                prev = post_ff(l, b - 1) if b else post_mix(l, n_rows[l] - 1)
                nxt = pre_ff(l, b + 1) if not last else pre_mix(l + 1, 0) if l + 1 < DEPTH else None
                if b == 0:
                    for k in range(KB):
                        high("pre", pre_ff(l, b), k)

                def outputs(g):
                    with act.Fori(0, FF_CH // 2) as i:
                        for s in range(2):
                            act.wait_ge(*lin_done.after(g + (2 * i + (FF_CH + s)), 1))
                            split_high(g + (2 * i + (FF_CH + 2 + s)), s)

                act.wait_ge(*lin_free.after(g0, 2))
                for j in range(FF_CH):
                    hidden(g0 + j, p.it * FF_GROUPS, j, j % 2, p.w)
                    if j == 0:
                        root_post(prev)
                outputs(g0)
                with act.Fori(1, FF_GROUPS - 1) as q_no:
                    g = q_no * (2 * FF_CH) + g0
                    act.wait_ge(*lin_free.after(g, 2))
                    act.sem_inc(wait_seat, 1)
                    with act.Fori(0, FF_CH // 2) as i:
                        for s in range(2):
                            hidden(g + (2 * i + s), q_no + p.it * FF_GROUPS, 2 * i + s, s, p.w)
                    outputs(g)
                g, grp = g0 + (FF_GROUPS - 1) * 2 * FF_CH, (p.it + 1) * FF_GROUPS - 1
                act.wait_ge(*lin_free.after(g, 2))
                for j in range(FF_CH):
                    hidden(g + j, grp, j, j % 2, p.w)
                    if nxt:
                        residual_square(nxt, j, FF_SUMS)
                for k in range(KB):
                    gi = g + FF_CH + k
                    act.wait_ge(*lin_done.after(gi, 1))
                    split_high(gi + 2, k % 2)
                    act.wait_ge(*lin_free.after(gi, EVACUATED))
                    square("post", post, k, POST_SUMS, y[:, k, 0:p.w])
                    if nxt and k:
                        high("pre", nxt, k - 1)
                    elif nxt:
                        root_pre(nxt, FF_SUMS)
                if nxt:
                    high("pre", nxt, KB - 1)
                if last:
                    root_post(post)

            act.wait_ge(consts_ready.sem, 1)
            for k in range(KB):
                residual_square(pre_mix(0, 0), k, S1_SUMS)
            root_pre(pre_mix(0, 0), S1_SUMS)
            for l in range(DEPTH):
                for b in range(NB + 1):
                    project(l, b, b == NB)
                fourier(l)
                attend(l)
                for b in range(n_rows[l]):
                    merge(l, b, b == n_rows[l] - 1)
                for b in range(n_rows[l]):
                    feed_forward(l, b, b == n_rows[l] - 1)

        @block.vector
        def _(dve):
            link = dve_chain.link

            def add_square(kind, n, k, buffers):
                sig, w = norms[kind], n.rows.w
                sums, slots = buffers
                part, first = part_of(kind, k)
                if first:
                    return
                dve.wait_ge(*sig["sq"].after(n.no, k + 1))
                total = tmp[:, sums[part], 0:w]
                nc.vector.tensor_tensor(total, total, tmp[:, slot_of(kind, slots, k), 0:w], ALU.add).then_inc(*sig["add"].one)
                dve.wait_ge(*sig["add"].after(n.no, adds_before(kind, k) + 1))

            def scale(kind, n, k, buffers):
                sig, p = norms[kind], n.rows
                part = part_of(kind, k)[0]
                dve.wait_ge(*sig["rstd"].after(n.no, part + 1))
                gain = g_m[:, p.l, k:k + 1] if kind == "mix" else column(p, n.gain + k)
                nc.vector.scalar_tensor_tensor(tmp[:, 2 + k % 2, 0:p.w], sources(n, kind, k), gain,
                                               tmp[:, buffers[0][part], 0:p.w], ALU.mult, ALU.mult).then_inc(*sig["scaled"].one)

            def low(kind, n, k):
                sig, p = norms[kind], n.rows
                hi, scaled = h_hi[:, k, 0:p.w].bitcast(F32), tmp[:, 2 + k % 2, 0:p.w]
                dve.wait_ge(*sig["hi"].after(n.no, k + 1))
                if kind == "mix":
                    ins = nc.vector.tensor_tensor(h_lo[:, k, 0:p.w], scaled, hi, ALU.subtract)
                else:
                    ins = nc.vector.scalar_tensor_tensor(h_lo[:, k, 0:p.w], scaled, column(p, n.shift + k), hi,
                                                         ALU.add, ALU.subtract)
                ins.then_inc(*sig["ready"].one)
                dve.wait_ge(*sig["ready"].after(n.no, k + 1))

            def split(kind, n, buffers):
                for k in range(KB + 1):
                    if k < KB:
                        scale(kind, n, k, buffers)
                    if k:
                        low(kind, n, k - 1)

            def update(n, k):
                p = n.rows
                if k == 0:
                    dve.wait_ge(*norms["post"]["rstd"].after(n.no, 1))
                link(nc.vector.tensor_tensor(y[:, k, 0:p.w], y[:, k, 0:p.w], rstd[:, 0:p.w], ALU.mult))
                nc.vector.scalar_tensor_tensor(residual(p, k), y[:, k, 0:p.w], column(p, n.gain + k), residual(p, k),
                                               ALU.mult, ALU.add).then_inc(*updated.one)
                dve.wait_ge(*updated.after(n.no, k + 1))

            def project(l, b, last):
                n, p, g = pre_mix(l, b), Rows(l, b), S1_AT[l] + b * IN2
                nxt = None if last else pre_mix(l, b + 1)
                if b or l == 0:
                    split("pre", n, S1_SUMS)
                if p.context and l:
                    return
                values = gvn[:, 0:p.tiles, :]
                n_heads = 4 * p.tiles
                by_head = values.rearrange("p t (h d) -> p (t h) d", d=64)
                squares = tmp[:, 0:2, :].rearrange("p a n -> p (a n)")[:, 0:n_heads * 64].rearrange("p (h d) -> p h d", d=64)
                dve.wait_ge(*lin_free.after(g + (GV2 + 1), EVACUATED))
                link(nc.vector.tensor_tensor(squares, by_head, by_head, ALU.mult))
                nc.vector.reduce_sum(ms[:, 0:n_heads], squares, AX_X).then_inc(*gv_ms.one)
                for r in range(6):
                    if r == (0 if p.context else 2):
                        dve.wait_ge(*gv_rs.after(p.it, 1))
                        nc.vector.tensor_tensor(by_head, by_head,
                                                ms[:, 0:n_heads].rearrange("p (h o) -> p h o", o=1).to_broadcast([P, n_heads, 64]),
                                                ALU.mult).then_inc(*gv_ready.one)
                    if r < 5 and not p.context:
                        rotate(p, g, r)
                    if nxt:
                        for k in S1_STATS[r]:
                            add_square("pre", nxt, k, S1_SUMS)
                dve.wait_ge(*sgu_mm.after(p.it, 1))
                sums = scores[0][:].rearrange("p (t c n) -> p c t n", c=2, n=P)
                dve.wait_ge(*lin_free.after(g + (U2 + 1), EVACUATED))
                for c in range(2):
                    gated = tmp[:, 4 + c, 0:p.w].rearrange("p (t n) -> p t n", n=P)
                    link(nc.vector.scalar_tensor_tensor(gated, sums[:, c, 0:p.tiles, :], g_s[:, p.l, c:c + 1],
                                                        b_s[:, p.l, c:c + 1, :].to_broadcast([P, p.tiles, P]),
                                                        ALU.mult, ALU.add))
                    ins = nc.vector.tensor_tensor(u[:, c, p.cols], u[:, c, p.cols], tmp[:, 4 + c, 0:p.w], ALU.mult)
                    if c == 0:
                        link(ins)
                ins.then_inc(*sgu_done.one)
                dve.wait_ge(*sgu_done.after(p.it, 1))

            def rotate(p, g, r):
                if r == 0:
                    dve.wait_ge(*table_in.after(p.latent_it, 16))
                dve.wait_ge(*lin_free.after(g + (Q2 + r), EVACUATED))
                nc.vector.tensor_tensor(tmp[:, 2 + r % 2, :], tmp[:, 6 + r % 2, :], table[:, 0, :], ALU.mult)
                dve.wait_ge(*rope_mm.after(p.latent_it, r + 1))
                link(nc.vector.tensor_tensor(tmp[:, 4 + r % 2, :], bank[4 + r % 2], table[:, 1, :], ALU.mult))
                if r < 4:
                    nc.vector.tensor_tensor(q[:, r, p.cols], tmp[:, 2 + r % 2, :], tmp[:, 4 + r % 2, :], ALU.add)\
                      .then_inc(*rope_done.one)
                else:
                    keys = slice(p.b * W + P, p.b * W + P + W)
                    link(nc.vector.tensor_tensor(kz[0:64, 0, keys], tmp[0:64, 2, :], tmp[0:64, 4, :], ALU.add))
                    nc.vector.tensor_tensor(kz[64:P, 1, keys], tmp[64:P, 2, :], tmp[64:P, 4, :], ALU.add)\
                      .then_inc(*rope_done.one)
                    dve.wait_ge(*rope_done.after(p.latent_it, 5))

            def fourier(l):
                for n in range(SEQ // P):
                    dve.wait_ge(*dim_hi.after(l, n + 1))
                    nc.vector.tensor_tensor(h_lo[:, n, :], bank[2 + n % 4], h_hi[:, n, :].bitcast(F32), ALU.subtract)\
                      .then_inc(*dim_ready.one)
                with dve.Fori(0, DFT // 8) as i:
                    for s in range(2):
                        dve.wait_ge(*lin_done.after(8 * i + (DFT_AT[l] + 4 * s), 4))
                        nc.vector.tensor_copy(f[:, :, bass.ds(i * (4 * P) + 2 * s * P, 2 * P)],
                                              scores[s][:].rearrange("p (c n) -> p c n", c=2)[:, :, 0:2 * P])\
                          .then_inc(lin_free.sem, 4)
                if l == 0:
                    dve.wait_ge(ctx_dft.sem, 1)
                    nc.vector.tensor_copy(f[:, :, SEQ:], bankT[:].rearrange("p (c n) -> p c n", c=2)[:, :, 0:CTX])\
                      .then_inc(*ctx_dft_done.one)

            def attend(l):
                def maximum(tile, no, j, keys):
                    dve.wait_ge(*s_ready.after(no, j + 1))
                    link(nc.vector.reduce_max(mx[:, j % 2:j % 2 + 1], scores[j % 2][:, keys], AX_X))
                    nc.vector.scalar_tensor_tensor(of_head(nmax, tile, j), mx[:, j % 2:j % 2 + 1], -ATT_SCALE,
                                                   neg_sink[:, l, j:j + 1], ALU.mult, ALU.min).then_inc(*nm_ready.one)
                    if j == 7:
                        dve.wait_ge(*nm_ready.after(no, 8))
                        nc.vector.tensor_tensor(of_tile(sink_arg, tile), of_tile(nmax, tile), neg_sink[:, l, :],
                                                ALU.subtract).then_inc(*sink_ready.one)

                def transposed(tile, no, j, n):
                    dve.wait_ge(*pt_done.after(no, j + 1))
                    if j >= 2 or not starts(no):
                        dve.wait_ge(*pv_done.after(no, j - 1))
                    half = (n + 1) // 2 * P
                    nc.vector.tensor_copy(probsT[j % 2][:, 0:half], bankT[:, 0:half]).then_inc(*pt_evac_d.one)

                def denominators(tile, no):
                    dve.wait_ge(*esink_ready.after(no, 1))
                    link(nc.vector.tensor_tensor(of_tile(esum, tile), of_tile(esum, tile), of_tile(esink, tile), ALU.add))
                    link(nc.vector.reciprocal(of_tile(rden, tile), of_tile(esum, tile)))

                def outputs(tile, no):
                    dve.wait_ge(*pv_done.after(no, 8))
                    if not starts(no):
                        dve.wait_ge(*ot_done.after(no, 0))
                    share = of_tile(rden, tile).rearrange("p (r k) -> p k r", k=2)
                    for kv in range(2):
                        half = slice(256 * kv, 256 * kv + 256)
                        ins = nc.vector.tensor_tensor(o_tile[:, half].rearrange("p (h d) -> p h d", d=64),
                                                      lin0[:, half].rearrange("p (h d) -> p h d", d=64),
                                                      share[:, kv, :].rearrange("p (h o) -> p h o", o=1)
                                                      .to_broadcast([P, 4, 64]), ALU.mult)
                        if kv == 0:
                            link(ins)
                    ins.then_inc(*o_done.one)

                def body(tile, no, mask_no, first, last):
                    keys, n = keys_of(mask_no)
                    for j in range(8):
                        maximum(tile, no, j, keys)
                        step = lagging(tile, no, j, 2, first)
                        if step:
                            transposed(*step, n)
                        if j == 1 and not first:
                            denominators(tile - 1, no - 1)
                        if j == 3 and not first:
                            outputs(tile - 1, no - 1)
                    if last:
                        for j in range(6, 8):
                            transposed(tile, no, j, n)
                        denominators(tile, no)
                        outputs(tile, no)

                attention_tiles(dve, l, body, dve_chain, 8 + 3)

            def merge(l, b, last):
                n, p, post = mix(l, b), Rows(l, b), post_mix(l, b)
                prev = post_mix(l, b - 1) if b else None
                nxt = None if last else mix(l, b + 1)
                ff = pre_ff(l, 0) if last else None
                if b == 0:
                    for k in range(KB):
                        add_square("mix", n, k, MIX_SUMS)
                split("mix", n, MIX_SUMS)
                for k in range(KB):
                    if prev:
                        update(prev, k)
                    add_square("post", post, k, POST_SUMS)
                    if nxt and k < 4:
                        for j in (2 * k, 2 * k + 1):
                            add_square("mix", nxt, j, MIX_SUMS)
                    if ff and k:
                        add_square("pre", ff, k - 1, FF_SUMS)
                if ff:
                    add_square("pre", ff, KB - 1, FF_SUMS)

            def hidden(gi, grp, j, s, w):
                unit = slice(j, j + 1) if isinstance(j, int) else bass.ds(j, 1)
                dve.wait_ge(*lin_free.after(gi, EVACUATED))
                nc.vector.tensor_tensor(tmp[:, 2 + s, 0:w], tmp[:, 4 + s, 0:w], tmp[:, 4 + s, 0:w], ALU.mult).then_inc(*a_sq.one)
                dve.wait_ge(*a_sq.after(grp, j + 1))
                dve.wait_ge(*a_hi_ready.after(grp, j + 1))
                nc.vector.tensor_tensor(a_lo[:, unit, 0:w].rearrange("p o n -> p (o n)"), tmp[:, 2 + s, 0:w],
                                        a_hi[:, unit, 0:w].rearrange("p o n -> p (o n)").bitcast(F32),
                                        ALU.subtract).then_inc(*a_ready.one)
                dve.wait_ge(*a_ready.after(grp, j + 1))
                dve.sem_inc(wait_seat, 1)

            def feed_forward(l, b, last):
                p, post, g0 = Rows(l, b), post_ff(l, b), FF_AT[l] + b * FF2
                prev = post_ff(l, b - 1) if b else post_mix(l, n_rows[l] - 1)
                nxt = pre_ff(l, b + 1) if not last else pre_mix(l + 1, 0) if l + 1 < DEPTH else None
                if b == 0:
                    split("pre", pre_ff(l, b), FF_SUMS)

                def outputs(g, first):
                    with dve.Fori(0, FF_CH // 2) as i:
                        for s in range(2):
                            output(g + (2 * i + (FF_CH + s)), s, y[:, bass.ds(2 * i + s, 1), 0:p.w].rearrange("p o n -> p (o n)"), first)

                def output(gi, s, part, first):
                    dve.wait_ge(*lin_done.after(gi, 1))
                    if first:
                        nc.vector.tensor_copy(part, bank[s][:, 0:p.w]).then_inc(*lin_free.one)
                    else:
                        nc.vector.tensor_tensor(part, bank[s][:, 0:p.w], part, ALU.add).then_inc(*lin_free.one)

                for j in range(FF_CH):
                    hidden(g0 + j, p.it * FF_GROUPS, j, j % 2, p.w)
                    if j:
                        update(prev, j - 1)
                update(prev, KB - 1)
                dve.sem_inc(wait_seat, 1)
                outputs(g0, True)
                with dve.Fori(1, FF_GROUPS - 1) as q_no:
                    g = q_no * (2 * FF_CH) + g0
                    with dve.Fori(0, FF_CH // 2) as i:
                        for s in range(2):
                            hidden(g + (2 * i + s), q_no + p.it * FF_GROUPS, 2 * i + s, s, p.w)
                    outputs(g, False)
                g, grp = g0 + (FF_GROUPS - 1) * 2 * FF_CH, (p.it + 1) * FF_GROUPS - 1
                for j in range(FF_CH):
                    hidden(g + j, grp, j, j % 2, p.w)
                    if nxt:
                        add_square("pre", nxt, j, FF_SUMS)
                for k in range(KB):
                    output(g + FF_CH + k, k % 2, y[:, k, 0:p.w], False)
                    if nxt and k:
                        scale("pre", nxt, k - 1, FF_SUMS)
                    add_square("post", post, k, POST_SUMS)
                    if nxt and k:
                        low("pre", nxt, k - 1)
                if nxt:
                    scale("pre", nxt, KB - 1, FF_SUMS)
                    low("pre", nxt, KB - 1)
                if last:
                    for k in range(KB):
                        update(post, k)

            dve.wait_ge(consts_in.sem, 16 * 10)
            link(nc.vector.tensor_copy(mask[:], mask_f))
            link(nc.vector.tensor_scalar(neg_sink[:], neg_sink[:], -1.0, None, ALU.mult))
            for pad in (kz[:], kcz[:], vx[:]):
                link(nc.vector.memset(pad, 0.0))
            dve.sem_inc(consts_ready.sem, 1)
            dve.sem_inc(a_ready.sem, 2)
            for k in range(KB):
                add_square("pre", pre_mix(0, 0), k, S1_SUMS)
            for l in range(DEPTH):
                for b in range(NB + 1):
                    project(l, b, b == NB)
                fourier(l)
                attend(l)
                for b in range(n_rows[l]):
                    merge(l, b, b == n_rows[l] - 1)
                for b in range(n_rows[l]):
                    feed_forward(l, b, b == n_rows[l] - 1)

        @block.tensor
        def _(pe):
            def sum_over_partitions(kind, n, part, ps, total):
                if kind == "mix":
                    adds = (3, 4, 5)[part]
                else:
                    adds = KB - 1
                pe.wait_ge(*norms[kind]["add"].after(n.no, adds))
                nc.tensor.matmul(ps[:, 0:n.rows.w], t["ones"][:], tmp[:, total, 0:n.rows.w], start=True, stop=True)\
                  .then_inc(*norms[kind]["sum"].one)

            def sum_pre(n, buffers):
                sum_over_partitions("pre", n, 0, bankT[:, 0:512], buffers[0][0])

            def sum_post(n):
                sum_over_partitions("post", n, 0, bankT[:, 512:1024], POST_SUMS[0][0])

            def sum_mix(n):
                for i in range(3):
                    sum_over_partitions("mix", n, i, bank[2 + i], MIX_SUMS[0][i])

            def product(g, s, p, parts, when=None):
                hi, lo = parts
                pe.wait_ge(*lin_free.after(g, 1))
                pe.wait_ge(*w_hi.after(g, 1))
                for k in range(KB):
                    if when:
                        pe.wait_ge(*when(k))
                    for h in (hi, lo):
                        nc.tensor.matmul(bank[s][:, 0:p.w], whi[:, s, k * P:(k + 1) * P], h[:, k, 0:p.w],
                                         start=(k == 0 and h is hi), stop=False)
                pe.wait_ge(*w_split.after(g, 1))
                for k in range(KB):
                    last = nc.tensor.matmul(bank[s][:, 0:p.w], wlo[:, s, k * P:(k + 1) * P], hi[:, k, 0:p.w],
                                            start=False, stop=(k == KB - 1))
                last.then_inc(*lin_done.one)

            def token_product(g, s, p):
                pe.wait_ge(*lin_free.after(g, 1))
                pe.wait_ge(*w_split.after(g, 1))
                for tile in range(p.tiles):
                    for k in range(KB):
                        for n, (h, w) in enumerate(((h_hi, whi), (h_lo, whi), (h_hi, wlo))):
                            last = nc.tensor.matmul(bank[s][:, tile * P:(tile + 1) * P],
                                                    h[:, k, tile * P:(tile + 1) * P], w[:, s, k * P:(k + 1) * P],
                                                    start=(k == 0 and n == 0), stop=(k == KB - 1 and n == 2))
                last.then_inc(*lin_done.one)

            def token_pair(g, p, when):
                pe.wait_ge(*lin_free.after(g, 2))
                pe.wait_ge(*w_hi.after(g, 2))
                for tile in range(p.tiles):
                    for n, (h, w) in enumerate(((h_hi, whi), (h_lo, whi), (h_hi, wlo))):
                        if n == 2 and tile == 0:
                            pe.wait_ge(*w_split.after(g, 2))
                        for k in range(KB):
                            if tile == n == 0:
                                pe.wait_ge(*when(k))
                            at = tile % 2 * 256
                            last = nc.tensor.matmul(bank[tile // 2][:, at:at + 256].rearrange("p (c n) -> p c n", n=P),
                                                    h[:, k, tile * P:(tile + 1) * P], w[:, 0:2, k * P:(k + 1) * P],
                                                    start=(k == n == 0), stop=(k == KB - 1 and n == 2))
                last.then_inc(lin_done.sem, 2)

            h_parts, a_parts = (h_hi, h_lo), (a_hi, a_lo)

            def project(l, b, last):
                n, p, g = pre_mix(l, b), Rows(l, b), S1_AT[l] + b * IN2
                nxt = None if last else pre_mix(l, b + 1)

                def part_ready(k):
                    return norms["pre"]["ready"].after(n.no, k + 1)

                if p.context and l:
                    product(g, 0, p, h_parts, part_ready)
                    token_product(g + 1, 1, p)
                    return
                token_pair(g + GV2, p, part_ready)
                for c in range(U2, U2 + 2):
                    product(g + c, c % 2, p, h_parts)

                def rotate(r):
                    pe.wait_ge(*lin_free.after(g + (Q2 + r), EVACUATED))
                    if r >= 2:
                        pe.wait_ge(*rope_done.after(p.latent_it, r - 1))
                    nc.tensor.matmul(bank[4 + r % 2], rot[:], tmp[:, 6 + r % 2, :], start=True, stop=True)\
                      .then_inc(*rope_mm.one)

                for r in range(5):
                    product(g + (Q2 + r), (Q2 + r) % 2, p, h_parts)
                    if r and not p.context:
                        rotate(r - 1)
                product(g + F2, F2 % 2, p, h_parts)
                if not p.context:
                    rotate(4)
                pe.wait_ge(*gv_ready.after(p.it, 1))
                if p.it:
                    pe.wait_ge(*sgu_done.after(p.it, 0))
                for tile in range(p.tiles):
                    for h in range(4):
                        at = (2 * tile + h // 2) * P
                        sgu = nc.tensor.matmul(scores[0][64 * (h % 2):64 * (h % 2) + 64, at:at + P],
                                               gvn[:, tile, 64 * h:64 * h + 64], w_s[:, p.l, h, :], start=True, stop=True)
                sgu.then_inc(*sgu_mm.one)
                product(g + (F2 + 1), (F2 + 1) % 2, p, h_parts)
                if nxt:
                    sum_pre(nxt, S1_SUMS)
                token_product(g + V2, V2 % 2, p)

            def fourier(l):
                pe.wait_ge(*lin_free.after(DFT_AT[l], 2))
                pe.wait_ge(*sgu_done.after(3 * l + n_rows[l], 0))
                for n in range(NDIM[l]):
                    if n >= 4:
                        pe.wait_ge(*dim_ready.after(l, n - 3))
                    for c in range(2):
                        last = nc.tensor.matmul(bank[2 + n % 4][:, 256 * c:256 * c + 256], f[:, c, n * P:(n + 1) * P],
                                                dims[:], start=True, stop=True)
                    last.then_inc(*dim_mm.one)
                pe.wait_ge(*dim_ready.after(l, SEQ // P))
                pe.wait_ge(*dim_hi.after(l, NDIM[l]))
                if l == 0:
                    for c in range(2):
                        for part in range(2):
                            for k in range(CTX // P):
                                at = 256 * c + P * part
                                last = nc.tensor.matmul(bankT[:, 512 * c:512 * c + CTX], tmp[:, k, at:at + P],
                                                        dft_ctx[:, part, k, :], start=(part == k == 0),
                                                        stop=(part == k == 1))
                    last.then_inc(*ctx_dft.one)
                pe.sem_inc(wait_seat, 1)
                with pe.Fori(0, DFT // 8) as i:
                    for s in range(2):
                        g = 8 * i + (DFT_AT[l] + 4 * s)
                        pe.wait_ge(*lin_free.after(g, -2))
                        for part in range(2):
                            def passes(n, h, w):
                                for c in range(2):
                                    cols = slice(256 * c + P * part, 256 * c + P * part + P)
                                    for k in range(KB):
                                        last = nc.tensor.matmul(scores[s][:, 512 * c:512 * c + 2 * P]
                                                                .rearrange("p (t n) -> p t n", t=2),
                                                                h[:, k, cols], w[:, 0:2, k * P:(k + 1) * P],
                                                                start=(part == k == n == 0),
                                                                stop=(part == 1 and k == KB - 1 and n == 2))
                                return last

                            pe.wait_ge(*w_hi.after(g + 2 * part, 2))
                            passes(0, h_hi, whi)
                            passes(1, h_lo, whi)
                            pe.wait_ge(*w_split.after(g + 2 * part, 2))
                            passes(2, h_hi, wlo).then_inc(lin_done.sem, 2)

            def attend(l):
                pe.wait_ge(*lin_free.after(WO_AT[l], 2))
                if l == 0:
                    pe.wait_ge(ctx_dft_done.sem, 1)

                def score(tile, no, j, mask_no):
                    r, kv = j // 2, j % 2
                    if j % 2 == 0:
                        pe.wait_ge(*qt_ready.after(no, r + 1))
                    if j >= 2 or not starts(no):
                        pe.wait_ge(*exp_done.after(no, j - 1))
                    if mask_no is not None:
                        local = scores[kv][:, P:4 * P]
                        keys = slice(tile * P, tile * P + 3 * P) if isinstance(tile, int) else bass.ds(tile * P, 3 * P)
                        nc.tensor.matmul(local, qt[:, r, :], kz[:, kv, keys], start=True, stop=False)
                        nc.tensor.matmul(local, t["identb"][:], mask[:, mask_no, :], start=False, stop=True)
                    nc.tensor.matmul(scores[kv][:, 4 * P:4 * P + CTX], qt[:, r, :], kcz[:, kv, :], start=True, stop=True)\
                      .then_inc(*s_ready.one)

                def transpose(tile, no, j, n):
                    pe.wait_ge(*exp_done.after(no, j + 1))
                    if j or not starts(no):
                        pe.wait_ge(*pt_evac_a.after(no, j))
                        pe.wait_ge(*pt_evac_d.after(no, j))
                    for k in range(n):
                        at = k * P if k < (n + 1) // 2 else 512 + (k - (n + 1) // 2) * P
                        last = nc.tensor.transpose(bankT[:, at:at + P], probs[j % 2][:, k * P:(k + 1) * P],
                                                   t["ident"][:])
                    last.then_inc(*pt_done.one)

                def values(tile, no, j, n):
                    r, kv = j // 2, j % 2
                    pe.wait_ge(*pt_evac_a.after(no, j + 1))
                    pe.wait_ge(*pt_evac_d.after(no, j + 1))
                    if j == 0 and not starts(no):
                        pe.wait_ge(*o_done.after(no, 0))
                    head = (r + 4 * kv) * 64
                    half = slice(64 * kv, 64 * kv + 64)
                    for k in range(n):
                        c = k - (n - CTX // P)
                        if c >= 0:
                            v = vc[:, c, half]
                        elif isinstance(tile, int):
                            v = vx[:, tile + k, half]
                        else:
                            v = vx[:, bass.ds(tile + k, 1), half].rearrange("p o n -> p (o n)")
                        last = nc.tensor.matmul(lin0[:, head:head + 64], probsT[j % 2][:, k * P:(k + 1) * P], v,
                                                start=(k == 0), stop=(k == n - 1))
                    last.then_inc(*pv_done.one)

                def outputs(tile, no):
                    pe.wait_ge(*o_done.after(no, 1))
                    if not starts(no):
                        pe.wait_ge(*attn_done.after(no, 0))
                    for c in range(4):
                        last = nc.tensor.transpose(lin1[:, c * P:(c + 1) * P], o_tile[:, c * P:(c + 1) * P], t["ident"][:])
                    last.then_inc(*ot_done.one)

                def body(tile, no, mask_no, first, last):
                    n = keys_of(mask_no)[1]
                    for j in range(8):
                        score(tile, no, j, mask_no)
                        for lag, work in ((2, transpose), (3, values)):
                            step = lagging(tile, no, j, lag, first)
                            if step:
                                work(*step, n)
                        if j == 4 and not first:
                            outputs(tile - 1, no - 1)
                    if last:
                        for j in range(5, 8):
                            if j > 5:
                                transpose(tile, no, j, n)
                            values(tile, no, j, n)
                        outputs(tile, no)

                attention_tiles(pe, l, body)

            def merge(l, b, last):
                n, p, post, g = mix(l, b), Rows(l, b), post_mix(l, b), WO_AT[l] + b * KB
                nxt = None if last else mix(l, b + 1)
                if b == 0:
                    sum_mix(n)
                else:
                    sum_post(post_mix(l, b - 1))
                for k in range(KB):
                    product(g + k, k % 2, p, h_parts, (lambda j: norms["mix"]["ready"].after(n.no, j + 1)) if k == 0 else None)
                    if nxt and k == 5:
                        sum_mix(nxt)
                if last:
                    sum_pre(pre_ff(l, 0), FF_SUMS)

            def feed_forward(l, b, last):
                n, p, g0 = pre_ff(l, b), Rows(l, b), FF_AT[l] + b * FF2
                prev = post_ff(l, b - 1) if b else post_mix(l, n_rows[l] - 1)
                nxt = pre_ff(l, b + 1) if not last else pre_mix(l + 1, 0) if l + 1 < DEPTH else None

                def run(g, parts, first):
                    with pe.Fori(first // 2, FF_CH // 2) as i:
                        for s in range(2):
                            product(g + (2 * i + s), s, p, parts)

                def hidden_ready(grp):
                    return lambda k: a_ready.after(grp, k + 1)

                product(g0, 0, p, h_parts, lambda k: norms["pre"]["ready"].after(n.no, k + 1))
                sum_post(prev)
                product(g0 + 1, 1, p, h_parts)
                run(g0, h_parts, 2)
                product(g0 + FF_CH, 0, p, a_parts, hidden_ready(p.it * FF_GROUPS))
                product(g0 + FF_CH + 1, 1, p, a_parts)
                run(g0 + FF_CH, a_parts, 2)
                with pe.Fori(1, FF_GROUPS - 1) as q_no:
                    g = q_no * (2 * FF_CH) + g0
                    run(g, h_parts, 0)
                    product(g + FF_CH, 0, p, a_parts, hidden_ready(q_no + p.it * FF_GROUPS))
                    product(g + (FF_CH + 1), 1, p, a_parts)
                    run(g + FF_CH, a_parts, 2)
                g = g0 + (FF_GROUPS - 1) * 2 * FF_CH
                run(g, h_parts, 0)
                product(g + FF_CH, 0, p, a_parts, hidden_ready((p.it + 1) * FF_GROUPS - 1))
                if nxt:
                    sum_pre(nxt, FF_SUMS)
                product(g + FF_CH + 1, 1, p, a_parts)
                run(g + FF_CH, a_parts, 2)
                if last:
                    sum_post(post_ff(l, b))

            pe.wait_ge(consts_ready.sem, 1)
            sum_pre(pre_mix(0, 0), S1_SUMS)
            for l in range(DEPTH):
                for b in range(NB + 1):
                    project(l, b, b == NB)
                fourier(l)
                attend(l)
                for b in range(n_rows[l]):
                    merge(l, b, b == n_rows[l] - 1)
                for b in range(n_rows[l]):
                    feed_forward(l, b, b == n_rows[l] - 1)


CONSTS1 = ["ones64", "rot1", "ret_mask", "ret_qdecay", "ret_kdecay", "ret_cdecay", "gla_heads", "gla_mask"]


def program(nc, a, out):
    with ExitStack() as ctx:
        def sem(name):
            return ctx.enter_context(nc.semaphore(name))

        def sb(name, shape, dt=F32):
            return ctx.enter_context(nc.sbuf_tensor(name, shape, dt))

        wide = D + KB * GATE_RANK
        t = {"x": sb("x", [P, KB, SEQ]), "wraw": sb("wraw", [P, 2, wide]), "whi": sb("whi", [P, 2, wide], F32R),
             "wlo": sb("wlo", [P, 2, wide], F32R), "ident": sb("ident", [P, P]), "ones": sb("ones", [P, P]),
             "identb": sb("identb", [P, P], BF16), "cols2": sb("cols2", [P, DEPTH, 2, 2 * 24])}
        t["x_in"], t["const_in"] = sem("x_in"), sem("const_in")
        t["raw_in"] = [Sig(sem(f"raw_in{s}"), 8 * CH1) for s in range(2)]
        t["w_hi"], t["w_split"] = Sig(sem("w_hi"), CH1), Sig(sem("w_split"), CH1)
        t["lin_done"], t["lin_free"] = Sig(sem("lin_done"), CH1), Sig(sem("lin_free"), CH1)
        with ExitStack() as first:
            def sb1(name, shape, dt=F32):
                return first.enter_context(nc.sbuf_tensor(name, shape, dt))

            t["cols1"], t["rope1"] = sb1("cols1", [P, DEPTH, NCOL1]), sb1("rope1", [P, 4, SEQ])
            t["mask1"] = sb1("mask1", [P, 2, 2 * P], BF16)
            t["gate_w"] = sb1("gate_w", [GATE_RANK, DEPTH, P])
            for name in CONSTS1:
                t[name] = sb1(name, list(a[name].shape), U8 if name == "gla_mask" else F32)
            load_and_modulate(nc, t, a, sem)
            first_block(nc, t, a, sem)
        second_block(nc, t, a, sem, out)


def chunked(w):
    k, n = w.shape
    return w.reshape(k // P, P, n // P, P).transpose(2, 1, 0, 3).reshape(n // P, P, k)


def columns(v):
    return np.moveaxis(v.reshape(*v.shape[:-1], -1, P), -1, 0)


def kernel(**inp):
    import concourse.bacc as bacc
    from concourse.bass_utils import run_bass_kernel_spmd as run

    inp = {k: np.asarray(v) for k, v in inp.items()}
    heads = np.concatenate([np.arange(64 * h, 64 * h + 64) for h in HEAD_PAIRS])
    order1 = np.concatenate([heads, np.arange(512, 640), np.arange(1280, 1792), np.arange(2304, 2560),
                             np.arange(640, 768), np.arange(1792, 2048), np.arange(2560, 2816),
                             768 + heads, np.arange(2048, 2304), np.arange(2816, 3072)])
    out_rows = np.concatenate([heads, np.arange(512, 1024)])
    a = {}
    a["x"] = inp["x"][0].T.reshape(KB, P, SEQ).transpose(1, 0, 2)
    a["c"] = np.stack([inp[n].reshape(KB, P).T for n in ("c", "c_2", "c_ctx_2")], 2)
    a["positions"] = np.broadcast_to(inp["positions"][0], (P, SEQ))
    a["w_mod"] = np.concatenate([chunked(w) for w in inp["w_mod"]])
    a["w_ada"] = np.concatenate([chunked(w) for w in inp["w_ada_2"]])
    a["b_mod"] = np.concatenate([columns(inp[n]).reshape(P, -1) for n in ("b_mod", "b_ada_2")], 1)
    a["gains2"] = np.stack([columns(inp[f"g_{n}_2"]) for n in ("pre_mix", "post_mix", "pre_ff", "post_ff")], 2)
    gn = np.tile(inp["gla_norm_gain"], (1, 2))
    a["gains1"] = np.concatenate([columns(inp["pre_norm_gain"]), columns(inp["post_norm_gain"]),
                                  inp["gla_gate_b"].T[:, :, None], gn.T[:, :, None]], 2)
    a["sinks1"] = np.broadcast_to(inp["attn_sinks"], (P, DEPTH, 8))
    a["gate_w"] = inp["gla_gate_w"].transpose(1, 0, 2)
    a["w1"] = np.stack([np.concatenate([chunked(inp["w_in"][l][:, order1]), chunked(inp["w_out"][l][out_rows])])
                        for l in range(DEPTH)])
    a["w1_gate"] = np.stack([inp["w_in"][l][:, 3072:].reshape(KB, P, GATE_RANK).transpose(1, 0, 2).reshape(P, -1)
                             for l in range(DEPTH)])
    order2 = np.concatenate([np.arange(1024, 1280), np.arange(768, 1024), heads, np.arange(512, 640),
                             np.arange(1280, 1536), np.arange(640, 768)])
    hidden = KB * P
    a["w2"] = np.stack([np.concatenate(
        [chunked(inp["w_in_2"][l][:, order2]), chunked(inp["w_out_2"][l])]
        + [chunked(w) for g in range(FF_GROUPS) for w in (inp["w_ff1_2"][l][:, g * hidden:(g + 1) * hidden],
                                                          inp["w_ff2_2"][l][g * hidden:(g + 1) * hidden])])
        for l in range(DEPTH)])
    a["w1_next"] = np.stack([a["w1"][0, :2], a["w1"][1, :2], a["w1"][1, :2], a["w2"][0, :2]])
    a["ctx"] = inp["ctx_2"][0].T.reshape(KB, P, CTX).transpose(1, 0, 2)
    a["sinks2"] = np.broadcast_to(inp["sink_2"][:, HEAD_PAIRS], (P, DEPTH, 8))
    a["w_sgu"] = inp["w_sgu_2"].transpose(3, 0, 1, 2)
    a["b_sgu"] = np.repeat(inp["b_sgu_2"].reshape(DEPTH, 2, 2, P).transpose(2, 0, 1, 3), 64, axis=0)
    a["g_sgu"] = columns(inp["g_sgu_2"].reshape(DEPTH, 256))
    a["g_mix"] = columns(inp["g_mix_2"])
    a.update(constants())

    nc = bacc.Bacc("TRN2", target_bir_lowering=False, num_devices=1)
    a = {k: np.ascontiguousarray(v) for k, v in a.items()}
    aps = {k: nc.dram_tensor(f"in_{k}", v.shape, mybir.dt.from_np(v.dtype), kind="ExternalInput").ap() for k, v in a.items()}
    out = nc.dram_tensor("out", (P, KB, SEQ), F32, kind="ExternalOutput").ap()
    program(nc, aps, out)
    r = run(nc, [{f"in_{k}": v for k, v in a.items()}], core_ids=[0])
    got = r.results[0]["out"]
    return got.transpose(2, 1, 0).reshape(1, SEQ, D)
```

```python
from contextlib import ExitStack

import numpy as np

import concourse.bass as bass
from concourse import mybir

F32 = mybir.dt.float32
F32R = mybir.dt.float32r
BF16 = mybir.dt.bfloat16
I32 = mybir.dt.int32
U8 = mybir.dt.uint8
ALU = mybir.AluOpType
ACT = mybir.ActivationFunctionType
AX_X = mybir.AxisListType.X

P = 128
D = 1024
KB = D // P
SEQ = 1024
W = 512
NB = SEQ // W
NT = W // P
DEPTH = 2
EPS = 1e-6

ROPE1 = 9
GQ, GK, AV, RV, GV = 9, 10, 11, 12, 14
GATE1 = 16
OUT1 = 24
CH1 = 32
GATE_RANK = 16
LEVELS = 7
ATT_SCALE = 64 ** -0.5
HEAD_PAIRS = [0, 4, 1, 5, 2, 6, 3, 7]

CTX = 256
GRID_W = 64
TOKENS = SEQ + CTX
VEC = 3
MOD1, MOD2 = 3 * KB, 6 * KB
GV2, U2, Q2, K2, F2, V2 = 0, 2, 4, 8, 9, 11
IN2 = 12
FF_GROUPS = 4
FF_CH = 8
FF2 = FF_GROUPS * 2 * FF_CH
CH2 = IN2 + KB + FF2
DFT = 16
A1, B1, G1, A2, B2, G2 = range(0, 48, 8)

C_A, C_B, C_G, C_GB, C_GN, C_ONE, C_SINK = 0, 8, 16, 24, 25, 26, 32
NCOL1 = 40


class Sig:

    def __init__(self, sem, per=0, start=0):
        self.sem, self.per, self.start = sem, per, start

    def after(self, it, n):
        if isinstance(it, int):
            return self.sem, self.start + it * self.per + n
        return self.sem, it * self.per + (self.start + n)

    @property
    def one(self):
        return self.sem, 1


class Order:

    def __init__(self, eng, sig):
        self.eng, self.sig, self.n, self.it = eng, sig, 0, 0

    def begin(self, it):
        self.it, self.n = it, 0

    def link(self, ins):
        self.n += 1
        ins.then_inc(self.sig.sem, 1)
        self.eng.wait_ge(*self.sig.after(self.it, self.n))

    def end(self):
        assert self.n == self.sig.per, (self.n, self.sig.per)


def constants():
    f = np.float32
    c = {}
    c["ident"] = np.eye(P, dtype=f)
    c["ones"] = np.ones((P, P), f)
    half = np.arange(P) // 64
    c["both_parts"] = np.tile(np.eye(VEC, dtype=f), (2, 1))
    c["ones64"] = (half[:, None] == half[None, :]).astype(f)
    rot = np.zeros((P, P), f)
    for m in range(P):
        d = m % 64
        if d < 32:
            rot[m + 32, m] = -1
        else:
            rot[m - 32, m] = 1
    c["rot1"] = rot
    inv_a = (10000.0 ** (-np.arange(0, 64, 2, dtype=np.float64) / 64)).astype(f)
    steps = np.arange(32, dtype=f) * f(1 / 31)
    steps[-1] = 1
    inv_r = f(1) / np.power(10000.0, steps.astype(np.float64)).astype(f)
    c["inv_freq"] = np.stack([np.tile(inv_a, 4), np.tile(inv_r, 4)], 1)
    i, j = np.arange(P)[:, None], np.arange(2 * P)[None, :]
    rel = i + P - j
    ok = (rel >= 0) & (rel < P)
    c["mask1"] = np.stack([np.where(ok & (j >= P), 0, -1e30), np.where(ok, 0, -1e30)], 1).astype(f)
    log_g = np.log(1.0 - 2.0 ** (-5.0 - np.arange(4)))
    idx = np.arange(P, dtype=np.float64)
    diff = idx[None, :] - idx[:, None]
    dm = np.where(diff >= 0, np.exp(log_g[:, None, None] * np.maximum(diff, 0)), 0) * 64 ** -0.5
    c["ret_mask"] = dm.transpose(1, 0, 2).astype(f)
    qd = np.exp(log_g[:, None] * (idx + 1))
    c["ret_qdecay"] = np.stack([qd[2 * n + half] for n in range(2)], 1).astype(f)
    kd = np.exp(log_g[:, None] * (P - 1 - idx)) * 64 ** -0.5
    c["ret_kdecay"] = np.repeat(kd.T, 64, axis=1).astype(f)
    c["ret_cdecay"] = np.stack([np.exp(log_g * P)[2 * n + half] for n in range(2)], 1).astype(f)
    c["gla_heads"] = (np.arange(P)[:, None] // 32 == np.arange(256)[None, :] // 64).astype(f)
    m = np.zeros((P, LEVELS + 1, P), f)
    a = np.arange(P)
    for lv in range(LEVELS):
        s = 64 >> lv
        m[:, lv] = (a[:, None] // s % 2 == 0) & (a[None, :] // s == a[:, None] // s + 1)
    m[:, LEVELS] = np.eye(P)
    c["gla_mask"] = m
    rot = np.zeros((P, P), f)
    for m in range(P):
        d = m % 32
        if d < 16:
            rot[m + 16, m] = -1
        else:
            rot[m - 16, m] = 1
    c["rot2"] = rot
    inv = (10000.0 ** (-np.arange(16, dtype=np.float64) / 16)).astype(f)
    tok = np.arange(SEQ)
    row, column = (tok // GRID_W).astype(f), (tok % GRID_W).astype(f)
    ang = np.concatenate([np.tile(inv[:, None] * row[None], (2, 1)), np.tile(inv[:, None] * column[None], (2, 1))])
    ang = np.tile(ang, (2, 1)).astype(np.float64)
    c["rope2"] = np.stack([np.cos(ang), np.sin(ang)], 1).astype(f)
    i, j = np.arange(P)[:, None], np.arange(3 * P)[None, :] - P
    band = np.abs(j - i) <= P
    c["mask2"] = np.stack([np.where(ok, 0, -1e30) for ok in (band & (j >= 0), band, band & (j < P))], 1).astype(f)
    w = 2 * np.pi * np.outer(np.arange(64), np.arange(64)) / 64
    two = np.kron(np.eye(2), np.ones((64, 64)))
    c["dft_dims"] = (np.concatenate([np.tile(np.cos(w), (2, 2)) * two, np.tile(np.sin(w), (2, 2)) * two], 1) / 256).astype(f)
    w = 2 * np.pi * (np.outer(np.arange(SEQ), np.arange(SEQ)) % SEQ) / SEQ
    c["dft_tokens"] = np.stack([chunked(v.astype(f)).reshape(-1, 2, P, SEQ) for v in (np.cos(w), -np.sin(w))], 1)\
        .reshape(-1, P, SEQ)
    w = 2 * np.pi * (np.outer(np.arange(CTX), np.arange(CTX)) % CTX) / CTX
    both = np.stack([2 * np.cos(w), -2 * np.sin(w)])
    c["dft_ctx"] = both.reshape(2, 2, P, CTX).transpose(2, 0, 1, 3).astype(f)
    return c


TWO_PI = 2 * np.pi
C1 = 6.28125
C2 = 0.0019350051879882812
C3 = TWO_PI - C1 - C2
MAGIC = 12582912.0
PI_IN = 3.1415925


def load_and_modulate(nc, t, a, sems):
    sem = sems
    GROUP = 4
    NRING = 2 * GROUP
    PAIR = 2
    K_POOL = 3
    PAIRS = NRING // PAIR
    n1, n2 = DEPTH * MOD1, DEPTH * MOD2
    chunks = n1 + n2
    passes = chunks // NRING
    early = (n1 + MOD2) // NRING
    with ExitStack() as ctx:
        ring = ctx.enter_context(nc.sbuf_tensor("mod_ring", [P, NRING, D], F32))
        pos_i = ctx.enter_context(nc.sbuf_tensor("pos_i", [P, SEQ], I32))
        pos_f = ctx.enter_context(nc.sbuf_tensor("pos_f", [P, SEQ], F32))
        ang = ctx.enter_context(nc.sbuf_tensor("ang", [P, SEQ], F32))
        turns = ctx.enter_context(nc.sbuf_tensor("turns", [P, SEQ], F32))
        arg = ctx.enter_context(nc.sbuf_tensor("arg", [P, 4, SEQ], F32))
        cvec = ctx.enter_context(nc.sbuf_tensor("cvec", [P, KB, VEC], F32))
        cact = ctx.enter_context(nc.sbuf_tensor("cact", [P, KB, VEC], F32))
        cparts = ctx.enter_context(nc.sbuf_tensor("cparts", [P, KB, 2 * VEC], F32R))
        both_parts = ctx.enter_context(nc.sbuf_tensor("both_parts", [2 * VEC, VEC], F32))
        bias = ctx.enter_context(nc.sbuf_tensor("mod_bias", [P, chunks], F32))
        mod = ctx.enter_context(nc.sbuf_tensor("mod", [P, DEPTH, MOD1], F32))
        mod2 = ctx.enter_context(nc.sbuf_tensor("mod2", [P, DEPTH, 2, MOD2], F32))
        gains2 = ctx.enter_context(nc.sbuf_tensor("gains2", [P, DEPTH, 4, KB], F32))
        gains = ctx.enter_context(nc.sbuf_tensor("gains", [P, DEPTH, 18], F32))
        sinks = ctx.enter_context(nc.sbuf_tensor("sinks", [P, DEPTH, 8], F32))
        mask_f = ctx.enter_context(nc.sbuf_tensor("mask_f", [P, 2, 2 * P], F32))
        levels_f = ctx.enter_context(nc.sbuf_tensor("levels_f", [P, LEVELS + 1, P], F32))
        inv = ctx.enter_context(nc.sbuf_tensor("inv", [P, 2], F32))
        psM = [ctx.enter_context(nc.psum_tensor(f"psM{n}", [P, 512], F32)) for n in range(2)]
        psR = [ctx.enter_context(nc.psum_tensor(f"psR{n}", [P, 512], F32)) for n in range(2)]
        row = ctx.enter_context(nc.sbuf_tensor("mod_row", [2 * VEC, 2, GROUP * P], F32))
        m_hi, m_lo = (t[n][:].rearrange("p k n -> p (k n)").rearrange("p (s k n) -> p s k n", s=2, k=KB)
                      for n in ("h_hi", "h_lo"))

        chunk_in = [sem(f"mod_chunk_in{s}") for s in range(NRING)]
        hi_ready, lo_pool, lo_dve, pair_done = sem("mod_hi"), sem("mod_lo_pool"), sem("mod_lo_dve"), sem("mod_pair_done")
        vec_in, pos_in, small_in = sem("vec_in"), sem("pos_in"), sem("small_in")
        cact_ready, args_ready = sem("cact_ready"), sem("args_ready")
        tables_ready, cols2_ready = sem("tables_ready"), sem("cols2_ready")
        ident_in = sem("ident_in")
        row_ready, row_used = sem("row_ready"), sem("row_used")
        order = Order(nc.vector, Sig(sem("prep_order")))
        block = ctx.enter_context(nc.Block())

        @block.sync
        def _(sp):
            sp.dma_start(cvec[:], a["c"]).then_inc(vec_in, 16)
            sp.dma_start(t["ident"][:], a["ident"]).then_inc(ident_in, 16)
            sp.dma_start(both_parts[:], a["both_parts"]).then_inc(ident_in, 16)
            sp.dma_start(pos_i[:], a["positions"]).then_inc(pos_in, 16)
            sp.dma_start(inv[:], a["inv_freq"]).then_inc(pos_in, 16)
            for s in range(NRING):
                sp.dma_start(ring[:, s, :], a["w_mod"][s]).then_inc(chunk_in[s], 16)
            loads = [(bias, "b_mod"), (gains, "gains1"), (sinks, "sinks1"), (mask_f, "mask1"), (gains2, "gains2"),
                     (levels_f, "gla_mask")]
            for dst, name in loads:
                sp.dma_start(dst[:], a[name]).then_inc(small_in, 16)
            with sp.Fori(0, n1 // NRING - 1) as i:
                for s in range(NRING):
                    sp.wait_ge(lo_pool, i * PAIRS + (s // 2 + 1))
                    sp.wait_ge(lo_dve, i * PAIRS + (s // 2 + 1))
                    sp.dma_start(ring[:, s, :], a["w_mod"][bass.ds(i * NRING + (NRING + s), 1)]
                                 .rearrange("o p n -> p (o n)")).then_inc(chunk_in[s], 16)
            with sp.Fori(n1 // NRING - 1, passes - 1) as i:
                for s in range(NRING):
                    sp.wait_ge(lo_pool, i * PAIRS + (s // 2 + 1))
                    sp.wait_ge(lo_dve, i * PAIRS + (s // 2 + 1))
                    sp.dma_start(ring[:, s, :], a["w_ada"][bass.ds(i * NRING + (NRING - n1 + s), 1)]
                                 .rearrange("o p n -> p (o n)")).then_inc(chunk_in[s], 16)

        def low_part(j, k0, k1):
            raw = ring[:, PAIR * j:PAIR * j + PAIR, k0 * P:k1 * P].rearrange("p c (k n) -> p k c n", n=P)
            lo, hi = (v[:, j % 2, k0:k1, :].rearrange("p k (c n) -> p k c n", c=PAIR) for v in (m_lo, m_hi))
            return lo, raw, hi.bitcast(F32)

        @block.gpsimd
        def _(pool):
            for name in ("ones", "ones64", "rot1", "ret_mask", "ret_qdecay", "ret_kdecay", "ret_cdecay",
                         "gla_heads", "gate_w"):
                pool.dma_start(t[name][:], a[name]).then_inc(t["const_in"], 16)
            pool.dma_start(t["x"][:], a["x"]).then_inc(t["x_in"], 16)
            with pool.Fori(0, passes) as i:
                for j in range(PAIRS):
                    pool.wait_ge(hi_ready, i * PAIRS + (j + 1))
                    nc.gpsimd.tensor_tensor(*low_part(j, 0, K_POOL), ALU.subtract).then_inc(lo_pool, 1)
            pool.wait_ge(t["x_in"], 16)
            pool.wait_ge(t["const_in"], 16 * 9)

        @block.scalar
        def _(act):
            act.wait_ge(vec_in, 16)
            nc.scalar.activation(cact[:], cvec[:], ACT.Silu).then_inc(cact_ready, 1)

            act.wait_ge(cact_ready, 1)
            nc.scalar.activation(cparts[:, :, 0:VEC], cact[:], ACT.Copy).then_inc(cact_ready, 1)

            def high(i, j):
                for c in range(PAIR):
                    act.wait_ge(chunk_in[PAIR * j + c], i * 16 + 16)
                if not isinstance(i, int) or j >= 2:
                    act.wait_ge(pair_done, i * PAIRS + (j - 1))
                raw = ring[:, PAIR * j:PAIR * j + PAIR, :].rearrange("p c (k n) -> p k c n", k=KB)
                nc.scalar.activation(m_hi[:, j % 2].rearrange("p k (c n) -> p k c n", c=PAIR), raw, ACT.Copy)\
                  .then_inc(hi_ready, 1)

            def row_out(i, s):
                act.wait_ge(pair_done, i * PAIRS + (2 * s + 2))
                act.wait_ge(row_used, i * 2 + (s + 1))
                nc.scalar.activation(row[:, s, :], psR[s][0:2 * VEC, :], ACT.Copy).then_inc(row_ready, 1)

            def run(first, last):
                with act.Fori(first - 1, last - 1) as before:
                    i = before + 1
                    high(i, 0)
                    high(i, 1)
                    row_out(before, 1)
                    high(i, 2)
                    high(i, 3)
                    row_out(i, 0)

            for j in range(PAIRS):
                high(0, j)
            row_out(0, 0)
            run(1, passes // 2 + 1)
            for n in range(4):
                act.wait_ge(args_ready, n + 1)
                nc.scalar.activation(t["rope1"][:, n, :], arg[:, n, :], ACT.Sin).then_inc(tables_ready, 1)
            run(passes // 2 + 1, passes)
            row_out(passes - 1, 1)
            act.wait_ge(tables_ready, 4)

        @block.tensor
        def _(pe):
            pe.wait_ge(cact_ready, 3)
            pe.sem_inc(row_used, 2)

            def products(i, s):
                for j in (2 * s, 2 * s + 1):
                    pe.wait_ge(lo_pool, i * PAIRS + (j + 1))
                    pe.wait_ge(lo_dve, i * PAIRS + (j + 1))
                    out = psR[s][0:2 * VEC, (j % 2) * PAIR * P:(j % 2 + 1) * PAIR * P]
                    for k in range(KB):
                        for n, part in enumerate((m_hi, m_lo)):
                            last = nc.tensor.matmul(out, cparts[:, k, :], part[:, j % 2, k, :],
                                                    start=(k + n == 0), stop=(k + n == KB))
                    last.then_inc(pair_done, 1)

            def to_columns(i, s, bank):
                pe.wait_ge(row_ready, i * 2 + (s + 1))
                for c in range(GROUP):
                    col = (i - bank * early) * (NRING * VEC) + (s * GROUP + c) * VEC
                    col = slice(col, col + VEC) if isinstance(i, int) else bass.ds(col, VEC)
                    last = nc.tensor.matmul(psM[bank][:, col], row[:, s, c * P:(c + 1) * P], both_parts[:],
                                            start=True, stop=True)
                last.then_inc(row_used, 1)

            products(0, 0)
            products(0, 1)
            pe.wait_ge(ident_in, 32)
            to_columns(0, 0, 0)

            def run(first, last, bank):
                with pe.Fori(first, last) as i:
                    products(i, 0)
                    to_columns(i - 1, 1, bank)
                    products(i, 1)
                    to_columns(i, 0, bank)

            run(1, early, 0)
            products(early, 0)
            to_columns(early - 1, 1, 0)
            products(early, 1)
            to_columns(early, 0, 1)
            run(early + 1, passes, 1)
            to_columns(passes - 1, 1, 1)

        @block.vector
        def _(dve):
            link = order.link

            def low(i, j):
                dve.wait_ge(hi_ready, i * PAIRS + (j + 1))
                nc.vector.tensor_tensor(*low_part(j, K_POOL, KB), ALU.subtract).then_inc(lo_dve, 1)

            def low_passes(first, last):
                with dve.Fori(first, last) as i:
                    for j in range(PAIRS):
                        low(i, j)

            def argument(j, cosine, step):
                out = arg[:, 2 * j + 1 - cosine, :]
                if step == 0:
                    if cosine:
                        link(nc.vector.tensor_scalar(ang[:], pos_f[:], inv[:, j:j + 1], None, ALU.mult))
                    link(nc.vector.tensor_scalar(turns[:], ang[:], 1 / TWO_PI, 0.25 * cosine, ALU.mult, ALU.add))
                elif step == 1:
                    link(nc.vector.tensor_scalar(turns[:], turns[:], MAGIC, None, ALU.add))
                elif step == 2:
                    link(nc.vector.tensor_scalar(turns[:], turns[:], MAGIC, None, ALU.subtract))
                elif step == 3:
                    link(nc.vector.scalar_tensor_tensor(out, turns[:], -C1, ang[:], ALU.mult, ALU.add))
                elif step == 4:
                    link(nc.vector.scalar_tensor_tensor(out, turns[:], -C2, out, ALU.mult, ALU.add))
                elif step == 5:
                    link(nc.vector.scalar_tensor_tensor(out, turns[:], -C3, out, ALU.mult, ALU.add))
                elif step == 6:
                    link(nc.vector.tensor_scalar(out, out, np.pi / 2 * cosine, PI_IN, ALU.add, ALU.min))
                else:
                    nc.vector.tensor_scalar(out, out, -PI_IN, None, ALU.max).then_inc(args_ready, 1)

            def columns2(l):
                part = slice(n1 + l * MOD2, n1 + (l + 1) * MOD2)
                at = part.start if l == 0 else 0
                products = psM[l][:, at * VEC:(at + MOD2) * VEC].rearrange("p (n v) -> p n v", v=VEC)
                for v in range(2):
                    link(nc.vector.tensor_tensor(mod2[:, l, v, :], products[:, :, 1 + v], bias[:, part], ALU.add))
                    for half in range(2):
                        m, out = mod2[:, l, v, 24 * half:], t["cols2"][:, l, v, 24 * half:]
                        nc.vector.scalar_tensor_tensor(out[:, A1:A1 + 8], m[:, 8:16], 1.0, gains2[:, l, 2 * half, :],
                                                       ALU.add, ALU.mult)
                        nc.vector.tensor_copy(out[:, B1:B1 + 8], m[:, 0:8])
                        nc.vector.tensor_tensor(out[:, G1:G1 + 8], m[:, 16:24], gains2[:, l, 2 * half + 1, :], ALU.mult)\
                          .then_inc(cols2_ready, 1)

            def columns1():
                cols = t["cols1"]
                products = psM[0][:, 0:n1 * VEC].rearrange("p (n v) -> p n v", v=VEC)
                link(nc.vector.tensor_tensor(mod[:].rearrange("p l n -> p (l n)"), products[:, :, 0], bias[:, 0:n1], ALU.add))
                link(nc.vector.scalar_tensor_tensor(cols[:, :, C_A:C_A + 8], mod[:, :, 8:16], 1.0, gains[:, :, 0:8],
                                                    ALU.add, ALU.mult))
                link(nc.vector.tensor_copy(cols[:, :, C_B:C_B + 8], mod[:, :, 0:8]))
                link(nc.vector.tensor_tensor(cols[:, :, C_G:C_G + 8], mod[:, :, 16:24], gains[:, :, 8:16], ALU.mult))
                for n in range(DEPTH * NB):
                    link(nc.vector.tensor_copy(t["ab1"][:, n, :], cols[:, n // NB, C_A:C_A + 2 * KB]))
                for n, at in enumerate((A1, B1)):
                    link(nc.vector.tensor_copy(t["ab1"][:, DEPTH * NB, n * KB:(n + 1) * KB], t["cols2"][:, 0, 0, at:at + KB]))
                link(nc.vector.tensor_copy(cols[:, :, C_GB:C_GB + 2], gains[:, :, 16:18]))
                link(nc.vector.memset(cols[:, :, C_ONE:C_ONE + 6], 1.0))
                link(nc.vector.tensor_scalar(cols[:, :, C_SINK:C_SINK + 8], sinks[:], -1.0, None, ALU.mult))

            dve.wait_ge(cact_ready, 2)
            nc.vector.tensor_tensor(cparts[:, :, VEC:], cact[:], cparts[:, :, 0:VEC].bitcast(F32), ALU.subtract)\
              .then_inc(cact_ready, 1)
            dve.wait_ge(pos_in, 32)
            link(nc.vector.tensor_copy(pos_f[:], pos_i[:]))
            for n in range(4):
                for step in range(8):
                    low(2 * n + step // PAIRS, step % PAIRS)
                    argument(n // 2, 1 - n % 2, step)
            dve.wait_ge(small_in, 16 * 6)
            link(nc.vector.tensor_copy(t["mask1"][:], mask_f[:]))
            link(nc.vector.tensor_copy(t["gla_mask"][:], levels_f[:]))
            dve.wait_ge(t["const_in"], 16 * 9)
            dve.wait_ge(ident_in, 32)
            link(nc.vector.tensor_copy(t["identb"][:], t["ident"][:]))
            low_passes(2 * 4, early + 2)
            dve.wait_ge(row_used, 2 + 2 * early)
            columns2(0)
            dve.wait_ge(cols2_ready, 4)
            columns1()
            low_passes(early + 2, passes)
            dve.wait_ge(row_used, 2 + 2 * passes)
            columns2(1)
            dve.wait_ge(cols2_ready, 8)


def first_block(nc, t, a, sems):
    sem = sems
    with ExitStack() as ctx:
        def sb(name, shape, dt=F32):
            return ctx.enter_context(nc.sbuf_tensor(name, shape, dt))

        x, wraw, whi, wlo = t["x"], t["wraw"], t["whi"], t["wlo"]
        cols1, rope1, mask1 = t["cols1"], t["rope1"], t["mask1"]
        h_hi, h_lo = t["h_hi"], t["h_lo"]
        aq = sb("aq", [P, 4, W])
        ak = sb("ak", [P, P + W])
        av = sb("av", [P, 1 + NT, P])
        rq, rk = sb("rq", [P, 2, W]), sb("rk", [P, 2, W])
        rv, gv = sb("rv", [P, NT, 256]), sb("gv", [P, NT, 256])
        gq, gk = sb("gq", [P, W]), sb("gk", [P, W])
        gate_y = sb("gate_y", [P, KB, W])
        ga = sb("ga", [GATE_RANK, W])
        gw = sb("gw", [GATE_RANK, P])
        col = sb("col", [P, NCOL1])
        next_ab = sb("next_ab", [P, 2 * KB])
        tmp = sb("tmp", [P, 8, W])
        rstd = sb("rstd", [P, W])
        probs = [tmp[:, 2 * n:2 * n + 2, :].rearrange("p a b -> p (a b)").rearrange("p (g k) -> p g k", g=4)
                 for n in range(2)]
        probsT = [tmp[:, 4 + 2 * n:6 + 2 * n, :] for n in range(2)]
        mx = sb("mx", [P, 2, 4])
        nmax, sink_arg, esum, esink, rden = (sb(n, [P, 2, 4]) for n in ("nmax", "sink_arg", "esum", "esink", "rden"))
        scm = sb("scm", [P, 2, 4, P])
        kd = sb("kd", [P, 2, 256])
        qd = sb("qd", [P, 2, 2, P])
        rstate, rnew = sb("rstate", [P, 2, P]), sb("rnew", [P, 2, P])
        gstate, gnew = sb("gstate", [P, 256]), rnew[:].rearrange("p c v -> p (c v)")
        bsum = sb("bsum", [P, W])
        zed = sb("zed", [P, 2, W])
        lk = tmp[:, 6:8, :]
        lq = [v.rearrange("p c n -> p (c n)") for v in (tmp[:, 4:6, :], rk[:])]
        gsc = aq[:].rearrange("p t (h i) -> p t h i", h=4)
        khT = sb("khT", [P, 2, P])
        elast = sb("elast", [P, NT])
        lin0, lin1 = (ctx.enter_context(nc.psum_tensor(f"lin{n}", [P, 512], F32)) for n in range(2))
        scores = [ctx.enter_context(nc.psum_tensor(f"scores{n}", [P, 1024], F32)) for n in range(2)]
        bank = [lin0[:], lin1[:]] + [s[:, 512 * n:512 * n + 512] for s in scores for n in range(2)]
        bankT = ctx.enter_context(nc.psum_tensor("bankT", [P, 2, 512], F32))
        bankS = bank[2:]
        eb, qe, khat = tmp[:, 0, :], tmp[:, 1, :], tmp[:, 2, :]

        def score(j):
            return scores[j % 2][:].rearrange("p (g k) -> p g k", g=4)

        def mixed(j):
            return rq[:, j, :] if j < 2 else gv[:, :, (j - 2) * P:(j - 1) * P]

        head_sq = [tmp[:, n, :] for n in (3, 2, 0, 1)]
        head_rstd = [scm[:, n].rearrange("p h i -> p (h i)") for n in range(2)] + [tmp[:, 6, :], tmp[:, 7, :]]
        head_sum = [bank[0], bank[1], bank[4], bank[5]]

        def in_pairs(v, lv, n):
            return v.rearrange("p (b t s) -> p b t s", t=2, s=P >> (lv + 1))[:, :, n, :]

        def sig(name, per, start=0):
            return Sig(sem(name), per, start)

        v_turned = sig("v_turned", 1)
        layer_ready = sig("layer_ready", 1)
        carried = sig("carried", 1)
        sq_ready, sq_used = sig("sq_ready", 4), sig("sq_used", 4)
        rstd_ready = sig("rstd_ready", 5)
        x_log = sig("x_log", 1)
        x_sq, x_add, x_sum, x_rstd = sig("x_sq", KB), sig("x_add", KB - 1), sig("x_sum", 1), sig("x_rstd", 1)
        ab_ready, scaled, h_high, h_ready = sig("ab_ready", 1), sig("scaled", KB), sig("h_high", KB), sig("h_ready", KB)
        y_sq, y_add, y_sum = sig("y_sq", KB), sig("y_add", KB - 1), sig("y_sum", 1)
        rope_raw, rope_mm, rope_done = sig("rope_raw", 9), sig("rope_mm", 9), sig("rope_done", 9)
        raw_in, w_hi, w_split = t["raw_in"], t["w_hi"], t["w_split"]
        lin_done, lin_free = t["lin_done"], t["lin_free"]
        ga_in = sig("ga_in", 16)
        ga_ready = sig("ga_ready", 1)
        logit_done, sig_ready = sig("logit_done", 1), sig("sig_ready", 1)
        bsum_ready = sig("bsum_ready", 1)
        s_ready, nm_ready, exp_done = sig("s_ready", 8), sig("nm_ready", 8), sig("exp_done", 8)
        rden_ready, pn_ready = sig("rden_ready", 8), sig("pn_ready", 8)
        pt_done, pt_evac_a, pt_evac_d = sig("pt_done", 8), sig("pt_evac_a", 8), sig("pt_evac_d", 8)
        pv_done, ao_done = sig("pv_done", 8), sig("ao_done", 4)
        r_scores, r_kd, r_qd = (sig(n, 4) for n in ("r_scores", "r_kd", "r_qd"))
        r_out, r_evac, r_state = (sig(n, 4) for n in ("r_out", "r_evac", "r_state"))
        z_ready, e_ready = sig("z_ready", LEVELS + 1), sig("e_ready", LEVELS + 1)
        eb_ready = sig("eb_ready", 2)
        lev_ready, lq_ready = sig("lev_ready", LEVELS), sig("lq_ready", LEVELS + 1)
        g_scores, g_picked = sig("g_scores", 4 * (LEVELS + 1)), sig("g_picked", 4 * (LEVELS + 1))
        qe_ready, kh_ready = sig("qe_ready", 1), sig("kh_ready", 1)
        kh_done, kh_evac = sig("kh_done", 4), sig("kh_evac", 4)
        g_out, g_evac, g_state = (sig(n, 4) for n in ("g_out", "g_evac", "g_state"))
        mix_hi, mix_ready = sig("mix_hi", 4), sig("mix_ready", 8)
        x_done = sig("x_done", 8, 1)
        dve_order = Order(nc.vector, sig("dve_order", 65))
        act_order = Order(nc.scalar, sig("act_order", 16))

        wait_seat = sem("wait_seat")
        block = ctx.enter_context(nc.Block())

        def layers_and_blocks(eng, layer_start=None):
            with eng.Fori(0, DEPTH) as l:
                if layer_start:
                    layer_start(l)
                with eng.Fori(0, NB) as b:
                    yield l, b, l * NB + b

        def rows(b):
            return bass.ds(b * W, W)

        def next_rows(b):
            return bass.ds(b * (-W) + W, W)

        def lin_product(it, c, out, slot):
            pe = nc.tensor
            pe.wait_ge(*lin_free.after(it, c + 1))
            pe.wait_ge(*w_hi.after(it, c + 1))
            for k in range(KB):
                if isinstance(c, int) and c == 0:
                    pe.wait_ge(*h_ready.after(it, k + 1))
                for h in (h_hi, h_lo):
                    nc.tensor.matmul(out, whi[:, slot, k * P:(k + 1) * P], h[:, k, :], start=(k == 0 and h is h_hi), stop=False)
            pe.wait_ge(*w_split.after(it, c + 1))
            for k in range(KB):
                last = nc.tensor.matmul(out, wlo[:, slot, k * P:(k + 1) * P], h_hi[:, k, :], start=False, stop=(k == KB - 1))
            return last

        def token_pair(it, c):
            pe = nc.tensor
            pe.wait_ge(*lin_free.after(it, c + 2))
            pe.wait_ge(*w_hi.after(it, c + 2))
            for tiles in ((0, 2), (1, 3)):
                for n, (h, w) in enumerate(((h_hi, whi), (h_lo, whi), (h_hi, wlo))):
                    if n == 2 and tiles[0] == 0:
                        pe.wait_ge(*w_split.after(it, c + 2))
                    for tile in tiles:
                        for k in range(KB):
                            at = tile % 2 * 256
                            last = nc.tensor.matmul(bank[tile // 2][:, at:at + 256].rearrange("p (c n) -> p c n", n=P),
                                                    h[:, k, tile * P:(tile + 1) * P], w[:, 0:2, k * P:(k + 1) * P],
                                                    start=(k == n == 0), stop=(k == KB - 1 and n == 2))
            last.then_inc(lin_done.sem, 2)

        @block.sync
        def _(sp):
            def load(dst, src, s):
                sp.dma_start(dst, src).then_inc(raw_in[s].sem, 16)

            for s in range(2):
                load(wraw[:, s, 0:D], a["w1"][0, s], s)
            for l, b, it in layers_and_blocks(sp):
                sp.dma_start(wraw[:, 1, D:], a["w1_gate"][bass.ds(l, 1)].rearrange("o p n -> p (o n)"))\
                  .then_inc(ga_in.sem, 16)
                with sp.Fori(0, CH1 // 2 - 1) as i:
                    for s in range(2):
                        sp.wait_ge(*w_split.after(it, 2 * i + (s + 1)))
                        load(wraw[:, s, 0:D], a["w1"][bass.ds(l, 1), bass.ds(2 * i + (s + 2), 1)]
                             .rearrange("l c p n -> p (l c n)"), s)
                for s in range(2):
                    sp.wait_ge(*w_split.after(it, CH1 - 1 + s))
                    load(wraw[:, s, 0:D], a["w1_next"][bass.ds(it, 1), s].rearrange("o p n -> p (o n)"), s)

        @block.gpsimd
        def _(pool):
            def split_low(it, c, s, n=D):
                pool.wait_ge(*w_hi.after(it, c + 1))
                nc.gpsimd.tensor_tensor(wlo[:, s, 0:n], wraw[:, s, 0:n], whi[:, s, 0:n].bitcast(F32), ALU.subtract)\
                  .then_inc(*w_split.one)

            for s in range(2):
                split_low(0, s, s)
            for l, b, it in layers_and_blocks(pool):
                with pool.Fori(1, AV // 2) as i:
                    for s in range(2):
                        split_low(it, 2 * i + s, s)
                split_low(it, AV - 1, 0)
                split_low(it, AV, 1, D + KB * GATE_RANK)
                with pool.Fori(AV // 2 + 1, OUT1 // 2 + 1) as i:
                    for s in range(2):
                        split_low(it, 2 * i + s, s)
                for s in range(8):
                    pool.wait_ge(*rden_ready.after(it, s + 1))
                    nc.gpsimd.tensor_tensor(probs[s % 2], probs[s % 2],
                                            rden[:, s % 2, :].rearrange("p (g o) -> p g o", o=1)
                                            .to_broadcast([P, 4, 2 * P]), ALU.mult).then_inc(*pn_ready.one)
                for n in range(NT):
                    pool.wait_ge(*rope_done.after(it, ROPE1))
                    if n >= 2:
                        pool.wait_ge(*r_out.after(it, n - 1))
                    nc.gpsimd.tensor_tensor(qd[:, n % 2], rq[:, :, n * P:(n + 1) * P], t["ret_qdecay"][:], ALU.mult)\
                      .then_inc(*r_qd.one)
                def z_of(lv):
                    if lv >= 2:
                        pool.wait_ge(*lev_ready.after(it, lv - 1))
                        pool.wait_ge(*lq_ready.after(it, lv - 1))
                    s = P >> (lv + 1)
                    if lv < LEVELS:
                        pairs = bsum[:].rearrange("p (n s) -> p n s", s=2 * s)
                        ref, n_ref, width = pairs[:, :, s - 1:s], W // (2 * s), 2 * s
                    else:
                        pairs = bsum[:].rearrange("p (n s) -> p n s", s=P)
                        ref, n_ref, width = pairs[:, :, P - 1:P], NT, P
                    nc.gpsimd.tensor_tensor(zed[:, lv % 2].rearrange("p (n s) -> p n s", s=width), pairs,
                                            ref.to_broadcast([P, n_ref, width]), ALU.subtract).then_inc(*z_ready.one)

                pool.wait_ge(*bsum_ready.after(it, 1))
                z_of(0)
                z_of(1)
                for lv in range(LEVELS):
                    pool.wait_ge(*e_ready.after(it, lv + 1))
                    if lv == 0:
                        pool.wait_ge(*pv_done.after(it, 8))
                    if lv >= 2:
                        pool.wait_ge(*g_scores.after(it, 4 * (lv - 1)))
                    nc.gpsimd.tensor_tensor(in_pairs(lk[:, lv % 2], lv, 0), in_pairs(gk[:], lv, 0), in_pairs(zed[:, lv % 2], lv, 0),
                                            ALU.mult).then_inc(*lev_ready.one)
                    if lv + 2 <= LEVELS:
                        z_of(lv + 2)
                pool.wait_ge(*eb_ready.after(it, 2))
                nc.gpsimd.tensor_tensor(qe, gq[:], eb, ALU.mult).then_inc(*qe_ready.one)
                pool.wait_ge(*e_ready.after(it, LEVELS + 1))
                pool.wait_ge(*mix_ready.after(it, 6))
                nc.gpsimd.tensor_tensor(khat, gk[:], zed[:, LEVELS % 2], ALU.mult).then_inc(*kh_ready.one)
                with pool.Fori(OUT1 // 2 + 1, CH1 // 2 + 1) as i:
                    for s in range(2):
                        split_low(it, 2 * i + s, s)

        @block.scalar
        def _(act):
            link = act_order.link

            def split_high(it, c, s, n=D):
                act.wait_ge(raw_in[s].sem, raw_in[s].after(it, 16 * (c // 2 + 1))[1] if isinstance(c, int)
                            else raw_in[s].after(it, c * 8 + (16 - 8 * s))[1])
                nc.scalar.activation(whi[:, s, 0:n], wraw[:, s, 0:n], ACT.Copy).then_inc(*w_hi.one)

            def product(it, c):
                act.wait_ge(*lin_done.after(it, c + 1))

            def head_square(it, j):
                src = mixed(j)
                nc.scalar.activation(head_sq[j] if len(src.shape) == 2 else head_sq[j].rearrange("p (a b) -> p a b", b=P),
                                     src, ACT.Square).then_inc(*sq_ready.one)

            def head_roots(it, first):
                for j in (first, first + 1):
                    act.wait_ge(*sq_used.after(it, j + 1))
                    link(nc.scalar.activation(head_rstd[j], head_sum[j], ACT.Ln, scale=1.0 / 64, bias=EPS))
                for j in (first, first + 1):
                    nc.scalar.activation(head_rstd[j], head_rstd[j], ACT.Exp, scale=-0.5).then_inc(*rstd_ready.one)

            def x_square(no, k, where):
                if k >= 3:
                    act.wait_ge(*x_add.after(no, k - 2))
                nc.scalar.activation(tmp[:, 4 + k % 2 if k else 6, :], x[:, k, where], ACT.Square).then_inc(*x_sq.one)

            def x_root(no):
                act.wait_ge(*x_sum.after(no, 1))
                nc.scalar.activation(tmp[:, 6, :], bank[3], ACT.Ln, scale=1.0 / D, bias=EPS).then_inc(*x_log.one)
                act.wait_ge(*x_log.after(no, 1))
                nc.scalar.activation(tmp[:, 6, :], tmp[:, 6, :], ACT.Exp, scale=-0.5).then_inc(*x_rstd.one)

            def x_high(no):
                act.wait_ge(*ab_ready.after(no, 1))
                for k in range(KB):
                    act.wait_ge(*scaled.after(no, k + 1))
                    nc.scalar.activation(h_hi[:, k, :], tmp[:, 2 + k % 2, :], ACT.Identity, bias=next_ab[:, KB + k:KB + k + 1])\
                      .then_inc(*h_high.one)

            act.sem_inc(lin_free.sem, 2)
            for k in range(KB):
                x_square(0, k, slice(0, W))
            for s in range(2):
                split_high(0, s, s)
            x_root(0)
            x_high(0)
            for l, b, it in layers_and_blocks(act):
                act_order.begin(it)
                for r in range(ROPE1):
                    product(it, r)
                    if r >= 2:
                        act.wait_ge(*rope_done.after(it, r - 1))
                    nc.scalar.activation(tmp[:, 6 + r % 2, :], bank[r % 2][:], ACT.Copy).then_inc(*rope_raw.one)
                    act.wait_ge(*rope_raw.after(it, r + 1))
                    act.sem_inc(lin_free.sem, 1)
                    split_high(it, r + 2, r % 2)
                product(it, GQ)
                nc.scalar.activation(gq[:], bank[1][:], ACT.Copy, scale=32 ** -0.5).then_inc(*lin_free.one)
                act.wait_ge(*ga_in.after(it, 16))
                split_high(it, AV, 1, D + KB * GATE_RANK)
                product(it, GK)
                nc.scalar.activation(gk[:], bank[0][:], ACT.Copy).then_inc(*lin_free.one)
                split_high(it, GK + 2, 0)
                product(it, AV)
                act.wait_ge(*layer_ready.after(l, 1))
                act.wait_ge(*carried.after(it, 1))
                nc.scalar.activation(ga[:], bank[4][0:GATE_RANK, :], ACT.Copy).then_inc(*ga_ready.one)
                act.wait_ge(*rope_done.after(it, ROPE1))
                nc.scalar.activation(tmp[:, 4, :], bank[1][:], ACT.Copy).then_inc(*lin_free.one)
                split_high(it, AV + 2, 1)
                for c, dst in ((RV, rv), (GV, gv)):
                    product(it, c + 1)
                    for s in range(2):
                        nc.scalar.activation(dst[:, 2 * s:2 * s + 2, :].rearrange("p t n -> p (t n)"), bank[s], ACT.Copy)\
                          .then_inc(*lin_free.one)
                    for s in range(2):
                        split_high(it, c + 2 + s, s)
                    if c == RV:
                        act.wait_ge(*v_turned.after(it, 1))
                        nc.scalar.activation(av[:, 1:, :].rearrange("p t n -> p (t n)"), bankT[:, 0, :], ACT.Copy)
                act.wait_ge(*logit_done.after(it, 1))
                link(nc.scalar.activation(zed[:, 0, :], bank[5][:], ACT.Identity, bias=col[:, C_GB:C_GB + 1]))
                link(nc.scalar.activation(zed[:, 1, :], zed[:, 0, :], ACT.Abs))
                link(nc.scalar.activation(zed[:, 1, :], zed[:, 1, :], ACT.Exp, scale=-1.0))
                nc.scalar.activation(zed[:, 1, :], zed[:, 1, :], ACT.Ln, bias=1.0).then_inc(*sig_ready.one)
                with act.Fori(0, (OUT1 - GATE1) // 2) as i:
                    for s in range(2):
                        product(it, 2 * i + (GATE1 + s))
                        nc.scalar.activation(gate_y[:, bass.ds(2 * i + s, 1), :].rearrange("p o n -> p (o n)"),
                                             bank[s][:], ACT.Silu).then_inc(*lin_free.one)
                        split_high(it, 2 * i + (GATE1 + s + 2), s)
                for j in range(10):
                    if j >= 2:
                        s = j - 2
                        act.wait_ge(*pt_done.after(it, s + 1))
                        if s >= 2:
                            act.wait_ge(*pv_done.after(it, s - 1))
                        nc.scalar.activation(probsT[s % 2][:, 0, :], bankT[:, 0, :], ACT.Copy).then_inc(*pt_evac_a.one)
                    if j < 8:
                        act.wait_ge(*nm_ready.after(it, j + 1))
                        if j >= 2:
                            act.wait_ge(*pt_done.after(it, j - 1))
                        for g in range(4):
                            nc.scalar.activation(probs[j % 2][:, g, :], score(j)[:, g, :], ACT.Exp, scale=ATT_SCALE,
                                                 bias=nmax[:, j % 2, g:g + 1], accum_out=esum[:, j % 2, g:g + 1])
                        nc.scalar.activation(esink[:, j % 2, :], sink_arg[:, j % 2, :], ACT.Exp).then_inc(*exp_done.one)
                act.wait_ge(*ao_done.after(it, NT))
                for j in range(4):
                    nc.scalar.activation(h_hi[:, j, :], aq[:, j, :], ACT.Copy).then_inc(*mix_hi.one)
                for n in range(NT):
                    act.wait_ge(*r_out.after(it, n + 1))
                    nc.scalar.activation(rq[:, :, n * P:(n + 1) * P],
                                         bank[n % 2][:, 0:256].rearrange("p (c n) -> p c n", n=P), ACT.Copy)\
                      .then_inc(*r_evac.one)
                act.wait_ge(*bsum_ready.after(it, 1))
                act.wait_ge(*pt_done.after(it, 8))
                nc.scalar.activation(eb, bsum[:], ACT.Exp).then_inc(*eb_ready.one)
                nc.scalar.activation(elast[:], bsum[:, P - 1::P], ACT.Exp).then_inc(*eb_ready.one)
                for lv in range(LEVELS + 1):
                    act.wait_ge(*z_ready.after(it, lv + 1))
                    link(nc.scalar.activation(zed[:, lv % 2], zed[:, lv % 2], ACT.Abs))
                    nc.scalar.activation(zed[:, lv % 2], zed[:, lv % 2], ACT.Exp, scale=-1.0).then_inc(*e_ready.one)
                    if lv == 1:
                        act.wait_ge(*r_evac.after(it, NT))
                        for j in range(2):
                            head_square(it, j)
                        head_roots(it, 0)
                for n in range(NT + 1):
                    if n < NT:
                        act.wait_ge(*kh_done.after(it, n + 1))
                        if n >= 2:
                            act.wait_ge(*g_out.after(it, n - 1))
                        nc.scalar.activation(khT[:, n % 2, :], bankT[:, n % 2, 0:P], ACT.Copy).then_inc(*kh_evac.one)
                    if n:
                        act.wait_ge(*g_out.after(it, n))
                        nc.scalar.activation(gv[:, n - 1, :], bank[(n - 1) % 2][:, 0:256], ACT.Copy)\
                          .then_inc(*g_evac.one)
                act.wait_ge(*g_evac.after(it, NT))
                for j in range(2, 4):
                    head_square(it, j)
                head_roots(it, 2)
                act.wait_ge(*x_done.after(it, 0))
                for k in range(KB):
                    product(it, OUT1 + k)
                    if k >= 2:
                        act.wait_ge(*y_add.after(it, k - 1))
                    nc.scalar.activation(tmp[:, 1 if k else 0, :], bank[k % 2][:], ACT.Square).then_inc(*y_sq.one)
                    nc.scalar.activation(gate_y[:, k, :], bank[k % 2][:], ACT.Copy).then_inc(*lin_free.one)
                    split_high(it, OUT1 + k + 2, k % 2)
                    if k < 4:
                        for j in (2 * k, 2 * k + 1):
                            x_square(it + 1, j, next_rows(b))
                    if k == 5:
                        x_root(it + 1)
                x_high(it + 1)
                act.wait_ge(*y_sum.after(it, 1))
                link(nc.scalar.activation(rstd[:], bank[2], ACT.Ln, scale=1.0 / D, bias=EPS))
                nc.scalar.activation(rstd[:], rstd[:], ACT.Exp, scale=-0.5).then_inc(*rstd_ready.one)
                act_order.end()

        @block.vector
        def _(dve):
            link = dve_order.link

            def layer_start(l):
                nc.vector.tensor_copy(col[:], cols1[:, bass.ds(l, 1), :].rearrange("p o n -> p (o n)"))
                nc.vector.tensor_copy(gw[:], t["gate_w"][:, bass.ds(l, 1), :].rearrange("p o n -> p (o n)"))
                for state in (ak[:], av[:], rstate[:], gstate[:]):
                    last = nc.vector.memset(state, 0.0)
                last.then_inc(*layer_ready.one)
                dve.wait_ge(*layer_ready.after(l, 1))
                dve.sem_inc(wait_seat, 1)

            def gated(it, j):
                view = (lambda v: v) if j < 2 else (lambda v: v.rearrange("p (t k) -> p t k", k=P))
                gain = C_ONE if j < 2 else C_GN
                dve.wait_ge(*rstd_ready.after(it, j + 1))
                link(nc.vector.tensor_tensor(view(head_rstd[j]), mixed(j), view(head_rstd[j]), ALU.mult))
                link(nc.vector.scalar_tensor_tensor(head_sq[j], head_rstd[j], col[:, gain:gain + 1], gate_y[:, 4 + j, :],
                                                    ALU.mult, ALU.mult))
                link(nc.vector.tensor_copy(h_hi[:, 4 + j, :], head_sq[j]))
                nc.vector.tensor_tensor(h_lo[:, 4 + j, :], head_sq[j], h_hi[:, 4 + j, :].bitcast(F32), ALU.subtract)\
                  .then_inc(*mix_ready.one)

            def x_added(no, k):
                dve.wait_ge(*x_sq.after(no, k + 1))
                nc.vector.tensor_tensor(tmp[:, 6, :], tmp[:, 6, :], tmp[:, 4 + k % 2, :], ALU.add).then_inc(*x_add.one)
                dve.wait_ge(*x_add.after(no, k))

            def x_split(no, where):
                nc.vector.tensor_copy(next_ab[:], t["ab1"][:, no, :] if isinstance(no, int) else
                                      t["ab1"][:, bass.ds(no, 1), :].rearrange("p o n -> p (o n)")).then_inc(*ab_ready.one)
                dve.wait_ge(*ab_ready.after(no, 1))
                dve.wait_ge(*x_rstd.after(no, 1))
                for k in range(KB + 1):
                    if k < KB:
                        nc.vector.scalar_tensor_tensor(tmp[:, 2 + k % 2, :], x[:, k, where], next_ab[:, k:k + 1], tmp[:, 6, :],
                                                       ALU.mult, ALU.mult).then_inc(*scaled.one)
                    if k:
                        j = k - 1
                        dve.wait_ge(*h_high.after(no, j + 1))
                        nc.vector.scalar_tensor_tensor(h_lo[:, j, :], tmp[:, 2 + j % 2, :], next_ab[:, KB + j:KB + j + 1],
                                                       h_hi[:, j, :].bitcast(F32), ALU.add, ALU.subtract).then_inc(*h_ready.one)
                        dve.wait_ge(*h_ready.after(no, j + 1))

            dve.sem_inc(x_done.sem, 1)
            for k in range(1, KB):
                x_added(0, k)
            x_split(0, slice(0, W))
            for l, b, it in layers_and_blocks(dve, layer_start):
                dve_order.begin(it)
                link(nc.vector.tensor_copy(ak[:, 0:P], ak[:, W:W + P]))
                nc.vector.tensor_copy(av[:, 0, :], av[:, NT, :]).then_inc(*carried.one)
                for r in range(ROPE1):
                    table = 0 if r < 5 else 2
                    out = aq[:, r, :] if r < 4 else ak[:, P:] if r == 4 else rq[:, r - 5, :] if r < 7 else rk[:, r - 7, :]
                    dve.wait_ge(*rope_raw.after(it, r + 1))
                    nc.vector.tensor_tensor(tmp[:, 2 + r % 2, :], tmp[:, 6 + r % 2, :], rope1[:, table, rows(b)],
                                            ALU.mult)
                    dve.wait_ge(*rope_mm.after(it, r + 1))
                    link(nc.vector.tensor_tensor(tmp[:, 4 + r % 2, :], bankS[r % 2][:], rope1[:, table + 1, rows(b)],
                                                 ALU.mult))
                    nc.vector.tensor_tensor(out, tmp[:, 2 + r % 2, :], tmp[:, 4 + r % 2, :], ALU.add)\
                      .then_inc(*rope_done.one)
                dve.wait_ge(*sig_ready.after(it, 1))
                link(nc.vector.tensor_scalar(zed[:, 0, :], zed[:, 0, :], 0.0, 1 / 16, ALU.min, ALU.mult))
                link(nc.vector.scalar_tensor_tensor(zed[:, 0, :], zed[:, 1, :], -1 / 16, zed[:, 0, :], ALU.mult, ALU.add))
                for n in range(NT):
                    part = slice(n * P, (n + 1) * P)
                    last = nc.vector.tensor_tensor_scan(bsum[:, part], t["ones"][:], zed[:, 0, part], 0.0,
                                                        ALU.mult, ALU.add)
                last.then_inc(*bsum_ready.one)
                dve.wait_ge(*bsum_ready.after(it, 1))
                for j in range(13):
                    if j < 8:
                        neg_sink = col[:, C_SINK + 4 * (j % 2):C_SINK + 4 * (j % 2) + 4]
                        dve.wait_ge(*s_ready.after(it, j + 1))
                        link(nc.vector.reduce_max(mx[:, j % 2, :], score(j), AX_X))
                        if j >= 2:
                            dve.wait_ge(*exp_done.after(it, j - 1))
                        link(nc.vector.scalar_tensor_tensor(nmax[:, j % 2, :], mx[:, j % 2, :], -ATT_SCALE, neg_sink,
                                                            ALU.mult, ALU.min))
                        nc.vector.tensor_tensor(sink_arg[:, j % 2, :], nmax[:, j % 2, :], neg_sink, ALU.subtract)\
                          .then_inc(*nm_ready.one)
                    if 1 <= j < 9:
                        s = j - 1
                        dve.wait_ge(*exp_done.after(it, s + 1))
                        link(nc.vector.tensor_tensor(esum[:, s % 2, :], esum[:, s % 2, :], esink[:, s % 2, :], ALU.add))
                        if s >= 2:
                            dve.wait_ge(*pn_ready.after(it, s - 1))
                        nc.vector.reciprocal(rden[:, s % 2, :], esum[:, s % 2, :]).then_inc(*rden_ready.one)
                    if 2 <= j < 10:
                        s = j - 2
                        dve.wait_ge(*pt_done.after(it, s + 1))
                        if s >= 2:
                            dve.wait_ge(*pv_done.after(it, s - 1))
                        nc.vector.tensor_copy(probsT[s % 2][:, 1, :], bankT[:, 1, :]).then_inc(*pt_evac_d.one)
                    if j >= 5 and j % 2:
                        n = (j - 5) // 2
                        part = slice(n * P, (n + 1) * P)
                        dve.wait_ge(*pv_done.after(it, 2 * n + 2))
                        nc.vector.tensor_tensor(aq[:, :, part], bank[n % 2][:].rearrange("p (g n) -> p g n", n=P),
                                                gate_y[:, 0:4, part], ALU.mult).then_inc(*ao_done.one)
                for j in range(4):
                    dve.wait_ge(*mix_hi.after(it, j + 1))
                    nc.vector.tensor_tensor(h_lo[:, j, :], aq[:, j, :], h_hi[:, j, :].bitcast(F32), ALU.subtract)\
                      .then_inc(*mix_ready.one)
                for n in range(NT + 1):
                    if n < NT:
                        dve.wait_ge(*r_scores.after(it, n + 1))
                        if n >= 2:
                            dve.wait_ge(*r_out.after(it, n - 1))
                        def by_parity(v):
                            return v.rearrange("p (c a) i -> p a c i", a=2)
                        nc.vector.tensor_tensor(by_parity(scm[:, n % 2]),
                                                scores[0][:].rearrange("p (a c i) -> p a c i", a=2, i=P)[:, :, 0:2, :],
                                                by_parity(t["ret_mask"][:]), ALU.mult)
                        nc.vector.tensor_tensor(kd[:, n % 2], bankS[2 + n % 2][:, 0:256], t["ret_kdecay"][:], ALU.mult)\
                          .then_inc(*r_kd.one)
                    if n:
                        dve.wait_ge(*r_out.after(it, n))
                        link(nc.vector.tensor_tensor(rnew[:], bankT[:, (n - 1) % 2, 0:256].rearrange("p (c v) -> p c v", c=2),
                                                     t["ones64"][:].rearrange("p (o v) -> p o v", o=1)
                                                     .to_broadcast([P, 2, P]), ALU.mult))
                        for c in range(2):
                            last = nc.vector.scalar_tensor_tensor(rstate[:, c, :], rstate[:, c, :],
                                                                  t["ret_cdecay"][:, c:c + 1], rnew[:, c, :],
                                                                  ALU.mult, ALU.add)
                        last.then_inc(*r_state.one)
                        dve.wait_ge(*r_state.after(it, n))
                def head_mask(h):
                    return t["gla_heads"][:, 64 * h:64 * h + 1]

                def queries(lv):
                    block = P >> (lv + 1)
                    dve.wait_ge(*e_ready.after(it, lv + 1))
                    if lv >= 2:
                        dve.wait_ge(*g_scores.after(it, 4 * (lv - 1)))
                    second = [v.rearrange("p (n b t s) -> p n b t s", n=NT, t=2, s=block)[:, :, :, 1, :] for v in (gq[:], zed[:, lv % 2])]
                    for h in range(4):
                        out = lq[lv % 2].rearrange("p (n h b s) -> p n h b s", n=NT, h=4, s=block)[:, :, h]
                        last = nc.vector.scalar_tensor_tensor(out, second[0], head_mask(h), second[1], ALU.mult, ALU.mult)
                    last.then_inc(*lq_ready.one)

                def pick(lv):
                    for n in range(NT):
                        dve.wait_ge(*g_scores.after(it, 4 * lv + n + 1))
                        dve.sem_inc(wait_seat, 1)
                        mask = t["gla_mask"][:, lv:lv + 1, :]
                        if lv < LEVELS:
                            block = P >> (lv + 1)
                            place, mask = (v.rearrange("p h (b t s) -> p h b t s", t=2, s=block)[:, :, :, 1, :]
                                           for v in (gsc[:, n], mask))
                            level = bankS[n][:, 0:256].rearrange("p (h b s) -> p h b s", h=4, s=block)
                            mask = mask.to_broadcast([P, 4, P // (2 * block), block])
                        else:
                            place, level = gsc[:, n], bankS[n].rearrange("p (h i) -> p h i", h=4)
                            mask = mask.to_broadcast([P, 4, P])
                        nc.vector.copy_predicated(place, mask, level).then_inc(*g_picked.one)

                queries(0)
                queries(1)
                dve.wait_ge(*mix_ready.after(it, 4))
                link(nc.vector.memset(aq[:], 0.0))
                for lv in range(LEVELS):
                    pick(lv)
                    if lv + 2 < LEVELS:
                        queries(lv + 2)
                    if lv in (2, 3):
                        gated(it, lv - 2)
                for h in range(4):
                    for n in range(2):
                        last = nc.vector.tensor_scalar(lq[n].rearrange("p (n h i) -> p n h i", n=2, h=4)[:, :, h, :],
                                                       gq[:, n * 2 * P:(n + 1) * 2 * P].rearrange("p (n i) -> p n i", n=2),
                                                       head_mask(h), None, ALU.mult)
                last.then_inc(*lq_ready.one)
                pick(LEVELS)
                for n in range(NT):
                    dve.wait_ge(*g_out.after(it, n + 1))
                    if n == 0:
                        dve.wait_ge(*eb_ready.after(it, 2))
                    link(nc.vector.tensor_tensor(gnew, bankS[n % 2][:, 0:256], t["gla_heads"][:], ALU.mult))
                    nc.vector.scalar_tensor_tensor(gstate[:], gstate[:], elast[:, n:n + 1], gnew, ALU.mult, ALU.add)\
                      .then_inc(*g_state.one)
                    dve.wait_ge(*g_state.after(it, n + 1))
                for j in range(2, 4):
                    gated(it, j)
                for k in range(KB):
                    if k:
                        dve.wait_ge(*y_sq.after(it, k + 1))
                        nc.vector.tensor_tensor(tmp[:, 0, :], tmp[:, 0, :], tmp[:, 1, :], ALU.add).then_inc(*y_add.one)
                        dve.wait_ge(*y_add.after(it, k))
                    if k < 4:
                        for j in (2 * k, 2 * k + 1):
                            if j:
                                x_added(it + 1, j)
                x_split(it + 1, next_rows(b))
                dve.wait_ge(*rstd_ready.after(it, 5))
                dve.wait_ge(*lin_free.after(it, CH1 + 2))
                for k in range(KB):
                    link(nc.vector.tensor_tensor(tmp[:, 2 + k % 2, :], gate_y[:, k, :], rstd[:], ALU.mult))
                    nc.vector.scalar_tensor_tensor(x[:, k, rows(b)], tmp[:, 2 + k % 2, :], col[:, C_G + k:C_G + k + 1],
                                                   x[:, k, rows(b)], ALU.mult, ALU.add).then_inc(*x_done.one)
                dve.wait_ge(*x_done.after(it, KB))
                dve_order.end()

        @block.tensor
        def _(pe):
            def sum_squares(it, j):
                pe.wait_ge(*sq_ready.after(it, j + 1))
                nc.tensor.matmul(head_sum[j], t["ones64"][:], head_sq[j], start=True, stop=True).then_inc(*sq_used.one)

            def x_summed(no):
                pe.wait_ge(*x_add.after(no, KB - 1))
                nc.tensor.matmul(bank[3][:], t["ones"][:], tmp[:, 6, :], start=True, stop=True).then_inc(*x_sum.one)

            def chunk(it, c, s):
                lin_product(it, c, bank[s][:], s).then_inc(*lin_done.one)

            def rotate(it, r, s):
                pe.wait_ge(*rope_raw.after(it, r + 1))
                if not isinstance(r, int) or r >= 2:
                    pe.wait_ge(*rope_done.after(it, r - 1))
                nc.tensor.matmul(bankS[s][:], t["rot1"][:], tmp[:, 6 + s, :], start=True, stop=True)\
                  .then_inc(*rope_mm.one)

            x_summed(0)
            for l, b, it in layers_and_blocks(pe):
                chunk(it, 0, 0)
                chunk(it, 1, 1)
                rotate(it, 0, 0)
                with pe.Fori(1, 5) as i:
                    chunk(it, 2 * i, 0)
                    rotate(it, 2 * i - 1, 1)
                    chunk(it, 2 * i + 1, 1)
                    rotate(it, 2 * i, 0)
                chunk(it, GK, 0)
                pe.wait_ge(*w_split.after(it, AV + 1))
                pe.wait_ge(*lin_free.after(it, AV + 1))
                for k in range(KB):
                    gate_cols = slice(D + k * GATE_RANK, D + (k + 1) * GATE_RANK)
                    for n, (w, h) in enumerate(((whi, h_hi), (whi, h_lo), (wlo, h_hi))):
                        nc.tensor.matmul(bank[4][0:GATE_RANK, :], w[:, 1, gate_cols], h[:, k, :],
                                         start=(k == 0 and n == 0), stop=(k == KB - 1 and n == 2))
                chunk(it, AV, 1)
                token_pair(it, RV)
                for n in range(NT):
                    last = nc.tensor.transpose(bankT[:, 0, n * P:(n + 1) * P], tmp[:, 4, n * P:(n + 1) * P], t["ident"][:])
                last.then_inc(*v_turned.one)
                pe.wait_ge(*ga_ready.after(it, 1))
                pe.wait_ge(*layer_ready.after(l, 1))
                nc.tensor.matmul(bank[5][:], gw[:], ga[:], start=True, stop=True).then_inc(*logit_done.one)
                token_pair(it, GV)
                with pe.Fori(GATE1 // 2, OUT1 // 2) as i:
                    for s in range(2):
                        chunk(it, 2 * i + s, s)
                pe.wait_ge(*rope_done.after(it, ROPE1))
                pe.wait_ge(*lin_free.after(it, OUT1 + 2))
                pe.wait_ge(*sig_ready.after(it, 1))
                for j in range(11):
                    if j < 8:
                        n, kv = j // 2, j % 2
                        half = slice(64 * kv, 64 * kv + 64)
                        if j >= 2:
                            pe.wait_ge(*exp_done.after(it, j - 1))
                        mask = mask1[:, bass.ds(b, 1), :].rearrange("p o n -> p (o n)") if n == 0 else mask1[:, 1, :]
                        for g in range(4):
                            nc.tensor.matmul(score(j)[:, g, :], aq[half, g, n * P:(n + 1) * P],
                                             ak[half, n * P:n * P + 2 * P], start=True, stop=False)
                            last = nc.tensor.matmul(score(j)[:, g, :], t["identb"][:], mask, start=False, stop=True)
                        last.then_inc(*s_ready.one)
                    if 2 <= j < 10:
                        s = j - 2
                        pe.wait_ge(*pn_ready.after(it, s + 1))
                        if s:
                            pe.wait_ge(*pt_evac_a.after(it, s))
                            pe.wait_ge(*pt_evac_d.after(it, s))
                        for kb in range(2):
                            for g in range(4):
                                last = nc.tensor.transpose(bankT[:, kb, g * P:(g + 1) * P],
                                                           probs[s % 2][:, g, kb * P:(kb + 1) * P], t["ident"][:])
                        last.then_inc(*pt_done.one)
                    if j >= 3:
                        s = j - 3
                        n, kv = s // 2, s % 2
                        half = slice(64 * kv, 64 * kv + 64)
                        pe.wait_ge(*pt_evac_a.after(it, s + 1))
                        pe.wait_ge(*pt_evac_d.after(it, s + 1))
                        if n >= 2:
                            pe.wait_ge(*ao_done.after(it, n - 1))
                        for kb in range(2):
                            last = nc.tensor.matmul(bank[n % 2][half, :], av[:, n + kb, half], probsT[s % 2][:, kb, :],
                                                    start=(kb == 0), stop=(kb == 1))
                        last.then_inc(*pv_done.one)
                pe.wait_ge(*ao_done.after(it, NT))
                for n in range(NT + 1):
                    if n < NT:
                        part = slice(n * P, (n + 1) * P)
                        if n:
                            pe.wait_ge(*r_kd.after(it, n))
                        for h in range(4):
                            half = slice(64 * (h % 2), 64 * (h % 2) + 64)
                            nc.tensor.matmul(bankS[h % 2][:, h // 2 * P:(h // 2 + 1) * P], rk[half, h // 2, part],
                                             rq[half, h // 2, part], start=True, stop=True)
                        for c in range(2):
                            last = nc.tensor.transpose(bankS[2 + n % 2][:, c * P:(c + 1) * P], rk[:, c, part], t["ident"][:])
                        last.then_inc(*r_scores.one)
                    if n:
                        m = n - 1
                        pe.wait_ge(*r_kd.after(it, m + 1))
                        pe.wait_ge(*r_qd.after(it, m + 1))
                        if m:
                            pe.wait_ge(*r_state.after(it, m))
                        if m >= 2:
                            pe.wait_ge(*r_evac.after(it, m - 1))
                        for c in range(2):
                            both = slice(c * P, (c + 1) * P)
                            nc.tensor.matmul(bankT[:, m % 2, both], kd[:, m % 2, both], rv[:, m, both],
                                             start=True, stop=True)
                        for c in range(2):
                            both = slice(c * P, (c + 1) * P)
                            nc.tensor.matmul(bank[m % 2][:, both], rstate[:, c, :], qd[:, m % 2, c, :],
                                             start=True, stop=False, skip_group_check=True)
                            for h in (2 * c, 2 * c + 1):
                                half = slice(64 * (h % 2), 64 * (h % 2) + 64)
                                last = nc.tensor.matmul(bank[m % 2][half, both], rv[:, m, 64 * h:64 * h + 64],
                                                        scm[:, m % 2, h, :], start=False, stop=(h % 2 == 1),
                                                        skip_group_check=True)
                        last.then_inc(*r_out.one)
                for lv in range(LEVELS + 1):
                    pe.wait_ge(*lq_ready.after(it, lv + 1))
                    if lv < LEVELS:
                        pe.wait_ge(*lev_ready.after(it, lv + 1))
                    if lv == 1:
                        for j in range(2):
                            sum_squares(it, j)
                    for n in range(NT):
                        part = slice(n * P, (n + 1) * P)
                        if lv:
                            pe.wait_ge(*g_picked.after(it, 4 * (lv - 1) + n + 1))
                        if lv < LEVELS:
                            last = nc.tensor.matmul(bankS[n][:, 0:256], lk[:, lv % 2, part], lq[lv % 2][:, n * 256:(n + 1) * 256],
                                                    start=True, stop=True)
                        else:
                            last = nc.tensor.matmul(bankS[n], gk[:, part], lq[n // 2][:, n % 2 * 512:(n % 2 + 1) * 512],
                                                    start=True, stop=True)
                        last.then_inc(*g_scores.one)
                pe.wait_ge(*kh_ready.after(it, 1))
                pe.wait_ge(*qe_ready.after(it, 1))
                pe.wait_ge(*r_evac.after(it, NT))
                pe.wait_ge(*r_state.after(it, NT))
                pe.wait_ge(*g_picked.after(it, 4 * (LEVELS + 1)))
                for n in range(NT + 1):
                    if n < NT:
                        if n >= 2:
                            pe.wait_ge(*kh_evac.after(it, n - 1))
                        nc.tensor.transpose(bankT[:, n % 2, 0:P], khat[:, n * P:(n + 1) * P], t["ident"][:])\
                          .then_inc(*kh_done.one)
                    if n:
                        m = n - 1
                        pe.wait_ge(*kh_evac.after(it, m + 1))
                        if m:
                            pe.wait_ge(*g_state.after(it, m))
                        if m >= 2:
                            pe.wait_ge(*g_evac.after(it, m - 1))
                        nc.tensor.matmul(bankS[m % 2][:, 0:256], khT[:, m % 2, :], gv[:, m, :], start=True, stop=True)
                        for c in range(2):
                            both = slice(c * P, (c + 1) * P)
                            nc.tensor.matmul(bank[m % 2][:, both], gstate[:, both], qe[:, m * P:(m + 1) * P],
                                             start=True, stop=False, skip_group_check=True)
                            for h in (2 * c, 2 * c + 1):
                                half = slice(64 * (h % 2), 64 * (h % 2) + 64)
                                last = nc.tensor.matmul(bank[m % 2][half, both], gv[:, m, 64 * h:64 * h + 64],
                                                        gsc[:, m, h, :], start=False, stop=(h % 2 == 1),
                                                        skip_group_check=True)
                        last.then_inc(*g_out.one)
                pe.wait_ge(*g_state.after(it, NT))
                pe.wait_ge(*g_evac.after(it, NT))
                for j in range(2, 4):
                    sum_squares(it, j)
                for channels in (range(6), range(6, KB)):
                    for c in range(2):
                        if channels[0] == 0:
                            pe.wait_ge(*lin_free.after(it, OUT1 + c + 1))
                            pe.wait_ge(*w_split.after(it, OUT1 + c + 1))
                        for k in channels:
                            if c == 0:
                                pe.wait_ge(*mix_ready.after(it, k + 1))
                            for n, (w, h) in enumerate(((whi, h_hi), (whi, h_lo), (wlo, h_hi))):
                                last = nc.tensor.matmul(bank[c], w[:, c, k * P:(k + 1) * P], h[:, k, :],
                                                        start=(k == n == 0), stop=(k == KB - 1 and n == 2))
                        if channels[0]:
                            last.then_inc(*lin_done.one)
                for k in range(2, KB):
                    chunk(it, OUT1 + k, k % 2)
                    if k == 4:
                        x_summed(it + 1)
                pe.wait_ge(*y_add.after(it, KB - 1))
                nc.tensor.matmul(bank[2][:], t["ones"][:], tmp[:, 0, :], start=True, stop=True).then_inc(*y_sum.one)


class Chain:

    def __init__(self, eng, sem):
        self.eng, self.sem, self.base, self.n = eng, sem, 0, 0
        self.reg, self.per, self.trips = 0, 0, 1

    def enter(self, reg, trips, per):
        self.base, self.n = self.base + self.n, 0
        self.reg, self.per, self.trips = reg, per, trips

    def leave(self):
        assert self.n == self.per, (self.n, self.per)
        self.base, self.n = self.base + self.per * self.trips, 0
        self.reg, self.per, self.trips = 0, 0, 1

    def link(self, ins):
        self.n += 1
        ins.then_inc(self.sem, 1)
        value = self.base + self.n
        self.eng.wait_ge(self.sem, value if isinstance(self.reg, int) else self.reg * self.per + value)


class Rows:

    def __init__(self, l, b):
        self.l, self.b, self.context = l, b, b == NB
        self.w = CTX if self.context else W
        self.tiles = self.w // P
        self.it = 3 * l + b
        self.latent_it = NB * l + b
        self.v = 1 if self.context else 0
        self.cols = slice(SEQ, TOKENS) if self.context else slice(b * W, b * W + W)


class Norm:

    def __init__(self, rows, no, gain=None, shift=None, after=None):
        self.rows, self.no, self.gain, self.shift = rows, no, gain, shift
        self.after = after


S1_AT, DFT_AT, WO_AT, FF_AT = [], [], [], []
_at = 0
for _l in range(DEPTH):
    _n = NB + 1 if _l == 0 else NB
    S1_AT.append(_at)
    _at += NB * IN2 + (IN2 if _l == 0 else 2)
    DFT_AT.append(_at)
    _at += DFT
    WO_AT.append(_at)
    _at += _n * KB
    FF_AT.append(_at)
    _at += _n * FF2
CHUNKS2 = _at
S1_STATS = [(), (0,), (1, 2), (3, 4), (5, 6), (7,)]


def second_block(nc, t, a, sems, out):
    sem = sems
    with ExitStack() as ctx:
        def sb(name, shape, dt=F32):
            return ctx.enter_context(nc.sbuf_tensor(name, shape, dt))

        x, wraw, whi, wlo, cols2 = t["x"], t["wraw"], t["whi"], t["wlo"], t["cols2"]
        xc = sb("xc", [P, KB, CTX])
        h_hi, h_lo = t["h_hi"], t["h_lo"]
        y, tmp, rstd = sb("y", [P, KB, W]), sb("tmp2", [P, 8, W]), sb("rstd2", [P, W])
        ALL_KEYS = CTX + SEQ + 2 * P
        k_own, k_swap = sb("k_own", [P, ALL_KEYS]), tmp[:, 2:5, :].rearrange("p a n -> p (a n)")
        vx, vc = sb("vx", [P, SEQ // P + 2, P]), sb("vc", [P, CTX // P, P])
        q_parts = sb("q_parts", [P, 4, 2, P], F32R)
        q_swap = sb("q_swap", [P, 4, P])
        stats = [sb(n, [P, TOKENS // P, 8]) for n in ("nmax2", "esum2", "sink_arg2", "esink2", "rden2")]
        nmax, esum, sink_arg, esink, rden = stats
        mx = sb("mx2", [P, 2])
        ms = sb("ms", [P, 16])
        rot, mask, dims = sb("rot", [P, P]), sb("mask_band", [P, 3, 3 * P], BF16), sb("dims", [P, 256])
        w_s, b_s = sb("w_s", [P, DEPTH, 4, P]), sb("b_s", [P, DEPTH, 2, P])
        g_s, g_m, neg_sink = sb("g_s", [P, DEPTH, 2]), sb("g_m", [P, DEPTH, KB]), sb("neg_sink", [P, DEPTH, 8])
        with ExitStack() as mixers:
            q, u, f = (mixers.enter_context(nc.sbuf_tensor(n, [P, c, TOKENS], F32))
                       for n, c in (("q", 4), ("u", 2), ("f", 2)))
        a_hi, a_lo = sb("a_hi", [P, FF_CH, W], F32R), sb("a_lo", [P, FF_CH, W], F32R)
        table, gvn = y[:, 0:2, :], y[:, 2:4, :].rearrange("p a (n c) -> p (a n) c", c=256)
        dft_ctx = y[:, 4:6, :].rearrange("p a (k n) -> p a k n", k=2)
        y_flat = y[:].rearrange("p a n -> p (a n)")
        KEYS = 3 * P + CTX
        probs = [y_flat[:, KEYS * n:KEYS * (n + 1)] for n in range(2)]
        probsT = [y_flat[:, KEYS * (2 + n):KEYS * (3 + n)] for n in range(2)]
        o_tile = y_flat[:, 4 * KEYS:4 * KEYS + 512]
        k_hi, k_lo = (v[:].rearrange("p k n -> p (k n)")[:, 0:2 * ALL_KEYS].rearrange("p (v n) -> p v n", v=2)
                      for v in (h_hi, h_lo))
        KEY_COLS = [slice(0, CTX + 3 * P), slice(CTX + 3 * P, ALL_KEYS)]
        mask_f = tmp[:, 0:3, 0:3 * P]

        lin0, lin1 = (ctx.enter_context(nc.psum_tensor(f"lin2_{n}", [P, 512], F32)) for n in range(2))
        scores = [ctx.enter_context(nc.psum_tensor(f"scores2_{n}", [P, 1024], F32)) for n in range(2)]
        bank = [lin0[:], lin1[:]] + [s[:, 512 * n:512 * n + 512] for s in scores for n in range(2)]
        bankT = ctx.enter_context(nc.psum_tensor("bankT2", [P, 1024], F32))

        def residual(p, k):
            return xc[:, k, :] if p.context else x[:, k, p.cols]

        def mixed(p, j):
            return (q[:, j, p.cols] if j < 4 else u[:, j - 4, p.cols] if j < 6 else f[:, j - 6, p.cols])

        def column(p, at):
            return cols2[:, p.l, p.v, at:at + 1]

        before = DEPTH * NB * CH1
        chunk_in = [Sig(t["raw_in"][s].sem, 8, before // 2 * 16 + 16 - 8 * s) for s in range(2)]
        w_hi, w_split = (Sig(t[n].sem, 1, before) for n in ("w_hi", "w_split"))
        lin_done, lin_free = (Sig(t[n].sem, 1, before) for n in ("lin_done", "lin_free"))
        EVACUATED = 3

        def sig(name, per, start=0):
            return Sig(sem("c_" + name), per, start)

        consts_in, consts_ready, table_in = sig("consts_in", 0), sig("consts_ready", 0), sig("table_in", 16)
        norms = {n: {s: sig(f"{n}_{s}", per) for s, per in
                     (("sq", KB), ("add", KB - sums), ("sum", sums), ("rstd", sums), ("scaled", KB), ("hi", KB), ("ready", KB))}
                 for n, sums in (("pre", 1), ("mix", 3), ("post", 1))}
        updated = sig("updated", KB)
        rope_mm, rope_done = sig("rope_mm", 5), sig("rope_done", 5)
        gv_ms, gv_rs, gv_ready = sig("gv_ms", 1), sig("gv_rs", 1), sig("gv_ready", 1)
        v_turned = sig("v_turned", 1)
        sgu_mm, sgu_done = sig("sgu_mm", 1), sig("sgu_done", 1)
        NDIM = [TOKENS // P, SEQ // P]
        dim_mm, dim_hi, dim_ready = sig("dim_mm", TOKENS // P), sig("dim_hi", TOKENS // P), sig("dim_ready", SEQ // P)
        ctx_dft, ctx_dft_done = sig("ctx_dft", 0), sig("ctx_dft_done", 0)
        s_ready, nm_ready, exp_done = sig("s_ready", 8), sig("nm_ready", 8), sig("exp_done", 8)
        pt_done, pt_evac_a, pt_evac_d, pv_done = (sig(n, 8) for n in ("pt_done", "pt_evac_a", "pt_evac_d", "pv_done"))
        q_split = sig("q_split", 12)
        q_swapped = sig("q_swapped", 32)
        k_swapped = sig("k_swapped", 32)
        k_hi_ready, k_lo_first, k_lo_rest = sig("k_hi_ready", 8), sig("k_lo_first", 4), sig("k_lo_rest", 4)
        sink_ready, esink_ready = sig("sink_ready", 1), sig("esink_ready", 1)
        o_done, ot_done, attn_done = sig("o_done", 1), sig("ot_done", 1), sig("attn_done", 1)
        a_sq = sig("a_sq", FF_CH)
        a_hi_ready, a_ready = sig("a_hi_ready", FF_CH), sig("a_ready", FF_CH, 2)
        saved = sig("saved", 0)
        wait_seat = sem("c_wait_seat")
        dve_chain, act_chain = Chain(nc.vector, sem("c_dve_chain")), Chain(nc.scalar, sem("c_act_chain"))
        block = ctx.enter_context(nc.Block())

        n_rows = [NB + 1 if l == 0 else NB for l in range(DEPTH)]

        def pre_mix(l, b):
            return Norm(Rows(l, b), 2 * 3 * l + b - 1, A1, B1, post_ff(l - 1, b) if l else None)

        def pre_ff(l, b):
            return Norm(Rows(l, b), 2 * 3 * l + 2 + b, A2, B2, post_mix(l, b))

        def mix(l, b):
            return Norm(Rows(l, b), 3 * l + b)

        def post_mix(l, b):
            return Norm(Rows(l, b), 2 * 3 * l + b, G1)

        def post_ff(l, b):
            return Norm(Rows(l, b), 2 * 3 * l + n_rows[l] + b, G2)

        def sources(n, kind, k):
            p = n.rows
            return mixed(p, k) if kind == "mix" else residual(p, k)

        S1_SUMS, FF_SUMS, MIX_SUMS, POST_SUMS = ([0], [1]), ([6], [7]), ([4, 5, 6], [7]), ([0], [1])
        MIX_OF = [0, 0, 0, 0, 1, 1, 2, 2]

        def part_of(kind, k):
            return (MIX_OF[k], k in (0, 4, 6)) if kind == "mix" else (0, k == 0)

        def adds_before(kind, k):
            return sum(not part_of(kind, j)[1] for j in range(k))

        def slot_of(kind, slots, k):
            return slots[adds_before(kind, k) % len(slots)]

        def attention_tiles(eng, l, body, chain=None, per=0):
            n = SEQ // P
            base = l * (TOKENS // P)
            body(0, base, 0, True, False)
            with eng.Fori(1, n - 1) as i:
                if chain:
                    chain.enter(i - 1, n - 2, per)
                body(i, i + base, 1, False, False)
            if chain:
                chain.leave()
            body(n - 1, base + n - 1, 2, False, True)
            if l == 0:
                body(n, base + n, None, True, False)
                body(n + 1, base + n + 1, None, False, True)

        def keys_of(mask_no):
            return (slice(P, 4 * P + CTX), 5) if mask_no is not None else (slice(4 * P, 4 * P + CTX), 2)

        def starts(no):
            return isinstance(no, int) and no == 0

        def lagging(tile, no, j, lag, first):
            if j >= lag:
                return tile, no, j - lag
            return None if first else (tile - 1, no - 1, j - lag + 8)

        def of_tile(v, tile):
            return v[:, tile, :] if isinstance(tile, int) else v[:, bass.ds(tile, 1), :].rearrange("p o h -> p (o h)")

        def of_head(v, tile, j):
            return v[:, tile, j:j + 1] if isinstance(tile, int) else v[:, bass.ds(tile, 1), j:j + 1].rearrange("p o h -> p (o h)")

        def is_first(tile):
            return isinstance(tile, int) and tile == 0

        def key_parts(part):
            for kv in range(2):
                for half in range(2):
                    rows = slice(64 * half, 64 * half + 64)
                    source = k_own if half == kv else k_swap
                    yield (*(v[rows, kv, KEY_COLS[part]] for v in (k_hi, k_lo)), source[rows, KEY_COLS[part]])

        def token_cols(tile):
            return slice(tile * P, (tile + 1) * P) if isinstance(tile, int) else bass.ds(tile * P, P)

        @block.sync
        def _(sp):
            def load(g, s, src):
                sp.wait_ge(*w_split.after(g, -1))
                sp.dma_start(wraw[:, s, 0:D], src).then_inc(chunk_in[s].sem, 16)

            def run(g, l, at, n, skip=0):
                with sp.Fori(skip // 2, n // 2) as i:
                    for s in range(2):
                        load(2 * i + (g + s), s, a["w2"][l, bass.ds(2 * i + (at + s), 1)].rearrange("o p n -> p (o n)"))

            for l in range(DEPTH):
                blocks = NB + 1 if l == 0 else NB
                for b in range(blocks):
                    run(S1_AT[l] + b * IN2, l, 0, IN2, 2 if l == b == 0 else 0)
                if l:
                    for s, c in enumerate((K2, V2)):
                        load(S1_AT[l] + NB * IN2 + s, s, a["w2"][l, c])
                def dft(first, last):
                    with sp.Fori(first, last) as i:
                        for s in range(2):
                            load(2 * i + (DFT_AT[l] + s), s, a["dft_tokens"][bass.ds(2 * i + s, 1)].rearrange("o p n -> p (o n)"))

                def swap_queries(tile, no):
                    if not starts(no):
                        sp.wait_ge(*q_split.after(no, 0))
                    for kv in range(2):
                        own, other = slice(64 * kv, 64 * kv + 64), slice(64 - 64 * kv, P - 64 * kv)
                        sp.dma_start(q_swap[other], q[own, :, token_cols(tile)]).then_inc(q_swapped.sem, 16)

                def tile_swaps(tile, no, mask_no, first, last):
                    if not is_first(tile):
                        swap_queries(tile, no)

                dft(0, 1)
                sp.wait_ge(*rope_done.after(NB * l + NB - 1, 5))
                sp.wait_ge(*lin_free.after(S1_AT[l] + NB * IN2 + (0 if l else K2), EVACUATED))
                sp.wait_ge(*sgu_done.after(3 * l + n_rows[l], 0))
                for kv in range(2):
                    own, other = slice(64 * kv, 64 * kv + 64), slice(64 - 64 * kv, P - 64 * kv)
                    sp.dma_start(k_swap[other, :], k_own[own, :]).then_inc(k_swapped.sem, 16)
                swap_queries(0, l * (TOKENS // P))
                dft(1, DFT // 2)
                for s in range(2):
                    load(WO_AT[l] + s, s, a["w2"][l, IN2 + s])
                attention_tiles(sp, l, tile_swaps)
                for b in range(blocks):
                    run(WO_AT[l] + b * KB, l, IN2, KB, 0 if b else 2)
                for b in range(blocks):
                    run(FF_AT[l] + b * FF2, l, IN2 + KB, FF2)
            for s in range(2):
                load(CHUNKS2 + s, s, a["w2"][0, s])
            ends = [post_ff(DEPTH - 1, b) for b in range(NB)]
            sp.wait_ge(*updated.after(ends[0].no, KB))
            sp.dma_start(out[:, :, ends[0].rows.cols], x[:, :, ends[0].rows.cols]).then_inc(saved.sem, 16)
            for k in range(KB):
                sp.wait_ge(*updated.after(ends[1].no, k + 1))
                sp.dma_start(out[:, k, ends[1].rows.cols], x[:, k, ends[1].rows.cols]).then_inc(saved.sem, 16)
            sp.wait_ge(saved.sem, 16 * (1 + KB))

        @block.gpsimd
        def _(pool):
            def split_low(g, s):
                pool.wait_ge(*w_hi.after(g, 1))
                nc.gpsimd.tensor_tensor(wlo[:, s, 0:D], wraw[:, s, 0:D], whi[:, s, 0:D].bitcast(F32), ALU.subtract)\
                  .then_inc(*w_split.one)

            def run(g, n):
                with pool.Fori(0, n // 2) as i:
                    for s in range(2):
                        split_low(2 * i + (g + 2 + s), s)

            for name, dst in (("ctx", xc[:]), ("rot2", rot[:]), ("mask2", mask_f), ("dft_dims", dims[:]),
                              ("dft_ctx", dft_ctx), ("w_sgu", w_s[:]), ("b_sgu", b_s[:]), ("g_sgu", g_s[:]),
                              ("g_mix", g_m[:]), ("sinks2", neg_sink[:])):
                pool.dma_start(dst, a[name]).then_inc(consts_in.sem, 16)
            for l in range(DEPTH):
                run(S1_AT[l], DFT_AT[l] - S1_AT[l])

                def queries(tile, no):
                    pool.wait_ge(*q_swapped.after(no, 32))
                    for n in range(2):
                        pair = slice(2 * n, 2 * n + 2)
                        if not starts(no):
                            pool.wait_ge(*s_ready.after(no - 1, 4 * n + 4))
                        step = 6 * n
                        for kv in range(2):
                            own, other = slice(64 * kv, 64 * kv + 64), slice(64 - 64 * kv, P - 64 * kv)
                            part = q_parts[other, pair, kv, :]
                            mine, swapped = q[own, pair, token_cols(tile)], q_swap[other, pair, :]
                            ones = [t["ones"][rows, :].rearrange("p (o n) -> p o n", o=1).to_broadcast([64, 2, P])
                                    for rows in (own, other)]
                            nc.gpsimd.tensor_tensor(q_parts[own, pair, kv, :], mine, ones[0], ALU.mult).then_inc(*q_split.one)
                            pool.wait_ge(*q_split.after(no, step + 3 * kv + 1))
                            nc.gpsimd.tensor_tensor(part, swapped, ones[1], ALU.mult).then_inc(*q_split.one)
                            pool.wait_ge(*q_split.after(no, step + 3 * kv + 2))
                            nc.gpsimd.tensor_tensor(part, swapped, part.bitcast(F32), ALU.subtract).then_inc(*q_split.one)
                            pool.wait_ge(*q_split.after(no, step + 3 * kv + 3))

                def tile_queries(tile, no, mask_no, first, last):
                    if not is_first(tile):
                        queries(tile, no)
                        return
                    pool.wait_ge(*w_split.after(WO_AT[l], 2))
                    for n, (hi, lo, source) in enumerate(key_parts(1)):
                        pool.wait_ge(*k_hi_ready.after(l, 4 + n + 1))
                        nc.gpsimd.tensor_tensor(lo, source, hi.bitcast(F32), ALU.subtract).then_inc(*k_lo_rest.one)
                        pool.wait_ge(*k_lo_rest.after(l, n + 1))

                pool.wait_ge(*lin_free.after(DFT_AT[l], 2))
                pool.wait_ge(*sgu_done.after(3 * l + n_rows[l], 0))
                pool.wait_ge(*w_split.after(DFT_AT[l], 2))
                queries(0, l * (TOKENS // P))
                run(DFT_AT[l], DFT)
                attention_tiles(pool, l, tile_queries)
                run(WO_AT[l], FF_AT[l] - WO_AT[l])
                run(FF_AT[l], (NB + 1 if l == 0 else NB) * FF2)

        @block.scalar
        def _(act):
            link = act_chain.link

            def split_high(g, s):
                act.wait_ge(*chunk_in[s].after(g, 0))
                nc.scalar.activation(whi[:, s, 0:D], wraw[:, s, 0:D], ACT.Copy).then_inc(*w_hi.one)

            def square(kind, n, k, buffers, src):
                sig, w = norms[kind], n.rows.w
                sums, slots = buffers
                part, first = part_of(kind, k)
                done = adds_before(kind, k)
                if first:
                    dst = tmp[:, sums[part], 0:w]
                else:
                    dst = tmp[:, slot_of(kind, slots, k), 0:w]
                    if done >= len(slots):
                        act.wait_ge(*sig["add"].after(n.no, done - len(slots) + 1))
                nc.scalar.activation(dst, src, ACT.Square).then_inc(*sig["sq"].one)

            def residual_square(n, k, buffers):
                if n.after:
                    act.wait_ge(*updated.after(n.after.no, k + 1))
                square("pre", n, k, buffers, residual(n.rows, k))

            def roots(kind, n, dsts, banks, widths):
                w = n.rows.w
                for i, (dst, ps, width) in enumerate(zip(dsts, banks, widths)):
                    act.wait_ge(*norms[kind]["sum"].after(n.no, i + 1))
                    link(nc.scalar.activation(dst[:, 0:w], ps[:, 0:w], ACT.Ln, scale=1.0 / width, bias=EPS))
                for dst in dsts:
                    nc.scalar.activation(dst[:, 0:w], dst[:, 0:w], ACT.Exp, scale=-0.5).then_inc(*norms[kind]["rstd"].one)

            def root_pre(n, buffers):
                roots("pre", n, [tmp[:, buffers[0][0], :]], [bankT[:, 0:512]], [D])

            def root_post(n):
                if n.no:
                    act.wait_ge(*updated.after(n.no - 1, KB))
                roots("post", n, [rstd[:]], [bankT[:, 512:1024]], [D])

            def high(kind, n, k):
                sig, w = norms[kind], n.rows.w
                act.wait_ge(*sig["scaled"].after(n.no, k + 1))
                if kind == "mix":
                    ins = nc.scalar.activation(h_hi[:, k, 0:w], tmp[:, 2 + k % 2, 0:w], ACT.Copy)
                else:
                    ins = nc.scalar.activation(h_hi[:, k, 0:w], tmp[:, 2 + k % 2, 0:w], ACT.Identity,
                                               bias=column(n.rows, n.shift + k))
                ins.then_inc(*sig["hi"].one)

            def evacuate(g, s, dst, src, func=ACT.Copy):
                act.wait_ge(*lin_done.after(g, 1))
                nc.scalar.activation(dst, src, func).then_inc(*lin_free.one)
                split_high(g + 2, s)

            def project(l, b, last):
                n, p, g = pre_mix(l, b), Rows(l, b), S1_AT[l] + b * IN2
                nxt = None if last else pre_mix(l, b + 1)
                if b:
                    for k in range(KB):
                        high("pre", n, k)
                if p.context and l:
                    for s, c in enumerate((K2, V2)):
                        context_kv(g + s, s, c, p)
                    return
                if not p.context:
                    if b:
                        act.wait_ge(*rope_done.after(p.latent_it, 0))
                    elif l:
                        act.wait_ge(*updated.after(post_ff(l - 1, NB).no, KB))
                    act.dma_start(table, a["rope2"][:, :, p.cols]).then_inc(table_in.sem, 16)
                if p.it:
                    act.wait_ge(*sgu_done.after(p.it, 0))
                act.wait_ge(*lin_done.after(g, 2))
                pairs = p.tiles // 2
                for s in range(pairs):
                    nc.scalar.activation(gvn[:, 2 * s:2 * s + 2, :].rearrange("p t n -> p (t n)"), bank[s], ACT.Gelu_apprx_tanh)\
                      .then_inc(lin_free.sem, 2 // pairs)
                for s in range(2):
                    split_high(g + 2 + s, s)
                for c in range(U2, U2 + 2):
                    evacuate(g + c, c % 2, u[:, c - U2, p.cols], bank[c % 2][:, 0:p.w], ACT.Gelu_apprx_tanh)
                for c in range(Q2, F2 + 2):
                    r = c - Q2
                    if r >= 5:
                        evacuate(g + c, c % 2, f[:, c - F2, p.cols], bank[c % 2][:, 0:p.w])
                    elif p.context:
                        if r < 4:
                            evacuate(g + c, c % 2, q[:, r, p.cols], bank[c % 2][:, 0:p.w])
                        else:
                            context_kv(g + c, c % 2, K2, p)
                    else:
                        if r >= 2:
                            act.wait_ge(*rope_done.after(p.latent_it, r - 1))
                        elif p.latent_it:
                            act.wait_ge(*rope_done.after(p.latent_it, 0))
                        evacuate(g + c, c % 2, tmp[:, 6 + r % 2, :], bank[c % 2][:])
                    if r == 1:
                        act.wait_ge(*gv_ms.after(p.it, 1))
                        part = ms[:, 0:4 * p.tiles]
                        link(nc.scalar.activation(part, part, ACT.Ln, scale=1.0 / 64, bias=EPS))
                        nc.scalar.activation(part, part, ACT.Exp, scale=-0.5).then_inc(*gv_rs.one)
                    if nxt and r < 6:
                        for k in S1_STATS[r]:
                            residual_square(nxt, k, S1_SUMS)
                if nxt:
                    root_pre(nxt, S1_SUMS)
                if p.context:
                    context_kv(g + V2, V2 % 2, V2, p)
                else:
                    if p.it == 0:
                        act.wait_ge(consts_ready.sem, 1)
                    values(g + V2, V2 % 2, p, vx[:, b * NT + 1:b * NT + 1 + NT, :])

            def values(g, s, p, dst):
                act.wait_ge(*rope_done.after(NB * p.l + min(p.b, NB - 1), 5))
                evacuate(g, s, tmp[:, 7, 0:p.w], bank[s][:, 0:p.w])
                act.wait_ge(*v_turned.after(p.it, 1))
                nc.scalar.activation(dst, bankT[:, 512:512 + p.w].rearrange("p (t n) -> p t n", n=P), ACT.Copy)

            def context_kv(g, s, c, p):
                if c == V2:
                    values(g, s, p, vc[:])
                    return
                evacuate(g, s, k_own[:, 0:CTX], bank[s][:, 0:CTX])

            def fourier(l):
                for n in range(NDIM[l]):
                    act.wait_ge(*dim_mm.after(l, n + 1))
                    if n < SEQ // P:
                        nc.scalar.activation(h_hi[:, n, :], bank[2 + n % 4], ACT.Copy).then_inc(*dim_hi.one)
                    else:
                        nc.scalar.activation(tmp[:, n - SEQ // P, :], bank[2 + n % 4], ACT.Copy).then_inc(*dim_hi.one)
                with act.Fori(0, DFT // 2) as i:
                    act.wait_ge(*lin_done.after(2 * i + DFT_AT[l], 2))
                    for s in range(2):
                        split_high(2 * i + (DFT_AT[l] + 2 + s), s)

            def attend(l):
                def sinks(tile, no):
                    act.wait_ge(*sink_ready.after(no, 1))
                    nc.scalar.activation(of_tile(esink, tile), of_tile(sink_arg, tile), ACT.Exp).then_inc(*esink_ready.one)

                def transposed(tile, no, j, n):
                    act.wait_ge(*pt_done.after(no, j + 1))
                    if j >= 2 or not starts(no):
                        act.wait_ge(*pv_done.after(no, j - 1))
                    rest = n // 2 * P
                    nc.scalar.activation(probsT[j % 2][:, n * P - rest:n * P], bankT[:, 512:512 + rest], ACT.Copy)\
                      .then_inc(*pt_evac_a.one)

                def outputs(tile, no):
                    act.wait_ge(*ot_done.after(no, 1))
                    nc.scalar.activation(q[:, :, token_cols(tile)], lin1[:].rearrange("p (c n) -> p c n", n=P), ACT.Copy)\
                      .then_inc(*attn_done.one)

                def body(tile, no, mask_no, first, last):
                    keys, n = keys_of(mask_no)
                    for j in range(8):
                        if j == 0 and not first:
                            sinks(tile - 1, no - 1)
                        step = lagging(tile, no, j, 2, first)
                        if step:
                            transposed(*step, n)
                        act.wait_ge(*nm_ready.after(no, j + 1))
                        if j >= 2 or not starts(no):
                            act.wait_ge(*pt_done.after(no, j - 1))
                        nc.scalar.activation(probs[j % 2][:, 0:n * P], scores[j % 2][:, keys], ACT.Exp, scale=ATT_SCALE,
                                             bias=of_head(nmax, tile, j), accum_out=of_head(esum, tile, j))\
                          .then_inc(*exp_done.one)
                        if j == 5 and not first:
                            outputs(tile - 1, no - 1)
                    if last:
                        sinks(tile, no)
                        for j in range(6, 8):
                            transposed(tile, no, j, n)
                        outputs(tile, no)

                act.wait_ge(*k_swapped.after(l, 32))
                for part in range(2):
                    for hi, lo, source in key_parts(part):
                        nc.scalar.activation(hi, source, ACT.Copy).then_inc(*k_hi_ready.one)
                attention_tiles(act, l, body)

            def mix_roots(n):
                roots("mix", n, [tmp[:, 4 + i, :] for i in range(3)], bank[2:5], (512, 256, 256))

            def merge(l, b, last):
                n, p, post, g = mix(l, b), Rows(l, b), post_mix(l, b), WO_AT[l] + b * KB
                prev = post_mix(l, b - 1) if b else None
                nxt = None if last else mix(l, b + 1)
                ff = pre_ff(l, 0) if last else None
                if b == 0:
                    act.wait_ge(*attn_done.after(l * (TOKENS // P), TOKENS // P if l == 0 else SEQ // P))
                    for k in range(KB):
                        square("mix", n, k, MIX_SUMS, mixed(p, k))
                    mix_roots(n)
                for k in range(KB):
                    high("mix", n, k)
                if prev:
                    root_post(prev)
                for k in range(KB):
                    s = k % 2
                    act.wait_ge(*lin_done.after(g + k, 1))
                    square("post", post, k, POST_SUMS, bank[s][:, 0:p.w])
                    if prev:
                        act.wait_ge(*updated.after(prev.no, k + 1))
                    nc.scalar.activation(y[:, k, 0:p.w], bank[s][:, 0:p.w], ACT.Copy).then_inc(*lin_free.one)
                    split_high(g + k + 2, s)
                    if nxt and k < 4:
                        for j in (2 * k, 2 * k + 1):
                            square("mix", nxt, j, MIX_SUMS, mixed(nxt.rows, j))
                    if nxt and k == 6:
                        mix_roots(nxt)
                    if ff and 3 <= k < 7:
                        for j in (2 * k - 6, 2 * k - 5):
                            residual_square(ff, j, FF_SUMS)
                if ff:
                    root_pre(ff, FF_SUMS)

            def hidden(gi, grp, j, s, w):
                act.wait_ge(*lin_done.after(gi, 1))
                act.wait_ge(*a_ready.after(grp, j - 1))
                nc.scalar.activation(tmp[:, 4 + s, 0:w], bank[s][:, 0:w], ACT.Relu).then_inc(*lin_free.one)
                split_high(gi + 2, s)
                act.wait_ge(*lin_free.after(gi, EVACUATED))
                unit = a_hi[:, j, 0:w] if isinstance(j, int) else a_hi[:, bass.ds(j, 1), 0:w].rearrange("p o n -> p (o n)")
                nc.scalar.activation(unit, tmp[:, 4 + s, 0:w], ACT.Square).then_inc(*a_hi_ready.one)

            def feed_forward(l, b, last):
                p, post, g0 = Rows(l, b), post_ff(l, b), FF_AT[l] + b * FF2
                prev = post_ff(l, b - 1) if b else post_mix(l, n_rows[l] - 1)
                nxt = pre_ff(l, b + 1) if not last else pre_mix(l + 1, 0) if l + 1 < DEPTH else None
                if b == 0:
                    for k in range(KB):
                        high("pre", pre_ff(l, b), k)

                def outputs(g):
                    with act.Fori(0, FF_CH // 2) as i:
                        for s in range(2):
                            act.wait_ge(*lin_done.after(g + (2 * i + (FF_CH + s)), 1))
                            split_high(g + (2 * i + (FF_CH + 2 + s)), s)

                act.wait_ge(*lin_free.after(g0, 2))
                for j in range(FF_CH):
                    hidden(g0 + j, p.it * FF_GROUPS, j, j % 2, p.w)
                    if j == 0:
                        root_post(prev)
                outputs(g0)
                with act.Fori(1, FF_GROUPS - 1) as q_no:
                    g = q_no * (2 * FF_CH) + g0
                    act.wait_ge(*lin_free.after(g, 2))
                    act.sem_inc(wait_seat, 1)
                    with act.Fori(0, FF_CH // 2) as i:
                        for s in range(2):
                            hidden(g + (2 * i + s), q_no + p.it * FF_GROUPS, 2 * i + s, s, p.w)
                    outputs(g)
                g, grp = g0 + (FF_GROUPS - 1) * 2 * FF_CH, (p.it + 1) * FF_GROUPS - 1
                act.wait_ge(*lin_free.after(g, 2))
                for j in range(FF_CH):
                    hidden(g + j, grp, j, j % 2, p.w)
                    if nxt:
                        residual_square(nxt, j, FF_SUMS)
                for k in range(KB):
                    gi = g + FF_CH + k
                    act.wait_ge(*lin_done.after(gi, 1))
                    split_high(gi + 2, k % 2)
                    act.wait_ge(*lin_free.after(gi, EVACUATED))
                    square("post", post, k, POST_SUMS, y[:, k, 0:p.w])
                    if nxt and k:
                        high("pre", nxt, k - 1)
                    elif nxt:
                        root_pre(nxt, FF_SUMS)
                if nxt:
                    high("pre", nxt, KB - 1)
                if last:
                    root_post(post)

            for l in range(DEPTH):
                for b in range(NB + 1):
                    project(l, b, b == NB)
                fourier(l)
                attend(l)
                for b in range(n_rows[l]):
                    merge(l, b, b == n_rows[l] - 1)
                for b in range(n_rows[l]):
                    feed_forward(l, b, b == n_rows[l] - 1)

        @block.vector
        def _(dve):
            link = dve_chain.link

            def add_square(kind, n, k, buffers):
                sig, w = norms[kind], n.rows.w
                sums, slots = buffers
                part, first = part_of(kind, k)
                if first:
                    return
                dve.wait_ge(*sig["sq"].after(n.no, k + 1))
                total = tmp[:, sums[part], 0:w]
                nc.vector.tensor_tensor(total, total, tmp[:, slot_of(kind, slots, k), 0:w], ALU.add).then_inc(*sig["add"].one)
                dve.wait_ge(*sig["add"].after(n.no, adds_before(kind, k) + 1))

            def scale(kind, n, k, buffers):
                sig, p = norms[kind], n.rows
                part = part_of(kind, k)[0]
                dve.wait_ge(*sig["rstd"].after(n.no, part + 1))
                gain = g_m[:, p.l, k:k + 1] if kind == "mix" else column(p, n.gain + k)
                nc.vector.scalar_tensor_tensor(tmp[:, 2 + k % 2, 0:p.w], sources(n, kind, k), gain,
                                               tmp[:, buffers[0][part], 0:p.w], ALU.mult, ALU.mult).then_inc(*sig["scaled"].one)

            def low(kind, n, k):
                sig, p = norms[kind], n.rows
                hi, scaled = h_hi[:, k, 0:p.w].bitcast(F32), tmp[:, 2 + k % 2, 0:p.w]
                dve.wait_ge(*sig["hi"].after(n.no, k + 1))
                if kind == "mix":
                    ins = nc.vector.tensor_tensor(h_lo[:, k, 0:p.w], scaled, hi, ALU.subtract)
                else:
                    ins = nc.vector.scalar_tensor_tensor(h_lo[:, k, 0:p.w], scaled, column(p, n.shift + k), hi,
                                                         ALU.add, ALU.subtract)
                ins.then_inc(*sig["ready"].one)
                dve.wait_ge(*sig["ready"].after(n.no, k + 1))

            def split(kind, n, buffers):
                for k in range(KB + 1):
                    if k < KB:
                        scale(kind, n, k, buffers)
                    if k:
                        low(kind, n, k - 1)

            def update(n, k):
                p = n.rows
                if k == 0:
                    dve.wait_ge(*norms["post"]["rstd"].after(n.no, 1))
                link(nc.vector.tensor_tensor(y[:, k, 0:p.w], y[:, k, 0:p.w], rstd[:, 0:p.w], ALU.mult))
                nc.vector.scalar_tensor_tensor(residual(p, k), y[:, k, 0:p.w], column(p, n.gain + k), residual(p, k),
                                               ALU.mult, ALU.add).then_inc(*updated.one)
                dve.wait_ge(*updated.after(n.no, k + 1))

            def project(l, b, last):
                n, p, g = pre_mix(l, b), Rows(l, b), S1_AT[l] + b * IN2
                nxt = None if last else pre_mix(l, b + 1)
                if b:
                    split("pre", n, S1_SUMS)
                if p.context and l:
                    return
                values = gvn[:, 0:p.tiles, :]
                n_heads = 4 * p.tiles
                by_head = values.rearrange("p t (h d) -> p (t h) d", d=64)
                squares = tmp[:, 0:2, :].rearrange("p a n -> p (a n)")[:, 0:n_heads * 64].rearrange("p (h d) -> p h d", d=64)
                dve.wait_ge(*lin_free.after(g + (GV2 + 1), EVACUATED))
                link(nc.vector.tensor_tensor(squares, by_head, by_head, ALU.mult))
                nc.vector.reduce_sum(ms[:, 0:n_heads], squares, AX_X).then_inc(*gv_ms.one)
                for r in range(6):
                    if r == (0 if p.context else 2):
                        dve.wait_ge(*gv_rs.after(p.it, 1))
                        nc.vector.tensor_tensor(by_head, by_head,
                                                ms[:, 0:n_heads].rearrange("p (h o) -> p h o", o=1).to_broadcast([P, n_heads, 64]),
                                                ALU.mult).then_inc(*gv_ready.one)
                    if r < 5 and not p.context:
                        rotate(p, g, r)
                    if nxt:
                        for k in S1_STATS[r]:
                            add_square("pre", nxt, k, S1_SUMS)
                dve.wait_ge(*sgu_mm.after(p.it, 1))
                sums = scores[0][:].rearrange("p (t c n) -> p c t n", c=2, n=P)
                dve.wait_ge(*lin_free.after(g + (U2 + 1), EVACUATED))
                for c in range(2):
                    gated = tmp[:, 4 + c, 0:p.w].rearrange("p (t n) -> p t n", n=P)
                    link(nc.vector.scalar_tensor_tensor(gated, sums[:, c, 0:p.tiles, :], g_s[:, p.l, c:c + 1],
                                                        b_s[:, p.l, c:c + 1, :].to_broadcast([P, p.tiles, P]),
                                                        ALU.mult, ALU.add))
                    ins = nc.vector.tensor_tensor(u[:, c, p.cols], u[:, c, p.cols], tmp[:, 4 + c, 0:p.w], ALU.mult)
                    if c == 0:
                        link(ins)
                ins.then_inc(*sgu_done.one)
                dve.wait_ge(*sgu_done.after(p.it, 1))

            def rotate(p, g, r):
                if r == 0:
                    dve.wait_ge(*table_in.after(p.latent_it, 16))
                dve.wait_ge(*lin_free.after(g + (Q2 + r), EVACUATED))
                nc.vector.tensor_tensor(tmp[:, 2 + r % 2, :], tmp[:, 6 + r % 2, :], table[:, 0, :], ALU.mult)
                dve.wait_ge(*rope_mm.after(p.latent_it, r + 1))
                link(nc.vector.tensor_tensor(tmp[:, 4 + r % 2, :], bank[4 + r % 2], table[:, 1, :], ALU.mult))
                if r < 4:
                    nc.vector.tensor_tensor(q[:, r, p.cols], tmp[:, 2 + r % 2, :], tmp[:, 4 + r % 2, :], ALU.add)\
                      .then_inc(*rope_done.one)
                else:
                    at = CTX + P + p.b * W
                    nc.vector.tensor_tensor(k_own[:, at:at + W], tmp[:, 2, :], tmp[:, 4, :], ALU.add).then_inc(*rope_done.one)
                    dve.wait_ge(*rope_done.after(p.latent_it, 5))

            def fourier(l):
                for n in range(SEQ // P):
                    dve.wait_ge(*dim_hi.after(l, n + 1))
                    nc.vector.tensor_tensor(h_lo[:, n, :], bank[2 + n % 4], h_hi[:, n, :].bitcast(F32), ALU.subtract)\
                      .then_inc(*dim_ready.one)
                with dve.Fori(0, DFT // 8) as i:
                    for s in range(2):
                        dve.wait_ge(*lin_done.after(8 * i + (DFT_AT[l] + 4 * s), 4))
                        nc.vector.tensor_copy(f[:, :, bass.ds(i * (4 * P) + 2 * s * P, 2 * P)],
                                              scores[s][:].rearrange("p (c n) -> p c n", c=2)[:, :, 0:2 * P])\
                          .then_inc(lin_free.sem, 4)
                if l == 0:
                    dve.wait_ge(ctx_dft.sem, 1)
                    nc.vector.tensor_copy(f[:, :, SEQ:], bankT[:].rearrange("p (c n) -> p c n", c=2)[:, :, 0:CTX])\
                      .then_inc(*ctx_dft_done.one)

            def attend(l):
                def maximum(tile, no, j, keys):
                    dve.wait_ge(*s_ready.after(no, j + 1))
                    link(nc.vector.reduce_max(mx[:, j % 2:j % 2 + 1], scores[j % 2][:, keys], AX_X))
                    nc.vector.scalar_tensor_tensor(of_head(nmax, tile, j), mx[:, j % 2:j % 2 + 1], -ATT_SCALE,
                                                   neg_sink[:, l, j:j + 1], ALU.mult, ALU.min).then_inc(*nm_ready.one)
                    if j == 7:
                        dve.wait_ge(*nm_ready.after(no, 8))
                        nc.vector.tensor_tensor(of_tile(sink_arg, tile), of_tile(nmax, tile), neg_sink[:, l, :],
                                                ALU.subtract).then_inc(*sink_ready.one)

                def transposed(tile, no, j, n):
                    dve.wait_ge(*pt_done.after(no, j + 1))
                    if j >= 2 or not starts(no):
                        dve.wait_ge(*pv_done.after(no, j - 1))
                    half = (n + 1) // 2 * P
                    nc.vector.tensor_copy(probsT[j % 2][:, 0:half], bankT[:, 0:half]).then_inc(*pt_evac_d.one)

                def denominators(tile, no):
                    dve.wait_ge(*esink_ready.after(no, 1))
                    link(nc.vector.tensor_tensor(of_tile(esum, tile), of_tile(esum, tile), of_tile(esink, tile), ALU.add))
                    link(nc.vector.reciprocal(of_tile(rden, tile), of_tile(esum, tile)))

                def outputs(tile, no):
                    dve.wait_ge(*pv_done.after(no, 8))
                    if not starts(no):
                        dve.wait_ge(*ot_done.after(no, 0))
                    share = of_tile(rden, tile).rearrange("p (r k) -> p k r", k=2)
                    for kv in range(2):
                        half = slice(256 * kv, 256 * kv + 256)
                        ins = nc.vector.tensor_tensor(o_tile[:, half].rearrange("p (h d) -> p h d", d=64),
                                                      lin0[:, half].rearrange("p (h d) -> p h d", d=64),
                                                      share[:, kv, :].rearrange("p (h o) -> p h o", o=1)
                                                      .to_broadcast([P, 4, 64]), ALU.mult)
                        if kv == 0:
                            link(ins)
                    ins.then_inc(*o_done.one)

                def body(tile, no, mask_no, first, last):
                    keys, n = keys_of(mask_no)
                    for j in range(8):
                        if j == 3 and not first:
                            outputs(tile - 1, no - 1)
                        maximum(tile, no, j, keys)
                        step = lagging(tile, no, j, 2, first)
                        if step:
                            transposed(*step, n)
                        if j == 1 and not first:
                            denominators(tile - 1, no - 1)
                    if last:
                        for j in range(6, 8):
                            transposed(tile, no, j, n)
                        denominators(tile, no)
                        outputs(tile, no)

                for n, (hi, lo, source) in enumerate(key_parts(0)):
                    dve.wait_ge(*k_hi_ready.after(l, n + 1))
                    nc.vector.tensor_tensor(lo, source, hi.bitcast(F32), ALU.subtract).then_inc(*k_lo_first.one)
                attention_tiles(dve, l, body, dve_chain, 8 + 3)

            def merge(l, b, last):
                n, p, post = mix(l, b), Rows(l, b), post_mix(l, b)
                prev = post_mix(l, b - 1) if b else None
                nxt = None if last else mix(l, b + 1)
                ff = pre_ff(l, 0) if last else None
                if b == 0:
                    for k in range(KB):
                        add_square("mix", n, k, MIX_SUMS)
                split("mix", n, MIX_SUMS)
                for k in range(KB):
                    if prev and k < 4:
                        update(prev, 2 * k)
                        update(prev, 2 * k + 1)
                    add_square("post", post, k, POST_SUMS)
                    if nxt and k < 4:
                        for j in (2 * k, 2 * k + 1):
                            add_square("mix", nxt, j, MIX_SUMS)
                    if ff and 3 <= k < 7:
                        for j in (2 * k - 6, 2 * k - 5):
                            add_square("pre", ff, j, FF_SUMS)

            def hidden(gi, grp, j, s, w):
                unit = slice(j, j + 1) if isinstance(j, int) else bass.ds(j, 1)
                dve.wait_ge(*lin_free.after(gi, EVACUATED))
                nc.vector.tensor_tensor(tmp[:, 2 + s, 0:w], tmp[:, 4 + s, 0:w], tmp[:, 4 + s, 0:w], ALU.mult).then_inc(*a_sq.one)
                dve.wait_ge(*a_sq.after(grp, j + 1))
                dve.wait_ge(*a_hi_ready.after(grp, j + 1))
                nc.vector.tensor_tensor(a_lo[:, unit, 0:w].rearrange("p o n -> p (o n)"), tmp[:, 2 + s, 0:w],
                                        a_hi[:, unit, 0:w].rearrange("p o n -> p (o n)").bitcast(F32),
                                        ALU.subtract).then_inc(*a_ready.one)
                dve.wait_ge(*a_ready.after(grp, j + 1))
                dve.sem_inc(wait_seat, 1)

            def feed_forward(l, b, last):
                p, post, g0 = Rows(l, b), post_ff(l, b), FF_AT[l] + b * FF2
                prev = post_ff(l, b - 1) if b else post_mix(l, n_rows[l] - 1)
                nxt = pre_ff(l, b + 1) if not last else pre_mix(l + 1, 0) if l + 1 < DEPTH else None
                if b == 0:
                    split("pre", pre_ff(l, b), FF_SUMS)

                def outputs(g, first):
                    with dve.Fori(0, FF_CH // 2) as i:
                        for s in range(2):
                            output(g + (2 * i + (FF_CH + s)), s, y[:, bass.ds(2 * i + s, 1), 0:p.w].rearrange("p o n -> p (o n)"), first)

                def output(gi, s, part, first):
                    dve.wait_ge(*lin_done.after(gi, 1))
                    if first:
                        nc.vector.tensor_copy(part, bank[s][:, 0:p.w]).then_inc(*lin_free.one)
                    else:
                        nc.vector.tensor_tensor(part, bank[s][:, 0:p.w], part, ALU.add).then_inc(*lin_free.one)

                for j in range(FF_CH):
                    hidden(g0 + j, p.it * FF_GROUPS, j, j % 2, p.w)
                    if j:
                        update(prev, j - 1)
                update(prev, KB - 1)
                dve.sem_inc(wait_seat, 1)
                outputs(g0, True)
                with dve.Fori(1, FF_GROUPS - 1) as q_no:
                    g = q_no * (2 * FF_CH) + g0
                    with dve.Fori(0, FF_CH // 2) as i:
                        for s in range(2):
                            hidden(g + (2 * i + s), q_no + p.it * FF_GROUPS, 2 * i + s, s, p.w)
                    outputs(g, False)
                g, grp = g0 + (FF_GROUPS - 1) * 2 * FF_CH, (p.it + 1) * FF_GROUPS - 1
                for j in range(FF_CH):
                    hidden(g + j, grp, j, j % 2, p.w)
                    if nxt:
                        add_square("pre", nxt, j, FF_SUMS)
                for k in range(KB):
                    output(g + FF_CH + k, k % 2, y[:, k, 0:p.w], False)
                    if nxt and k:
                        scale("pre", nxt, k - 1, FF_SUMS)
                    add_square("post", post, k, POST_SUMS)
                    if nxt and k:
                        low("pre", nxt, k - 1)
                if nxt:
                    scale("pre", nxt, KB - 1, FF_SUMS)
                    low("pre", nxt, KB - 1)
                if last:
                    for k in range(KB):
                        update(post, k)

            dve.wait_ge(consts_in.sem, 16 * 10)
            link(nc.vector.tensor_copy(mask[:], mask_f))
            link(nc.vector.tensor_scalar(neg_sink[:], neg_sink[:], -1.0, None, ALU.mult))
            for pad in (k_own[:], vx[:]):
                link(nc.vector.memset(pad, 0.0))
            dve.sem_inc(consts_ready.sem, 1)
            dve.sem_inc(a_ready.sem, 2)
            for l in range(DEPTH):
                for b in range(NB + 1):
                    project(l, b, b == NB)
                fourier(l)
                attend(l)
                for b in range(n_rows[l]):
                    merge(l, b, b == n_rows[l] - 1)
                for b in range(n_rows[l]):
                    feed_forward(l, b, b == n_rows[l] - 1)

        @block.tensor
        def _(pe):
            def sum_over_partitions(kind, n, part, ps, total):
                if kind == "mix":
                    adds = (3, 4, 5)[part]
                else:
                    adds = KB - 1
                pe.wait_ge(*norms[kind]["add"].after(n.no, adds))
                nc.tensor.matmul(ps[:, 0:n.rows.w], t["ones"][:], tmp[:, total, 0:n.rows.w], start=True, stop=True)\
                  .then_inc(*norms[kind]["sum"].one)

            def sum_pre(n, buffers):
                sum_over_partitions("pre", n, 0, bankT[:, 0:512], buffers[0][0])

            def sum_post(n):
                sum_over_partitions("post", n, 0, bankT[:, 512:1024], POST_SUMS[0][0])

            def sum_mix(n):
                for i in range(3):
                    sum_over_partitions("mix", n, i, bank[2 + i], MIX_SUMS[0][i])

            def product(g, s, p, parts, when=None):
                hi, lo = parts
                pe.wait_ge(*lin_free.after(g, 1))
                pe.wait_ge(*w_hi.after(g, 1))
                for k in range(KB):
                    if when:
                        pe.wait_ge(*when(k))
                    for h in (hi, lo):
                        nc.tensor.matmul(bank[s][:, 0:p.w], whi[:, s, k * P:(k + 1) * P], h[:, k, 0:p.w],
                                         start=(k == 0 and h is hi), stop=False)
                pe.wait_ge(*w_split.after(g, 1))
                for k in range(KB):
                    last = nc.tensor.matmul(bank[s][:, 0:p.w], wlo[:, s, k * P:(k + 1) * P], hi[:, k, 0:p.w],
                                            start=False, stop=(k == KB - 1))
                last.then_inc(*lin_done.one)

            def values(g, s, p):
                product(g, s, p, h_parts)
                pe.wait_ge(*lin_free.after(g, EVACUATED))
                for n in range(p.tiles):
                    tile = slice(n * P, (n + 1) * P)
                    last = nc.tensor.transpose(bankT[:, 512:1024][:, tile], tmp[:, 7, tile], t["ident"][:])
                last.then_inc(*v_turned.one)

            def token_pair(g, p, when):
                pe.wait_ge(*lin_free.after(g, 2))
                pe.wait_ge(*w_hi.after(g, 2))
                for tiles in ((0, 2), (1, 3)) if p.tiles == 4 else ((0,), (1,)):
                    for n, (h, w) in enumerate(((h_hi, whi), (h_lo, whi), (h_hi, wlo))):
                        if n == 2 and tiles[0] == 0:
                            pe.wait_ge(*w_split.after(g, 2))
                        for tile in tiles:
                            for k in range(KB):
                                if when and tile == n == 0:
                                    pe.wait_ge(*when(k))
                                at = tile % 2 * 256
                                last = nc.tensor.matmul(bank[tile // 2][:, at:at + 256].rearrange("p (c n) -> p c n", n=P),
                                                        h[:, k, tile * P:(tile + 1) * P], w[:, 0:2, k * P:(k + 1) * P],
                                                        start=(k == n == 0), stop=(k == KB - 1 and n == 2))
                last.then_inc(lin_done.sem, 2)

            h_parts, a_parts = (h_hi, h_lo), (a_hi, a_lo)

            def project(l, b, last):
                n, p, g = pre_mix(l, b), Rows(l, b), S1_AT[l] + b * IN2
                nxt = None if last else pre_mix(l, b + 1)

                def part_ready(k):
                    return norms["pre"]["ready"].after(n.no, k + 1)

                if n.no < 0:
                    part_ready = None
                if p.context and l:
                    product(g, 0, p, h_parts, part_ready)
                    values(g + 1, 1, p)
                    return
                token_pair(g + GV2, p, part_ready)
                for c in range(U2, U2 + 2):
                    product(g + c, c % 2, p, h_parts)

                def rotate(r):
                    pe.wait_ge(*lin_free.after(g + (Q2 + r), EVACUATED))
                    if r == p.it == 0:
                        pe.wait_ge(consts_ready.sem, 1)
                    if r >= 2:
                        pe.wait_ge(*rope_done.after(p.latent_it, r - 1))
                    nc.tensor.matmul(bank[4 + r % 2], rot[:], tmp[:, 6 + r % 2, :], start=True, stop=True)\
                      .then_inc(*rope_mm.one)

                for r in range(5):
                    product(g + (Q2 + r), (Q2 + r) % 2, p, h_parts)
                    if r and not p.context:
                        rotate(r - 1)
                product(g + F2, F2 % 2, p, h_parts)
                if not p.context:
                    rotate(4)
                pe.wait_ge(*gv_ready.after(p.it, 1))
                if p.it:
                    pe.wait_ge(*sgu_done.after(p.it, 0))
                for tile in range(p.tiles):
                    for h in range(4):
                        at = (2 * tile + h // 2) * P
                        sgu = nc.tensor.matmul(scores[0][64 * (h % 2):64 * (h % 2) + 64, at:at + P],
                                               gvn[:, tile, 64 * h:64 * h + 64], w_s[:, p.l, h, :], start=True, stop=True)
                sgu.then_inc(*sgu_mm.one)
                product(g + (F2 + 1), (F2 + 1) % 2, p, h_parts)
                if nxt:
                    sum_pre(nxt, S1_SUMS)
                values(g + V2, V2 % 2, p)

            def fourier(l):
                pe.wait_ge(*lin_free.after(DFT_AT[l], 2))
                pe.wait_ge(*sgu_done.after(3 * l + n_rows[l], 0))
                for n in range(NDIM[l]):
                    if n >= 4:
                        pe.wait_ge(*dim_ready.after(l, n - 3))
                    for c in range(2):
                        last = nc.tensor.matmul(bank[2 + n % 4][:, 256 * c:256 * c + 256], f[:, c, n * P:(n + 1) * P],
                                                dims[:], start=True, stop=True)
                    last.then_inc(*dim_mm.one)
                pe.wait_ge(*dim_ready.after(l, SEQ // P))
                pe.wait_ge(*dim_hi.after(l, NDIM[l]))
                if l == 0:
                    for c in range(2):
                        for part in range(2):
                            for k in range(CTX // P):
                                at = 256 * c + P * part
                                last = nc.tensor.matmul(bankT[:, 512 * c:512 * c + CTX], tmp[:, k, at:at + P],
                                                        dft_ctx[:, part, k, :], start=(part == k == 0),
                                                        stop=(part == k == 1))
                    last.then_inc(*ctx_dft.one)
                pe.sem_inc(wait_seat, 1)
                with pe.Fori(0, DFT // 8) as i:
                    for s in range(2):
                        g = 8 * i + (DFT_AT[l] + 4 * s)
                        pe.wait_ge(*lin_free.after(g, -2))
                        for part in range(2):
                            def passes(n, h, w):
                                for c in range(2):
                                    cols = slice(256 * c + P * part, 256 * c + P * part + P)
                                    for k in range(KB):
                                        last = nc.tensor.matmul(scores[s][:, 512 * c:512 * c + 2 * P]
                                                                .rearrange("p (t n) -> p t n", t=2),
                                                                h[:, k, cols], w[:, 0:2, k * P:(k + 1) * P],
                                                                start=(part == k == n == 0),
                                                                stop=(part == 1 and k == KB - 1 and n == 2))
                                return last

                            pe.wait_ge(*w_hi.after(g + 2 * part, 2))
                            passes(0, h_hi, whi)
                            passes(1, h_lo, whi)
                            pe.wait_ge(*w_split.after(g + 2 * part, 2))
                            passes(2, h_hi, wlo).then_inc(lin_done.sem, 2)

            def attend(l):
                pe.wait_ge(*lin_free.after(WO_AT[l], 2))
                if l == 0:
                    pe.wait_ge(ctx_dft_done.sem, 1)

                def score(tile, no, j, mask_no):
                    r, kv = j // 2, j % 2
                    if j % 4 == 0:
                        pe.wait_ge(*q_split.after(no, j // 4 * 6 + 6))
                    if is_first(tile) and j < 2:
                        pe.wait_ge(*k_lo_first.after(l, 2 * kv + 2))
                    if not isinstance(tile, int) and j == 0:
                        pe.wait_ge(*k_lo_rest.after(l, 4))
                    if j >= 2 or not starts(no):
                        pe.wait_ge(*exp_done.after(no, j - 1))
                    parts = (k_hi, k_lo)
                    if mask_no is not None:
                        local = scores[kv][:, P:4 * P]
                        at = tile * P + CTX
                        keys = slice(at, at + 3 * P) if isinstance(tile, int) else bass.ds(at, 3 * P)
                        for n, k in enumerate(parts):
                            nc.tensor.matmul(local, q_parts[:, r, kv, :], k[:, kv, keys], start=(n == 0), stop=False)
                        nc.tensor.matmul(local, t["identb"][:], mask[:, mask_no, :], start=False, stop=True)
                    for n, k in enumerate(parts):
                        last = nc.tensor.matmul(scores[kv][:, 4 * P:4 * P + CTX], q_parts[:, r, kv, :], k[:, kv, 0:CTX],
                                                start=(n == 0), stop=(n == 1))
                    last.then_inc(*s_ready.one)

                def transpose(tile, no, j, n):
                    pe.wait_ge(*exp_done.after(no, j + 1))
                    if j or not starts(no):
                        pe.wait_ge(*pt_evac_a.after(no, j))
                        pe.wait_ge(*pt_evac_d.after(no, j))
                    for k in range(n):
                        at = k * P if k < (n + 1) // 2 else 512 + (k - (n + 1) // 2) * P
                        last = nc.tensor.transpose(bankT[:, at:at + P], probs[j % 2][:, k * P:(k + 1) * P],
                                                   t["ident"][:])
                    last.then_inc(*pt_done.one)

                def values(tile, no, j, n):
                    r, kv = j // 2, j % 2
                    pe.wait_ge(*pt_evac_a.after(no, j + 1))
                    pe.wait_ge(*pt_evac_d.after(no, j + 1))
                    if j == 0 and not starts(no):
                        pe.wait_ge(*o_done.after(no, 0))
                    head = (r + 4 * kv) * 64
                    half = slice(64 * kv, 64 * kv + 64)
                    for k in range(n):
                        c = k - (n - CTX // P)
                        if c >= 0:
                            v = vc[:, c, half]
                        elif isinstance(tile, int):
                            v = vx[:, tile + k, half]
                        else:
                            v = vx[:, bass.ds(tile + k, 1), half].rearrange("p o n -> p (o n)")
                        last = nc.tensor.matmul(lin0[:, head:head + 64], probsT[j % 2][:, k * P:(k + 1) * P], v,
                                                start=(k == 0), stop=(k == n - 1))
                    last.then_inc(*pv_done.one)

                def outputs(tile, no):
                    pe.wait_ge(*o_done.after(no, 1))
                    if not starts(no):
                        pe.wait_ge(*attn_done.after(no, 0))
                    for c in range(4):
                        last = nc.tensor.transpose(lin1[:, c * P:(c + 1) * P], o_tile[:, c * P:(c + 1) * P], t["ident"][:])
                    last.then_inc(*ot_done.one)

                def body(tile, no, mask_no, first, last):
                    n = keys_of(mask_no)[1]
                    for j in range(8):
                        score(tile, no, j, mask_no)
                        for lag, work in ((2, transpose), (3, values)):
                            step = lagging(tile, no, j, lag, first)
                            if step:
                                work(*step, n)
                        if j == 4 and not first:
                            outputs(tile - 1, no - 1)
                    if last:
                        for j in range(5, 8):
                            if j > 5:
                                transpose(tile, no, j, n)
                            values(tile, no, j, n)
                        outputs(tile, no)

                attention_tiles(pe, l, body)

            def merge(l, b, last):
                n, p, post, g = mix(l, b), Rows(l, b), post_mix(l, b), WO_AT[l] + b * KB
                nxt = None if last else mix(l, b + 1)
                if b == 0:
                    sum_mix(n)
                else:
                    sum_post(post_mix(l, b - 1))
                for k in range(KB):
                    product(g + k, k % 2, p, h_parts, (lambda j: norms["mix"]["ready"].after(n.no, j + 1)) if k == 0 else None)
                    if nxt and k == 5:
                        sum_mix(nxt)
                    if last and k == 6:
                        sum_pre(pre_ff(l, 0), FF_SUMS)

            def feed_forward(l, b, last):
                n, p, g0 = pre_ff(l, b), Rows(l, b), FF_AT[l] + b * FF2
                prev = post_ff(l, b - 1) if b else post_mix(l, n_rows[l] - 1)
                nxt = pre_ff(l, b + 1) if not last else pre_mix(l + 1, 0) if l + 1 < DEPTH else None

                def run(g, parts, first):
                    with pe.Fori(first // 2, FF_CH // 2) as i:
                        for s in range(2):
                            product(g + (2 * i + s), s, p, parts)

                def hidden_ready(grp):
                    return lambda k: a_ready.after(grp, k + 1)

                product(g0, 0, p, h_parts, lambda k: norms["pre"]["ready"].after(n.no, k + 1))
                sum_post(prev)
                product(g0 + 1, 1, p, h_parts)
                run(g0, h_parts, 2)
                product(g0 + FF_CH, 0, p, a_parts, hidden_ready(p.it * FF_GROUPS))
                product(g0 + FF_CH + 1, 1, p, a_parts)
                run(g0 + FF_CH, a_parts, 2)
                with pe.Fori(1, FF_GROUPS - 1) as q_no:
                    g = q_no * (2 * FF_CH) + g0
                    run(g, h_parts, 0)
                    product(g + FF_CH, 0, p, a_parts, hidden_ready(q_no + p.it * FF_GROUPS))
                    product(g + (FF_CH + 1), 1, p, a_parts)
                    run(g + FF_CH, a_parts, 2)
                g = g0 + (FF_GROUPS - 1) * 2 * FF_CH
                run(g, h_parts, 0)
                product(g + FF_CH, 0, p, a_parts, hidden_ready((p.it + 1) * FF_GROUPS - 1))
                if nxt:
                    sum_pre(nxt, FF_SUMS)
                product(g + FF_CH + 1, 1, p, a_parts)
                run(g + FF_CH, a_parts, 2)
                if last:
                    sum_post(post_ff(l, b))

            for l in range(DEPTH):
                for b in range(NB + 1):
                    project(l, b, b == NB)
                fourier(l)
                attend(l)
                for b in range(n_rows[l]):
                    merge(l, b, b == n_rows[l] - 1)
                for b in range(n_rows[l]):
                    feed_forward(l, b, b == n_rows[l] - 1)


CONSTS1 = ["ones64", "rot1", "ret_mask", "ret_qdecay", "ret_kdecay", "ret_cdecay", "gla_heads", "gla_mask"]


def program(nc, a, out):
    with ExitStack() as ctx:
        def sem(name):
            return ctx.enter_context(nc.semaphore(name))

        def sb(name, shape, dt=F32):
            return ctx.enter_context(nc.sbuf_tensor(name, shape, dt))

        wide = D + KB * GATE_RANK
        t = {"x": sb("x", [P, KB, SEQ]), "wraw": sb("wraw", [P, 2, wide]), "whi": sb("whi", [P, 2, wide], F32R),
             "wlo": sb("wlo", [P, 2, wide], F32R), "ident": sb("ident", [P, P]), "ones": sb("ones", [P, P]),
             "identb": sb("identb", [P, P], BF16), "h_hi": sb("h_hi", [P, KB, W], F32R), "h_lo": sb("h_lo", [P, KB, W], F32R),
             "cols2": sb("cols2", [P, DEPTH, 2, 2 * 24])}
        t["x_in"], t["const_in"] = sem("x_in"), sem("const_in")
        t["raw_in"] = [Sig(sem(f"raw_in{s}"), 8 * CH1) for s in range(2)]
        t["w_hi"], t["w_split"] = Sig(sem("w_hi"), CH1), Sig(sem("w_split"), CH1)
        t["lin_done"], t["lin_free"] = Sig(sem("lin_done"), CH1), Sig(sem("lin_free"), CH1)
        with ExitStack() as first:
            def sb1(name, shape, dt=F32):
                return first.enter_context(nc.sbuf_tensor(name, shape, dt))

            t["cols1"], t["rope1"] = sb1("cols1", [P, DEPTH, NCOL1]), sb1("rope1", [P, 4, SEQ])
            t["mask1"] = sb1("mask1", [P, 2, 2 * P], BF16)
            t["gate_w"] = sb1("gate_w", [GATE_RANK, DEPTH, P])
            t["ab1"] = sb1("ab1", [P, DEPTH * NB + 1, 2 * KB])
            for name in CONSTS1:
                t[name] = sb1(name, list(a[name].shape), U8 if name == "gla_mask" else F32)
            load_and_modulate(nc, t, a, sem)
            first_block(nc, t, a, sem)
        second_block(nc, t, a, sem, out)


def chunked(w):
    k, n = w.shape
    return w.reshape(k // P, P, n // P, P).transpose(2, 1, 0, 3).reshape(n // P, P, k)


def columns(v):
    return np.moveaxis(v.reshape(*v.shape[:-1], -1, P), -1, 0)


def kernel(**inp):
    import concourse.bacc as bacc
    from concourse.bass_utils import run_bass_kernel_spmd as run

    inp = {k: np.asarray(v) for k, v in inp.items()}
    heads = np.concatenate([np.arange(64 * h, 64 * h + 64) for h in HEAD_PAIRS])
    order1 = np.concatenate([heads, np.arange(512, 640), np.arange(1280, 1792), np.arange(2304, 2560),
                             np.arange(640, 768), np.arange(1792, 2048), np.arange(2560, 2816),
                             768 + heads, np.arange(2048, 2304), np.arange(2816, 3072)])
    out_rows = np.concatenate([heads, np.arange(512, 1024)])
    a = {}
    a["x"] = inp["x"][0].T.reshape(KB, P, SEQ).transpose(1, 0, 2)
    a["c"] = np.stack([inp[n].reshape(KB, P).T for n in ("c", "c_2", "c_ctx_2")], 2)
    a["positions"] = np.broadcast_to(inp["positions"][0], (P, SEQ))
    a["w_mod"] = np.concatenate([chunked(w) for w in inp["w_mod"]])
    a["w_ada"] = np.concatenate([chunked(w) for w in inp["w_ada_2"]])
    a["b_mod"] = np.concatenate([columns(inp[n]).reshape(P, -1) for n in ("b_mod", "b_ada_2")], 1)
    a["gains2"] = np.stack([columns(inp[f"g_{n}_2"]) for n in ("pre_mix", "post_mix", "pre_ff", "post_ff")], 2)
    gn = np.tile(inp["gla_norm_gain"], (1, 2))
    a["gains1"] = np.concatenate([columns(inp["pre_norm_gain"]), columns(inp["post_norm_gain"]),
                                  inp["gla_gate_b"].T[:, :, None], gn.T[:, :, None]], 2)
    a["sinks1"] = np.broadcast_to(inp["attn_sinks"], (P, DEPTH, 8))
    a["gate_w"] = inp["gla_gate_w"].transpose(1, 0, 2)
    a["w1"] = np.stack([np.concatenate([chunked(inp["w_in"][l][:, order1]), chunked(inp["w_out"][l][out_rows])])
                        for l in range(DEPTH)])
    a["w1_gate"] = np.stack([inp["w_in"][l][:, 3072:].reshape(KB, P, GATE_RANK).transpose(1, 0, 2).reshape(P, -1)
                             for l in range(DEPTH)])
    order2 = np.concatenate([np.arange(1024, 1280), np.arange(768, 1024), heads, np.arange(512, 640),
                             np.arange(1280, 1536), np.arange(640, 768)])
    hidden = KB * P
    a["w2"] = np.stack([np.concatenate(
        [chunked(inp["w_in_2"][l][:, order2]), chunked(inp["w_out_2"][l])]
        + [chunked(w) for g in range(FF_GROUPS) for w in (inp["w_ff1_2"][l][:, g * hidden:(g + 1) * hidden],
                                                          inp["w_ff2_2"][l][g * hidden:(g + 1) * hidden])])
        for l in range(DEPTH)])
    a["w1_next"] = np.stack([a["w1"][0, :2], a["w1"][1, :2], a["w1"][1, :2], a["w2"][0, :2]])
    a["ctx"] = inp["ctx_2"][0].T.reshape(KB, P, CTX).transpose(1, 0, 2)
    a["sinks2"] = np.broadcast_to(inp["sink_2"][:, HEAD_PAIRS], (P, DEPTH, 8))
    a["w_sgu"] = inp["w_sgu_2"].transpose(3, 0, 1, 2)
    a["b_sgu"] = np.repeat(inp["b_sgu_2"].reshape(DEPTH, 2, 2, P).transpose(2, 0, 1, 3), 64, axis=0)
    a["g_sgu"] = columns(inp["g_sgu_2"].reshape(DEPTH, 256))
    a["g_mix"] = columns(inp["g_mix_2"])
    a.update(constants())

    nc = bacc.Bacc("TRN2", target_bir_lowering=False, num_devices=1)
    a = {k: np.ascontiguousarray(v) for k, v in a.items()}
    aps = {k: nc.dram_tensor(f"in_{k}", v.shape, mybir.dt.from_np(v.dtype), kind="ExternalInput").ap() for k, v in a.items()}
    out = nc.dram_tensor("out", (P, KB, SEQ), F32, kind="ExternalOutput").ap()
    program(nc, aps, out)
    r = run(nc, [{f"in_{k}": v for k, v in a.items()}], core_ids=[0])
    got = r.results[0]["out"]
    return got.transpose(2, 1, 0).reshape(1, SEQ, D)
```
